# Optimizing a Trainium2 kernel written in Bass

```python
import math
import jax, jax.numpy as jnp
from jax import lax
import numpy as np

D_MODEL = 1024
BATCH = 1
SEQ = 1024
DEPTH = 1

RWKV_HEAD = 64
D_RWKV = D_MODEL // 2
N_RWKV_HEADS = D_RWKV // RWKV_HEAD
DECAY_LORA = 64
AAA_LORA = 64
GATE_LORA = 160
LN_X_EPS = 64e-5
D_CONV = D_MODEL // 2
CONV_WIDTH = 3
N_MEM = 256
N_XHEADS = 4
XHEAD_DIM = D_MODEL // N_XHEADS
D_FF = 4 * D_MODEL
RMS_EPS = 1e-6

SPLITS = (D_RWKV, D_RWKV, D_RWKV, DECAY_LORA, AAA_LORA, GATE_LORA,
          D_CONV, D_CONV, D_CONV,
          D_MODEL, D_MODEL)
D_IN = sum(SPLITS)
RWKV_COLS = 3 * D_RWKV + DECAY_LORA + AAA_LORA + GATE_LORA


def rms_norm(x, g):
    xf = x.astype(jnp.float32)
    y = xf * lax.rsqrt(jnp.mean(xf * xf, axis=-1, keepdims=True) + RMS_EPS)
    return (y * g.astype(jnp.float32)).astype(x.dtype)

def token_shift(p):
    return jnp.pad(p[:, :-1], ((0, 0), (1, 0), (0, 0)))

def wkv7_scan(r, w, k, v, a, b):
    bsz, _, h, n = r.shape

    def step(state, inp):
        r_t, w_t, k_t, v_t, a_t, b_t = inp
        sa = jnp.einsum("bhvk,bhk->bhv", state, a_t)
        state = (state * w_t[:, :, None, :]
                 + sa[..., None] * b_t[:, :, None, :]
                 + v_t[..., None] * k_t[:, :, None, :])
        return state, jnp.einsum("bhvk,bhk->bhv", state, r_t)

    xs = tuple(jnp.moveaxis(t, 1, 0) for t in (r, w, k, v, a, b))
    s0 = jnp.zeros((bsz, h, n, n), jnp.float32)
    _, ys = lax.scan(step, s0, xs)
    return jnp.moveaxis(ys, 0, 1)

def rwkv7_branch(r, k, v, wd, ad, gd, w0, w_lora_w, a0, w_lora_a, w_lora_g,
                 k_k, k_a, r_k, ln_x_w, ln_x_b):
    bsz, s, _ = r.shape
    f32 = jnp.float32
    log_w = -jax.nn.softplus(-(w0 + jnp.tanh(wd) @ w_lora_w)) - 0.5
    decay = jnp.exp(-jnp.exp(log_w.astype(f32)))
    a = jax.nn.sigmoid(a0 + ad @ w_lora_a)
    g = jax.nn.sigmoid(gd) @ w_lora_g

    def heads(t):
        return t.reshape(bsz, s, N_RWKV_HEADS, RWKV_HEAD).astype(f32)

    kk = heads(k * k_k)
    kk = kk / jnp.maximum(jnp.sqrt(jnp.sum(kk * kk, axis=-1, keepdims=True)), 1e-12)
    k = k * (1.0 + (a - 1.0) * k_a)
    rh, kh, vh, ah, wh = heads(r), heads(k), heads(v), heads(a), heads(decay)
    y = wkv7_scan(rh, wh, kh, vh, -kk, kk * ah)
    mu = jnp.mean(y, axis=-1, keepdims=True)
    var = jnp.mean(jnp.square(y - mu), axis=-1, keepdims=True)
    y = (y - mu) * lax.rsqrt(var + LN_X_EPS)
    y = y.reshape(bsz, s, D_RWKV) * ln_x_w.astype(f32) + ln_x_b.astype(f32)
    bonus = jnp.sum(rh * kh * r_k.astype(f32), axis=-1, keepdims=True) * vh
    y = y + bonus.reshape(bsz, s, D_RWKV)
    return y.astype(r.dtype) * g

def short_conv_branch(bg, cg, xc, conv_w):
    u = cg * xc
    y = lax.conv_general_dilated(
        u, conv_w.astype(u.dtype), window_strides=(1,),
        padding=[(CONV_WIDTH - 1, 0)],
        dimension_numbers=("NWC", "WIO", "NWC"),
        feature_group_count=D_CONV)
    return bg * y

def memory_cross_attention(h, mem_n, w_q, w_kv, w_xo):
    bsz, s, _ = h.shape
    n_mem = mem_n.shape[1]
    q = (h @ w_q).reshape(bsz, s, N_XHEADS, XHEAD_DIM)
    k, v = jnp.split(mem_n @ w_kv, 2, axis=-1)
    k = k.reshape(bsz, n_mem, N_XHEADS, XHEAD_DIM)
    v = v.reshape(bsz, n_mem, N_XHEADS, XHEAD_DIM)
    scores = jnp.einsum("bshd,bmhd->bhsm", q, k).astype(jnp.float32) / math.sqrt(XHEAD_DIM)
    probs = jax.nn.softmax(scores, axis=-1).astype(v.dtype)
    o = jnp.einsum("bhsm,bmhd->bshd", probs, v).reshape(bsz, s, D_MODEL)
    return o @ w_xo

def first_inputs(seed: int = 0) -> dict:
    key = jax.random.key(seed)
    ks = jax.random.split(key, 32)
    it = iter(range(32))
    f32 = jnp.float32
    L = DEPTH

    def nrm(shape, scale):
        return scale * jax.random.normal(ks[next(it)], shape, f32)

    def gain(shape):
        return 1.0 + 0.05 * jax.random.normal(ks[next(it)], shape, f32)

    return {
        "x": nrm((BATCH, SEQ, D_MODEL), 1.0),
        "mem": nrm((BATCH, N_MEM, D_MODEL), 1.0),
        "norm_mix": gain((L, D_MODEL)),
        "w_in": nrm((L, D_MODEL, D_IN), D_MODEL ** -0.5),
        "b_gate": nrm((L, 2 * D_MODEL), 0.01),
        "mu_shift": jax.random.uniform(ks[next(it)], (L, RWKV_COLS), f32),
        "w0": jax.random.uniform(ks[next(it)], (L, D_RWKV), f32, -6.0, -1.0),
        "w_lora_w": nrm((L, DECAY_LORA, D_RWKV), 0.1 * DECAY_LORA ** -0.5),
        "a0": nrm((L, D_RWKV), 0.1),
        "w_lora_a": nrm((L, AAA_LORA, D_RWKV), AAA_LORA ** -0.5),
        "w_lora_g": nrm((L, GATE_LORA, D_RWKV), GATE_LORA ** -0.5),
        "k_k": 0.85 + nrm((L, D_RWKV), 0.05),
        "k_a": gain((L, D_RWKV)),
        "r_k": nrm((L, N_RWKV_HEADS, RWKV_HEAD), 0.1),
        "ln_x_w": gain((L, D_RWKV)),
        "ln_x_b": nrm((L, D_RWKV), 0.01),
        "conv_w": nrm((L, CONV_WIDTH, 1, D_CONV), CONV_WIDTH ** -0.5),
        "w_proj_a": nrm((L, D_RWKV, D_MODEL), D_RWKV ** -0.5),
        "w_proj_b": nrm((L, D_CONV, D_MODEL), D_CONV ** -0.5),
        "w_out_mix": nrm((L, D_MODEL, D_MODEL), D_MODEL ** -0.5),
        "norm_xattn": gain((L, D_MODEL)),
        "norm_mem": gain((L, D_MODEL)),
        "w_q": nrm((L, D_MODEL, D_MODEL), D_MODEL ** -0.5),
        "w_kv": nrm((L, D_MODEL, 2 * D_MODEL), D_MODEL ** -0.5),
        "w_xo": nrm((L, D_MODEL, D_MODEL), D_MODEL ** -0.5),
        "norm_mlp": gain((L, D_MODEL)),
        "w_up": nrm((L, D_MODEL, D_FF), D_MODEL ** -0.5),
        "w_down": nrm((L, D_FF, D_MODEL), D_FF ** -0.5),
        "norm_final": gain((D_MODEL,)),
    }

def first_block(x, mem, norm_mix, w_in, b_gate, mu_shift, w0, w_lora_w, a0, w_lora_a,
              w_lora_g, k_k, k_a, r_k, ln_x_w, ln_x_b, conv_w, w_proj_a, w_proj_b,
              w_out_mix, norm_xattn, norm_mem, w_q, w_kv, w_xo, norm_mlp, w_up,
              w_down, norm_final):
    offsets = np.cumsum(SPLITS)[:-1].tolist()
    for i in range(DEPTH):
        h = rms_norm(x, norm_mix[i])
        p = h @ w_in[i]
        p_rw = p[..., :RWKV_COLS]
        p_rw = p_rw + (token_shift(p_rw) - p_rw) * mu_shift[i]
        p = jnp.concatenate([p_rw, p[..., RWKV_COLS:]], axis=-1)
        r, k, v, wd, ad, gd, cb, cc, cx, ga, gb = jnp.split(p, offsets, axis=-1)
        out_a = rwkv7_branch(r, k, v, wd, ad, gd, w0[i], w_lora_w[i], a0[i], w_lora_a[i],
                             w_lora_g[i], k_k[i], k_a[i], r_k[i], ln_x_w[i], ln_x_b[i])
        out_b = short_conv_branch(cb, cc, cx, conv_w[i])
        bg_a, bg_b = jnp.split(b_gate[i], 2)
        merged = (jax.nn.sigmoid(ga + bg_a) * (out_a @ w_proj_a[i])
                  + jax.nn.sigmoid(gb + bg_b) * (out_b @ w_proj_b[i]))
        x = x + merged @ w_out_mix[i]
        mem_n = rms_norm(mem, norm_mem[i])
        x = x + memory_cross_attention(rms_norm(x, norm_xattn[i]), mem_n,
                                       w_q[i], w_kv[i], w_xo[i])
        hm = rms_norm(x, norm_mlp[i])
        x = x + jnp.square(jax.nn.relu(hm @ w_up[i])) @ w_down[i]
    return rms_norm(x, norm_final)


CHUNK = 64
SB_BLOCK = 128
EPS = 1e-6
DN_HEADS = 4
DN_DK = 128
DN_DV = 128
DN_CONV = 4
SB_HEADS = 8
SB_DH = 64
DN_WIDTH = DN_HEADS * DN_DV
SB_WIDTH = SB_HEADS * SB_DH
N_BRANCH = 2
A_QKV1 = 2 * DN_HEADS * DN_DK + DN_WIDTH
A_Z1 = A_QKV1 + DN_WIDTH
A_B1 = A_Z1 + DN_HEADS
A_A1 = A_B1 + DN_HEADS
B_QKV1 = A_A1 + 3 * SB_WIDTH
B_Z1 = B_QKV1 + SB_WIDTH
G1 = B_Z1 + N_BRANCH * D_MODEL
PROJ_WIDTH = G1


def _rms(x, gain):
    xf = x.astype(jnp.float32)
    return xf * lax.rsqrt(jnp.mean(xf * xf, axis=-1, keepdims=True) + EPS) * gain.astype(jnp.float32)

def _l2n(x):
    return x * lax.rsqrt(jnp.sum(x * x, axis=-1, keepdims=True) + EPS)

def _causal_dwconv(u, w):
    k_len, c = w.shape
    return lax.conv_general_dilated(u, w[:, None, :].astype(u.dtype), window_strides=(1,),
                                    padding=[(k_len - 1, 0)],
                                    dimension_numbers=('NWC', 'WIO', 'NWC'),
                                    feature_group_count=c)

def _gated_delta_rule(q, k, v, g, beta):
    b, s, h, dk = q.shape
    dv = v.shape[-1]
    n = s // CHUNK

    def blocks(t):
        return jnp.moveaxis(t.reshape(b, n, CHUNK, h, -1), 3, 1)

    q = blocks(q) * dk ** -0.5
    k = blocks(k)
    v = blocks(v)
    g = jnp.moveaxis(g.reshape(b, n, CHUNK, h), 3, 1)
    beta = jnp.moveaxis(beta.reshape(b, n, CHUNK, h), 3, 1)
    gc = jnp.cumsum(g, axis=-1)
    causal = jnp.tril(jnp.ones((CHUNK, CHUNK), dtype=bool))
    strict = jnp.tril(jnp.ones((CHUNK, CHUNK), dtype=bool), -1)
    decay = jnp.exp(jnp.where(causal, gc[..., :, None] - gc[..., None, :], -jnp.inf))
    kk = jnp.einsum('bhnid,bhnjd->bhnij', k, k)
    m = jnp.where(strict, beta[..., :, None] * kk * decay, 0.0)
    eye = jnp.eye(CHUNK, dtype=m.dtype)
    rhs = jnp.concatenate([beta[..., None] * v,
                           beta[..., None] * k * jnp.exp(gc)[..., None]], axis=-1)
    sol = lax.linalg.triangular_solve(eye + m, rhs, left_side=True, lower=True, unit_diagonal=True)
    u, w = sol[..., :dv], sol[..., dv:]
    qk = jnp.where(causal, jnp.einsum('bhnid,bhnjd->bhnij', q, k) * decay, 0.0)
    q_dec = q * jnp.exp(gc)[..., None]
    k_dec = k * jnp.exp(gc[..., -1:] - gc)[..., None]
    g_end = jnp.exp(gc[..., -1])

    def step(state, inp):
        qk_c, qd_c, kd_c, u_c, w_c, ge_c = inp
        v_new = u_c - jnp.einsum('bhck,bhkv->bhcv', w_c, state)
        o = (jnp.einsum('bhck,bhkv->bhcv', qd_c, state)
             + jnp.einsum('bhij,bhjv->bhiv', qk_c, v_new))
        state = state * ge_c[..., None, None] + jnp.einsum('bhck,bhcv->bhkv', kd_c, v_new)
        return state, o

    xs = tuple(jnp.moveaxis(t, 2, 0) for t in (qk, q_dec, k_dec, u, w, g_end))
    state0 = jnp.zeros((b, h, dk, dv), q.dtype)
    _, o = lax.scan(step, state0, xs)
    return jnp.transpose(o, (1, 0, 3, 2, 4)).reshape(b, s, h, dv)

def _stick_breaking(q, k, v):
    _, _, s, d = q.shape
    scale = d ** -0.5
    outs = []
    for blk in range(s // SB_BLOCK):
        q0 = blk * SB_BLOCK
        end = q0 + SB_BLOCK
        z = jnp.einsum('bhqd,bhkd->bhqk', q[:, :, q0:end], k[:, :, :end]) * scale
        qi = q0 + jnp.arange(SB_BLOCK)[:, None]
        kj = jnp.arange(end)[None, :]
        mask = kj < qi
        log_keep = jnp.where(mask, jax.nn.log_sigmoid(-z), 0.0)
        rest = lax.cumsum(log_keep, axis=3, reverse=True) - log_keep
        a = jnp.where(mask, jnp.exp(jax.nn.log_sigmoid(z) + rest), 0.0)
        outs.append(jnp.einsum('bhqk,bhkd->bhqd', a, v[:, :, :end]))
    return jnp.concatenate(outs, axis=2)

def _layer(x, norm_gain, w_in, b_gate, conv_w, a_log, dt_bias, dn_out_gain,
           sb_q_gain, sb_k_gain, w_up_a, w_up_b, w_out):
    f32 = jnp.float32
    b, s, _ = x.shape
    xn = _rms(x, norm_gain).astype(x.dtype)
    proj = jnp.einsum('bsd,dp->bsp', xn, w_in)

    nqk = DN_HEADS * DN_DK
    qkv_a = jax.nn.silu(_causal_dwconv(proj[..., :A_QKV1], conv_w)).astype(f32)
    q_a = _l2n(qkv_a[..., :nqk].reshape(b, s, DN_HEADS, DN_DK))
    k_a = _l2n(qkv_a[..., nqk:2 * nqk].reshape(b, s, DN_HEADS, DN_DK))
    v_a = qkv_a[..., 2 * nqk:].reshape(b, s, DN_HEADS, DN_DV)
    z_a = proj[..., A_QKV1:A_Z1].astype(f32)
    beta = jax.nn.sigmoid(proj[..., A_Z1:A_B1].astype(f32))
    g = -jnp.exp(a_log.astype(f32)) * jax.nn.softplus(proj[..., A_B1:A_A1].astype(f32)
                                                       + dt_bias.astype(f32))
    o_a = _gated_delta_rule(q_a, k_a, v_a, g, beta)
    o_a = _rms(o_a, dn_out_gain).reshape(b, s, DN_WIDTH) * jax.nn.silu(z_a)
    y_a = jnp.einsum('bsc,cd->bsd', o_a.astype(x.dtype), w_up_a)

    qkv_b = proj[..., A_A1:B_QKV1].astype(f32).reshape(b, s, 3, SB_HEADS, SB_DH)
    q_b = jnp.swapaxes(_rms(qkv_b[:, :, 0], sb_q_gain), 1, 2)
    k_b = jnp.swapaxes(_rms(qkv_b[:, :, 1], sb_k_gain), 1, 2)
    v_b = jnp.swapaxes(qkv_b[:, :, 2], 1, 2)
    z_b = proj[..., B_QKV1:B_Z1].astype(f32)
    o_b = jnp.swapaxes(_stick_breaking(q_b, k_b, v_b), 1, 2).reshape(b, s, SB_WIDTH)
    o_b = o_b * jax.nn.silu(z_b)
    y_b = jnp.einsum('bsc,cd->bsd', o_b.astype(x.dtype), w_up_b)

    gates = jax.nn.sigmoid(proj[..., B_Z1:G1].astype(f32) + b_gate.astype(f32))
    merged = gates[..., :D_MODEL] * y_a.astype(f32) + gates[..., D_MODEL:] * y_b.astype(f32)
    return x + jnp.einsum('bsd,de->bse', merged.astype(x.dtype), w_out)

def second_inputs(seed: int = 0) -> dict:
    key = jax.random.key(seed)
    ks = jax.random.split(key, 14)
    f32 = jnp.float32
    nl = DEPTH
    nrm = jax.random.normal
    x = nrm(ks[0], (BATCH, SEQ, D_MODEL), f32)
    norm_gain = 1.0 + 0.02 * nrm(ks[1], (nl, D_MODEL), f32)
    w_in = nrm(ks[2], (nl, D_MODEL, PROJ_WIDTH), f32) * D_MODEL ** -0.5
    b_gate = 0.02 * nrm(ks[3], (nl, N_BRANCH * D_MODEL), f32)
    conv_w = nrm(ks[4], (nl, DN_CONV, A_QKV1), f32) * DN_CONV ** -0.5
    a_log = jnp.log(jax.random.uniform(ks[5], (nl, DN_HEADS), f32, minval=1.0, maxval=16.0))
    dt = jnp.exp(jax.random.uniform(ks[6], (nl, DN_HEADS), f32,
                                    minval=math.log(1e-3), maxval=math.log(1e-1)))
    dt_bias = dt + jnp.log(-jnp.expm1(-dt))
    dn_out_gain = 1.0 + 0.02 * nrm(ks[7], (nl, DN_DV), f32)
    sb_q_gain = 1.0 + 0.02 * nrm(ks[8], (nl, SB_DH), f32)
    sb_k_gain = 1.0 + 0.02 * nrm(ks[9], (nl, SB_DH), f32)
    w_up_a = nrm(ks[10], (nl, DN_WIDTH, D_MODEL), f32) * DN_WIDTH ** -0.5
    w_up_b = nrm(ks[11], (nl, SB_WIDTH, D_MODEL), f32) * SB_WIDTH ** -0.5
    w_out = nrm(ks[12], (nl, D_MODEL, D_MODEL), f32) * D_MODEL ** -0.5
    return {'x': x, 'norm_gain': norm_gain, 'w_in': w_in, 'b_gate': b_gate, 'conv_w': conv_w,
            'a_log': a_log, 'dt_bias': dt_bias, 'dn_out_gain': dn_out_gain,
            'sb_q_gain': sb_q_gain, 'sb_k_gain': sb_k_gain, 'w_up_a': w_up_a,
            'w_up_b': w_up_b, 'w_out': w_out}

def second_block(x, norm_gain, w_in, b_gate, conv_w, a_log, dt_bias, dn_out_gain,
              sb_q_gain, sb_k_gain, w_up_a, w_up_b, w_out):
    h = x
    for layer in range(DEPTH):
        h = _layer(h, norm_gain[layer], w_in[layer], b_gate[layer], conv_w[layer],
                   a_log[layer], dt_bias[layer], dn_out_gain[layer], sb_q_gain[layer],
                   sb_k_gain[layer], w_up_a[layer], w_up_b[layer], w_out[layer])
    return h


def setup_inputs(seed=0):
    out = dict(first_inputs(seed))
    for name, value in second_inputs(seed + 1).items():
        if name != "x":
            out[name + "_2"] = value
    return out


def reference(
    x, mem, norm_mix, w_in, b_gate, mu_shift, w0, w_lora_w, a0, w_lora_a, w_lora_g, k_k, k_a,
    r_k, ln_x_w, ln_x_b, conv_w, w_proj_a, w_proj_b, w_out_mix, norm_xattn, norm_mem, w_q, w_kv,
    w_xo, norm_mlp, w_up, w_down, norm_final, norm_gain_2, w_in_2, b_gate_2, conv_w_2, a_log_2,
    dt_bias_2, dn_out_gain_2, sb_q_gain_2, sb_k_gain_2, w_up_a_2, w_up_b_2, w_out_2,
):
    x = first_block(
        x, mem, norm_mix, w_in, b_gate, mu_shift, w0, w_lora_w, a0, w_lora_a, w_lora_g, k_k,
        k_a, r_k, ln_x_w, ln_x_b, conv_w, w_proj_a, w_proj_b, w_out_mix, norm_xattn, norm_mem,
        w_q, w_kv, w_xo, norm_mlp, w_up, w_down, norm_final,
    )
    return second_block(
        x, norm_gain_2, w_in_2, b_gate_2, conv_w_2, a_log_2, dt_bias_2, dn_out_gain_2,
        sb_q_gain_2, sb_k_gain_2, w_up_a_2, w_up_b_2, w_out_2,
    )


_drawn_inputs = setup_inputs


def setup_inputs(seed=0):
    import zlib

    import numpy as np

    out = dict(_drawn_inputs(seed))
    spreads = {}
    factors = {'b_gate': 8.0,
     'w_lora_w': 8.0,
     'a0': 5.452,
     'k_k': 3.851,
     'k_a': 3.616,
     'ln_x_w': 3.795,
     'ln_x_b': 8.0,
     'norm_xattn': 8.0,
     'norm_mem': 6.83,
     'norm_gain_2': 4.627,
     'b_gate_2': 8.0,
     'dn_out_gain_2': 8.0,
     'sb_q_gain_2': 8.0,
     'sb_k_gain_2': 8.0}
    for name, (base, spread) in spreads.items():
        noise = np.random.default_rng([zlib.crc32(name.encode()), seed]).standard_normal(out[name].shape)
        drawn = base * np.exp(spread * noise) if base else spread * noise
        out[name] = __import__('jax').numpy.asarray(drawn.astype(out[name].dtype))
    for name, factor in factors.items():
        out[name] = (out[name] * factor).astype(out[name].dtype)
    return out
```

```python
from contextlib import ExitStack

import concourse.bass as bass
from concourse import mybir

F32 = mybir.dt.float32
F32R = mybir.dt.float32r
ALU = mybir.AluOpType
ACT = mybir.ActivationFunctionType
AX_X = mybir.AxisListType.X

P = 128
SEQ = 1024
HALF = 512
D = 1024
KT = D // P
N_MEM = 256
EPS = 1e-6
LN_X_EPS = 64e-5

_INS = [
    "x", "mem", "norm_mix", "w_in", "b_gate", "mu_shift", "w0", "w_lora_w", "a0", "w_lora_a", "w_lora_g",
    "k_k", "k_a", "r_k", "ln_x_w", "ln_x_b", "conv_w", "w_proj_a", "w_proj_b", "w_out_mix", "norm_xattn",
    "norm_mem", "w_q", "w_kv", "w_xo", "norm_mlp", "w_up", "w_down", "norm_final", "norm_gain_2", "w_in_2",
    "b_gate_2", "conv_w_2", "a_log_2", "dt_bias_2", "dn_out_gain_2", "sb_q_gain_2", "sb_k_gain_2",
    "w_up_a_2", "w_up_b_2", "w_out_2",
]

VECTORS = [
    ("norm_mix", 8), ("b_gate", 16), ("mu_shift", 15), ("w0", 4), ("a0", 4), ("k_k", 4), ("k_a", 4),
    ("r_k", 4), ("ln_x_w", 4), ("ln_x_b", 4), ("conv_w", 12), ("norm_xattn", 8), ("norm_mem", 8),
    ("norm_mlp", 8), ("norm_final", 8), ("norm_gain_2", 8),
    ("b_gate_2", 16), ("conv_w_2", 48), ("dn_out_gain_2", 1), ("sb_q_gain_2", 1), ("sb_k_gain_2", 1),
]


def wait(eng, sem, value):
    if not (isinstance(value, int) and value <= 0):
        eng.wait_ge(sem, value)


def apart(c, eng):
    eng.sem_inc(c.passed, 1)


class Steps:

    def __init__(self, sem):
        self.sem, self.total, self.shift = sem, 0, 0

    def mark(self, ins):
        ins.then_inc(self.sem, 1)
        self.total += 1
        return self.total + self.shift

    def wait(self, eng, value=None):
        wait(eng, self.sem, self.total + self.shift if value is None else value)


def rolled(eng, n, body, *steps):
    starts = [s.total for s in steps]
    body(0)
    if n > 1:
        per = [s.total - a for s, a in zip(steps, starts)]
        with eng.Fori(1, n) as i:
            for s, a, p in zip(steps, starts, per):
                s.total, s.shift = a, i * p
            body(i)
        assert [s.total - a for s, a in zip(steps, starts)] == per, "turns count alike"
        for s, a, p in zip(steps, starts, per):
            s.total, s.shift = a + n * p, 0


def first(i):
    return isinstance(i, int) and i == 0


def columns(i, width):
    return bass.ds(i * width, width)


class Weights:

    def __init__(self, core, sources, turns):
        self.core, self.sources, self.turns = core, sources, turns
        self.per = len(sources)
        self.slots = 3 if self.per % 3 == 0 else 2
        self.total = self.per * turns
        self.parts = [2 if isinstance(s(0), tuple) else 1 for s in sources]
        assert self.per % self.slots == 0

    def begin(self):
        self.t0 = self.core.tiles
        self.l0 = list(self.core.loads)
        self.core.tiles += self.total
        for s in range(self.slots):
            self.core.loads[s] += self.total // self.slots * self.parts[s]

    def fetch(self, sp, u, i):
        c, s, src = self.core, u % self.slots, self.sources[u](i)
        if self.parts[u] == 2:
            for half, part in enumerate(src):
                sp.dma_start(c.w_raw[:, s, half * KT // 2:(half + 1) * KT // 2], part).then_inc(c.w_loaded[s], 16)
        else:
            sp.dma_start(c.w_raw[:, s], src).then_inc(c.w_loaded[s], 16)

    def load_first(self, sp):
        for u in range(self.slots):
            self.fetch(sp, u, 0)

    def load_all(self, sp):
        for u in range(self.slots):
            sp.wait_ge(self.core.w_split, self.t0 + (u - self.slots + 1))
            self.fetch(sp, u, 0)
        self.load_rest(sp)

    def load_rest(self, sp):
        c, n = self.core, self.slots

        def turn(i):
            for u in range(self.per):
                if first(i) and u < n:
                    continue
                sp.wait_ge(c.w_split, self.t0 + i * self.per + (u - n + 1))
                apart(c, sp)
                self.fetch(sp, u, i)

        rolled(sp, self.turns, turn)

    def split(self, pool):
        c, n = self.core, self.slots

        def turn(i):
            for u in range(self.per):
                s = u % n
                each = 16 * self.parts[u]
                pool.wait_ge(c.w_loaded[s], 16 * self.l0[s] + i * (each * (self.per // n)) + each * (u // n + 1))
                wait(pool, c.tile_done, self.t0 + i * self.per + (u - n + 1))
                pool.tensor_tensor(c.w_hi[:, s], c.w_raw[:, s], c.ones[:].unsqueeze(1).broadcast_to([P, KT, P]),
                                   ALU.mult).then_inc(c.w_rounded, 1)
                pool.wait_ge(c.w_rounded, self.t0 + i * self.per + (u + 1))
                pool.tensor_tensor(c.w_lo[:, s], c.w_raw[:, s], c.w_hi[:, s].bitcast(F32),
                                   ALU.subtract).then_inc(c.w_split, 1)

        rolled(pool, self.turns, turn)

    def round_on(self, act):
        c, n = self.core, self.slots

        def turn(i):
            for u in range(self.per):
                s = u % n
                act.wait_ge(c.w_loaded[s], 16 * self.l0[s] + i * (16 * (self.per // n)) + 16 * (u // n + 1))
                wait(act, c.tile_done, self.t0 + i * self.per + (u - n + 1))
                act.copy(c.w_hi[:, s], c.w_raw[:, s]).then_inc(c.w_rounded, 1)

        rolled(act, self.turns, turn)

    def subtract(self, pool):
        c, n = self.core, self.slots

        def turn(i):
            for u in range(self.per):
                s = u % n
                pool.wait_ge(c.w_rounded, self.t0 + i * self.per + (u + 1))
                pool.tensor_tensor(c.w_lo[:, s], c.w_raw[:, s], c.w_hi[:, s].bitcast(F32),
                                   ALU.subtract).then_inc(c.w_split, 1)

        rolled(pool, self.turns, turn)

    def ready(self, pe, i, u):
        pe.wait_ge(self.core.w_split, self.t0 + i * self.per + (u + 1))

    def done(self, eng, i, u):
        eng.wait_ge(self.core.tile_done, self.t0 + i * self.per + (u + 1))

    def multiply(self, pe, u, out, hi, lo, kts=range(KT), offset=0, width=HALF, before=None):
        c, s = self.core, u % self.slots
        kts = list(kts)
        for k in kts:
            if before:
                before(k)
            for w, a in ((c.w_hi, hi), (c.w_hi, lo), (c.w_lo, hi)):
                for h, o in enumerate(out):
                    last = pe.matmul(o, w[:, s, k], a[:, k - offset, h * width:(h + 1) * width],
                                     start=(k == kts[0] and w is c.w_hi and a is hi),
                                     stop=(k == kts[-1] and w is c.w_lo))
        return last


class Core:
    pass


def open_core(nc, ctx, dram):
    c = Core()
    c.nc, c.ctx, c.dram = nc, ctx, dram

    def sb(name, shape, dt=F32):
        return ctx.enter_context(nc.sbuf_tensor(name, shape, dt))

    c.sb = sb
    c.stage_sems = []

    def sem(name):
        c.stage_sems.append(ctx.enter_context(nc.semaphore(name)))
        return c.stage_sems[-1]

    c.sem = sem
    c.x = sb("x_t", [P, KT, SEQ])
    c.h_base = (nc.sbuf_base + 31) // 32 * 32
    c.h_hi = sb("h_hi", [P, KT, SEQ], F32R)
    c.h_lo = sb("h_lo", [P, KT, SEQ], F32R)
    c.w_raw = sb("w_raw", [P, 3, KT, P])
    c.w_base = (nc.sbuf_base + 31) // 32 * 32
    c.w_hi = sb("w_hi", [P, 3, KT, P], F32R)
    c.w_lo = sb("w_lo", [P, 3, KT, P], F32R)
    c.vec = sb("vec", [P, 2 * P])
    c.ident = sb("ident", [P, P])
    c.ones = sb("ones", [P, P])
    c.ones_64 = sb("ones_64", [P, P])
    c.upper = sb("upper", [P, P])
    c.upper_eq = sb("upper_eq", [P, P])
    c.lower = sb("lower", [P, P])
    c.level_t = sb("level_t", [P, P])
    c.eps = sb("eps", [P, 5])
    c.lmid = sb("lmid", [P, CT, TILES + 1])
    c.lend = sb("lend", [P, CT, TILES])
    c.beta_col, c.decay_col, c.beta_decay = (sb(n, [P, TILES, DN_HEADS]) for n in ("beta_col", "decay_col", "beta_decay"))
    c.aux_base = nc.sbuf_base
    c.ps = ctx.enter_context(nc.psum_tensor("ps", [P, 8, HALF], F32))
    c.w_loaded = [c.sem(f"w_loaded{s}") for s in range(3)]
    c.w_rounded, c.w_split, c.tile_done = c.sem("w_rounded"), c.sem("w_split"), c.sem("tile_done")
    c.tiles, c.loads = 0, [0, 0, 0]
    c.a_steps, c.v_steps = Steps(c.sem("act_steps")), Steps(c.sem("dve_steps"))
    c.g_steps, c.t_steps = Steps(c.sem("pool_steps")), Steps(c.sem("pe_steps"))
    c.norm_sems = [c.sem(f"norm_{x}") for x in ("squared", "summed", "rooted", "scaled", "rounded", "split")]
    c.norm_tiles = c.norm_roots = c.norm_splits = 0
    c.begun, c.passed = c.sem("ident_ready"), c.sem("waits_passed")
    c.scratch = {}
    c.col, row = {}, 0
    for name, rows in VECTORS:
        c.col[name] = row
        row += rows
    assert row <= 2 * P
    c.stage_sems = []
    return c


def at(c, off, name, shape, dt=F32):
    return c.nc.alloc_sbuf_tensor_at(name, shape, dt, offset=(c.aux_base + 31) // 32 * 32 + off)


def at_h(c, off, name, shape, dt=F32):
    return c.nc.alloc_sbuf_tensor_at(name, shape, dt, offset=c.h_base + off)


def nth(events, name, i=0):
    return i * len(events) + (events.index(name) + 1)


def scratch(c, name, shape):
    c.scratch[name] = c.nc.dram_tensor(name, shape, F32, kind="Internal").ap()
    return c.scratch[name]


def vec(c, name, i=0):
    k = c.col[name]
    return c.vec[:, k + i:k + i + 1] if isinstance(i, int) else c.vec[:, bass.ds(i + k, 1)]


def setup(c):
    nc, d = c.nc, c.dram
    rows = at(c, 0, "vec_rows", [P, 2, P])
    xin = at(c, 2048, "x_in", [P, 2, D])
    c.mem_t = at(c, 16384, "mem_t", [P, KT, N_MEM])
    cleared, rows_in = c.sem("rows_cleared"), c.sem("rows_loaded")
    x_in = [c.sem("x_loaded0"), c.sem("x_loaded1")]
    ident_ready, turned, copied = c.begun, c.sem("tile_turned"), c.sem("tile_copied")
    n_rows = [0]
    with nc.Block() as block:

        @block.sync
        def _(sp):
            sp.dma_start(xin[:, 0], d["x"][0, 0:P, :]).then_inc(x_in[0], 16)
            sp.dma_start(xin[:, 1], d["x"][0, P:2 * P, :]).then_inc(x_in[1], 16)
            sp.wait_ge(cleared, 1)
            for name, n in VECTORS:
                r = c.col[name]
                flat = d[name]
                if name == "mu_shift":
                    mu = flat.rearrange("a n -> (a n)")
                    parts = [(r, mu[0:14 * P].rearrange("(n p) -> n p", p=P)),
                             (r + 14, mu[14 * P:1824].rearrange("(n p) -> n p", n=1))]
                elif name.startswith("sb_"):
                    parts = [(r, flat), (r, flat)]
                elif len(flat.shape) == 1:
                    parts = [(r, flat.rearrange("(n p) -> n p", p=P))]
                elif len(flat.shape) == 2:
                    parts = [(r, flat.rearrange("a (n p) -> (a n) p", p=P))]
                elif name == "r_k":
                    parts = [(r, flat.rearrange("a (n b) p -> (a n) (b p)", b=2))]
                elif len(flat.shape) == 3:
                    parts = [(r, flat.rearrange("a t (n p) -> (a t n) p", p=P))]
                else:
                    parts = [(r, flat.rearrange("a t b (n p) -> (a t b n) p", p=P))]
                for k, (at_row, src) in enumerate(parts):
                    done = 0
                    while done < src.shape[0]:
                        s, q = divmod(at_row + done, P)
                        m = min(src.shape[0] - done, P - q)
                        w = src.shape[1]
                        first = k * 64 if name.startswith("sb_") else 0
                        sp.dma_start(rows[q:q + m, s, first:first + w], src[done:done + m, :]).then_inc(rows_in, 16)
                        n_rows[0] += 1
                        done += m
            for t in range(2, SEQ // P + 2):
                sp.wait_ge(turned, t - 1)
                src = d["x"][0, t * P:(t + 1) * P, :] if t < 8 else d["mem"][0, (t - 8) * P:(t - 7) * P, :]
                sp.dma_start(xin[:, t % 2], src).then_inc(x_in[t % 2], 16)

        @block.gpsimd
        def _(pool):
            g = c.g_steps

            def fill(buf, value):
                return g.mark(pool.memset(buf, value))

            def keep(buf, pattern, base, mult, op=ALU.is_ge, fill=0.0):
                g.mark(pool.affine_select(out=buf, in_=buf, compare_op=op, fill=fill, base=base,
                                          pattern=pattern, channel_multiplier=mult))
                g.wait(pool)

            pool.memset(rows[:], 0.0).then_inc(cleared, 1)
            for buf, value in ((c.ident, 0.0), (c.ones, 1.0), (c.ones_64, 1.0), (c.upper, 1.0),
                               (c.upper_eq, 1.0), (c.lower, 1.0), (c.level_t, 0.0)):
                fill(buf[:], value)
            for k, value in enumerate((EPS, LN_X_EPS, 1.0, 0.0, EPS * SB_HEAD)):
                fill(c.eps[:, k:k + 1], value)
            g.wait(pool)
            pool.affine_select(out=c.ident[:], in_=c.ident[:], compare_op=ALU.not_equal, fill=1.0, base=0,
                               pattern=[[-1, P]], channel_multiplier=1).then_inc(ident_ready, 1)
            keep(c.ones_64[:, 0:64], [[0, 64]], 63, -1)
            keep(c.ones_64[:, 64:128], [[0, 64]], -64, 1)
            keep(c.upper[:], [[1, P]], -1, -1)
            keep(c.upper_eq[:], [[1, P]], 0, -1)
            keep(c.lower[:], [[-1, P]], -1, 1)
            odd = c.level_t[:].rearrange("p (b w) -> p b w", w=2)[:, :, 1:2]
            keep(odd, [[-2, P // 2]], 0, 1, op=ALU.not_equal, fill=1.0)

        @block.tensor
        def _(pe):
            pe.wait_ge(ident_ready, 1)
            for t in range(SEQ // P + 2):
                pe.wait_ge(x_in[t % 2], 16 * (t // 2 + 1))
                wait(pe, copied, t - 1)
                for k in range(KT):
                    last = pe.transpose(c.ps[:, 2 * (t % 2) + k // 4, (k % 4) * P:(k % 4 + 1) * P],
                                        xin[:, t % 2, k * P:(k + 1) * P], c.ident[:])
                last.then_inc(turned, 1)
            pe.wait_ge(rows_in, 16 * n_rows[0])
            for s in range(2):
                last = pe.transpose(c.ps[:, 4, s * P:(s + 1) * P], rows[:, s, :], c.ident[:])
            last.then_inc(turned, 1)

        @block.scalar
        def _(act):
            for t in range(SEQ // P + 2):
                act.wait_ge(turned, t + 1)
                dst = c.x[:, :, t * P:(t + 1) * P] if t < 8 else c.mem_t[:, :, (t - 8) * P:(t - 7) * P]
                act.copy(dst, c.ps[:, 2 * (t % 2):2 * (t % 2) + 2, :]
                         .rearrange("p b (k n) -> p (b k) n", n=P)).then_inc(copied, 1)
            act.wait_ge(turned, SEQ // P + 3)
            act.copy(c.vec[:], c.ps[:, 4, 0:2 * P]).then_inc(copied, 1)


def rms_norm(c, name, src, gain, tokens, hi=None, lo=None, dst=None, following=None):
    nc = c.nc
    width = min(HALF, tokens)
    sq = at(c, c.norm_at, f"{name}_sq", [P, 4, HALF])
    root = at(c, c.norm_at + 8192, f"{name}_root", [P, 2, HALF])
    whole = at(c, c.norm_at + 12288, f"{name}_whole", [P, 3, HALF])
    squared, summed, rooted, scaled, rounded, split = c.norm_sems
    halves = tokens // width
    n0, r0, s0 = c.norm_tiles, c.norm_roots, c.norm_splits
    c.norm_tiles += halves * KT
    c.norm_roots += halves
    c.norm_splits += halves * KT if hi is not None else 0
    with nc.Block() as block:

        @block.sync
        def _(sp):
            if following:
                following.load_first(sp)

        @block.tensor
        def _(pe):
            for h in range(halves):
                for k in range(KT):
                    pe.wait_ge(squared, n0 + h * KT + k + 1)
                    pe.matmul(c.ps[:, h, 0:width], c.ones[:], sq[:, k % 4, 0:width], start=k == 0,
                              stop=k == KT - 1).then_inc(summed, 1)

        @block.scalar
        def _(act):
            for h in range(halves):
                for k in range(KT):
                    wait(act, summed, n0 + h * KT + k - 3)
                    act.activation(sq[:, k % 4, 0:width], src[:, k, h * width:(h + 1) * width],
                                   ACT.Square).then_inc(squared, 1)
            for h in range(halves):
                act.wait_ge(summed, n0 + (h + 1) * KT)
                act.activation(root[:, h, 0:width], c.ps[:, h, 0:width], ACT.Sqrt, bias=c.eps[:, 0:1],
                               scale=1.0 / D).then_inc(rooted, 1)
            if hi is not None:
                for n in range(halves * KT):
                    h, k = divmod(n, KT)
                    act.wait_ge(scaled, n0 + n + 1)
                    act.copy(hi[:, k, h * width:(h + 1) * width], whole[:, n % 3, 0:width]).then_inc(rounded, 1)

        @block.vector
        def _(dve):
            v = c.v_steps
            for h in range(halves):
                dve.wait_ge(rooted, r0 + h + 1)
                v.mark(dve.reciprocal(root[:, h, 0:width], root[:, h, 0:width]))
            v.wait(dve)

            def take(n):
                h, k = divmod(n, KT)
                dve.wait_ge(rounded, s0 + n + 1)
                dve.tensor_tensor(lo[:, k, h * width:(h + 1) * width], whole[:, n % 3, 0:width],
                                  hi[:, k, h * width:(h + 1) * width].bitcast(F32), ALU.subtract).then_inc(split, 1)

            for n in range(halves * KT):
                h, k = divmod(n, KT)
                if hi is None:
                    out = dst[:, k, h * width:(h + 1) * width]
                else:
                    wait(dve, split, s0 + n - 2)
                    out = whole[:, n % 3, 0:width]
                dve.scalar_tensor_tensor(out=out, in0=src[:, k, h * width:(h + 1) * width], scalar=vec(c, gain, k),
                                         in1=root[:, h, 0:width], op0=ALU.mult, op1=ALU.mult).then_inc(scaled, 1)
                if hi is not None and n >= 1:
                    take(n - 1)
            if hi is not None:
                take(halves * KT - 1)


def add_product(c, name, weights, following):
    nc = c.nc
    weights.begin()
    free = [c.sem(f"{name}_free{q}") for q in range(2)]
    with nc.Block() as block:

        @block.sync
        def _(sp):
            weights.load_rest(sp)
            if following:
                sp.wait_ge(c.w_split, weights.t0 + weights.total)
                following.load_first(sp)

        @block.gpsimd
        def _(pool):
            weights.split(pool)

        @block.tensor
        def _(pe):
            def turn(i):
                for u in range(2):
                    weights.ready(pe, i, u)
                    wait(pe, free[u], i)
                    weights.multiply(pe, u, [c.ps[:, 2 * u], c.ps[:, 2 * u + 1]], c.h_hi, c.h_lo).then_inc(c.tile_done, 1)

            rolled(pe, weights.turns, turn)

        @block.vector
        def _(dve):
            def turn(i):
                for u in range(2):
                    weights.done(dve, i, u)
                    rows = c.x[:, bass.ds(i * 2 + u, 1), :].rearrange("p a n -> p (a n)")
                    dve.tensor_tensor(rows, rows, c.ps[:, 2 * u:2 * u + 2, :].rearrange("p b n -> p (b n)"),
                                      ALU.add).then_inc(free[u], 1)

            rolled(dve, weights.turns, turn)


def tile_of(src, first=0):
    view = src.rearrange("(k p) n -> p k n", p=P)
    return lambda i, step=1, off=0: view[:, :, bass.ds(i * (step * P) + (first + off * P), P)]


def finish(c, out):
    nc = c.nc
    tok = at(c, 0, "out_tok", [P, 2, D])
    turned, copied = c.sem("out_turned"), c.sem("out_copied")
    stored = [c.sem("out_stored0"), c.sem("out_stored1")]
    with nc.Block() as block:

        @block.tensor
        def _(pe):
            for t in range(SEQ // P):
                wait(pe, copied, t - 1)
                for k in range(KT):
                    last = pe.transpose(c.ps[:, 2 * (t % 2) + k // 4, (k % 4) * P:(k % 4 + 1) * P],
                                        c.x[:, k, t * P:(t + 1) * P], c.ident[:])
                last.then_inc(turned, 1)

        @block.scalar
        def _(act):
            for t in range(SEQ // P):
                act.wait_ge(turned, t + 1)
                wait(act, stored[t % 2], 16 * (t // 2))
                act.copy(tok[:, t % 2], c.ps[:, 2 * (t % 2):2 * (t % 2) + 2, :].rearrange("p b n -> p (b n)")).then_inc(copied, 1)

        @block.sync
        def _(sp):
            for t in range(SEQ // P):
                sp.wait_ge(copied, t + 1)
                sp.dma_start(out[0, t * P:(t + 1) * P, :], tok[:, t % 2]).then_inc(stored[t % 2], 16)
            for s in range(2):
                sp.wait_ge(stored[s], 16 * (SEQ // P // 2))


def mlp(c, following):
    nc, d = c.nc, c.dram
    groups, pairs = 4, KT // 2
    up, down = tile_of(d["w_up"][0]), d["w_down"][0]
    hid_hi = at(c, 0, "hid_hi", [P, KT, SEQ], F32R)
    hid_lo = at(c, 32768, "hid_lo", [P, KT, SEQ], F32R)
    relu = c.w_raw[:, 2].rearrange("p (h k) n -> p h (k n)", h=2)
    rectified, squared, rounded = c.sem("hid_rectified"), c.sem("hid_squared"), c.sem("hid_rounded")
    ready = c.sem("hid_ready")
    down_free = [c.sem("down_free0"), c.sem("down_free1")]
    streams = []
    for g in range(groups):
        rows = tile_of(down[g * D:(g + 1) * D, :])
        streams.append((Weights(c, [lambda i, g=g, u=u: up(i, 2, g * KT + u) for u in range(2)], pairs),
                        Weights(c, [lambda i, rows=rows, u=u: rows(i, 2, u) for u in range(2)], pairs)))
    c.mlp_first = streams[0][0]

    def build():
        for pair in streams:
            for w in pair:
                w.begin()
        every = [w for pair in streams for w in pair]
        with nc.Block() as block:

            @block.sync
            def _(sp):
                every[0].load_rest(sp)
                for w in every[1:]:
                    w.load_all(sp)
                if following:
                    sp.wait_ge(c.w_split, c.tiles)
                    following.load_first(sp)

            @block.gpsimd
            def _(pool):
                for w in every:
                    w.split(pool)

            @block.tensor
            def _(pe):
                for g, (w_up, w_down) in enumerate(streams):
                    def up_turn(i):
                        for u in range(2):
                            w_up.ready(pe, i, u)
                            wait(pe, rectified, (g * pairs + i) * 4 + (2 * u - 2))
                            w_up.multiply(pe, u, [c.ps[:, 2 * u], c.ps[:, 2 * u + 1]], c.h_hi,
                                          c.h_lo).then_inc(c.tile_done, 1)

                    def down_turn(i):
                        for u in range(2):
                            w_down.ready(pe, i, u)
                            wait(pe, down_free[u], g * pairs + i)
                            waits = first(i) and u == 0
                            w_down.multiply(pe, u, [c.ps[:, 4 + 2 * u], c.ps[:, 5 + 2 * u]], hid_hi, hid_lo,
                                            before=(lambda k: pe.wait_ge(ready, g * 16 + 2 * k + 2)) if waits
                                            else None).then_inc(c.tile_done, 1)

                    rolled(pe, pairs, up_turn)
                    rolled(pe, pairs, down_turn)

            @block.scalar
            def _(act):
                for g, (w_up, w_down) in enumerate(streams):
                    def turn(i):
                        for u in range(2):
                            w_up.done(act, i, u)
                            k = bass.ds(i * 2 + u, 1)
                            n = (g * pairs + i) * 4 + 2 * u
                            for h in range(2):
                                wait(act, ready, n + (h - 1))
                                act.activation(relu[:, h], c.ps[:, 2 * u + h], ACT.Relu).then_inc(rectified, 1)
                            for h in range(2):
                                act.wait_ge(squared, n + (h + 1))
                                act.copy(hid_hi[:, k, h * HALF:(h + 1) * HALF].rearrange("p a n -> p (a n)"),
                                         relu[:, h]).then_inc(rounded, 1)

                    rolled(act, pairs, turn)

            @block.vector
            def _(dve):
                for g, (w_up, w_down) in enumerate(streams):
                    def up_turn(i):
                        for u in range(2):
                            k = bass.ds(i * 2 + u, 1)
                            n = (g * pairs + i) * 4 + 2 * u
                            for h in range(2):
                                dve.wait_ge(rectified, n + (h + 1))
                                dve.tensor_tensor(relu[:, h], relu[:, h], relu[:, h], ALU.mult).then_inc(squared, 1)
                            for h in range(2):
                                dve.wait_ge(rounded, n + (h + 1))
                                cut = slice(h * HALF, (h + 1) * HALF)
                                dve.tensor_tensor(hid_lo[:, k, cut].rearrange("p a n -> p (a n)"), relu[:, h],
                                                  hid_hi[:, k, cut].rearrange("p a n -> p (a n)").bitcast(F32),
                                                  ALU.subtract).then_inc(ready, 1)

                    def down_turn(i):
                        for u in range(2):
                            w_down.done(dve, i, u)
                            if g:
                                dve.wait_ge(down_free[u], (g - 1) * pairs + i + 1)
                            rows = c.x[:, bass.ds(i * 2 + u, 1), :].rearrange("p a n -> p (a n)")
                            dve.tensor_tensor(rows, rows, c.ps[:, 4 + 2 * u:6 + 2 * u, :].rearrange("p b n -> p (b n)"),
                                              ALU.add).then_inc(down_free[u], 1)

                    rolled(dve, pairs, up_turn)
                    rolled(dve, pairs, down_turn)

    return streams[0][0], build


N_HEADS = 8
HEAD = 64
D_RWKV = N_HEADS * HEAD
CT = D_RWKV // P
RWKV_COLS = 3 * D_RWKV + 288
TILES = SEQ // P
DECAY = -0.6065306597126334
STORED = ["a_t", "r_t", "k_t", "b_t", "v_t", "bonus_t", "gate_t"]


def rwkv_lora_inputs(c):
    nc, d = c.nc, c.dram
    tile = tile_of(d["w_in"][0])
    c.lora_in = at(c, 0, "lora_in", [P, SEQ])
    c.gate_in = at(c, 4096, "gate_in", [P, SEQ])
    c.gate_in2 = at(c, 8192, "gate_in2", [P, SEQ])
    c.gate_w2 = c.gate_in2[32:64, 0:D_RWKV]
    c.lora_w = at(c, 12288, "lora_w", [P, D_RWKV])
    c.gate_w = at(c, 14336, "gate_w", [P, D_RWKV])
    plain = at(c, 20480, "lora_plain", [P, 3, SEQ + 1])
    mixed = at(c, 20480 + 12320, "lora_mixed", [P, 3, SEQ])
    weights = Weights(c, [lambda i, u=u: tile(i, 3, 12 + u) for u in range(3)], 1)
    cleared, copied, moved = c.sem("lora_cleared"), c.sem("lora_copied"), c.sem("lora_mixed_done")
    c.lora_loaded = c.sem("lora_loaded")
    mu = c.col["mu_shift"] + 12

    def build(following):
        weights.begin()
        with nc.Block() as block:

            @block.sync
            def _(sp):
                weights.load_rest(sp)
                sp.dma_start(c.lora_w[0:64, :], d["w_lora_w"][0]).then_inc(c.lora_loaded, 16)
                sp.dma_start(c.lora_w[64:128, :], d["w_lora_a"][0]).then_inc(c.lora_loaded, 16)
                sp.dma_start(c.gate_w[:], d["w_lora_g"][0, 0:P, :]).then_inc(c.lora_loaded, 16)
                sp.dma_start(c.gate_w2, d["w_lora_g"][0, P:160, :]).then_inc(c.lora_loaded, 16)
                sp.wait_ge(c.w_split, weights.t0 + weights.total)
                following.load_first(sp)

            @block.gpsimd
            def _(pool):
                pool.memset(plain[:, :, 0:1], 0.0).then_inc(cleared, 1)
                weights.split(pool)

            @block.tensor
            def _(pe):
                for u in range(3):
                    weights.ready(pe, 0, u)
                    weights.multiply(pe, u, [c.ps[:, 2 * u], c.ps[:, 2 * u + 1]], c.h_hi, c.h_lo).then_inc(c.tile_done, 1)

            @block.scalar
            def _(act):
                for u in range(3):
                    weights.done(act, 0, u)
                    act.copy(plain[:, u, 1:SEQ + 1], c.ps[:, 2 * u:2 * u + 2].rearrange("p b n -> p (b n)")).then_inc(copied, 1)
                act.wait_ge(moved, 1)
                act.activation(c.lora_in[0:64, :], mixed[0:64, 0, :], ACT.Tanh)
                act.copy(c.lora_in[64:128, :], mixed[64:128, 0, :])
                act.wait_ge(moved, 2)
                act.activation(c.gate_in[:], mixed[:, 1, :], ACT.Sigmoid)
                act.wait_ge(moved, 3)
                act.activation(c.gate_in2[0:32, :], mixed[0:32, 2, :], ACT.Sigmoid)

            @block.vector
            def _(dve):
                v = c.v_steps
                dve.wait_ge(cleared, 1)
                for u in range(3):
                    dve.wait_ge(copied, u + 1)
                    v.mark(dve.tensor_tensor(mixed[:, u], plain[:, u, 0:SEQ], plain[:, u, 1:SEQ + 1], ALU.subtract))
                    v.wait(dve)
                    dve.scalar_tensor_tensor(out=mixed[:, u], in0=mixed[:, u], scalar=c.vec[:, mu + u:mu + u + 1],
                                             in1=plain[:, u, 1:SEQ + 1], op0=ALU.mult, op1=ALU.add).then_inc(moved, 1)

    return weights, build


def rwkv_features(c):
    nc, d = c.nc, c.dram
    tile = tile_of(d["w_in"][0])
    out = [scratch(c, f"rwkv_{name}", [CT, P, SEQ]) for name in STORED]
    order = [4, 0, 8]
    weights = Weights(c, [lambda i, o=o: tile(i, 1, o) for o in order], CT)
    mid = SEQ // TILES // 2 - 1
    base = 16384

    def buf(name, width=HALF):
        nonlocal base
        b = at(c, base, f"rw_{name}", [P, width])
        base += 4 * ((width + 7) // 8 * 8)
        return b

    plain = [[buf(f"plain_{n}{h}", HALF + 1) for h in range(2)] for n in "krv"]
    log_w, a_gate, gate = buf("log_w", SEQ), buf("a_gate", SEQ), buf("gate", SEQ)
    k, r, v_b, kk, kf, b_b, bonus, root, rk, l_b, l_prev, e_neg = (
        buf(n) for n in ("k", "r", "v", "kk", "kf", "b", "bonus", "root", "rk", "l", "l_prev", "e_neg"))
    lora_s = buf("lora_s", 3 * P)
    assert base <= 229368 - c.aux_base, base
    copied, mixed, cleared = c.sem("rw_copied"), c.sem("rw_mixed"), c.sem("rw_cleared")
    aux, taken = [[c.sem(f"rw_{n}{h}") for h in range(2)] for n in ("aux", "taken")]
    staged, squared, keyed = c.sem("rw_staged"), c.sem("rw_squared"), c.sem("rw_keyed")
    decayed, negated, exps = c.sem("rw_decayed"), c.sem("rw_negated"), c.sem("rw_exps")
    made, stored = c.sem("rw_made"), c.sem("rw_stored")
    outputs = [None, None, None, None, None, None, None]

    def build(following):
        weights.begin()
        with nc.Block() as block:

            @block.sync
            def _(sp):
                def store(i, h):
                    sp.wait_ge(taken[h], i * 5 + 3)
                    apart(c, sp)
                    sp.wait_ge(made, i * 2 + (h + 1))
                    apart(c, sp)
                    cut = slice(h * HALF, (h + 1) * HALF)
                    for dst, src in zip(out, (kk[:], r[:], kf[:], b_b[:], v_b[:], bonus[:], gate[:, cut])):
                        view = dst[bass.ds(i, 1), :, cut].rearrange("a p n -> p (a n)")
                        sp.dma_start(view, src).then_inc(stored, 16)

                def turn(i):
                    for u in range(3):
                        sp.wait_ge(c.w_split, weights.t0 + i * 3 + (u + 1))
                        apart(c, sp)
                        sp.dma_start(c.w_raw[:, u], weights.sources[u](i + 1)).then_inc(c.w_loaded[u], 16)
                    for h in range(2):
                        store(i, h)

                rolled(sp, CT - 1, turn)
                for h in range(2):
                    store(CT - 1, h)
                following(sp)
                sp.wait_ge(stored, 16 * 7 * 2 * CT)

            @block.gpsimd
            def _(pool):
                pool.memset(c.lmid[:], 0.0).then_inc(cleared, 1)
                for n in range(3):
                    pool.memset(plain[n][0][:, 0:1], 0.0).then_inc(cleared, 1)
                weights.split(pool)

            @block.tensor
            def _(pe):
                def lora(i, n, h):
                    wait(pe, taken[h], i * 5 + n)
                    cut = slice(h * HALF, (h + 1) * HALF)
                    o = c.ps[:, 6 + h]
                    if n == 0:
                        last = pe.matmul(o, lora_s[0:64, 0:P], c.lora_in[0:64, cut], start=True, stop=True)
                    elif n == 1:
                        last = pe.matmul(o, lora_s[64:128, 0:P], c.lora_in[64:128, cut], start=True, stop=True)
                    else:
                        pe.matmul(o, lora_s[:, P:2 * P], c.gate_in[:, cut], start=True, stop=False)
                        last = pe.matmul(o, lora_s[0:32, 2 * P:3 * P], c.gate_in2[0:32, cut], start=False, stop=True)
                    last.then_inc(aux[h], 1)

                def sums_of(i, h):
                    wait(pe, taken[h], i * 5 + 3)
                    pe.wait_ge(squared, i * 2 + (h + 1))
                    pe.matmul(c.ps[:, 6 + h], c.ones_64[:], root[:], start=True, stop=True).then_inc(aux[h], 1)
                    wait(pe, taken[h], i * 5 + 4)
                    pe.wait_ge(keyed, i * 2 + (h + 1))
                    pe.matmul(c.ps[:, 6 + h], c.ones_64[:], rk[:], start=True, stop=True).then_inc(aux[h], 1)

                def turn(i):
                    for u in range(3):
                        weights.ready(pe, i, u)
                        wait(pe, copied, i * 6 + (2 * u - 4))
                        weights.multiply(pe, u, [c.ps[:, 2 * u], c.ps[:, 2 * u + 1]], c.h_hi, c.h_lo).then_inc(c.tile_done, 1)
                        if u == 0:
                            if not first(i):
                                sums_of(i - 1, 1)
                            pe.wait_ge(staged, i + 1)
                            for n in range(3):
                                for h in range(2):
                                    lora(i, n, h)
                    sums_of(i, 0)

                rolled(pe, CT, turn)
                sums_of(CT - 1, 1)

            @block.scalar
            def _(act):
                act.wait_ge(c.lora_loaded, 64)
                act.wait_ge(cleared, 4)
                a = c.a_steps

                def copies(i, n):
                    weights.done(act, i, n)
                    for h in range(2):
                        wait(act, mixed, (i - 1) * 6 + (3 * h + n + 1) if not first(i) else 0)
                        flat = c.ps[:, 2 * n:2 * n + 2].rearrange("p b m -> p (b m)")
                        if h == 0:
                            act.copy(plain[n][0][:, 1:HALF + 1], flat[:, 0:HALF]).then_inc(copied, 1)
                        else:
                            act.copy(plain[n][1][:], flat[:, HALF - 1:SEQ]).then_inc(copied, 1)

                def half(i, h):
                    act.wait_ge(mixed, i * 6 + (3 * h + 1))
                    if h == 0:
                        wait(act, made, i * 2)
                    else:
                        act.wait_ge(made, i * 2 + 1)
                    act.activation(root[:], kk[:], ACT.Square).then_inc(squared, 1)
                    act.wait_ge(aux[h], i * 5 + 4)
                    act.activation(root[:], c.ps[:, 6 + h], ACT.Sqrt, bias=c.eps[:, 3:4]).then_inc(taken[h], 1)
                    act.wait_ge(decayed, i * 2 + (h + 1))
                    act.activation(l_prev[:], l_prev[:], ACT.Exp)
                    act.activation(e_neg[:], l_b[:], ACT.Exp, scale=-1.0).then_inc(negated, 1)
                    act.wait_ge(negated, i * 2 + (h + 1))
                    act.activation(l_b[:], l_b[:], ACT.Exp).then_inc(exps, 1)

                def turn(i):
                    wait(act, aux[1], i * 5 - 2)
                    apart(c, act)
                    at_i = columns(i, P)
                    a.mark(act.copy(lora_s[:, 0:P], c.lora_w[:, at_i]))
                    a.mark(act.copy(lora_s[:, P:2 * P], c.gate_w[:, at_i]))
                    a.mark(act.copy(lora_s[0:32, 2 * P:3 * P], c.gate_in2[32:64, at_i]))
                    a.wait(act)
                    act.sem_inc(staged, 1)
                    copies(i, 0)
                    if not first(i):
                        half(i - 1, 1)
                    for n, (dst, bias) in enumerate(((log_w, vec(c, "w0", i)), (a_gate, vec(c, "a0", i)))):
                        for h in range(2):
                            act.wait_ge(aux[h], i * 5 + (n + 1))
                            wait(act, made, (i - 1) * 2 + (h + 1) if not first(i) else 0)
                            apart(c, act)
                            act.activation(dst[:, h * HALF:(h + 1) * HALF], c.ps[:, 6 + h], ACT.Sigmoid,
                                           bias=bias).then_inc(taken[h], 1)
                    for h in range(2):
                        act.wait_ge(aux[h], i * 5 + 3)
                        wait(act, stored, i * (16 * 14) + (h - 1) * 16 * 7 if not first(i) else 0)
                        act.copy(gate[:, h * HALF:(h + 1) * HALF], c.ps[:, 6 + h]).then_inc(taken[h], 1)
                    for n in range(1, 3):
                        copies(i, n)
                    half(i, 0)

                rolled(act, CT, turn, a)
                half(CT - 1, 1)

            @block.vector
            def _(dve):
                v = c.v_steps
                mu = c.col["mu_shift"]
                dve.wait_ge(cleared, 4)

                def mix(i, n, h, dst):
                    p = plain[n][h]
                    dve.wait_ge(copied, i * 6 + (2 * n + h + 1))
                    v.mark(dve.tensor_tensor(dst[:], p[:, 0:HALF], p[:, 1:HALF + 1], ALU.subtract))
                    v.wait(dve)
                    col = i + (mu + order[n])
                    scale = c.vec[:, col:col + 1] if isinstance(i, int) else c.vec[:, bass.ds(col, 1)]
                    v.mark(dve.scalar_tensor_tensor(out=dst[:], in0=dst[:], scalar=scale, in1=p[:, 1:HALF + 1],
                                                    op0=ALU.mult, op1=ALU.add))
                    v.wait(dve)

                def half(i, h):
                    cut = slice(h * HALF, (h + 1) * HALF)
                    if h == 0:
                        wait(dve, stored, i * (16 * 14))
                    else:
                        dve.wait_ge(stored, i * (16 * 14) + 16 * 7)
                    mix(i, 0, h, k)
                    dve.tensor_scalar(kk[:], k[:], vec(c, "k_k", i), None, ALU.mult).then_inc(mixed, 1)
                    dve.wait_ge(taken[h], i * 5 + 2)
                    v.mark(dve.tensor_scalar(log_w[:, cut], log_w[:, cut], DECAY, None, ALU.mult))
                    v.wait(dve)
                    for q in range(HALF // P):
                        chunk = slice(q * P, (q + 1) * P)
                        v.mark(dve.tensor_tensor_scan(l_b[:, chunk], c.ones[:], log_w[:, cut][:, chunk], 0.0,
                                                      ALU.mult, ALU.add))
                    v.wait(dve)
                    chunks = l_b[:].rearrange("p (t n) -> p t n", n=P)
                    t0 = h * (TILES // 2)
                    mids = c.lmid[:, bass.ds(i, 1), t0:t0 + 4].rearrange("p a t -> p (a t)")
                    v.mark(dve.tensor_copy(mids, chunks[:, :, mid]))
                    v.wait(dve)
                    v.mark(dve.tensor_tensor(chunks, chunks, mids.unsqueeze(2).broadcast_to([P, 4, P]), ALU.subtract))
                    v.wait(dve)
                    v.mark(dve.tensor_copy(c.lend[:, bass.ds(i, 1), t0:t0 + 4].rearrange("p a t -> p (a t)"),
                                           chunks[:, :, P - 1]))
                    v.mark(dve.tensor_tensor(l_prev[:], l_b[:], log_w[:, cut], ALU.subtract))
                    v.wait(dve)
                    dve.sem_inc(decayed, 1)
                    v.mark(dve.tensor_scalar(kf[:], a_gate[:, cut], -1.0, vec(c, "k_a", i), ALU.add, ALU.mult))
                    v.wait(dve)
                    v.mark(dve.scalar_tensor_tensor(out=kf[:], in0=kf[:], scalar=1.0, in1=k[:], op0=ALU.add, op1=ALU.mult))
                    mix(i, 1, h, r)
                    dve.sem_inc(mixed, 1)
                    v.mark(dve.scalar_tensor_tensor(out=rk[:], in0=r[:], scalar=vec(c, "r_k", i), in1=kf[:],
                                                    op0=ALU.mult, op1=ALU.mult))
                    v.wait(dve)
                    dve.sem_inc(keyed, 1)
                    mix(i, 2, h, v_b)
                    dve.sem_inc(mixed, 1)
                    dve.wait_ge(taken[h], i * 5 + 4)
                    v.mark(dve.tensor_scalar(root[:], root[:], 1e-12, None, ALU.max))
                    v.wait(dve)
                    v.mark(dve.reciprocal(root[:], root[:]))
                    v.wait(dve)
                    v.mark(dve.tensor_tensor(kk[:], kk[:], root[:], ALU.mult))
                    v.wait(dve)
                    v.mark(dve.tensor_tensor(b_b[:], kk[:], a_gate[:, cut], ALU.mult))
                    dve.wait_ge(aux[h], i * 5 + 5)
                    v.mark(dve.tensor_tensor(bonus[:], c.ps[:, 6 + h], v_b[:], ALU.mult))
                    v.wait(dve)
                    dve.sem_inc(taken[h], 1)
                    dve.wait_ge(exps, i * 2 + (h + 1))
                    v.mark(dve.tensor_tensor(r[:], r[:], l_b[:], ALU.mult))
                    v.mark(dve.scalar_tensor_tensor(out=kk[:], in0=kk[:], scalar=-1.0, in1=l_prev[:], op0=ALU.mult, op1=ALU.mult))
                    v.mark(dve.tensor_tensor(kf[:], kf[:], e_neg[:], ALU.mult))
                    v.mark(dve.tensor_tensor(b_b[:], b_b[:], e_neg[:], ALU.mult))
                    v.wait(dve)
                    dve.sem_inc(made, 1)

                def turn(i):
                    for h in range(2):
                        half(i, h)

                rolled(dve, CT, turn, v)
                v.mark(dve.tensor_tensor(c.lend[:], c.lend[:], c.lmid[:, :, 1:TILES + 1], ALU.add))

    return weights, build


def make_levels(c, pool):
    g = c.g_steps
    g.mark(pool.memset(c.level[:], 0.0))
    for n in range(LEVELS):
        s = 1 << n
        blocks = P // (2 * s)
        quarter = c.level[:, n, :].rearrange("p (b w) -> p b w", w=2 * s)[:, :, 0:s]
        g.wait(pool)
        g.mark(pool.memset(quarter, 1.0))
        for pattern, base, sign in (([[-2 * s, blocks], [0, s]], -s, 1), ([[2 * s, blocks], [0, s]], 2 * s - 1, -1)):
            g.wait(pool)
            g.mark(pool.affine_select(out=quarter, in_=quarter, compare_op=ALU.is_ge, fill=0.0, base=base,
                                      pattern=pattern, channel_multiplier=sign))
    g.wait(pool)


LEVELS = 7
LEVEL_PE = [f"{what}{n}" for n in range(1, LEVELS) for what in ("x", "t")]
LEVEL_DVE = [f"{what}{n}" for n in range(1, LEVELS) for what in (("xm", "t", "tt") if n < LEVELS - 1 else ("xm", "tt"))]


def inverse_pe(pe, n, products, masks, i, pe_events, dve_events, banks, n_t, t, t_t, x):
    px, pt, ptt = banks
    pe.wait_ge(masks, nth(dve_events, "tt0" if n == 1 else f"tt{n - 1}", i))
    for h in range(4):
        last = pe.matmul(px[:, h * P:(h + 1) * P], n_t[:, h], t[:, h], start=True, stop=True)
    last.then_inc(products, 1)


def inverse_pe_update(pe, n, products, masks, i, dve_events, banks, t, t_t, x):
    px, pt, ptt = banks
    pe.wait_ge(masks, nth(dve_events, f"xm{n}", i))
    for h in range(4):
        cut = slice(h * P, (h + 1) * P)
        if n < LEVELS - 1:
            pe.matmul(pt[:, cut], t_t[:, h], x[:, h], start=True, stop=True)
        last = pe.matmul(ptt[:, cut], x[:, h], t_t[:, h], start=True, stop=True)
    last.then_inc(products, 1)


def heads_of(bank):
    return bank.rearrange("p (h n) -> p h n", n=P)


def inverse_start_dve(c, dve, masks, i, dve_events, n_plain, n_t, t, t_t):
    def over_heads(m):
        return m.unsqueeze(1).broadcast_to([P, 4, P])

    dve.wait_ge(masks, nth(dve_events, "n", i))
    dve.tensor_tensor(t[:], n_plain[:], over_heads(c.level[:, 0]), ALU.mult).then_inc(masks, 1)
    dve.wait_ge(masks, nth(dve_events, "t_block", i))
    dve.tensor_tensor(t[:], t[:], over_heads(c.ident[:]), ALU.add).then_inc(masks, 1)
    dve.wait_ge(masks, nth(dve_events, "n_t", i))
    dve.tensor_tensor(t_t[:], n_t[:], over_heads(c.level_t[:]), ALU.mult).then_inc(masks, 1)
    dve.wait_ge(masks, nth(dve_events, "tt_block", i))
    dve.tensor_tensor(t_t[:], t_t[:], over_heads(c.ident[:]), ALU.add).then_inc(masks, 1)


def inverse_mask_dve(c, dve, n, products, masks, i, pe_events, banks, x):
    dve.wait_ge(products, nth(pe_events, f"x{n}", i))
    dve.tensor_tensor(x[:], heads_of(banks[0]), c.level[:, n].unsqueeze(1).broadcast_to([P, 4, P]),
                      ALU.mult).then_inc(masks, 1)


def inverse_add_dve(dve, n, products, masks, i, pe_events, banks, t, t_t):
    dve.wait_ge(products, nth(pe_events, f"t{n}", i))
    if n < LEVELS - 1:
        dve.tensor_tensor(t[:], t[:], heads_of(banks[1]), ALU.add).then_inc(masks, 1)
    dve.tensor_tensor(t_t[:], t_t[:], heads_of(banks[2]), ALU.add).then_inc(masks, 1)


def rwkv_scan(c):
    nc = c.nc
    base = 0

    def buf(name, shape):
        nonlocal base
        b = at(c, base, f"scan_{name}", shape)
        n = 4
        for m in shape[1:]:
            n *= m
        base += n
        return b

    a_r, k_in, b_in, v_in = (buf("a_r", [P, 2, CT, 2, P]), buf("k", [P, 2, CT, P]), buf("b", [P, 2, CT, P]),
                             buf("v", [P, 2, CT, P]))
    nat = {n: buf(f"{n}_nat", [P, CT, P]) for n in "vkb"}
    groups = range(2)
    ak, rk, ab, rb, n_p = ([buf(f"{n}{g}", [P, 4, P]) for g in groups] for n in ("ak", "rk", "ab", "rb", "n"))
    t, t_t, x = ([buf(f"{n}{g}", [P, 4, P]) for g in groups] for n in ("t", "tt", "x"))
    u_b, sa = ([buf(f"{n}{g}", [P, 2, P]) for g in groups] for n in ("u", "sa"))
    state = buf("state", [P, CT, P])
    new = [buf(f"new{g}", [P, 2, P]) for g in groups]
    factor = c.lend
    assert c.aux_base + base <= 229376
    c.y_t = c.nc.alloc_sbuf_tensor_at("y_t", [P, CT, SEQ], F32, offset=c.w_base)
    c.level = c.nc.alloc_sbuf_tensor_at("scan_level", [P, LEVELS, P], F32, offset=c.w_base + 16384)

    PE_EVENTS = ["n", "k", "b"] + LEVEL_PE
    DVE_EVENTS = ["n", "ak", "rk", "n_t", "rb", "t_block", "t0", "tt_block", "tt0"] + LEVEL_DVE
    CHAIN_PE, CHAIN_DVE, CHAIN_ACT = ["u", "sa", "s", "y"], ["s_sum", "s_new"], ["u", "sa", "y"]
    loaded = [c.sem("scan_loaded0"), c.sem("scan_loaded1")]
    turned, natural, cleared = c.sem("scan_turned"), c.sem("scan_natural"), c.sem("scan_cleared")
    products, masks = ([c.sem(f"scan_{n}{g}") for g in groups] for n in ("products", "masks"))
    chained, copies, states = ([c.sem(f"scan_{n}{e}") for e in groups] for n in ("chained", "copies", "states"))
    factored = c.sem("scan_factored")
    ps = c.ps
    src = [c.scratch[f"rwkv_{n}"].rearrange("a p n -> p a n") for n in STORED[:5]]
    level_banks = [(ps[:, g], ps[:, 2 + g], ps[:, 4 + g]) for g in groups]
    n_bank = [4, 5]
    k_banks = [slice(0, 2), slice(6, 8)]
    b_banks = [slice(2, 4), slice(4, 6)]
    turns = TILES // 2

    with nc.Block() as block:

        @block.sync
        def _(sp):
            def turn(j):
                for q in range(2):
                    i = j * 2 + q
                    if not first(j):
                        for e in groups:
                            sp.wait_ge(chained[e], nth(CHAIN_PE, "y", i - 2))
                        apart(c, sp)
                    cut = columns(i, P)
                    for part, dst in zip(src, (a_r[:, q, :, 0], a_r[:, q, :, 1], k_in[:, q], b_in[:, q], v_in[:, q])):
                        sp.dma_start(dst, part[:, :, cut]).then_inc(loaded[q], 16)

            rolled(sp, turns, turn)

        @block.gpsimd
        def _(pool):
            for g in groups:
                for m in (ak[g], rk[g], ab[g], rb[g], n_p[g]):
                    pool.memset(m[:], 0.0).then_inc(cleared, 1)
            make_levels(c, pool)
            pool.memset(state[:], 0.0).then_inc(cleared, 1)

        @block.tensor
        def _(pe):
            pe.wait_ge(cleared, 11)

            def scores(q, i):
                rows = [slice(0, 64), slice(64, P)]
                for ct in range(CT):
                    for g in groups:
                        last = pe.matmul(ps[:, n_bank[g], ct * P:(ct + 1) * P], a_r[rows[g], q, ct, 0],
                                         b_in[rows[g], q, ct], start=True, stop=True)
                        if ct == CT - 1:
                            last.then_inc(products[g], 1)
                pe.wait_ge(natural, i * 3 + 3)
                for operand, banks in ((k_in, k_banks), (b_in, b_banks)):
                    if operand is b_in:
                        for g in groups:
                            pe.wait_ge(masks[g], nth(DVE_EVENTS, "n", i))
                    for ct in range(CT):
                        for g in groups:
                            pair = ps[:, banks[g]].rearrange("p b (h m) -> p (b h) m", m=2 * P)
                            last = pe.matmul(pair[:, ct], operand[rows[g], q, ct],
                                             a_r[rows[g], q, ct].rearrange("p a n -> p (a n)"), start=True, stop=True)
                            if ct == CT - 1:
                                last.then_inc(products[g], 1)

            def chunk(i, q, use):
                pe.wait_ge(loaded[q], use * 80 + 80)
                for e in groups:
                    wait(pe, states[e], nth(CHAIN_DVE, "s_new", i - 1))
                    wait(pe, copies[e], nth(CHAIN_ACT, "y", i - 1))
                for b, (n, part) in enumerate((("v", v_in), ("k", k_in), ("b", b_in))):
                    for ct in range(CT):
                        last = pe.transpose(ps[:, (3, 6, 7)[b], ct * P:(ct + 1) * P], part[:, q, ct], c.ident[:])
                    last.then_inc(turned, 1)
                scores(q, i)
                for g in groups:
                    pe.wait_ge(masks[g], nth(DVE_EVENTS, "rk", i))
                for e in groups:
                    out = ps[:, 6 + e]
                    for k in range(2):
                        ct = 2 * e + k
                        pe.matmul(out[:, k * P:(k + 1) * P], a_r[:, q, ct, 0], state[:, ct], start=True, stop=False,
                                  skip_group_check=True)
                        for g in groups:
                            cut = slice(k * P + g * 64, k * P + g * 64 + 64)
                            last = pe.matmul(out[:, cut], ak[g][:, ct], nat["v"][:, ct, g * 64:g * 64 + 64],
                                             start=False, stop=True, skip_group_check=True)
                    last.then_inc(chained[e], 1)
                for n in range(1, LEVELS):
                    for g in groups:
                        if n == 1:
                            pe.wait_ge(masks[1], nth(DVE_EVENTS, "rb", i))
                        inverse_pe(pe, n, products[g], masks[g], i, PE_EVENTS, DVE_EVENTS, level_banks[g], ab[g], t[g], t_t[g], x[g])
                    for g in groups:
                        inverse_pe_update(pe, n, products[g], masks[g], i, DVE_EVENTS, level_banks[g], t[g], t_t[g], x[g])
                for g in groups:
                    pe.wait_ge(masks[g], nth(DVE_EVENTS, f"tt{LEVELS - 1}", i))
                for e in groups:
                    pe.wait_ge(copies[e], nth(CHAIN_ACT, "u", i))
                    for k in range(2):
                        for g in groups:
                            last = pe.matmul(ps[:, e, k * P + g * 64:k * P + g * 64 + 64], t_t[g][:, 2 * e + k],
                                             u_b[e][:, k, g * 64:g * 64 + 64], start=True, stop=True)
                    last.then_inc(chained[e], 1)
                for e in groups:
                    pe.wait_ge(copies[e], nth(CHAIN_ACT, "sa", i))
                    for k in range(2):
                        ct = 2 * e + k
                        o = ps[:, 2 + e, k * P:(k + 1) * P]
                        pe.matmul(o, nat["b"][:, ct], sa[e][:, k], start=True, stop=False, skip_group_check=True)
                        last = pe.matmul(o, nat["k"][:, ct], nat["v"][:, ct], start=False, stop=True, skip_group_check=True)
                    last.then_inc(chained[e], 1)
                    for k in range(2):
                        ct = 2 * e + k
                        cut = slice(k * P, (k + 1) * P)
                        pe.matmul(ps[:, 4 + e, cut], state[:, ct], a_r[:, q, ct, 1], start=True, stop=False,
                                  skip_group_check=True)
                        for g in groups:
                            rows = slice(64 * g, 64 * g + 64)
                            pe.matmul(ps[rows, 4 + e, cut], sa[e][:, k, rows], rb[g][:, ct], start=False,
                                      stop=False, skip_group_check=True)
                            last = pe.matmul(ps[rows, 4 + e, cut], nat["v"][:, ct, rows], rk[g][:, ct], start=False,
                                             stop=True, skip_group_check=True)
                    last.then_inc(chained[e], 1)

            def turn(j):
                for q in range(2):
                    chunk(j * 2 + q, q, j)

            rolled(pe, turns, turn)

        @block.scalar
        def _(act):
            act.activation(factor[:], c.lend[:], ACT.Exp).then_inc(factored, 1)

            def chunk(i):
                for b, n in enumerate("vkb"):
                    act.wait_ge(turned, i * 3 + (b + 1))
                    act.copy(nat[n][:], heads_of(ps[:, (3, 6, 7)[b]])).then_inc(natural, 1)
                for bank, name, into in ((6, "u", u_b), (0, "sa", sa), (4, "y", None)):
                    for e in groups:
                        act.wait_ge(chained[e], nth(CHAIN_PE, name, i))
                        if name == "y":
                            apart(c, act)
                            dst = c.y_t[:, 2 * e:2 * e + 2, columns(i, P)]
                        else:
                            dst = into[e][:]
                        act.copy(dst, ps[:, bank + e, 0:2 * P].rearrange("p (k n) -> p k n", n=P)).then_inc(copies[e], 1)

            def turn(j):
                for q in range(2):
                    chunk(j * 2 + q)

            rolled(act, turns, turn)

        @block.vector
        def _(dve):
            dve.wait_ge(cleared, 11)
            dve.wait_ge(factored, 1)

            def over(m):
                return m[:].unsqueeze(1).broadcast_to([P, 4, P]).bitcast(mybir.dt.int32)

            def pair(banks):
                return ps[:, banks].rearrange("p b (h a n) -> p (b h) a n", a=2, n=P)

            def chunk(i):
                for e in groups:
                    wait(dve, chained[e], nth(CHAIN_PE, "y", i - 1))
                for g in groups:
                    dve.wait_ge(products[g], nth(PE_EVENTS, "n", i))
                    apart(c, dve)
                    dve.copy_predicated(n_p[g][:], over(c.lower), heads_of(ps[:, n_bank[g]])).then_inc(masks[g], 1)
                for g in groups:
                    dve.wait_ge(products[g], nth(PE_EVENTS, "k", i))
                    apart(c, dve)
                    dve.copy_predicated(ak[g][:], over(c.upper), pair(k_banks[g])[:, :, 0]).then_inc(masks[g], 1)
                    dve.copy_predicated(rk[g][:], over(c.upper_eq), pair(k_banks[g])[:, :, 1]).then_inc(masks[g], 1)
                for g in groups:
                    dve.wait_ge(products[g], nth(PE_EVENTS, "b", i))
                    apart(c, dve)
                    dve.copy_predicated(ab[g][:], over(c.upper), pair(b_banks[g])[:, :, 0]).then_inc(masks[g], 1)
                    dve.copy_predicated(rb[g][:], over(c.upper_eq), pair(b_banks[g])[:, :, 1]).then_inc(masks[g], 1)
                for g in groups:
                    inverse_start_dve(c, dve, masks[g], i, DVE_EVENTS, n_p[g], ab[g], t[g], t_t[g])
                for n in range(1, LEVELS):
                    for g in groups:
                        inverse_mask_dve(c, dve, n, products[g], masks[g], i, PE_EVENTS, level_banks[g], x[g])
                    for g in groups:
                        inverse_add_dve(dve, n, products[g], masks[g], i, PE_EVENTS, level_banks[g], t[g], t_t[g])
                for e in groups:
                    two = slice(2 * e, 2 * e + 2)
                    dve.wait_ge(chained[e], nth(CHAIN_PE, "y", i))
                    dve.tensor_tensor(new[e][:], state[:, two], ps[:, 2 + e, 0:2 * P].rearrange("p (k n) -> p k n", n=P),
                                      ALU.add).then_inc(states[e], 1)
                    dve.wait_ge(states[e], nth(CHAIN_DVE, "s_sum", i))
                    for k in range(2):
                        last = dve.scalar_tensor_tensor(
                            out=state[:, 2 * e + k], in0=new[e][:, k],
                            scalar=factor[:, 2 * e + k, bass.ds(i, 1)], in1=c.ones_64[:], op0=ALU.mult, op1=ALU.mult)
                    last.then_inc(states[e], 1)

            def turn(j):
                for q in range(2):
                    chunk(j * 2 + q)

            rolled(dve, turns, turn)


def rwkv_output(c, following):
    nc = c.nc
    c.br_hi = at(c, 0, "branch_hi", [P, KT, SEQ], F32R)
    c.br_lo = at(c, 32768, "branch_lo", [P, KT, SEQ], F32R)
    six = c.w_raw[:].rearrange("p s (a k) n -> p (s a) (k n)", a=2)
    dev, sq, root, bonus, gate = (six[:, n] for n in range(5))
    centred, squared, rooted = c.sem("ro_centred"), c.sem("ro_squared"), c.sem("ro_rooted")
    summed, loaded, made, rounded, split = (c.sem(f"ro_{n}") for n in ("summed", "loaded", "made", "rounded", "split"))
    src = [c.scratch["rwkv_bonus_t"], c.scratch["rwkv_gate_t"]]
    with nc.Block() as block:

        @block.sync
        def _(sp):
            def turn(i):
                for h in range(2):
                    wait(sp, made, i * 2 + h)
                    apart(c, sp)
                    cut = slice(h * HALF, (h + 1) * HALF)
                    for part, dst in zip(src, (bonus, gate)):
                        sp.dma_start(dst, part[bass.ds(i, 1), :, cut].rearrange("a p n -> p (a n)")).then_inc(loaded, 16)

            rolled(sp, CT, turn)
            if following:
                sp.wait_ge(split, 2 * CT)
                following.load_first(sp)

        @block.tensor
        def _(pe):
            def turn(i):
                for h in range(2):
                    cut = slice(h * HALF, (h + 1) * HALF)
                    wait(pe, centred, i * 2 + (h - 1))
                    pe.matmul(c.ps[:, h], c.ones_64[:], c.y_t[:, bass.ds(i, 1), cut].rearrange("p a n -> p (a n)"),
                              start=True, stop=True).then_inc(summed, 1)
                    pe.wait_ge(squared, i * 2 + (h + 1))
                    pe.matmul(c.ps[:, 2 + h], c.ones_64[:], sq, start=True, stop=True).then_inc(summed, 1)

            rolled(pe, CT, turn)

        @block.scalar
        def _(act):
            def turn(i):
                for h in range(2):
                    cut = slice(h * HALF, (h + 1) * HALF)
                    act.wait_ge(centred, i * 2 + (h + 1))
                    act.activation(sq, dev, ACT.Square).then_inc(squared, 1)
                    act.wait_ge(summed, i * 4 + (2 * h + 2))
                    wait(act, made, i * 2 + h)
                    act.activation(root, c.ps[:, 2 + h], ACT.Sqrt, bias=c.eps[:, 1:2],
                                   scale=1.0 / HEAD).then_inc(rooted, 1)
                    act.wait_ge(made, i * 2 + (h + 1))
                    apart(c, act)
                    act.copy(c.br_hi[:, bass.ds(i, 1), cut].rearrange("p a n -> p (a n)"), dev).then_inc(rounded, 1)

            rolled(act, CT, turn)

        @block.vector
        def _(dve):
            v = c.v_steps

            def turn(i):
                for h in range(2):
                    cut = slice(h * HALF, (h + 1) * HALF)
                    dve.wait_ge(summed, i * 4 + (2 * h + 1))
                    wait(dve, split, i * 2 + h)
                    dve.scalar_tensor_tensor(out=dev, in0=c.ps[:, h], scalar=-1.0 / HEAD,
                                             in1=c.y_t[:, bass.ds(i, 1), cut].rearrange("p a n -> p (a n)"),
                                             op0=ALU.mult, op1=ALU.add).then_inc(centred, 1)
                    dve.wait_ge(rooted, i * 2 + (h + 1))
                    v.mark(dve.reciprocal(root, root))
                    v.wait(dve)
                    v.mark(dve.tensor_tensor(dev, dev, root, ALU.mult))
                    v.wait(dve)
                    v.mark(dve.tensor_scalar(dev, dev, vec(c, "ln_x_w", i), vec(c, "ln_x_b", i), ALU.mult, ALU.add))
                    v.wait(dve)
                    dve.wait_ge(loaded, i * 64 + (32 * h + 32))
                    v.mark(dve.tensor_tensor(dev, dev, bonus, ALU.add))
                    v.wait(dve)
                    dve.tensor_tensor(dev, dev, gate, ALU.mult).then_inc(made, 1)
                    dve.wait_ge(rounded, i * 2 + (h + 1))
                    dve.tensor_tensor(c.br_lo[:, bass.ds(i, 1), cut].rearrange("p a n -> p (a n)"), dev,
                                      c.br_hi[:, bass.ds(i, 1), cut].rearrange("p a n -> p (a n)").bitcast(F32),
                                      ALU.subtract).then_inc(split, 1)

            rolled(dve, CT, turn, v)


def short_conv(c):
    nc, d = c.nc, c.dram
    tile = tile_of(d["w_in"][0], RWKV_COLS)
    weights = Weights(c, [lambda i, o=o: tile(i, 1, o * CT) for o in (1, 2, 0)], CT)
    u_b = at(c, 65536, "conv_u", [P, HALF + 2])
    y_b = at(c, 65536 + 2080, "conv_y", [P, HALF])
    cleared, copied, product, ended, made, rounded, split = (
        c.sem(f"conv_{n}") for n in ("cleared", "copied", "product", "ended", "made", "rounded", "split"))

    def build(following):
        weights.begin()
        with nc.Block() as block:

            @block.sync
            def _(sp):
                weights.load_rest(sp)
                sp.wait_ge(c.w_split, weights.t0 + weights.total)
                following.load_first(sp)

            @block.gpsimd
            def _(pool):
                weights.split(pool)

            @block.tensor
            def _(pe):
                def turn(i):
                    for u in range(3):
                        weights.ready(pe, i, u)
                        wait(pe, (copied, product, made)[u], i * 2)
                        weights.multiply(pe, u, [c.ps[:, 2 * u], c.ps[:, 2 * u + 1]], c.h_hi, c.h_lo).then_inc(c.tile_done, 1)

                rolled(pe, CT, turn)

            @block.scalar
            def _(act):
                def turn(i):
                    for h in range(2):
                        cut = slice(h * HALF, (h + 1) * HALF)
                        weights.done(act, i, 0)
                        wait(act, ended, i * 2 + h)
                        act.copy(u_b[:, 2:HALF + 2], c.ps[:, h]).then_inc(copied, 1)
                        act.wait_ge(made, i * 2 + (h + 1))
                        apart(c, act)
                        act.copy(c.br_hi[:, bass.ds(i + CT, 1), cut].rearrange("p a n -> p (a n)"), y_b[:]).then_inc(rounded, 1)

                rolled(act, CT, turn)

            @block.vector
            def _(dve):
                v = c.v_steps

                def turn(i):
                    v.mark(dve.memset(u_b[:, 0:2], 0.0))
                    for h in range(2):
                        cut = slice(h * HALF, (h + 1) * HALF)
                        weights.done(dve, i, 1)
                        dve.wait_ge(copied, i * 2 + (h + 1))
                        v.wait(dve)
                        dve.tensor_tensor(u_b[:, 2:HALF + 2], u_b[:, 2:HALF + 2], c.ps[:, 2 + h], ALU.mult).then_inc(product, 1)
                        dve.wait_ge(product, i * 2 + (h + 1))
                        wait(dve, split, i * 2 + h)
                        v.mark(dve.tensor_scalar(y_b[:], u_b[:, 2:HALF + 2], vec(c, "conv_w", i + 2 * CT), None, ALU.mult))
                        for tap in (1, 0):
                            v.wait(dve)
                            v.mark(dve.scalar_tensor_tensor(out=y_b[:], in0=u_b[:, tap:HALF + tap],
                                                            scalar=vec(c, "conv_w", i + tap * CT), in1=y_b[:],
                                                            op0=ALU.mult, op1=ALU.add))
                        v.wait(dve)
                        v.mark(dve.tensor_copy(u_b[:, 0:2], u_b[:, HALF:HALF + 2]))
                        v.wait(dve)
                        dve.sem_inc(ended, 1)
                        weights.done(dve, i, 2)
                        dve.tensor_tensor(y_b[:], y_b[:], c.ps[:, 4 + h], ALU.mult).then_inc(made, 1)
                        dve.wait_ge(rounded, i * 2 + (h + 1))
                        dve.tensor_tensor(c.br_lo[:, bass.ds(i + CT, 1), cut].rearrange("p a n -> p (a n)"), y_b[:],
                                          c.br_hi[:, bass.ds(i + CT, 1), cut].rearrange("p a n -> p (a n)").bitcast(F32),
                                          ALU.subtract).then_inc(split, 1)

                rolled(dve, CT, turn, v)

    return weights, build


def merge_branches(c, name, w_in, first, w_a, w_b, bias):
    nc = c.nc
    gates, top, low = tile_of(w_in, first), w_a.rearrange("(k p) n -> p k n", p=P), w_b.rearrange("(k p) n -> p k n", p=P)
    out = scratch(c, f"{name}_merged", [KT, P, SEQ])
    weights = Weights(c, [lambda i: gates(i, 1, 0), lambda i: gates(i, 1, KT),
                          lambda i: (top[:, :, columns(i, P)], low[:, :, columns(i, P)])], KT)
    sig = at(c, 65536, f"{name}_sig", [P, 2, HALF])
    gated, scaled, made, stored = (c.sem(f"{name}_{n}") for n in ("gated", "scaled", "made", "stored"))

    def build():
        weights.begin()
        with nc.Block() as block:

            @block.sync
            def _(sp):
                def turn(i):
                    for u in range(3):
                        sp.wait_ge(c.w_split, weights.t0 + i * 3 + (u + 1))
                        apart(c, sp)
                        weights.fetch(sp, u, i + 1)
                    store(i)

                def store(i):
                    for h in range(2):
                        sp.wait_ge(made, i * 2 + (h + 1))
                        apart(c, sp)
                        view = out[bass.ds(i, 1), :, h * HALF:(h + 1) * HALF].rearrange("a p n -> p (a n)")
                        sp.dma_start(view, sig[:, 0]).then_inc(stored, 16)

                rolled(sp, KT - 1, turn)
                store(KT - 1)
                sp.wait_ge(stored, 16 * 2 * KT)

            @block.gpsimd
            def _(pool):
                weights.split(pool)

            @block.tensor
            def _(pe):
                def turn(i):
                    for u in range(2):
                        weights.ready(pe, i, u)
                        wait(pe, gated, i * 4 + (u - 1))
                        weights.multiply(pe, u, [c.ps[:, 2 * u], c.ps[:, 2 * u + 1]], c.h_hi, c.h_lo).then_inc(c.tile_done, 1)
                    weights.ready(pe, i, 2)
                    wait(pe, scaled, i * 4)
                    weights.multiply(pe, 2, [c.ps[:, 4], c.ps[:, 5]], c.br_hi, c.br_lo, kts=range(KT // 2))
                    weights.multiply(pe, 2, [c.ps[:, 6], c.ps[:, 7]], c.br_hi, c.br_lo,
                                     kts=range(KT // 2, KT)).then_inc(c.tile_done, 1)

                rolled(pe, KT, turn)

            @block.scalar
            def _(act):
                def turn(i):
                    for h in range(2):
                        for g in range(2):
                            weights.done(act, i, g)
                            if g == 0:
                                wait(act, stored, i * 32 + 16 * h)
                            else:
                                wait(act, made, i * 2 + h)
                            apart(c, act)
                            act.activation(sig[:, g], c.ps[:, 2 * g + h], ACT.Sigmoid,
                                           bias=vec(c, bias, i + g * KT)).then_inc(gated, 1)

                rolled(act, KT, turn)

            @block.vector
            def _(dve):
                def turn(i):
                    for h in range(2):
                        for g in range(2):
                            weights.done(dve, i, 2)
                            dve.wait_ge(gated, i * 4 + (2 * h + g + 1))
                            dve.tensor_tensor(sig[:, g], sig[:, g], c.ps[:, 4 + 2 * g + h], ALU.mult).then_inc(scaled, 1)
                        dve.wait_ge(scaled, i * 4 + (2 * h + 2))
                        dve.tensor_tensor(sig[:, 0], sig[:, 0], sig[:, 1], ALU.add).then_inc(made, 1)

                rolled(dve, KT, turn)

    return weights, build


def take_back(c, name, following):
    nc = c.nc
    whole = at(c, 0, f"{name}_whole", [P, KT, SEQ])
    src = c.scratch[f"{name}_merged"]
    loaded = [c.sem(f"{name}_in{k}") for k in range(2)]
    rounded = c.sem(f"{name}_rounded")
    with nc.Block() as block:

        @block.sync
        def _(sp):
            for k in range(2):
                sp.dma_start(whole[:, 4 * k:4 * k + 4], src[4 * k:4 * k + 4].rearrange("k p n -> p k n")).then_inc(loaded[k], 16)
            following.load_first(sp)

        @block.scalar
        def _(act):
            for k in range(KT):
                act.wait_ge(loaded[k // 4], 16)
                act.copy(c.h_hi[:, k], whole[:, k]).then_inc(rounded, 1)

        @block.vector
        def _(dve):
            for k in range(KT):
                dve.wait_ge(rounded, k + 1)
                dve.tensor_tensor(c.h_lo[:, k], whole[:, k], c.h_hi[:, k].bitcast(F32), ALU.subtract)


def residual_weights(c, w):
    tile = tile_of(w)
    return Weights(c, [lambda i, u=u: tile(i, 2, u) for u in range(2)], KT // 2)


N_XHEADS = 4
XD = D // N_XHEADS


def memory_keys(c):
    nc, d = c.nc, c.dram
    tile = tile_of(d["w_kv"][0])
    keys = Weights(c, [lambda i, u=u: tile(i, 2, u) for u in range(2)], KT // 2)
    values = Weights(c, [lambda i, u=u: tile(i, 2, KT + u) for u in range(2)], KT // 2)
    mem_hi = at(c, 0, "mem_hi", [P, KT, N_MEM], F32R)
    mem_lo = at(c, 8192, "mem_lo", [P, KT, N_MEM], F32R)
    k_all = at(c, 24576, "k_all", [P, KT, N_MEM])
    v_all = at(c, 32768, "v_all", [P, 2, D])
    scratch(c, "mem_k", [KT, P, N_MEM])
    scratch(c, "mem_v", [2, P, D])
    copied, stored = [c.sem("mem_copied0"), c.sem("mem_copied1")], c.sem("mem_stored")
    rms_norm(c, "norm_mem", c.mem_t, "norm_mem", N_MEM, mem_hi, mem_lo, following=keys)

    def build(following):
        for w in (keys, values):
            w.begin()
        with nc.Block() as block:

            @block.sync
            def _(sp):
                keys.load_rest(sp)
                values.load_all(sp)
                sp.wait_ge(c.w_split, c.tiles)
                following.load_first(sp)
                for s in range(2):
                    sp.wait_ge(copied[s], KT)
                sp.dma_start(c.scratch["mem_k"].rearrange("k p n -> p k n"), k_all[:]).then_inc(stored, 16)
                sp.dma_start(c.scratch["mem_v"].rearrange("m p n -> p m n"), v_all[:]).then_inc(stored, 16)
                sp.wait_ge(stored, 32)

            @block.scalar
            def _(act):
                keys.round_on(act)
                values.round_on(act)

            @block.gpsimd
            def _(pool):
                keys.subtract(pool)
                values.subtract(pool)

            @block.tensor
            def _(pe):
                def key_turn(i):
                    for u in range(2):
                        keys.ready(pe, i, u)
                        wait(pe, copied[u], i)
                        keys.multiply(pe, u, [c.ps[:, u, 0:N_MEM]], mem_hi, mem_lo, width=N_MEM).then_inc(c.tile_done, 1)

                def value_turn(i):
                    for u in range(2):
                        values.ready(pe, i, u)
                        pe.wait_ge(copied[u], i + KT // 2)
                        for m in range(2):
                            rows = slice(m * P, (m + 1) * P)
                            for k in range(KT):
                                for a, w in ((mem_hi, c.w_hi), (mem_lo, c.w_hi), (mem_hi, c.w_lo)):
                                    last = pe.matmul(c.ps[:, u, rows], a[:, k, rows], w[:, u, k],
                                                     start=(k == 0 and w is c.w_hi and a is mem_hi),
                                                     stop=(k == KT - 1 and w is c.w_lo))
                        last.then_inc(c.tile_done, 1)

                rolled(pe, KT // 2, key_turn)
                rolled(pe, KT // 2, value_turn)

            @block.vector
            def _(dve):
                def key_turn(i):
                    for u in range(2):
                        keys.done(dve, i, u)
                        apart(c, dve)
                        dve.tensor_copy(k_all[:, bass.ds(i * 2 + u, 1), :].rearrange("p a n -> p (a n)"),
                                        c.ps[:, u, 0:N_MEM]).then_inc(copied[u], 1)

                def value_turn(i):
                    for u in range(2):
                        values.done(dve, i, u)
                        apart(c, dve)
                        dve.tensor_copy(v_all[:, :, bass.ds(i * (2 * P) + u * P, P)],
                                        c.ps[:, u, 0:N_MEM].rearrange("p (m n) -> p m n", n=P)).then_inc(copied[u], 1)

                rolled(dve, KT // 2, key_turn)
                rolled(dve, KT // 2, value_turn)

    return build


def queries(c):
    nc = c.nc
    weights = residual_weights(c, c.dram["w_q"][0])
    out = scratch(c, "queries", [KT, P, SEQ])
    q_b = at(c, 0, "q_tile", [P, 2, SEQ])
    copied = [c.sem("q_copied0"), c.sem("q_copied1")]
    stored = [c.sem("q_stored0"), c.sem("q_stored1")]

    def build():
        weights.begin()
        with nc.Block() as block:

            @block.sync
            def _(sp):
                def store(i):
                    for u in range(2):
                        sp.wait_ge(copied[u], i + 1)
                        apart(c, sp)
                        sp.dma_start(out[bass.ds(i * 2 + u, 1)].rearrange("a p n -> p (a n)"), q_b[:, u]).then_inc(stored[u], 16)

                def turn(i):
                    for u in range(2):
                        sp.wait_ge(c.w_split, weights.t0 + i * 2 + (u + 1))
                        apart(c, sp)
                        weights.fetch(sp, u, i + 1)
                    store(i)

                rolled(sp, KT // 2 - 1, turn)
                store(KT // 2 - 1)
                for u in range(2):
                    sp.wait_ge(stored[u], 16 * KT // 2)

            @block.gpsimd
            def _(pool):
                weights.split(pool)

            @block.tensor
            def _(pe):
                def turn(i):
                    for u in range(2):
                        weights.ready(pe, i, u)
                        wait(pe, copied[u], i)
                        weights.multiply(pe, u, [c.ps[:, 2 * u], c.ps[:, 2 * u + 1]], c.h_hi, c.h_lo).then_inc(c.tile_done, 1)

                rolled(pe, KT // 2, turn)

            @block.scalar
            def _(act):
                def turn(i):
                    for u in range(2):
                        weights.done(act, i, u)
                        wait(act, stored[u], i * 16)
                        act.activation(q_b[:, u], c.ps[:, 2 * u:2 * u + 2].rearrange("p b n -> p (b n)"), ACT.Copy,
                                       scale=XD ** -0.5).then_inc(copied[u], 1)

                rolled(act, KT // 2, turn)

    return weights, build


def attention(c, following):
    nc = c.nc
    q_in = at(c, 0, "xa_q", [P, 2, 2, SEQ])
    k_in = at(c, 16384, "xa_k", [P, 2, 2, N_MEM])
    v_in = at(c, 20480, "xa_v", [P, 2, 2, XD])
    prob = at(c, 24576, "xa_prob", [P, 2, N_MEM])
    p_t = at(c, 26624, "xa_prob_t", [P, 2, 2, HALF])
    top = at(c, 34816, "xa_top", [P, 2])
    neg = at(c, 34848, "xa_neg", [P, 2])
    total = at(c, 34880, "xa_total", [P, 2])
    loaded = [c.sem("xa_loaded0"), c.sem("xa_loaded1")]
    scored, turned, summed = c.sem("xa_scored"), c.sem("xa_turned"), c.sem("xa_summed")
    exps, copied, rounded = c.sem("xa_exps"), c.sem("xa_copied"), c.sem("xa_rounded")
    tops, normed, split = c.sem("xa_tops"), c.sem("xa_normed"), c.sem("xa_split")
    ps = c.ps
    q_src, k_src, v_src = c.scratch["queries"], c.scratch["mem_k"], c.scratch["mem_v"]

    with nc.Block() as block:

        @block.sync
        def _(sp):
            following.load_first(sp)

            def turn(j):
                for s in range(2):
                    hd = j * 2 + s
                    wait(sp, summed, 2 * (hd - 1) if not first(j) else 0)
                    apart(c, sp)
                    sp.dma_start(q_in[:, s], q_src[bass.ds(hd * 2, 2)].rearrange("k p n -> p k n")).then_inc(loaded[s], 16)
                    sp.dma_start(k_in[:, s], k_src[bass.ds(hd * 2, 2)].rearrange("k p n -> p k n")).then_inc(loaded[s], 16)
                    sp.dma_start(v_in[:, s], v_src[:, :, columns(hd, XD)].rearrange("m p n -> p m n")).then_inc(loaded[s], 16)

            rolled(sp, 2, turn)

        @block.tensor
        def _(pe):
            def turn(j):
                for s in range(2):
                    hd = j * 2 + s
                    pe.wait_ge(loaded[s], j * 48 + 48)

                    def score(t):
                        wait(pe, exps, hd * 8 + (t - 1))
                        for k in range(2):
                            last = pe.matmul(ps[:, t % 2, 0:N_MEM], q_in[:, s, k, t * P:(t + 1) * P], k_in[:, s, k],
                                             start=k == 0, stop=k == 1)
                        last.then_inc(scored, 1)

                    score(0)
                    for t in range(TILES):
                        if t + 1 < TILES:
                            score(t + 1)
                        pe.wait_ge(normed, hd * 8 + (t + 1))
                        wait(pe, copied, hd * 8 + (t - 1))
                        for m in range(2):
                            last = pe.transpose(ps[:, 2 + t % 2, m * P:(m + 1) * P], prob[:, t % 2, m * P:(m + 1) * P],
                                                c.ident[:])
                        last.then_inc(turned, 1)
                        if t % 4 == 3:
                            h = t // 4
                            pe.wait_ge(copied, hd * 8 + (t + 1))
                            wait(pe, split, hd * 4 + (2 * h - 2))
                            for e in range(2):
                                for m in range(2):
                                    last = pe.matmul(ps[:, 4 + 2 * h + e], v_in[:, s, m, e * P:(e + 1) * P], p_t[:, h, m],
                                                     start=m == 0, stop=m == 1)
                            last.then_inc(summed, 1)

            rolled(pe, 2, turn)

        @block.scalar
        def _(act):
            def turn(j):
                for s in range(2):
                    hd = j * 2 + s

                    def exp(t):
                        act.wait_ge(tops, hd * 16 + (2 * t + 2))
                        wait(act, turned, hd * 8 + (t - 1))
                        act.activation(prob[:, t % 2], ps[:, t % 2, 0:N_MEM], ACT.Exp, bias=neg[:, t % 2:t % 2 + 1],
                                       accum_out=total[:, t % 2:t % 2 + 1]).then_inc(exps, 1)

                    exp(0)
                    for t in range(TILES):
                        if t + 1 < TILES:
                            exp(t + 1)
                        act.wait_ge(turned, hd * 8 + (t + 1))
                        wait(act, summed, hd * 2 + (t // 4 - 1))
                        act.copy(p_t[:, t // 4, :, (t % 4) * P:(t % 4 + 1) * P],
                                 ps[:, 2 + t % 2, 0:2 * P].rearrange("p (m n) -> p m n", n=P)).then_inc(copied, 1)
                        if t % 4 == 3:
                            h = t // 4
                            act.wait_ge(summed, hd * 2 + (h + 1))
                            apart(c, act)
                            for e in range(2):
                                act.copy(c.h_hi[:, bass.ds(hd * 2 + e, 1), h * HALF:(h + 1) * HALF]
                                         .rearrange("p a n -> p (a n)"), ps[:, 4 + 2 * h + e]).then_inc(rounded, 1)

            rolled(act, 2, turn)

        @block.vector
        def _(dve):
            v = c.v_steps

            def turn(j):
                for s in range(2):
                    hd = j * 2 + s

                    def peak(t):
                        one = slice(t % 2, t % 2 + 1)
                        dve.wait_ge(scored, hd * 8 + (t + 1))
                        dve.tensor_reduce(top[:, one], ps[:, t % 2, 0:N_MEM], AX_X, ALU.max).then_inc(tops, 1)
                        dve.wait_ge(tops, hd * 16 + (2 * t + 1))
                        dve.tensor_scalar(neg[:, one], top[:, one], -1.0, None, ALU.mult).then_inc(tops, 1)

                    peak(0)
                    for t in range(TILES):
                        if t + 1 < TILES:
                            peak(t + 1)
                        one = slice(t % 2, t % 2 + 1)
                        dve.wait_ge(exps, hd * 8 + (t + 1))
                        v.mark(dve.reciprocal(total[:, one], total[:, one]))
                        v.wait(dve)
                        dve.tensor_scalar(prob[:, t % 2], prob[:, t % 2], total[:, one], None, ALU.mult).then_inc(normed, 1)
                        if t % 4 == 3:
                            h = t // 4
                            for e in range(2):
                                cut = (slice(None), bass.ds(hd * 2 + e, 1), slice(h * HALF, (h + 1) * HALF))
                                dve.wait_ge(rounded, hd * 4 + (2 * h + e + 1))
                                dve.tensor_tensor(c.h_lo[cut].rearrange("p a n -> p (a n)"), ps[:, 4 + 2 * h + e],
                                                  c.h_hi[cut].rearrange("p a n -> p (a n)").bitcast(F32),
                                                  ALU.subtract).then_inc(split, 1)

            rolled(dve, 2, turn, v)


DN_HEADS = 4
SB_HEAD = 64
BETA_COLUMN = 4 * D_RWKV
SB_COLUMN = BETA_COLUMN + 2 * DN_HEADS
GATE_COLUMN_2 = SB_COLUMN + 4 * D_RWKV


def second_projections(c):
    nc, d = c.nc, c.dram
    w = d["w_in_2"][0]
    kinds = ["q", "z", "k", "v", "sq", "sv", "sk", "zb"]
    at_column = dict(q=0, k=D_RWKV, v=2 * D_RWKV, z=3 * D_RWKV, sq=SB_COLUMN, sk=SB_COLUMN + D_RWKV,
                     sv=SB_COLUMN + 2 * D_RWKV, zb=SB_COLUMN + 3 * D_RWKV)
    conv_row = dict(q=0, k=CT, v=2 * CT)
    out = {n: scratch(c, f"second_{n}", [CT, P, SEQ]) for n in kinds}
    rows_out = {n: scratch(c, f"second_{n}", [2 * DN_HEADS, SEQ]) for n in ("beta", "decay")}
    weights = Weights(c, [tile_of(w, at_column[n]) for n in kinds], CT)
    raw = at(c, 0, "p2_raw", [P, 2, SEQ + 8])
    y = at(c, 8256, "p2_y", [P, 4, SEQ])
    sig = at(c, 24640, "p2_sig", [P, SEQ])
    sq = at(c, 28736, "p2_sq", [P, SEQ])
    root = at(c, 32832, "p2_root", [P, SEQ])
    n_rows = 2 * DN_HEADS
    beta, pre, soft, cum, keep = (at(c, 36928 + 4096 * n, f"p2_{name}", [n_rows, SEQ])
                                  for n, name in enumerate(("beta", "pre", "soft", "cum", "keep")))
    few = at(c, 57408, "p2_few", [P, KT, n_rows])
    few_hi = at(c, 57664, "p2_few_hi", [P, KT, n_rows], F32R)
    few_lo = at(c, 57920, "p2_few_lo", [P, KT, n_rows], F32R)
    params = at(c, 58176, "p2_params", [n_rows, 4])
    cols = at(c, 58208, "p2_cols", [P, TILES, 2, n_rows])
    ACT_EVENTS = ["q_copy", "z_copy", "q_root", "z_sig", "k_copy", "v_copy", "k_root", "sq_copy", "sv_copy", "sq_root",
                  "sk_copy", "zb_copy", "sk_root", "zb_sig"]
    few_loaded, prepared, few_split = c.sem("p2_few_loaded"), c.sem("p2_prepared"), c.sem("p2_few_split")
    rows_made, turned, cols_made = c.sem("p2_rows"), c.sem("p2_turned"), c.sem("p2_cols_made")
    few_done = c.sem("p2_few_done")
    copied, sigmoid, squared, summed, rooted = (c.sem(f"p2_{n}") for n in ("copied", "sigmoid", "squared", "summed", "rooted"))
    tapped, gated, normed, plain = (c.sem(f"p2_{n}") for n in ("tapped", "gated", "normed", "plain"))
    stored = [c.sem(f"p2_stored{s}") for s in range(4)]
    rows_stored = c.sem("p2_rows_stored")
    CONV, NORM, SILU = ["q", "k", "v"], ["q", "k", "sq", "sk"], ["q", "z", "k", "v", "zb"]
    gain = dict(sq="sb_q_gain_2", sk="sb_k_gain_2")

    def finished(eng, n, i):
        if n in NORM:
            eng.wait_ge(normed, nth(NORM, n, i))
        elif n in SILU:
            eng.wait_ge(gated, nth(SILU, n, i))
        else:
            eng.wait_ge(plain, i + 1)

    def build():
        weights.begin()
        with nc.Block() as block:

            @block.sync
            def _(sp):
                sp.dma_start(few[:], w.rearrange("(k p) n -> p k n", p=P)[:, :, BETA_COLUMN:SB_COLUMN]).then_inc(few_loaded, 16)
                sp.wait_ge(prepared, 1)
                for k, name in enumerate(("dt_bias_2", "a_log_2")):
                    sp.dma_start(params[DN_HEADS:n_rows, k:k + 1], d[name].rearrange("a n -> n a")).then_inc(few_loaded, 16)

                def store(u, i):
                    finished(sp, kinds[u], i)
                    apart(c, sp)
                    sp.dma_start(out[kinds[u]][bass.ds(i, 1)].rearrange("a p n -> p (a n)"), y[:, u % 4]).then_inc(stored[u % 4], 16)

                def fetch(u, i):
                    v = u + 2
                    sp.wait_ge(c.w_split, weights.t0 + i * len(kinds) + (u + 1))
                    apart(c, sp)
                    weights.fetch(sp, v % len(kinds), i + v // len(kinds))

                def turn(i):
                    for u in range(len(kinds)):
                        fetch(u, i)
                        if u >= 2:
                            store(u - 2, i)
                    for u in (6, 7):
                        store(u, i)

                rolled(sp, CT - 1, turn)
                for u in range(len(kinds)):
                    if u < 6:
                        fetch(u, CT - 1)
                    if u >= 2:
                        store(u - 2, CT - 1)
                for u in (6, 7):
                    store(u, CT - 1)
                sp.wait_ge(rows_made, 9)
                for n, src in (("beta", beta), ("decay", cum)):
                    sp.dma_start(rows_out[n], src[:]).then_inc(rows_stored, 16)
                for s in range(4):
                    sp.wait_ge(stored[s], 16 * 2 * CT)
                sp.wait_ge(rows_stored, 32)

            @block.gpsimd
            def _(pool):
                pool.memset(params[:], 0.0).then_inc(prepared, 1)
                pool.memset(keep[:], 1.0).then_inc(prepared, 1)
                pool.wait_ge(prepared, 2)
                pool.memset(keep[:].rearrange("p (t n) -> p t n", n=P)[:, :, 0:1], 0.0).then_inc(prepared, 1)
                pool.memset(raw[:, :, 0:8], 0.0).then_inc(prepared, 1)
                weights.split(pool)

            @block.tensor
            def _(pe):
                pe.wait_ge(few_split, 2)
                for k in range(KT):
                    for wt, a in ((few_hi, c.h_hi), (few_hi, c.h_lo), (few_lo, c.h_hi)):
                        for h in range(2):
                            last = pe.matmul(c.ps[0:n_rows, 6 + h], wt[:, k], a[:, k, h * HALF:(h + 1) * HALF],
                                             start=(k == 0 and wt is few_hi and a is c.h_hi),
                                             stop=(k == KT - 1 and wt is few_lo))
                last.then_inc(few_done, 1)

                def sums(n, i):
                    ones = c.ones if n in CONV else c.ones_64
                    pe.wait_ge(squared, nth(NORM, n, i))
                    wait(pe, rooted, nth(NORM, n, i) - 1)
                    for h in range(2):
                        last = pe.matmul(c.ps[:, 4 + h], ones[:], sq[:, h * HALF:(h + 1) * HALF], start=True, stop=True)
                    last.then_inc(summed, 1)

                def turn(i):
                    for u, n in enumerate(kinds):
                        weights.ready(pe, i, u)
                        wait(pe, copied, i * len(kinds) + (u - 1))
                        s = u % 2
                        weights.multiply(pe, u, [c.ps[:, 2 * s], c.ps[:, 2 * s + 1]], c.h_hi, c.h_lo).then_inc(c.tile_done, 1)
                        if u and kinds[u - 1] in NORM:
                            sums(kinds[u - 1], i)

                rolled(pe, CT, turn)
                pe.wait_ge(rows_made, 9)
                for t in range(TILES):
                    for b, src in enumerate((beta, cum)):
                        last = pe.transpose(c.ps[:, 6, (2 * t + b) * n_rows:(2 * t + b + 1) * n_rows],
                                            src[:, t * P:(t + 1) * P], c.ident[0:n_rows, 0:n_rows])
                last.then_inc(turned, 1)

            @block.scalar
            def _(act):
                act.wait_ge(few_loaded, 48)
                act.copy(few_hi[:], few[:]).then_inc(few_split, 1)
                act.activation(params[:, 2:3], params[:, 1:2], ACT.Exp).then_inc(rows_made, 1)
                act.wait_ge(few_done, 1)
                act.activation(beta[:], c.ps[0:n_rows, 6:8].rearrange("p b n -> p (b n)"), ACT.Sigmoid).then_inc(rows_made, 1)
                act.wait_ge(rows_made, 3)
                act.activation(soft[:], pre[:], ACT.Abs).then_inc(rows_made, 1)
                act.wait_ge(rows_made, 4)
                act.activation(soft[:], soft[:], ACT.Exp, scale=-1.0).then_inc(rows_made, 1)
                act.wait_ge(rows_made, 5)
                act.activation(soft[:], soft[:], ACT.Ln, bias=c.eps[0:n_rows, 2:3]).then_inc(rows_made, 1)
                act.wait_ge(prepared, 4)

                def turn(i):
                    for u, n in enumerate(kinds):
                        ps = c.ps[:, 2 * (u % 2):2 * (u % 2) + 2].rearrange("p b n -> p (b n)")
                        weights.done(act, i, u)
                        if n == "sv":
                            wait(act, stored[u % 4], i * 32 + (u // 4) * 16)
                            act.copy(y[:, u % 4], ps).then_inc(plain, 1)
                            act.wait_ge(plain, i + 1)
                            act.sem_inc(copied, 1)
                        else:
                            if u >= 2:
                                finished(act, kinds[u - 2], i)
                            elif not first(i):
                                finished(act, kinds[u + 6], i - 1)
                            act.copy(raw[:, u % 2, 8:SEQ + 8], ps).then_inc(copied, 1)
                        if u and kinds[u - 1] in NORM:
                            m = kinds[u - 1]
                            act.wait_ge(summed, nth(NORM, m, i))
                            wait(act, normed, nth(NORM, m, i) - 1)
                            act.activation(root[:], c.ps[:, 4:6].rearrange("p b n -> p (b n)"), ACT.Sqrt,
                                           bias=c.eps[:, 4:5] if m == "sq" else c.eps[:, 0:1],
                                           scale=1.0 / SB_HEAD if m == "sk" else 1.0).then_inc(rooted, 1)
                        if n in SILU:
                            wait(act, gated, nth(SILU, n, i) - 1)
                            if n in CONV:
                                act.wait_ge(tapped, nth(CONV, n, i))
                                act.activation(sig[:], y[:, u % 4], ACT.Sigmoid).then_inc(sigmoid, 1)
                            else:
                                act.wait_ge(copied, i * len(kinds) + (u + 1))
                                act.activation(sig[:], raw[:, u % 2, 8:SEQ + 8], ACT.Sigmoid).then_inc(sigmoid, 1)
                        if n in NORM:
                            wait(act, summed, nth(NORM, n, i) - 1)
                            if n in CONV:
                                act.wait_ge(gated, nth(SILU, n, i))
                                src = y[:, u % 4]
                            else:
                                act.wait_ge(copied, i * len(kinds) + (u + 1))
                                src = raw[:, u % 2, 8:SEQ + 8]
                            act.activation(sq[:], src, ACT.Square).then_inc(squared, 1)

                rolled(act, CT, turn)
                act.wait_ge(turned, 1)
                act.copy(cols[:].rearrange("p t b n -> p (t b n)"), c.ps[:, 6, 0:TILES * 2 * n_rows]).then_inc(cols_made, 1)
                act.wait_ge(cols_made, 1)
                act.activation(c.beta_decay[:], cols[:, :, 1, DN_HEADS:n_rows], ACT.Exp).then_inc(cols_made, 1)

            @block.vector
            def _(dve):
                v = c.v_steps
                dve.wait_ge(few_split, 1)
                dve.tensor_tensor(few_lo[:], few[:], few_hi[:].bitcast(F32), ALU.subtract).then_inc(few_split, 1)
                dve.wait_ge(few_done, 1)
                dve.wait_ge(rows_made, 2)
                dve.tensor_scalar(pre[:], c.ps[0:n_rows, 6:8].rearrange("p b n -> p (b n)"), params[:, 0:1], None,
                                  ALU.add).then_inc(rows_made, 1)
                dve.wait_ge(rows_made, 6)
                dve.scalar_tensor_tensor(out=pre[:], in0=pre[:], scalar=0.0, in1=soft[:], op0=ALU.max,
                                         op1=ALU.add).then_inc(rows_made, 1)
                dve.wait_ge(rows_made, 7)
                dve.tensor_scalar(pre[:], pre[:], params[:, 2:3], -1.0, ALU.mult, ALU.mult).then_inc(rows_made, 1)
                dve.wait_ge(rows_made, 8)
                dve.wait_ge(prepared, 3)
                dve.tensor_tensor_scan(cum[:], keep[:], pre[:], 0.0, ALU.mult, ALU.add).then_inc(rows_made, 1)

                def turn(i):
                    for u, n in enumerate(kinds):
                        dst = y[:, u % 4]
                        if n != "sv":
                            wait(dve, stored[u % 4], i * 32 + (u // 4) * 16)
                        if n in CONV:
                            dve.wait_ge(copied, i * len(kinds) + (u + 1))
                            for tap in (3, 2, 1, 0):
                                scale = vec(c, "conv_w_2", i + (tap * 3 * CT + conv_row[n]))
                                src = raw[:, u % 2, 5 + tap:5 + tap + SEQ]
                                if tap == 3:
                                    ins = dve.tensor_scalar(dst, src, scale, None, ALU.mult)
                                else:
                                    v.wait(dve)
                                    ins = dve.scalar_tensor_tensor(out=dst, in0=src, scalar=scale, in1=dst,
                                                                   op0=ALU.mult, op1=ALU.add)
                                v.mark(ins)
                            v.wait(dve)
                            dve.sem_inc(tapped, 1)
                        if u and kinds[u - 1] in NORM:
                            m, p = kinds[u - 1], u - 1
                            dve.wait_ge(rooted, nth(NORM, m, i))
                            v.mark(dve.reciprocal(root[:], root[:]))
                            v.wait(dve)
                            o = y[:, p % 4]
                            if m in CONV:
                                dve.scalar_tensor_tensor(out=o, in0=o, scalar=P ** -0.5 if m == "q" else 1.0, in1=root[:],
                                                         op0=ALU.mult, op1=ALU.mult).then_inc(normed, 1)
                            else:
                                dve.scalar_tensor_tensor(out=o, in0=raw[:, p % 2, 8:SEQ + 8], scalar=vec(c, gain[m]),
                                                         in1=root[:], op0=ALU.mult, op1=ALU.mult).then_inc(normed, 1)
                        if n in SILU:
                            dve.wait_ge(sigmoid, nth(SILU, n, i))
                            src = dst if n in CONV else raw[:, u % 2, 8:SEQ + 8]
                            dve.tensor_tensor(dst, src, sig[:], ALU.mult).then_inc(gated, 1)

                rolled(dve, CT, turn, v)
                dve.wait_ge(cols_made, 2)
                v.mark(dve.tensor_copy(c.beta_col[:], cols[:, :, 0, 0:DN_HEADS]))
                v.mark(dve.tensor_copy(c.decay_col[:], cols[:, :, 1, DN_HEADS:n_rows]))
                v.mark(dve.scalar_tensor_tensor(out=c.beta_decay[:], in0=c.beta_decay[:], scalar=-1.0,
                                                in1=cols[:, :, 0, 0:DN_HEADS], op0=ALU.mult, op1=ALU.mult))
                v.wait(dve)

    return weights, build


def delta_rule(c):
    nc = c.nc
    base, w_off = 0, 0
    wide = [P, DN_HEADS, P]

    def buf(name):
        nonlocal base
        b = at(c, base, f"dn_{name}", wide)
        base += 4 * DN_HEADS * P
        return b

    def buf_w(name, shape):
        nonlocal w_off
        b = nc.alloc_sbuf_tensor_at(f"dn_{name}", shape, F32, offset=c.w_base + w_off)
        n = 4
        for m in shape[1:]:
            n *= m
        w_off += n
        return b

    groups = range(2)
    q_in, k_in, v_in, g_in, b_in = ([buf(f"{n}_in{g}") for g in groups] for n in ("q", "k", "v", "decay", "beta"))
    low, up, q_dec, a_t, q_k = ([buf(f"{n}{g}") for g in groups] for n in ("low", "up", "q_dec", "a_t", "q_k"))
    t, t_t, x = ([buf(f"{n}{g}") for g in groups] for n in ("t", "tt", "x"))
    v_beta, k_dec = ([buf(f"{n}{g}") for g in groups] for n in ("v_beta", "k_dec"))
    rest, v_new, o_b = ([buf_w(f"{n}{g}", wide) for g in groups] for n in ("rest", "v_new", "o"))
    state = buf_w("state", wide)
    c.level = buf_w("level", [P, LEVELS, P])
    ends = [buf_w(f"ends{g}", [P, 2, DN_HEADS]) for g in groups]
    assert w_off <= 24576 and c.aux_base + 32 + base <= 229376

    PE_EVENTS = ["kk", "qk", "k_nat", "v_nat"] + LEVEL_PE + ["ks", "v_new", "o", "s"]
    DVE_EVENTS = ["low_in", "up_in", "ends_in", "low_beta", "n", "qm", "qk", "up_beta", "up_mask", "n_t", "q_dec", "v_beta", "k_dec",
                  "t_block", "t0", "tt_block", "tt0"] + LEVEL_DVE + ["rest", "s_new"]
    ACT_EVENTS = ["low", "up", "grown", "end", "to_end", "v_new", "o"]
    loaded, stored = ([c.sem(f"dn_{n}{g}") for g in groups] for n in ("loaded", "stored"))
    products, masks, acts = ([c.sem(f"dn_{n}{g}") for g in groups] for n in ("products", "masks", "acts"))
    cleared = c.sem("dn_cleared")
    src = {n: c.scratch[f"second_{n}"].rearrange("h p n -> p h n") for n in "qkv"}
    row_src = {n: c.scratch[f"second_{n}"] for n in ("decay", "beta")}
    out = scratch(c, "second_oa", [CT, P, SEQ])
    ps = c.ps
    level_banks = [(ps[:, g], ps[:, 2 + g], ps[:, 4 + g]) for g in groups]
    turns = TILES // 2

    def over(m):
        return m.unsqueeze(1).broadcast_to(wide)

    with nc.Block() as block:

        @block.sync
        def _(sp):
            def load(j, g):
                cut = columns(j * 2 + g, P)
                for n, dst in (("q", q_in), ("k", k_in), ("v", v_in)):
                    sp.dma_start(dst[g][:], src[n][:, :, cut]).then_inc(loaded[g], 16)
                for n, dst, r in (("decay", g_in, DN_HEADS), ("beta", b_in, 0)):
                    rows = row_src[n][r:r + DN_HEADS, cut]
                    sp.dma_start(dst[g][:], rows.unsqueeze(0).broadcast_to(wide)).then_inc(loaded[g], 16)

            def store(j, g):
                sp.wait_ge(acts[g], nth(ACT_EVENTS, "o", j))
                apart(c, sp)
                sp.dma_start(out.rearrange("h p n -> p h n")[:, :, columns(j * 2 + g, P)], o_b[g][:]).then_inc(stored[g], 16)

            def turn(j):
                for g in groups:
                    sp.wait_ge(products[g], nth(PE_EVENTS, "ks", j))
                    apart(c, sp)
                    load(j + 1, g)
                    store(j, g)

            for g in groups:
                load(0, g)
            rolled(sp, turns - 1, turn)
            for g in groups:
                store(turns - 1, g)
            for g in groups:
                sp.wait_ge(stored[g], 16 * turns)

        @block.gpsimd
        def _(pool):
            make_levels(c, pool)
            pool.memset(state[:], 0.0).then_inc(cleared, 1)

        @block.tensor
        def _(pe):
            def four(out, lhs, rhs, start=True, stop=True):
                for h in range(DN_HEADS):
                    last = pe.matmul(out[:, h * P:(h + 1) * P], lhs[:, h], rhs[:, h], start=start and h == 0, stop=stop,
                                     skip_group_check=True)
                return last

            def turn(j):
                for g in groups:
                    pe.wait_ge(loaded[g], j * 80 + 80)
                    wait(pe, masks[g], nth(DVE_EVENTS, "s_new", j - 1))
                    wait(pe, acts[g], nth(ACT_EVENTS, "o", j - 1))
                    four(ps[:, 6 + g], k_in[g], k_in[g]).then_inc(products[g], 1)
                    four(ps[:, 4 + g], k_in[g], q_in[g]).then_inc(products[g], 1)
                    for bank, part in ((g, k_in), (2 + g, v_in)):
                        for h in range(DN_HEADS):
                            last = pe.transpose(ps[:, bank, h * P:(h + 1) * P], part[g][:, h], c.ident[:])
                        last.then_inc(products[g], 1)
                for n in range(1, LEVELS):
                    for g in groups:
                        inverse_pe(pe, n, products[g], masks[g], j, PE_EVENTS, DVE_EVENTS, level_banks[g], a_t[g], t[g], t_t[g], x[g])
                    for g in groups:
                        inverse_pe_update(pe, n, products[g], masks[g], j, DVE_EVENTS, level_banks[g], t[g], t_t[g], x[g])
                for g in groups:
                    if g == 0:
                        pe.wait_ge(cleared, 1)
                        wait(pe, masks[1], nth(DVE_EVENTS, "s_new", j - 1))
                    else:
                        pe.wait_ge(masks[0], nth(DVE_EVENTS, "s_new", j))
                    four(ps[:, 6 + g], k_in[g], state).then_inc(products[g], 1)
                    pe.wait_ge(masks[g], nth(DVE_EVENTS, "rest", j))
                    four(ps[:, g], t_t[g], rest[g]).then_inc(products[g], 1)
                    four(ps[:, 2 + g], state, q_dec[g], stop=False)
                    pe.wait_ge(acts[g], nth(ACT_EVENTS, "v_new", j))
                    four(ps[:, 2 + g], v_new[g], q_k[g], start=False).then_inc(products[g], 1)
                    four(ps[:, 4 + g], k_dec[g], v_new[g]).then_inc(products[g], 1)

            rolled(pe, turns, turn)

        @block.scalar
        def _(act):
            def turn(j):
                for g in groups:
                    act.wait_ge(masks[g], nth(DVE_EVENTS, "low_in", j))
                    act.activation(low[g][:], low[g][:], ACT.Exp, scale=-1.0).then_inc(acts[g], 1)
                    act.wait_ge(masks[g], nth(DVE_EVENTS, "up_in", j))
                    act.activation(up[g][:], up[g][:], ACT.Exp).then_inc(acts[g], 1)
                    wait(act, products[g], nth(PE_EVENTS, "o", j - 1))
                    act.activation(q_dec[g][:], g_in[g][:], ACT.Exp).then_inc(acts[g], 1)
                    act.wait_ge(masks[g], nth(DVE_EVENTS, "ends_in", j))
                    act.activation(ends[g][:, 1], g_in[g][:, :, P - 1], ACT.Exp).then_inc(acts[g], 1)
                    act.activation(ends[g][:, 0], ends[g][:, 0], ACT.Exp).then_inc(acts[g], 1)
                for g in groups:
                    act.wait_ge(products[g], nth(PE_EVENTS, "v_new", j))
                    act.copy(v_new[g][:], heads_of(ps[:, g])).then_inc(acts[g], 1)
                    act.wait_ge(products[g], nth(PE_EVENTS, "o", j))
                    wait(act, stored[g], j * 16)
                    act.copy(o_b[g][:], heads_of(ps[:, 2 + g])).then_inc(acts[g], 1)

            rolled(act, turns, turn)

        @block.vector
        def _(dve):
            dve.wait_ge(cleared, 1)

            def turn(j):
                def col(buf, g, h):
                    return buf[:, bass.ds(j * 2 + g, 1), h:h + 1].rearrange("p a b -> p (a b)")

                def after(g, name):
                    dve.wait_ge(masks[g], nth(DVE_EVENTS, name, j))

                for g in groups:
                    dve.wait_ge(loaded[g], j * 80 + 80)
                    wait(dve, products[g], nth(PE_EVENTS, "s", j - 1))
                    wait(dve, masks[g], nth(DVE_EVENTS, "s_new", j - 1))
                    for buf, op, in ((low, ALU.max), (up, ALU.min)):
                        for h in range(DN_HEADS):
                            last = dve.tensor_scalar(buf[g][:, h], g_in[g][:, h], col(c.decay_col, g, h), 0.0, ALU.subtract, op)
                        last.then_inc(masks[g], 1)
                    dve.tensor_tensor(ends[g][:, 0], g_in[g][:, :, P - 1],
                                      c.decay_col[:, bass.ds(j * 2 + g, 1), :].rearrange("p a n -> p (a n)"),
                                      ALU.subtract).then_inc(masks[g], 1)
                for g in groups:
                    dve.wait_ge(acts[g], nth(ACT_EVENTS, "low", j))
                    for h in range(DN_HEADS):
                        last = dve.scalar_tensor_tensor(out=low[g][:, h], in0=low[g][:, h], scalar=col(c.beta_col, g, h),
                                                        in1=c.lower[:], op0=ALU.mult, op1=ALU.mult)
                    last.then_inc(masks[g], 1)
                    after(g, "low_beta")
                    dve.wait_ge(products[g], nth(PE_EVENTS, "kk", j))
                    dve.scalar_tensor_tensor(out=low[g][:], in0=heads_of(ps[:, 6 + g]), scalar=-1.0, in1=low[g][:],
                                             op0=ALU.mult, op1=ALU.mult).then_inc(masks[g], 1)
                    dve.wait_ge(acts[g], nth(ACT_EVENTS, "up", j))
                    dve.tensor_tensor(q_k[g][:], up[g][:], over(c.upper_eq[:]), ALU.mult).then_inc(masks[g], 1)
                    after(g, "qm")
                    dve.wait_ge(products[g], nth(PE_EVENTS, "qk", j))
                    dve.tensor_tensor(q_k[g][:], heads_of(ps[:, 4 + g]), q_k[g][:], ALU.mult).then_inc(masks[g], 1)
                    dve.scalar_tensor_tensor(out=a_t[g][:], in0=up[g][:], scalar=-1.0, in1=b_in[g][:],
                                             op0=ALU.mult, op1=ALU.mult).then_inc(masks[g], 1)
                    after(g, "up_beta")
                    dve.tensor_tensor(a_t[g][:], a_t[g][:], over(c.upper[:]), ALU.mult).then_inc(masks[g], 1)
                    after(g, "up_mask")
                    dve.tensor_tensor(a_t[g][:], heads_of(ps[:, 6 + g]), a_t[g][:], ALU.mult).then_inc(masks[g], 1)
                    dve.wait_ge(acts[g], nth(ACT_EVENTS, "grown", j))
                    dve.tensor_tensor(q_dec[g][:], q_in[g][:], q_dec[g][:], ALU.mult).then_inc(masks[g], 1)
                    dve.wait_ge(products[g], nth(PE_EVENTS, "v_nat", j))
                    beta = c.beta_col[:, bass.ds(j * 2 + g, 1), :].rearrange("p a n -> p (a n)")
                    dve.tensor_tensor(v_beta[g][:], heads_of(ps[:, 2 + g]), beta.unsqueeze(2).broadcast_to(wide),
                                      ALU.mult).then_inc(masks[g], 1)
                    dve.wait_ge(acts[g], nth(ACT_EVENTS, "to_end", j))
                    dve.tensor_tensor(k_dec[g][:], heads_of(ps[:, g]), ends[g][:, 0].unsqueeze(2).broadcast_to(wide),
                                      ALU.mult).then_inc(masks[g], 1)
                for g in groups:
                    inverse_start_dve(c, dve, masks[g], j, DVE_EVENTS, low[g], a_t[g], t[g], t_t[g])
                for n in range(1, LEVELS):
                    for g in groups:
                        inverse_mask_dve(c, dve, n, products[g], masks[g], j, PE_EVENTS, level_banks[g], x[g])
                    for g in groups:
                        inverse_add_dve(dve, n, products[g], masks[g], j, PE_EVENTS, level_banks[g], t[g], t_t[g])
                for g in groups:
                    dve.wait_ge(products[g], nth(PE_EVENTS, "ks", j))
                    for h in range(DN_HEADS):
                        last = dve.scalar_tensor_tensor(out=rest[g][:, h], in0=ps[:, 6 + g, h * P:(h + 1) * P],
                                                        scalar=col(c.beta_decay, g, h), in1=v_beta[g][:, h],
                                                        op0=ALU.mult, op1=ALU.add)
                    last.then_inc(masks[g], 1)
                    dve.wait_ge(products[g], nth(PE_EVENTS, "s", j))
                    for h in range(DN_HEADS):
                        last = dve.scalar_tensor_tensor(out=state[:, h], in0=state[:, h], scalar=ends[g][:, 1, h:h + 1],
                                                        in1=ps[:, 4 + g, h * P:(h + 1) * P], op0=ALU.mult, op1=ALU.add)
                    last.then_inc(masks[g], 1)

            rolled(dve, turns, turn)


def stick_breaking(c):
    nc = c.nc
    offset = 0

    def buf(name, shape):
        nonlocal offset
        b = at(c, offset, f"sb_{name}", shape)
        n = 4
        for m in shape[1:]:
            n *= m
        offset += n
        return b

    heads = range(2)
    q_in, k_in, v_in = (buf(f"{n}_in", [P, 2, SEQ]) for n in "qkv")
    v_nat = buf("v_nat", [P, 2, TILES, P])
    soft, over, later, a = (buf(n, [P, 2, 2, HALF]) for n in ("soft", "over", "later", "a"))
    o_b = buf("o", [P, 2, HALF])
    neg_tri = buf("neg_tri", [P, P])
    neg_ones = buf("neg_ones", [P, P])
    forbid = buf("forbid", [P, P])
    assert c.aux_base + 32 + offset <= 229376
    steps = [(h, kb, max(0, kb * P - h * HALF), kb // 4 == h) for h in range(2) for kb in range(4 * h + 3, -1, -1)]
    n_steps = len(steps)
    last_of = [max(n for n, st in enumerate(steps) if st[0] == h) for h in range(2)]
    firsts = [min(n for n, st in enumerate(steps) if st[0] == h) for h in range(2)]
    loaded = [c.sem("sb_loaded0"), c.sem("sb_loaded1")]
    made, scored, logs, summed = (c.sem(f"sb_{n}") for n in ("made", "scored", "logs", "summed"))
    turned, natural, chain, exps = (c.sem(f"sb_{n}") for n in ("turned", "natural", "chain", "exps"))
    softened, added, taken = (c.sem(f"sb_{n}") for n in ("softened", "added", "taken"))
    stored = [c.sem("sb_stored0"), c.sem("sb_stored1")]
    src = [c.scratch[f"second_{n}"] for n in ("sq", "sk", "sv")]
    out = scratch(c, "second_ob", [CT, P, SEQ])
    ps = c.ps

    with nc.Block() as block:

        @block.sync
        def _(sp):
            def load(j, s):
                for part, dst in zip(src, (q_in, k_in, v_in)):
                    sp.dma_start(dst[:, s], part[bass.ds(j * 2 + s, 1)].rearrange("a p n -> p (a n)")).then_inc(loaded[s], 16)

            def store(j, s):
                for h in range(2):
                    sp.wait_ge(taken, (j * 2 + s) * 2 + (h + 1))
                    apart(c, sp)
                    sp.dma_start(out[bass.ds(j * 2 + s, 1), :, h * HALF:(h + 1) * HALF].rearrange("a p n -> p (a n)"),
                                 o_b[:, h]).then_inc(stored[h], 16)

            for s in range(2):
                load(0, s)
            for s in range(2):
                store(0, s)
                load(1, s)
            for s in range(2):
                store(1, s)
            for h in range(2):
                sp.wait_ge(stored[h], 16 * CT)

        @block.gpsimd
        def _(pool):
            g = c.g_steps
            for buf_, value in ((neg_ones, -1.0), (neg_tri, -1.0), (forbid, -1e30)):
                g.mark(pool.memset(buf_[:], value))
            g.wait(pool)
            for buf_ in (neg_tri, forbid):
                g.mark(pool.affine_select(out=buf_[:], in_=buf_[:], compare_op=ALU.is_ge, fill=0.0, base=0,
                                          pattern=[[-1, P]], channel_multiplier=1))
            g.wait(pool)
            pool.sem_inc(made, 1)

        @block.tensor
        def _(pe):
            pe.wait_ge(made, 1)

            def turn(j):
                for s in range(2):
                    ct = j * 2 + s
                    at0 = ct * n_steps
                    pe.wait_ge(loaded[s], j * 48 + 48)
                    for h in range(2):
                        wait(pe, natural, ct * 2 + (h - 1))
                        for t in range(4):
                            last = pe.transpose(ps[:, 6 + h, t * P:(t + 1) * P], v_in[:, s, (4 * h + t) * P:(4 * h + t + 1) * P],
                                                c.ident[:])
                        last.then_inc(turned, 1)

                    def score(n):
                        h, kb, first_q, diagonal = steps[n]
                        wait(pe, exps, at0 + (n - 1))
                        for hd in heads:
                            rows = slice(SB_HEAD * hd, SB_HEAD * (hd + 1))
                            last = pe.matmul(ps[:, 2 * (n % 2) + hd, first_q:HALF], k_in[rows, s, kb * P:(kb + 1) * P],
                                             q_in[rows, s, h * HALF + first_q:(h + 1) * HALF], start=True, stop=False,
                                             skip_group_check=True)
                        last.then_inc(scored, 1)

                    def logarithm(n):
                        h, kb, first_q, diagonal = steps[n]
                        pe.wait_ge(softened, at0 + (n + 1))
                        begun = first_q + P if diagonal else 0
                        for hd in heads:
                            bank = ps[:, 2 * (n % 2) + hd]
                            last = pe.matmul(bank[:, first_q:HALF], neg_tri[:], over[:, n % 2, hd, first_q:HALF],
                                             start=False, stop=False, skip_group_check=True)
                            if diagonal:
                                last = pe.matmul(bank[:, first_q:first_q + P], c.ident[:], forbid[:], start=False,
                                                 stop=False, skip_group_check=True)
                        if n != firsts[h]:
                            pe.wait_ge(added, ct * (n_steps - 2) + (n - h))
                            for hd in heads:
                                last = pe.matmul(ps[:, 2 * (n % 2) + hd, begun:HALF], neg_ones[:],
                                                 later[:, (n - 1) % 2, hd, begun:HALF], start=False, stop=True,
                                                 skip_group_check=True)
                        last.then_inc(logs, 1)

                    def take_values(n):
                        h, kb, first_q, diagonal = steps[n]
                        pe.wait_ge(exps, at0 + (n + 1))
                        if n == firsts[h]:
                            wait(pe, taken, ct * 2 + (h - 1))
                            pe.wait_ge(natural, ct * 2 + 2)
                        for hd in heads:
                            rows = slice(SB_HEAD * hd, SB_HEAD * (hd + 1))
                            last = pe.matmul(ps[rows, 4 + h, first_q:HALF], v_nat[:, s, kb, rows], a[:, n % 2, hd, first_q:HALF],
                                             start=n == firsts[h], stop=n == last_of[h], skip_group_check=True)
                        last.then_inc(summed, 1)

                    score(0)
                    for n in range(n_steps):
                        if n + 1 < n_steps:
                            score(n + 1)
                        logarithm(n)
                        if n:
                            take_values(n - 1)
                    take_values(n_steps - 1)

            rolled(pe, CT // 2, turn)

        @block.scalar
        def _(act):
            def turn(j):
                for s in range(2):
                    ct = j * 2 + s
                    at0 = ct * n_steps
                    for h in range(2):
                        act.wait_ge(turned, ct * 2 + (h + 1))
                        act.copy(v_nat[:, s, 4 * h:4 * h + 4], heads_of(ps[:, 6 + h])).then_inc(natural, 1)

                    def softplus(n):
                        h, kb, first_q, diagonal = steps[n]
                        act.wait_ge(scored, at0 + (n + 1))
                        wait(act, softened, at0 + (n - 1))
                        z = ps[:, 2 * (n % 2):2 * (n % 2) + 2, first_q:HALF]
                        l = soft[:, n % 2, :, first_q:HALF]
                        act.activation(l, z, ACT.Abs).then_inc(chain, 1)
                        act.wait_ge(chain, (at0 + n) * 3 + 1)
                        act.activation(l, l, ACT.Exp, scale=-1.0).then_inc(chain, 1)
                        act.wait_ge(chain, (at0 + n) * 3 + 2)
                        act.activation(l, l, ACT.Ln, bias=c.eps[:, 2:3]).then_inc(chain, 1)

                    softplus(0)
                    for n, (h, kb, first_q, diagonal) in enumerate(steps):
                        if n + 1 < n_steps:
                            softplus(n + 1)
                        act.wait_ge(logs, at0 + (n + 1))
                        wait(act, summed, at0 + (n - 1))
                        act.activation(a[:, n % 2, :, first_q:HALF], ps[:, 2 * (n % 2):2 * (n % 2) + 2, first_q:HALF],
                                       ACT.Exp).then_inc(exps, 1)

            rolled(act, CT // 2, turn)

        @block.vector
        def _(dve):
            v = c.v_steps

            def turn(j):
                for s in range(2):
                    ct = j * 2 + s
                    at0 = ct * n_steps

                    def take(h):
                        dve.wait_ge(summed, at0 + (last_of[h] + 1))
                        wait(dve, stored[h], ct * 16)
                        dve.tensor_copy(o_b[:, h], ps[:, 4 + h]).then_inc(taken, 1)

                    for n, (h, kb, first_q, diagonal) in enumerate(steps):
                        dve.wait_ge(chain, (at0 + n) * 3 + 3)
                        wait(dve, logs, at0 + (n - 1))
                        p = over[:, n % 2, :, first_q:HALF]
                        v.mark(dve.scalar_tensor_tensor(out=p, in0=ps[:, 2 * (n % 2):2 * (n % 2) + 2, first_q:HALF], scalar=0.0,
                                                        in1=soft[:, n % 2, :, first_q:HALF], op0=ALU.max, op1=ALU.add))
                        v.wait(dve)
                        if diagonal:
                            block_p = over[:, n % 2, :, first_q:first_q + P]
                            v.mark(dve.tensor_tensor(block_p, block_p, c.upper[:].unsqueeze(1).broadcast_to([P, 2, P]), ALU.mult))
                            v.wait(dve)
                        dve.sem_inc(softened, 1)
                        if n != last_of[h]:
                            wait(dve, logs, at0 + n)
                            begun = first_q + P if diagonal else 0
                            if diagonal:
                                v.mark(dve.tensor_copy(later[:, n % 2, :, first_q:begun], over[:, n % 2, :, first_q:begun]))
                            if begun < HALF:
                                v.mark(dve.tensor_tensor(later[:, n % 2, :, begun:HALF], over[:, n % 2, :, begun:HALF],
                                                         later[:, (n - 1) % 2, :, begun:HALF], ALU.add))
                            v.wait(dve)
                            dve.sem_inc(added, 1)
                        if n == last_of[0] + 2:
                            take(0)
                    take(1)

            rolled(dve, CT // 2, turn, v)


def branch_outputs(c, following):
    nc = c.nc
    c.br_hi = at(c, 0, "branch_2_hi", [P, KT, SEQ], F32R)
    c.br_lo = at(c, 32768, "branch_2_lo", [P, KT, SEQ], F32R)
    six = c.w_raw[:].rearrange("p s (a k) n -> p (s a) (k n)", a=2)
    o_a, z_a, o_2, z_2, sq, root = (six[:, n] for n in range(6))
    squared, summed, rooted = c.sem("bo_squared"), c.sem("bo_summed"), c.sem("bo_rooted")
    loaded, made, rounded, split = (c.sem(f"bo_{n}") for n in ("loaded", "made", "rounded", "split"))
    src = [c.scratch[f"second_{n}"] for n in ("oa", "z", "ob", "zb")]

    def place(buf, i, h):
        return buf[:, bass.ds(i, 1), h * HALF:(h + 1) * HALF].rearrange("p a n -> p (a n)")

    with nc.Block() as block:

        @block.sync
        def _(sp):
            def turn(i):
                for h in range(2):
                    wait(sp, split, i * 4 + 2 * h)
                    apart(c, sp)
                    cut = slice(h * HALF, (h + 1) * HALF)
                    for part, dst in zip(src, (o_a, z_a, o_2, z_2)):
                        sp.dma_start(dst, part[bass.ds(i, 1), :, cut].rearrange("a p n -> p (a n)")).then_inc(loaded, 16)

            rolled(sp, CT, turn)
            sp.wait_ge(split, 4 * CT)
            following.load_first(sp)

        @block.tensor
        def _(pe):
            def turn(i):
                for h in range(2):
                    pe.wait_ge(squared, i * 2 + (h + 1))
                    wait(pe, rooted, i * 2 + (h - 1))
                    pe.matmul(c.ps[:, h], c.ones[:], sq, start=True, stop=True).then_inc(summed, 1)

            rolled(pe, CT, turn)

        @block.scalar
        def _(act):
            def turn(i):
                for h in range(2):
                    act.wait_ge(loaded, i * 128 + (64 * h + 64))
                    wait(act, summed, i * 2 + h)
                    act.activation(sq, o_a, ACT.Square).then_inc(squared, 1)
                    act.wait_ge(summed, i * 2 + (h + 1))
                    wait(act, made, i * 4 + 2 * h)
                    act.activation(root, c.ps[:, h], ACT.Sqrt, bias=c.eps[:, 0:1], scale=1.0 / P).then_inc(rooted, 1)
                    for b, (o, k) in enumerate(((o_2, i + CT), (o_a, i))):
                        act.wait_ge(made, i * 4 + (2 * h + b + 1))
                        apart(c, act)
                        act.copy(place(c.br_hi, k, h), o).then_inc(rounded, 1)

            rolled(act, CT, turn)

        @block.vector
        def _(dve):
            v = c.v_steps

            def turn(i):
                for h in range(2):
                    dve.wait_ge(loaded, i * 128 + (64 * h + 64))
                    dve.tensor_tensor(o_2, o_2, z_2, ALU.mult).then_inc(made, 1)
                    dve.wait_ge(rooted, i * 2 + (h + 1))
                    v.mark(dve.reciprocal(root, root))
                    v.wait(dve)
                    v.mark(dve.scalar_tensor_tensor(out=o_a, in0=o_a, scalar=vec(c, "dn_out_gain_2"), in1=root,
                                                    op0=ALU.mult, op1=ALU.mult))
                    v.wait(dve)
                    dve.tensor_tensor(o_a, o_a, z_a, ALU.mult).then_inc(made, 1)
                    for b, (o, k) in enumerate(((o_2, i + CT), (o_a, i))):
                        dve.wait_ge(rounded, i * 4 + (2 * h + b + 1))
                        dve.tensor_tensor(place(c.br_lo, k, h), o, place(c.br_hi, k, h).bitcast(F32),
                                          ALU.subtract).then_inc(split, 1)

            rolled(dve, CT, turn, v)


def renew(c):
    c.nc.clear_and_free_semaphores(c.stage_sems)
    c.stage_sems = []
    with c.nc.Block() as block:

        @block.gpsimd
        def _(pool):
            pass


def second_block(c, out):
    d = c.dram
    rms_norm(c, "norm_final", c.x, "norm_final", SEQ, dst=c.x)
    first_weights, project = second_projections(c)
    rms_norm(c, "norm_gain_2", c.x, "norm_gain_2", SEQ, c.h_hi, c.h_lo, following=first_weights)
    project()
    delta_rule(c)
    stick_breaking(c)
    merge_weights, merge = merge_branches(c, "mix_2", d["w_in_2"][0], GATE_COLUMN_2, d["w_up_a_2"][0], d["w_up_b_2"][0], "b_gate_2")
    branch_outputs(c, merge_weights)
    merge()
    out_weights = residual_weights(c, d["w_out_2"][0])
    take_back(c, "mix_2", out_weights)
    add_product(c, "out_2", out_weights, None)
    finish(c, out)


def first_block(c):
    d = c.dram
    memory = memory_keys(c)
    lora_weights, lora = rwkv_lora_inputs(c)
    memory(lora_weights)
    rms_norm(c, "norm_mix", c.x, "norm_mix", SEQ, c.h_hi, c.h_lo)
    feature_weights, features = rwkv_features(c)
    lora(feature_weights)
    features(lambda sp: None)
    rwkv_scan(c)
    conv_weights, conv = short_conv(c)
    rwkv_output(c, conv_weights)
    merge_weights, merge = merge_branches(c, "mix", d["w_in"][0], RWKV_COLS + 3 * D_RWKV, d["w_proj_a"][0], d["w_proj_b"][0], "b_gate")
    conv(merge_weights)
    merge()
    out_weights = residual_weights(c, d["w_out_mix"][0])
    take_back(c, "mix", out_weights)
    query_weights, query = queries(c)
    add_product(c, "out_mix", out_weights, query_weights)
    rms_norm(c, "norm_xattn", c.x, "norm_xattn", SEQ, c.h_hi, c.h_lo)
    query()
    xo_weights = residual_weights(c, d["w_xo"][0])
    attention(c, xo_weights)
    up_weights, hidden = mlp(c, None)
    add_product(c, "xo", xo_weights, up_weights)
    rms_norm(c, "norm_mlp", c.x, "norm_mlp", SEQ, c.h_hi, c.h_lo)
    hidden()


def build(nc, dram, out):
    with ExitStack() as ctx:
        c = open_core(nc, ctx, dram)
        c.norm_at = 40000
        setup(c)
        first_block(c)
        renew(c)
        second_block(c, out)


def kernel(**inputs):
    from concourse import bacc
    from concourse.bass_utils import run_bass_kernel_spmd
    import numpy as np

    arrays = {f"in_{name}_dram": np.ascontiguousarray(inputs[name]) for name in _INS}
    nc = bacc.Bacc("TRN2", target_bir_lowering=False, num_devices=1)
    dram = {name: nc.dram_tensor(f"in_{name}_dram", list(arrays[f"in_{name}_dram"].shape), F32, kind="ExternalInput").ap()
            for name in _INS}
    out = nc.dram_tensor("out_0_dram", [1, SEQ, D], F32, kind="ExternalOutput").ap()
    build(nc, dram, out)
    nc.finalize()
    results = run_bass_kernel_spmd(nc, [arrays], core_ids=[0])
    return results.results[0]["out_0_dram"]
```

```python
from contextlib import ExitStack

import concourse.bass as bass
from concourse import mybir

F32 = mybir.dt.float32
F32R = mybir.dt.float32r
ALU = mybir.AluOpType
ACT = mybir.ActivationFunctionType
AX_X = mybir.AxisListType.X

P = 128
SEQ = 1024
HALF = 512
D = 1024
KT = D // P
N_MEM = 256
EPS = 1e-6
LN_X_EPS = 64e-5

_INS = [
    "x", "mem", "norm_mix", "w_in", "b_gate", "mu_shift", "w0", "w_lora_w", "a0", "w_lora_a", "w_lora_g",
    "k_k", "k_a", "r_k", "ln_x_w", "ln_x_b", "conv_w", "w_proj_a", "w_proj_b", "w_out_mix", "norm_xattn",
    "norm_mem", "w_q", "w_kv", "w_xo", "norm_mlp", "w_up", "w_down", "norm_final", "norm_gain_2", "w_in_2",
    "b_gate_2", "conv_w_2", "a_log_2", "dt_bias_2", "dn_out_gain_2", "sb_q_gain_2", "sb_k_gain_2",
    "w_up_a_2", "w_up_b_2", "w_out_2",
]

VECTORS = [
    ("norm_mix", 8), ("b_gate", 16), ("mu_shift", 15), ("w0", 4), ("a0", 4), ("k_k", 4), ("k_a", 4),
    ("r_k", 4), ("ln_x_w", 4), ("ln_x_b", 4), ("conv_w", 12), ("norm_xattn", 8), ("norm_mem", 8),
    ("norm_mlp", 8), ("norm_final", 8), ("norm_gain_2", 8),
    ("b_gate_2", 16), ("conv_w_2", 48), ("dn_out_gain_2", 1), ("sb_q_gain_2", 1), ("sb_k_gain_2", 1),
]


def wait(eng, sem, value):
    if not (isinstance(value, int) and value <= 0):
        eng.wait_ge(sem, value)


def apart(c, eng):
    eng.sem_inc(c.passed, 1)


class Steps:

    def __init__(self, sem):
        self.sem, self.total, self.shift = sem, 0, 0

    def mark(self, ins):
        ins.then_inc(self.sem, 1)
        self.total += 1
        return self.total + self.shift

    def wait(self, eng, value=None):
        wait(eng, self.sem, self.total + self.shift if value is None else value)


def rolled(eng, n, body, *steps):
    starts = [s.total for s in steps]
    body(0)
    if n > 1:
        per = [s.total - a for s, a in zip(steps, starts)]
        with eng.Fori(1, n) as i:
            for s, a, p in zip(steps, starts, per):
                s.total, s.shift = a, i * p
            body(i)
        assert [s.total - a for s, a in zip(steps, starts)] == per, "turns count alike"
        for s, a, p in zip(steps, starts, per):
            s.total, s.shift = a + n * p, 0


def first(i):
    return isinstance(i, int) and i == 0


def columns(i, width):
    return bass.ds(i * width, width)


class Weights:

    def __init__(self, core, sources, turns):
        self.core, self.sources, self.turns = core, sources, turns
        self.per = len(sources)
        self.slots = 3 if self.per % 3 == 0 else 2
        self.total = self.per * turns
        self.parts = [2 if isinstance(s(0), tuple) else 1 for s in sources]
        assert self.per % self.slots == 0

    def begin(self):
        self.t0 = self.core.tiles
        self.l0 = list(self.core.loads)
        self.core.tiles += self.total
        for s in range(self.slots):
            self.core.loads[s] += self.total // self.slots * self.parts[s]

    def fetch(self, sp, u, i):
        c, s, src = self.core, u % self.slots, self.sources[u](i)
        if self.parts[u] == 2:
            for half, part in enumerate(src):
                sp.dma_start(c.w_raw[:, s, half * KT // 2:(half + 1) * KT // 2], part).then_inc(c.w_loaded[s], 16)
        else:
            sp.dma_start(c.w_raw[:, s], src).then_inc(c.w_loaded[s], 16)

    def load_first(self, sp):
        for u in range(self.slots):
            self.fetch(sp, u, 0)

    def load_all(self, sp):
        for u in range(self.slots):
            sp.wait_ge(self.core.w_split, self.t0 + (u - self.slots + 1))
            self.fetch(sp, u, 0)
        self.load_rest(sp)

    def load_rest(self, sp):
        c, n = self.core, self.slots

        def turn(i):
            for u in range(self.per):
                if first(i) and u < n:
                    continue
                sp.wait_ge(c.w_split, self.t0 + i * self.per + (u - n + 1))
                apart(c, sp)
                self.fetch(sp, u, i)

        rolled(sp, self.turns, turn)

    def split(self, pool, beside=None):
        c, n = self.core, self.slots

        def turn(i):
            for u in range(self.per):
                s = u % n
                each = 16 * self.parts[u]
                pool.wait_ge(c.w_loaded[s], 16 * self.l0[s] + i * (each * (self.per // n)) + each * (u // n + 1))
                wait(pool, c.tile_done, self.t0 + i * self.per + (u - n + 1))
                pool.tensor_tensor(c.w_hi[:, s], c.w_raw[:, s], c.ones[:].unsqueeze(1).broadcast_to([P, KT, P]),
                                   ALU.mult).then_inc(c.w_rounded, 1)
                pool.wait_ge(c.w_rounded, self.t0 + i * self.per + (u + 1))
                pool.tensor_tensor(c.w_lo[:, s], c.w_raw[:, s], c.w_hi[:, s].bitcast(F32),
                                   ALU.subtract).then_inc(c.w_split, 1)
                if beside:
                    beside(i, u)

        rolled(pool, self.turns, turn)

    def round_on(self, act):
        c, n = self.core, self.slots

        def turn(i):
            for u in range(self.per):
                s = u % n
                act.wait_ge(c.w_loaded[s], 16 * self.l0[s] + i * (16 * (self.per // n)) + 16 * (u // n + 1))
                wait(act, c.tile_done, self.t0 + i * self.per + (u - n + 1))
                act.copy(c.w_hi[:, s], c.w_raw[:, s]).then_inc(c.w_rounded, 1)

        rolled(act, self.turns, turn)

    def subtract(self, eng, beside=None):
        c, n = self.core, self.slots

        def turn(i):
            for u in range(self.per):
                s = u % n
                eng.wait_ge(c.w_rounded, self.t0 + i * self.per + (u + 1))
                eng.tensor_tensor(c.w_lo[:, s], c.w_raw[:, s], c.w_hi[:, s].bitcast(F32),
                                   ALU.subtract).then_inc(c.w_split, 1)
                if beside:
                    beside(i, u)

        rolled(eng, self.turns, turn)

    def ready(self, pe, i, u):
        pe.wait_ge(self.core.w_split, self.t0 + i * self.per + (u + 1))

    def done(self, eng, i, u):
        eng.wait_ge(self.core.tile_done, self.t0 + i * self.per + (u + 1))

    def multiply(self, pe, u, out, hi, lo, kts=range(KT), offset=0, width=HALF, before=None, half=0):
        c, s = self.core, u % self.slots
        kts = list(kts)
        for k in kts:
            if before:
                before(k)
            for w, a in ((c.w_hi, hi), (c.w_hi, lo), (c.w_lo, hi)):
                for h, o in enumerate(out):
                    last = pe.matmul(o, w[:, s, k], a[:, k - offset, (half + h) * width:(half + h + 1) * width],
                                     start=(k == kts[0] and w is c.w_hi and a is hi),
                                     stop=(k == kts[-1] and w is c.w_lo))
        return last


NORM_EVENTS = dict(squared=KT, added=KT, summed=2, rooted=2, scaled=2 * KT, rounded=2 * KT, split=2 * KT)
NORM_AT = 59392


class Norm:

    def __init__(self, c, name, gain, events=tuple(NORM_EVENTS), acc=None):
        self.c, self.gain = c, gain
        self.root = at(c, NORM_AT, f"{name}_root", [P, 2, HALF])
        self.whole = at(c, NORM_AT + 4096, f"{name}_whole", [P, 2, HALF])
        self.acc = acc if acc is not None else at(c, NORM_AT + 8192, f"{name}_acc", [P, SEQ])
        self.events = events
        self.before = dict(c.norm_totals)
        for n in events:
            c.norm_totals[n] += NORM_EVENTS[n]

    def wait(self, eng, name, n):
        wait(eng, self.c.norm_sems[name], self.before[name] + n)

    def mark(self, ins, name):
        ins.then_inc(self.c.norm_sems[name], 1)

    def square(self, act, dst, src, n):
        self.mark(act.activation(dst, src, ACT.Square), "squared")

    def add_squares(self, pool, sq, n):
        self.wait(pool, "squared", n + 1)
        self.wait(pool, "added", n)
        self.mark(pool.tensor_tensor(self.acc[:], self.acc[:], sq, ALU.add), "added")

    def pe_sums(self, pe):
        for h in range(2) if "summed" in self.events else ():
            self.mark(pe.matmul(self.c.ps[:, 4 + h], self.c.ones[:], self.acc[:, h * HALF:(h + 1) * HALF], start=True, stop=True),
                      "summed")

    def act_roots(self, act):
        for h in range(2):
            if "summed" in self.events:
                self.wait(act, "summed", h + 1)
            self.mark(act.activation(self.root[:, h], self.c.ps[:, 4 + h], ACT.Sqrt, bias=self.c.eps[:, 0:1], scale=1.0 / D),
                      "rooted")

    def act(self, act):
        self.act_roots(act)
        for n in range(2 * KT):
            self.wait(act, "scaled", n + 1)
            h, k = divmod(n, KT)
            self.mark(act.copy(self.c.h_hi[:, k, h * HALF:(h + 1) * HALF], self.whole[:, n % 2]), "rounded")

    def dve(self, dve):
        c, v = self.c, self.c.v_steps

        def take(n):
            h, k = divmod(n, KT)
            cut = slice(h * HALF, (h + 1) * HALF)
            self.wait(dve, "rounded", n + 1)
            self.mark(dve.tensor_tensor(c.h_lo[:, k, cut], self.whole[:, n % 2], c.h_hi[:, k, cut].bitcast(F32), ALU.subtract),
                      "split")

        for n in range(2 * KT):
            h, k = divmod(n, KT)
            if k == 0:
                self.wait(dve, "rooted", h + 1)
                v.mark(dve.reciprocal(self.root[:, h], self.root[:, h]))
                v.wait(dve)
            if n >= 2:
                self.wait(dve, "split", n - 1)
            self.mark(dve.scalar_tensor_tensor(out=self.whole[:, n % 2], in0=c.x[:, k, h * HALF:(h + 1) * HALF],
                                               scalar=vec(c, self.gain, k), in1=self.root[:, h], op0=ALU.mult, op1=ALU.mult),
                      "scaled")
            if n:
                take(n - 1)
        take(2 * KT - 1)

    def first_tiles(self, pe, weights):
        c = self.c
        for h in range(2):
            for u in range(2):
                if h == 0:
                    weights.ready(pe, 0, u)
                last = weights.multiply(pe, u, [c.ps[:, 2 * u + h]], c.h_hi, c.h_lo, half=h,
                                        before=(lambda k: self.wait(pe, "split", h * KT + k + 1)) if u == 0 else None)
                if h:
                    last.then_inc(c.tile_done, 1)


class Core:
    pass


def open_core(nc, ctx, dram):
    c = Core()
    c.nc, c.ctx, c.dram = nc, ctx, dram

    def sb(name, shape, dt=F32):
        return ctx.enter_context(nc.sbuf_tensor(name, shape, dt))

    c.sb = sb
    c.stage_sems = []

    def sem(name):
        c.stage_sems.append(ctx.enter_context(nc.semaphore(name)))
        return c.stage_sems[-1]

    c.sem = sem
    c.x = sb("x_t", [P, KT, SEQ])
    c.h_base = (nc.sbuf_base + 31) // 32 * 32
    c.h_hi = sb("h_hi", [P, KT, SEQ], F32R)
    c.h_lo = sb("h_lo", [P, KT, SEQ], F32R)
    c.w_raw = sb("w_raw", [P, 3, KT, P])
    c.w_base = (nc.sbuf_base + 31) // 32 * 32
    c.w_hi = sb("w_hi", [P, 3, KT, P], F32R)
    c.w_lo = sb("w_lo", [P, 3, KT, P], F32R)
    c.vec = sb("vec", [P, 2 * P])
    c.ident = sb("ident", [P, P])
    c.ones = sb("ones", [P, P])
    c.ones_64 = sb("ones_64", [P, P])
    c.upper = sb("upper", [P, P])
    c.upper_eq = sb("upper_eq", [P, P])
    c.lower = sb("lower", [P, P])
    c.level_t = sb("level_t", [P, P])
    c.eps = sb("eps", [P, 5])
    c.lmid = sb("lmid", [P, CT, TILES + 1])
    c.lend = sb("lend", [P, CT, TILES])
    c.beta_col, c.decay_col, c.beta_decay = (sb(n, [P, TILES, DN_HEADS]) for n in ("beta_col", "decay_col", "beta_decay"))
    c.aux_base = nc.sbuf_base
    c.ps = ctx.enter_context(nc.psum_tensor("ps", [P, 8, HALF], F32))
    c.w_loaded = [c.sem(f"w_loaded{s}") for s in range(3)]
    c.w_rounded, c.w_split, c.tile_done = c.sem("w_rounded"), c.sem("w_split"), c.sem("tile_done")
    c.tiles, c.loads = 0, [0, 0, 0]
    c.a_steps, c.v_steps = Steps(c.sem("act_steps")), Steps(c.sem("dve_steps"))
    c.g_steps, c.t_steps = Steps(c.sem("pool_steps")), Steps(c.sem("pe_steps"))
    c.norm_sems = {n: c.sem(f"norm_{n}") for n in NORM_EVENTS}
    c.norm_totals = dict.fromkeys(NORM_EVENTS, 0)
    c.begun, c.passed = c.sem("ident_ready"), c.sem("waits_passed")
    c.scratch = {}
    c.col, row = {}, 0
    for name, rows in VECTORS:
        c.col[name] = row
        row += rows
    assert row <= 2 * P
    c.stage_sems = []
    return c


def at(c, off, name, shape, dt=F32):
    return c.nc.alloc_sbuf_tensor_at(name, shape, dt, offset=(c.aux_base + 31) // 32 * 32 + off)


def at_h(c, off, name, shape, dt=F32):
    return c.nc.alloc_sbuf_tensor_at(name, shape, dt, offset=c.h_base + off)


def nth(events, name, i=0):
    return i * len(events) + (events.index(name) + 1)


def scratch(c, name, shape):
    c.scratch[name] = c.nc.dram_tensor(name, shape, F32, kind="Internal").ap()
    return c.scratch[name]


def vec(c, name, i=0):
    k = c.col[name]
    return c.vec[:, k + i:k + i + 1] if isinstance(i, int) else c.vec[:, bass.ds(i + k, 1)]


def setup(c):
    nc, d = c.nc, c.dram
    rows = at(c, 0, "vec_rows", [P, 2, P])
    xin = at(c, 2048, "x_in", [P, 2, D])
    c.mem_t = at(c, 16384, "mem_t", [P, KT, N_MEM])
    cleared, rows_in = c.sem("rows_cleared"), c.sem("rows_loaded")
    x_in = [c.sem("x_loaded0"), c.sem("x_loaded1")]
    ident_ready, turned, copied = c.begun, c.sem("tile_turned"), c.sem("tile_copied")
    n_rows = [0]
    with nc.Block() as block:

        @block.sync
        def _(sp):
            sp.dma_start(xin[:, 0], d["x"][0, 0:P, :]).then_inc(x_in[0], 16)
            sp.dma_start(xin[:, 1], d["x"][0, P:2 * P, :]).then_inc(x_in[1], 16)
            sp.wait_ge(cleared, 1)
            for name, n in VECTORS:
                r = c.col[name]
                flat = d[name]
                if name == "mu_shift":
                    mu = flat.rearrange("a n -> (a n)")
                    parts = [(r, mu[0:14 * P].rearrange("(n p) -> n p", p=P)),
                             (r + 14, mu[14 * P:1824].rearrange("(n p) -> n p", n=1))]
                elif name.startswith("sb_"):
                    parts = [(r, flat), (r, flat)]
                elif len(flat.shape) == 1:
                    parts = [(r, flat.rearrange("(n p) -> n p", p=P))]
                elif len(flat.shape) == 2:
                    parts = [(r, flat.rearrange("a (n p) -> (a n) p", p=P))]
                elif name == "r_k":
                    parts = [(r, flat.rearrange("a (n b) p -> (a n) (b p)", b=2))]
                elif len(flat.shape) == 3:
                    parts = [(r, flat.rearrange("a t (n p) -> (a t n) p", p=P))]
                else:
                    parts = [(r, flat.rearrange("a t b (n p) -> (a t b n) p", p=P))]
                for k, (at_row, src) in enumerate(parts):
                    done = 0
                    while done < src.shape[0]:
                        s, q = divmod(at_row + done, P)
                        m = min(src.shape[0] - done, P - q)
                        w = src.shape[1]
                        first = k * 64 if name.startswith("sb_") else 0
                        sp.dma_start(rows[q:q + m, s, first:first + w], src[done:done + m, :]).then_inc(rows_in, 16)
                        n_rows[0] += 1
                        done += m
            for t in range(2, SEQ // P + 2):
                sp.wait_ge(turned, t - 1)
                src = d["x"][0, t * P:(t + 1) * P, :] if t < 8 else d["mem"][0, (t - 8) * P:(t - 7) * P, :]
                sp.dma_start(xin[:, t % 2], src).then_inc(x_in[t % 2], 16)

        @block.gpsimd
        def _(pool):
            g = c.g_steps

            def fill(buf, value):
                return g.mark(pool.memset(buf, value))

            def keep(buf, pattern, base, mult, op=ALU.is_ge, fill=0.0):
                g.mark(pool.affine_select(out=buf, in_=buf, compare_op=op, fill=fill, base=base,
                                          pattern=pattern, channel_multiplier=mult))
                g.wait(pool)

            pool.memset(rows[:], 0.0).then_inc(cleared, 1)
            for buf, value in ((c.ident, 0.0), (c.ones, 1.0), (c.ones_64, 1.0), (c.upper, 1.0),
                               (c.upper_eq, 1.0), (c.lower, 1.0), (c.level_t, 0.0)):
                fill(buf[:], value)
            for k, value in enumerate((EPS, LN_X_EPS, 1.0, 0.0, EPS * SB_HEAD)):
                fill(c.eps[:, k:k + 1], value)
            g.wait(pool)
            pool.affine_select(out=c.ident[:], in_=c.ident[:], compare_op=ALU.not_equal, fill=1.0, base=0,
                               pattern=[[-1, P]], channel_multiplier=1).then_inc(ident_ready, 1)
            keep(c.ones_64[:, 0:64], [[0, 64]], 63, -1)
            keep(c.ones_64[:, 64:128], [[0, 64]], -64, 1)
            keep(c.upper[:], [[1, P]], -1, -1)
            keep(c.upper_eq[:], [[1, P]], 0, -1)
            keep(c.lower[:], [[-1, P]], -1, 1)
            odd = c.level_t[:].rearrange("p (b w) -> p b w", w=2)[:, :, 1:2]
            keep(odd, [[-2, P // 2]], 0, 1, op=ALU.not_equal, fill=1.0)

        @block.tensor
        def _(pe):
            pe.wait_ge(ident_ready, 1)
            for t in range(SEQ // P + 2):
                pe.wait_ge(x_in[t % 2], 16 * (t // 2 + 1))
                wait(pe, copied, t - 1)
                for k in range(KT):
                    last = pe.transpose(c.ps[:, 2 * (t % 2) + k // 4, (k % 4) * P:(k % 4 + 1) * P],
                                        xin[:, t % 2, k * P:(k + 1) * P], c.ident[:])
                last.then_inc(turned, 1)
            pe.wait_ge(rows_in, 16 * n_rows[0])
            for s in range(2):
                last = pe.transpose(c.ps[:, 4, s * P:(s + 1) * P], rows[:, s, :], c.ident[:])
            last.then_inc(turned, 1)

        @block.scalar
        def _(act):
            for t in range(SEQ // P + 2):
                act.wait_ge(turned, t + 1)
                dst = c.x[:, :, t * P:(t + 1) * P] if t < 8 else c.mem_t[:, :, (t - 8) * P:(t - 7) * P]
                act.copy(dst, c.ps[:, 2 * (t % 2):2 * (t % 2) + 2, :]
                         .rearrange("p b (k n) -> p (b k) n", n=P)).then_inc(copied, 1)
            act.wait_ge(turned, SEQ // P + 3)
            act.copy(c.vec[:], c.ps[:, 4, 0:2 * P]).then_inc(copied, 1)


def memory_norm(c, hi, lo, following):
    gain, src, width = "norm_mem", c.mem_t, N_MEM
    sq = at(c, 40960, "mem_sq", [P, KT, width])
    root = at(c, 49152, "mem_root", [P, width])
    whole = at(c, 50176, "mem_whole", [P, KT, width])
    squared, summed, rooted, scaled, rounded, split = (
        c.sem(f"mem_{n}") for n in ("squared", "summed", "rooted", "scaled", "rounded", "split"))
    with c.nc.Block() as block:

        @block.sync
        def _(sp):
            following.load_first(sp)

        @block.tensor
        def _(pe):
            for k in range(KT):
                pe.wait_ge(squared, k + 1)
                pe.matmul(c.ps[:, 0, 0:width], c.ones[:], sq[:, k], start=k == 0, stop=k == KT - 1).then_inc(summed, 1)

        @block.scalar
        def _(act):
            for k in range(KT):
                act.activation(sq[:, k], src[:, k], ACT.Square).then_inc(squared, 1)
            act.wait_ge(summed, KT)
            act.activation(root[:], c.ps[:, 0, 0:width], ACT.Sqrt, bias=c.eps[:, 0:1], scale=1.0 / D).then_inc(rooted, 1)
            for k in range(KT):
                act.wait_ge(scaled, k + 1)
                act.copy(hi[:, k], whole[:, k]).then_inc(rounded, 1)

        @block.vector
        def _(dve):
            v = c.v_steps
            dve.wait_ge(rooted, 1)
            v.mark(dve.reciprocal(root[:], root[:]))
            v.wait(dve)
            for k in range(KT):
                dve.scalar_tensor_tensor(out=whole[:, k], in0=src[:, k], scalar=vec(c, gain, k), in1=root[:],
                                         op0=ALU.mult, op1=ALU.mult).then_inc(scaled, 1)
            for k in range(KT):
                dve.wait_ge(rounded, k + 1)
                dve.tensor_tensor(lo[:, k], whole[:, k], hi[:, k].bitcast(F32), ALU.subtract).then_inc(split, 1)


def add_product(c, name, weights, following, norm=None):
    nc = c.nc
    weights.begin()
    free = [c.sem(f"{name}_free{q}") for q in range(2)]
    cleared = c.sem(f"{name}_cleared")
    sq = at(c, 0, f"{name}_sq", [P, 2, SEQ])

    def row(k):
        return c.x[:, bass.ds(k, 1), :].rearrange("p a n -> p (a n)")

    with nc.Block() as block:

        @block.sync
        def _(sp):
            weights.load_rest(sp)
            if following:
                sp.wait_ge(c.w_split, weights.t0 + weights.total)
                following.load_first(sp)

        @block.gpsimd
        def _(pool):
            if not norm:
                weights.split(pool)
                return
            pool.memset(norm.acc[:], 0.0).then_inc(cleared, 1)
            pool.wait_ge(cleared, 1)

            def beside(i, u):
                if not first(i):
                    norm.add_squares(pool, sq[:, u], i * 2 + (u - 2))

            weights.split(pool, beside)
            for k in (KT - 2, KT - 1):
                norm.add_squares(pool, sq[:, k % 2], k)

        @block.tensor
        def _(pe):
            def turn(i):
                for u in range(2):
                    weights.ready(pe, i, u)
                    wait(pe, free[u], i)
                    weights.multiply(pe, u, [c.ps[:, 2 * u], c.ps[:, 2 * u + 1]], c.h_hi, c.h_lo).then_inc(c.tile_done, 1)

            rolled(pe, weights.turns, turn)

        @block.scalar
        def _(act):
            def turn(i):
                for u in range(2):
                    act.wait_ge(free[u], i + 1)
                    if not first(i):
                        norm.wait(act, "added", i * 2 + (u - 1))
                    apart(c, act)
                    norm.square(act, sq[:, u], row(i * 2 + u), i * 2 + u)

            if norm:
                rolled(act, weights.turns, turn)

        @block.vector
        def _(dve):
            def turn(i):
                for u in range(2):
                    weights.done(dve, i, u)
                    dve.tensor_tensor(row(i * 2 + u), row(i * 2 + u), c.ps[:, 2 * u:2 * u + 2, :].rearrange("p b n -> p (b n)"),
                                      ALU.add).then_inc(free[u], 1)

            rolled(dve, weights.turns, turn)


def tile_of(src, first=0):
    view = src.rearrange("(k p) n -> p k n", p=P)
    return lambda i, step=1, off=0: view[:, :, bass.ds(i * (step * P) + (first + off * P), P)]


def finish(c, out):
    nc = c.nc
    tok = at(c, 0, "out_tok", [P, 2, D])
    turned, copied = c.sem("out_turned"), c.sem("out_copied")
    stored = [c.sem("out_stored0"), c.sem("out_stored1")]
    with nc.Block() as block:

        @block.tensor
        def _(pe):
            for t in range(SEQ // P):
                wait(pe, copied, t - 1)
                for k in range(KT):
                    last = pe.transpose(c.ps[:, 2 * (t % 2) + k // 4, (k % 4) * P:(k % 4 + 1) * P],
                                        c.x[:, k, t * P:(t + 1) * P], c.ident[:])
                last.then_inc(turned, 1)

        @block.scalar
        def _(act):
            for t in range(SEQ // P):
                act.wait_ge(turned, t + 1)
                wait(act, stored[t % 2], 16 * (t // 2))
                act.copy(tok[:, t % 2], c.ps[:, 2 * (t % 2):2 * (t % 2) + 2, :].rearrange("p b n -> p (b n)")).then_inc(copied, 1)

        @block.sync
        def _(sp):
            for t in range(SEQ // P):
                sp.wait_ge(copied, t + 1)
                sp.dma_start(out[0, t * P:(t + 1) * P, :], tok[:, t % 2]).then_inc(stored[t % 2], 16)
            for s in range(2):
                sp.wait_ge(stored[s], 16 * (SEQ // P // 2))


def mlp(c):
    nc, d = c.nc, c.dram
    groups, pairs = 4, KT // 2
    up, down = tile_of(d["w_up"][0]), d["w_down"][0]
    hid_hi = at(c, 0, "hid_hi", [P, KT, SEQ], F32R)
    hid_lo = at(c, 32768, "hid_lo", [P, KT, SEQ], F32R)
    relu = c.w_raw[:, 2].rearrange("p (h k) n -> p h (k n)", h=2)
    rectified, squared, rounded = c.sem("hid_rectified"), c.sem("hid_squared"), c.sem("hid_rounded")
    ready, cleared = c.sem("hid_ready"), c.sem("final_cleared")
    sq = c.w_raw[:, 2].rearrange("p k n -> p (k n)")
    down_free = [c.sem("down_free0"), c.sem("down_free1")]
    streams = []
    for g in range(groups):
        rows = tile_of(down[g * D:(g + 1) * D, :])
        streams.append((Weights(c, [lambda i, g=g, u=u: up(i, 2, g * KT + u) for u in range(2)], pairs),
                        Weights(c, [lambda i, rows=rows, u=u: rows(i, 2, u) for u in range(2)], pairs)))
    c.mlp_first = streams[0][0]

    def build(norm, after):
        for pair in streams:
            for w in pair:
                w.begin()
        every = [w for pair in streams for w in pair]
        with nc.Block() as block:

            @block.sync
            def _(sp):
                every[0].load_rest(sp)
                for w in every[1:]:
                    w.load_all(sp)

            @block.gpsimd
            def _(pool):
                for w in every[:-1]:
                    w.split(pool)
                pool.memset(after.acc[:], 0.0).then_inc(cleared, 1)
                pool.wait_ge(cleared, 1)

                def beside(i, u):
                    if not first(i):
                        after.add_squares(pool, sq, i * 2 + (u - 2))

                every[-1].split(pool, beside)
                for k in (KT - 2, KT - 1):
                    after.add_squares(pool, sq, k)

            @block.tensor
            def _(pe):
                norm.pe_sums(pe)
                for g, (w_up, w_down) in enumerate(streams):
                    def up_turn(i):
                        if g == 0 and first(i):
                            norm.first_tiles(pe, w_up)
                            return
                        for u in range(2):
                            w_up.ready(pe, i, u)
                            wait(pe, rectified, (g * pairs + i) * 4 + (2 * u - 2))
                            w_up.multiply(pe, u, [c.ps[:, 2 * u], c.ps[:, 2 * u + 1]], c.h_hi,
                                          c.h_lo).then_inc(c.tile_done, 1)

                    def down_turn(i):
                        for u in range(2):
                            w_down.ready(pe, i, u)
                            wait(pe, down_free[u], g * pairs + i)
                            waits = first(i) and u == 0
                            w_down.multiply(pe, u, [c.ps[:, 4 + 2 * u], c.ps[:, 5 + 2 * u]], hid_hi, hid_lo,
                                            before=(lambda k: pe.wait_ge(ready, g * 16 + 2 * k + 2)) if waits
                                            else None).then_inc(c.tile_done, 1)

                    rolled(pe, pairs, up_turn)
                    rolled(pe, pairs, down_turn)

            @block.scalar
            def _(act):
                norm.act(act)
                for g, (w_up, w_down) in enumerate(streams):
                    def turn(i):
                        for u in range(2):
                            w_up.done(act, i, u)
                            k = bass.ds(i * 2 + u, 1)
                            n = (g * pairs + i) * 4 + 2 * u
                            for h in range(2):
                                wait(act, ready, n + (h - 1))
                                act.activation(relu[:, h], c.ps[:, 2 * u + h], ACT.Relu).then_inc(rectified, 1)
                            for h in range(2):
                                act.wait_ge(squared, n + (h + 1))
                                act.copy(hid_hi[:, k, h * HALF:(h + 1) * HALF].rearrange("p a n -> p (a n)"),
                                         relu[:, h]).then_inc(rounded, 1)

                    rolled(act, pairs, turn)

                def squares(i):
                    for u in range(2):
                        act.wait_ge(down_free[u], (groups - 1) * pairs + i + 1)
                        if u or not first(i):
                            after.wait(act, "added", i * 2 + u)
                        apart(c, act)
                        after.square(act, sq, c.x[:, bass.ds(i * 2 + u, 1), :].rearrange("p a n -> p (a n)"), i * 2 + u)

                act.wait_ge(ready, groups * pairs * 4)
                rolled(act, pairs, squares)

            @block.vector
            def _(dve):
                norm.dve(dve)
                for g, (w_up, w_down) in enumerate(streams):
                    def up_turn(i):
                        for u in range(2):
                            k = bass.ds(i * 2 + u, 1)
                            n = (g * pairs + i) * 4 + 2 * u
                            for h in range(2):
                                dve.wait_ge(rectified, n + (h + 1))
                                dve.tensor_tensor(relu[:, h], relu[:, h], relu[:, h], ALU.mult).then_inc(squared, 1)
                            for h in range(2):
                                dve.wait_ge(rounded, n + (h + 1))
                                cut = slice(h * HALF, (h + 1) * HALF)
                                dve.tensor_tensor(hid_lo[:, k, cut].rearrange("p a n -> p (a n)"), relu[:, h],
                                                  hid_hi[:, k, cut].rearrange("p a n -> p (a n)").bitcast(F32),
                                                  ALU.subtract).then_inc(ready, 1)

                    def down_turn(i):
                        for u in range(2):
                            w_down.done(dve, i, u)
                            if g:
                                dve.wait_ge(down_free[u], (g - 1) * pairs + i + 1)
                            rows = c.x[:, bass.ds(i * 2 + u, 1), :].rearrange("p a n -> p (a n)")
                            dve.tensor_tensor(rows, rows, c.ps[:, 4 + 2 * u:6 + 2 * u, :].rearrange("p b n -> p (b n)"),
                                              ALU.add).then_inc(down_free[u], 1)

                    rolled(dve, pairs, up_turn)
                    rolled(dve, pairs, down_turn)

    return streams[0][0], build


N_HEADS = 8
HEAD = 64
D_RWKV = N_HEADS * HEAD
CT = D_RWKV // P
RWKV_COLS = 3 * D_RWKV + 288
TILES = SEQ // P
DECAY = -0.6065306597126334
STORED = ["a_t", "r_t", "k_t", "b_t", "v_t", "bonus_t", "gate_t"]


def rwkv_lora_inputs(c):
    nc, d = c.nc, c.dram
    tile = tile_of(d["w_in"][0])
    c.lora_in = at(c, 0, "lora_in", [P, SEQ])
    c.gate_in = at(c, 4096, "gate_in", [P, SEQ])
    c.gate_in2 = at(c, 8192, "gate_in2", [P, SEQ])
    c.gate_w2 = c.gate_in2[32:64, 0:D_RWKV]
    c.lora_w = at(c, 12288, "lora_w", [P, D_RWKV])
    c.gate_w = at(c, 14336, "gate_w", [P, D_RWKV])
    plain = at(c, 20480, "lora_plain", [P, 3, SEQ + 1])
    mixed = at(c, 20480 + 12320, "lora_mixed", [P, 3, SEQ])
    weights = Weights(c, [lambda i, u=u: tile(i, 3, 12 + u) for u in range(3)], 1)
    cleared, copied, moved = c.sem("lora_cleared"), c.sem("lora_copied"), c.sem("lora_mixed_done")
    c.lora_loaded = c.sem("lora_loaded")
    mu = c.col["mu_shift"] + 12

    def build(following, norm):
        weights.begin()
        with nc.Block() as block:

            @block.sync
            def _(sp):
                weights.load_rest(sp)
                sp.dma_start(c.lora_w[0:64, :], d["w_lora_w"][0]).then_inc(c.lora_loaded, 16)
                sp.dma_start(c.lora_w[64:128, :], d["w_lora_a"][0]).then_inc(c.lora_loaded, 16)
                sp.dma_start(c.gate_w[:], d["w_lora_g"][0, 0:P, :]).then_inc(c.lora_loaded, 16)
                sp.dma_start(c.gate_w2, d["w_lora_g"][0, P:160, :]).then_inc(c.lora_loaded, 16)
                sp.wait_ge(c.w_split, weights.t0 + weights.total)
                following.load_first(sp)

            @block.gpsimd
            def _(pool):
                pool.memset(plain[:, :, 0:1], 0.0).then_inc(cleared, 1)
                weights.split(pool)

            @block.tensor
            def _(pe):
                norm.pe_sums(pe)
                norm.first_tiles(pe, weights)
                weights.ready(pe, 0, 2)
                weights.multiply(pe, 2, [c.ps[:, 4], c.ps[:, 5]], c.h_hi, c.h_lo).then_inc(c.tile_done, 1)

            @block.scalar
            def _(act):
                norm.act(act)
                for u in range(3):
                    weights.done(act, 0, u)
                    act.copy(plain[:, u, 1:SEQ + 1], c.ps[:, 2 * u:2 * u + 2].rearrange("p b n -> p (b n)")).then_inc(copied, 1)
                act.wait_ge(moved, 1)
                act.activation(c.lora_in[0:64, :], mixed[0:64, 0, :], ACT.Tanh)
                act.copy(c.lora_in[64:128, :], mixed[64:128, 0, :])
                act.wait_ge(moved, 2)
                act.activation(c.gate_in[:], mixed[:, 1, :], ACT.Sigmoid)
                act.wait_ge(moved, 3)
                act.activation(c.gate_in2[0:32, :], mixed[0:32, 2, :], ACT.Sigmoid)

            @block.vector
            def _(dve):
                v = c.v_steps
                norm.dve(dve)
                dve.wait_ge(cleared, 1)
                for u in range(3):
                    dve.wait_ge(copied, u + 1)
                    v.mark(dve.tensor_tensor(mixed[:, u], plain[:, u, 0:SEQ], plain[:, u, 1:SEQ + 1], ALU.subtract))
                    v.wait(dve)
                    dve.scalar_tensor_tensor(out=mixed[:, u], in0=mixed[:, u], scalar=c.vec[:, mu + u:mu + u + 1],
                                             in1=plain[:, u, 1:SEQ + 1], op0=ALU.mult, op1=ALU.add).then_inc(moved, 1)

    return weights, build


def rwkv_features(c):
    nc, d = c.nc, c.dram
    tile = tile_of(d["w_in"][0])
    out = [scratch(c, f"rwkv_{name}", [CT, P, SEQ]) for name in STORED]
    order = [4, 0, 8]
    weights = Weights(c, [lambda i, o=o: tile(i, 1, o) for o in order], CT)
    mid = SEQ // TILES // 2 - 1
    base = 16384

    def buf(name, width=HALF):
        nonlocal base
        b = at(c, base, f"rw_{name}", [P, width])
        base += 4 * ((width + 7) // 8 * 8)
        return b

    plain = [[buf(f"plain_{n}{h}", HALF + 1) for h in range(2)] for n in "krv"]
    log_w, a_gate, gate = buf("log_w", SEQ), buf("a_gate", SEQ), buf("gate", SEQ)
    k, r, v_b, kk, kf, b_b, bonus, root, rk, l_b, l_prev, e_neg = (
        buf(n) for n in ("k", "r", "v", "kk", "kf", "b", "bonus", "root", "rk", "l", "l_prev", "e_neg"))
    lora_s = buf("lora_s", 3 * P)
    assert base <= 229368 - c.aux_base, base
    copied, mixed, cleared = c.sem("rw_copied"), c.sem("rw_mixed"), c.sem("rw_cleared")
    aux, taken = [[c.sem(f"rw_{n}{h}") for h in range(2)] for n in ("aux", "taken")]
    staged, squared, keyed = c.sem("rw_staged"), c.sem("rw_squared"), c.sem("rw_keyed")
    decayed, negated, exps = c.sem("rw_decayed"), c.sem("rw_negated"), c.sem("rw_exps")
    made, stored = c.sem("rw_made"), c.sem("rw_stored")
    outputs = [None, None, None, None, None, None, None]

    def build(following):
        weights.begin()
        with nc.Block() as block:

            @block.sync
            def _(sp):
                def store(i, h):
                    sp.wait_ge(taken[h], i * 5 + 3)
                    apart(c, sp)
                    sp.wait_ge(made, i * 2 + (h + 1))
                    apart(c, sp)
                    cut = slice(h * HALF, (h + 1) * HALF)
                    for dst, src in zip(out, (kk[:], r[:], kf[:], b_b[:], v_b[:], bonus[:], gate[:, cut])):
                        view = dst[bass.ds(i, 1), :, cut].rearrange("a p n -> p (a n)")
                        sp.dma_start(view, src).then_inc(stored, 16)

                def turn(i):
                    for u in range(3):
                        sp.wait_ge(c.w_split, weights.t0 + i * 3 + (u + 1))
                        apart(c, sp)
                        sp.dma_start(c.w_raw[:, u], weights.sources[u](i + 1)).then_inc(c.w_loaded[u], 16)
                    for h in range(2):
                        store(i, h)

                rolled(sp, CT - 1, turn)
                for h in range(2):
                    store(CT - 1, h)
                following(sp)
                sp.wait_ge(stored, 16 * 7 * 2 * CT)

            @block.gpsimd
            def _(pool):
                pool.memset(c.lmid[:], 0.0).then_inc(cleared, 1)
                for n in range(3):
                    pool.memset(plain[n][0][:, 0:1], 0.0).then_inc(cleared, 1)
                weights.split(pool)

            @block.tensor
            def _(pe):
                def lora(i, n, h):
                    wait(pe, taken[h], i * 5 + n)
                    cut = slice(h * HALF, (h + 1) * HALF)
                    o = c.ps[:, 6 + h]
                    if n == 0:
                        last = pe.matmul(o, lora_s[0:64, 0:P], c.lora_in[0:64, cut], start=True, stop=True)
                    elif n == 1:
                        last = pe.matmul(o, lora_s[64:128, 0:P], c.lora_in[64:128, cut], start=True, stop=True)
                    else:
                        pe.matmul(o, lora_s[:, P:2 * P], c.gate_in[:, cut], start=True, stop=False)
                        last = pe.matmul(o, lora_s[0:32, 2 * P:3 * P], c.gate_in2[0:32, cut], start=False, stop=True)
                    last.then_inc(aux[h], 1)

                def sums_of(i, h):
                    wait(pe, taken[h], i * 5 + 3)
                    pe.wait_ge(squared, i * 2 + (h + 1))
                    pe.matmul(c.ps[:, 6 + h], c.ones_64[:], root[:], start=True, stop=True).then_inc(aux[h], 1)
                    wait(pe, taken[h], i * 5 + 4)
                    pe.wait_ge(keyed, i * 2 + (h + 1))
                    pe.matmul(c.ps[:, 6 + h], c.ones_64[:], rk[:], start=True, stop=True).then_inc(aux[h], 1)

                def turn(i):
                    for u in range(3):
                        weights.ready(pe, i, u)
                        wait(pe, copied, i * 6 + (2 * u - 4))
                        weights.multiply(pe, u, [c.ps[:, 2 * u], c.ps[:, 2 * u + 1]], c.h_hi, c.h_lo).then_inc(c.tile_done, 1)
                        if u == 1:
                            if not first(i):
                                sums_of(i - 1, 1)
                            pe.wait_ge(staged, i + 1)
                            for n in range(3):
                                for h in range(2):
                                    lora(i, n, h)
                    sums_of(i, 0)

                rolled(pe, CT, turn)
                sums_of(CT - 1, 1)

            @block.scalar
            def _(act):
                act.wait_ge(c.lora_loaded, 64)
                act.wait_ge(cleared, 4)
                a = c.a_steps

                def copies(i, n):
                    weights.done(act, i, n)
                    for h in range(2):
                        wait(act, mixed, (i - 1) * 6 + (3 * h + n + 1) if not first(i) else 0)
                        flat = c.ps[:, 2 * n:2 * n + 2].rearrange("p b m -> p (b m)")
                        if h == 0:
                            act.copy(plain[n][0][:, 1:HALF + 1], flat[:, 0:HALF]).then_inc(copied, 1)
                        else:
                            act.copy(plain[n][1][:], flat[:, HALF - 1:SEQ]).then_inc(copied, 1)

                def half(i, h):
                    act.wait_ge(mixed, i * 6 + (3 * h + 1))
                    if h == 0:
                        wait(act, made, i * 2)
                    else:
                        act.wait_ge(made, i * 2 + 1)
                    act.activation(root[:], kk[:], ACT.Square).then_inc(squared, 1)
                    act.wait_ge(aux[h], i * 5 + 4)
                    act.activation(root[:], c.ps[:, 6 + h], ACT.Sqrt, bias=c.eps[:, 3:4]).then_inc(taken[h], 1)
                    act.wait_ge(decayed, i * 2 + (h + 1))
                    act.activation(l_prev[:], l_prev[:], ACT.Exp)
                    act.activation(e_neg[:], l_b[:], ACT.Exp, scale=-1.0).then_inc(negated, 1)
                    act.wait_ge(negated, i * 2 + (h + 1))
                    act.activation(l_b[:], l_b[:], ACT.Exp).then_inc(exps, 1)

                def turn(i):
                    wait(act, aux[1], i * 5 - 2)
                    apart(c, act)
                    at_i = columns(i, P)
                    a.mark(act.copy(lora_s[:, 0:P], c.lora_w[:, at_i]))
                    a.mark(act.copy(lora_s[:, P:2 * P], c.gate_w[:, at_i]))
                    a.mark(act.copy(lora_s[0:32, 2 * P:3 * P], c.gate_in2[32:64, at_i]))
                    a.wait(act)
                    act.sem_inc(staged, 1)
                    for n in range(2):
                        copies(i, n)
                    if not first(i):
                        half(i - 1, 1)
                    for n, (dst, bias) in enumerate(((log_w, vec(c, "w0", i)), (a_gate, vec(c, "a0", i)))):
                        for h in range(2):
                            act.wait_ge(aux[h], i * 5 + (n + 1))
                            wait(act, made, (i - 1) * 2 + (h + 1) if not first(i) else 0)
                            apart(c, act)
                            act.activation(dst[:, h * HALF:(h + 1) * HALF], c.ps[:, 6 + h], ACT.Sigmoid,
                                           bias=bias).then_inc(taken[h], 1)
                    for h in range(2):
                        act.wait_ge(aux[h], i * 5 + 3)
                        wait(act, stored, i * (16 * 14) + (h - 1) * 16 * 7 if not first(i) else 0)
                        act.copy(gate[:, h * HALF:(h + 1) * HALF], c.ps[:, 6 + h]).then_inc(taken[h], 1)
                    copies(i, 2)
                    half(i, 0)

                rolled(act, CT, turn, a)
                half(CT - 1, 1)

            @block.vector
            def _(dve):
                v = c.v_steps
                mu = c.col["mu_shift"]
                dve.wait_ge(cleared, 4)

                def mix(i, n, h, dst):
                    p = plain[n][h]
                    dve.wait_ge(copied, i * 6 + (2 * n + h + 1))
                    v.mark(dve.tensor_tensor(dst[:], p[:, 0:HALF], p[:, 1:HALF + 1], ALU.subtract))
                    v.wait(dve)
                    col = i + (mu + order[n])
                    scale = c.vec[:, col:col + 1] if isinstance(i, int) else c.vec[:, bass.ds(col, 1)]
                    v.mark(dve.scalar_tensor_tensor(out=dst[:], in0=dst[:], scalar=scale, in1=p[:, 1:HALF + 1],
                                                    op0=ALU.mult, op1=ALU.add))
                    v.wait(dve)

                def half(i, h):
                    cut = slice(h * HALF, (h + 1) * HALF)
                    if h == 0:
                        wait(dve, stored, i * (16 * 14))
                    else:
                        dve.wait_ge(stored, i * (16 * 14) + 16 * 7)
                    mix(i, 0, h, k)
                    dve.tensor_scalar(kk[:], k[:], vec(c, "k_k", i), None, ALU.mult).then_inc(mixed, 1)
                    dve.wait_ge(taken[h], i * 5 + 2)
                    v.mark(dve.tensor_scalar(log_w[:, cut], log_w[:, cut], DECAY, None, ALU.mult))
                    v.wait(dve)
                    for q in range(HALF // P):
                        chunk = slice(q * P, (q + 1) * P)
                        v.mark(dve.tensor_tensor_scan(l_b[:, chunk], c.ones[:], log_w[:, cut][:, chunk], 0.0,
                                                      ALU.mult, ALU.add))
                    v.wait(dve)
                    chunks = l_b[:].rearrange("p (t n) -> p t n", n=P)
                    t0 = h * (TILES // 2)
                    mids = c.lmid[:, bass.ds(i, 1), t0:t0 + 4].rearrange("p a t -> p (a t)")
                    v.mark(dve.tensor_copy(mids, chunks[:, :, mid]))
                    v.wait(dve)
                    v.mark(dve.tensor_tensor(chunks, chunks, mids.unsqueeze(2).broadcast_to([P, 4, P]), ALU.subtract))
                    v.wait(dve)
                    v.mark(dve.tensor_copy(c.lend[:, bass.ds(i, 1), t0:t0 + 4].rearrange("p a t -> p (a t)"),
                                           chunks[:, :, P - 1]))
                    v.mark(dve.tensor_tensor(l_prev[:], l_b[:], log_w[:, cut], ALU.subtract))
                    v.wait(dve)
                    dve.sem_inc(decayed, 1)
                    v.mark(dve.tensor_scalar(kf[:], a_gate[:, cut], -1.0, vec(c, "k_a", i), ALU.add, ALU.mult))
                    v.wait(dve)
                    v.mark(dve.scalar_tensor_tensor(out=kf[:], in0=kf[:], scalar=1.0, in1=k[:], op0=ALU.add, op1=ALU.mult))
                    mix(i, 1, h, r)
                    dve.sem_inc(mixed, 1)
                    v.mark(dve.scalar_tensor_tensor(out=rk[:], in0=r[:], scalar=vec(c, "r_k", i), in1=kf[:],
                                                    op0=ALU.mult, op1=ALU.mult))
                    v.wait(dve)
                    dve.sem_inc(keyed, 1)
                    mix(i, 2, h, v_b)
                    dve.sem_inc(mixed, 1)
                    dve.wait_ge(taken[h], i * 5 + 4)
                    v.mark(dve.tensor_scalar(root[:], root[:], 1e-12, None, ALU.max))
                    v.wait(dve)
                    v.mark(dve.reciprocal(root[:], root[:]))
                    v.wait(dve)
                    v.mark(dve.tensor_tensor(kk[:], kk[:], root[:], ALU.mult))
                    v.wait(dve)
                    v.mark(dve.tensor_tensor(b_b[:], kk[:], a_gate[:, cut], ALU.mult))
                    dve.wait_ge(aux[h], i * 5 + 5)
                    v.mark(dve.tensor_tensor(bonus[:], c.ps[:, 6 + h], v_b[:], ALU.mult))
                    v.wait(dve)
                    dve.sem_inc(taken[h], 1)
                    dve.wait_ge(exps, i * 2 + (h + 1))
                    v.mark(dve.tensor_tensor(r[:], r[:], l_b[:], ALU.mult))
                    v.mark(dve.scalar_tensor_tensor(out=kk[:], in0=kk[:], scalar=-1.0, in1=l_prev[:], op0=ALU.mult, op1=ALU.mult))
                    v.mark(dve.tensor_tensor(kf[:], kf[:], e_neg[:], ALU.mult))
                    v.mark(dve.tensor_tensor(b_b[:], b_b[:], e_neg[:], ALU.mult))
                    v.wait(dve)
                    dve.sem_inc(made, 1)

                def turn(i):
                    for h in range(2):
                        half(i, h)

                rolled(dve, CT, turn, v)
                v.mark(dve.tensor_tensor(c.lend[:], c.lend[:], c.lmid[:, :, 1:TILES + 1], ALU.add))

    return weights, build


def make_levels(c, pool):
    g = c.g_steps
    g.mark(pool.memset(c.level[:], 0.0))
    for n in range(LEVELS):
        s = 1 << n
        blocks = P // (2 * s)
        quarter = c.level[:, n, :].rearrange("p (b w) -> p b w", w=2 * s)[:, :, 0:s]
        g.wait(pool)
        g.mark(pool.memset(quarter, 1.0))
        for pattern, base, sign in (([[-2 * s, blocks], [0, s]], -s, 1), ([[2 * s, blocks], [0, s]], 2 * s - 1, -1)):
            g.wait(pool)
            g.mark(pool.affine_select(out=quarter, in_=quarter, compare_op=ALU.is_ge, fill=0.0, base=base,
                                      pattern=pattern, channel_multiplier=sign))
    g.wait(pool)


LEVELS = 7
LEVEL_PE = [f"{what}{n}" for n in range(1, LEVELS) for what in ("x", "t")]
LEVEL_DVE = [f"{what}{n}" for n in range(1, LEVELS) for what in (("xm", "t", "tt") if n < LEVELS - 1 else ("xm", "tt"))]


def side_of(buf, n, which):
    return buf.rearrange("p (b two s) -> p b two s", two=2, s=1 << n)[:, :, which]


def inverse_pe(pe, n, products, masks, i, dve_events, banks, n_t, t):
    pe.wait_ge(masks, nth(dve_events, "tt0" if n == 1 else f"tt{n - 1}", i))
    for h in range(4):
        cut = slice(h * P, (h + 1) * P)
        last = pe.matmul(banks[0][:, cut], n_t[:, h], t[:, h], start=True, stop=True)
    last.then_inc(products, 1)


def inverse_pe_update(pe, n, products, masks, i, dve_events, banks, t, t_t, x):
    pe.wait_ge(masks, nth(dve_events, f"xm{n}", i))
    for h in range(4):
        cut = slice(h * P, (h + 1) * P)
        if n < LEVELS - 1:
            pe.matmul(banks[1][:, cut], t_t[:, h], x[:, h], start=True, stop=True)
        last = pe.matmul(banks[2][:, cut], x[:, h], t_t[:, h], start=True, stop=True)
    last.then_inc(products, 1)


def heads_of(bank):
    return bank.rearrange("p (h n) -> p h n", n=P)


def inverse_start_dve(c, dve, masks, i, dve_events, n_plain, n_t, t, t_t):
    def over_heads(m):
        return m.unsqueeze(1).broadcast_to([P, 4, P])

    dve.wait_ge(masks, nth(dve_events, "n", i))
    dve.tensor_tensor(t[:], n_plain[:], over_heads(c.level[:, 0]), ALU.mult).then_inc(masks, 1)
    dve.wait_ge(masks, nth(dve_events, "t_block", i))
    dve.tensor_tensor(t[:], t[:], over_heads(c.ident[:]), ALU.add).then_inc(masks, 1)
    dve.wait_ge(masks, nth(dve_events, "n_t", i))
    dve.tensor_tensor(t_t[:], n_t[:], over_heads(c.level_t[:]), ALU.mult).then_inc(masks, 1)
    dve.wait_ge(masks, nth(dve_events, "tt_block", i))
    dve.tensor_tensor(t_t[:], t_t[:], over_heads(c.ident[:]), ALU.add).then_inc(masks, 1)


def inverse_mask_dve(c, dve, n, products, masks, i, pe_events, banks, x):
    dve.wait_ge(products, nth(pe_events, f"x{n}", i))
    dve.tensor_tensor(x[:], heads_of(banks[0]), c.level[:, n].unsqueeze(1).broadcast_to([P, 4, P]),
                      ALU.mult).then_inc(masks, 1)


def inverse_add_dve(dve, n, products, masks, i, pe_events, banks, t, t_t):
    dve.wait_ge(products, nth(pe_events, f"t{n}", i))
    for bank, buf, which in ((banks[1], t, 0), (banks[2], t_t, 1)):
        if which or n < LEVELS - 1:
            dst = side_of(buf[:].rearrange("p h n -> p (h n)"), n, which)
            dve.tensor_tensor(dst, dst, side_of(bank, n, which), ALU.add).then_inc(masks, 1)


def rwkv_scan(c, following):
    nc = c.nc
    base = 0

    def buf(name, shape):
        nonlocal base
        b = at(c, base, f"scan_{name}", shape)
        n = 4
        for m in shape[1:]:
            n *= m
        base += n
        return b

    a_r, k_in, b_in, v_in = (buf("a_r", [P, 2, CT, 2, P]), buf("k", [P, 2, CT, P]), buf("b", [P, 2, CT, P]),
                             buf("v", [P, 2, CT, P]))
    nat = {n: buf(f"{n}_nat", [P, CT, P]) for n in "vkb"}
    groups = range(2)
    ak, rk, ab, rb, n_p = ([buf(f"{n}{g}", [P, 4, P]) for g in groups] for n in ("ak", "rk", "ab", "rb", "n"))
    t, t_t, x = ([buf(f"{n}{g}", [P, 4, P]) for g in groups] for n in ("t", "tt", "x"))
    u_b = [buf(f"u{g}", [P, 2, 2 * P]) for g in groups]
    sa = [buf(f"sa{g}", [P, 2, P]) for g in groups]
    state = buf("state", [P, CT, P])
    factor = c.lend
    assert c.aux_base + base <= 229376
    y_t = c.nc.alloc_sbuf_tensor_at("y_t", [P, CT, SEQ], F32, offset=c.w_base)
    c.level = c.nc.alloc_sbuf_tensor_at("scan_level", [P, LEVELS, P], F32, offset=c.w_base + 16384)
    v_two = c.nc.alloc_sbuf_tensor_at("scan_v_two", [P, CT, 2 * P], F32, offset=c.w_base + 16384 + 3584)

    def own(two):
        return two.rearrange("p c (x y) -> p c x y", y=64)[:, :, 0:4:3]

    PE_EVENTS = ["n", "k", "b"] + LEVEL_PE
    DVE_EVENTS = ["n", "ak", "rk", "n_t", "rb", "t_block", "t0", "tt_block", "tt0"] + LEVEL_DVE
    CHAIN_PE, CHAIN_DVE, CHAIN_ACT = ["u", "sa", "s", "y"], ["s_sum", "s_new"], ["u", "sa", "y"]
    loaded = [c.sem("scan_loaded0"), c.sem("scan_loaded1")]
    turned, natural, cleared = c.sem("scan_turned"), c.sem("scan_natural"), c.sem("scan_cleared")
    products, masks = ([c.sem(f"scan_{n}{g}") for g in groups] for n in ("products", "masks"))
    chained, copies, states = ([c.sem(f"scan_{n}{e}") for e in groups] for n in ("chained", "copies", "states"))
    factored, stored = c.sem("scan_factored"), c.sem("scan_stored")
    y_out = scratch(c, "rwkv_y", [CT, P, SEQ]).rearrange("a p n -> p a n")
    ps = c.ps
    src = [c.scratch[f"rwkv_{n}"].rearrange("a p n -> p a n") for n in STORED[:5]]
    level_banks = [(ps[:, g], ps[:, 2 + g], ps[:, 4 + g]) for g in groups]
    n_bank = [4, 5]
    k_banks = [slice(0, 2), slice(6, 8)]
    b_banks = [slice(2, 4), slice(4, 6)]
    turns = TILES // 2

    with nc.Block() as block:

        @block.sync
        def _(sp):
            def turn(j):
                for q in range(2):
                    i = j * 2 + q
                    if not first(j):
                        for e in groups:
                            sp.wait_ge(chained[e], nth(CHAIN_PE, "y", i - 2))
                        apart(c, sp)
                        store(i - 2)
                    cut = columns(i, P)
                    for part, dst in zip(src, (a_r[:, q, :, 0], a_r[:, q, :, 1], k_in[:, q], b_in[:, q], v_in[:, q])):
                        sp.dma_start(dst, part[:, :, cut]).then_inc(loaded[q], 16)

            def store(i):
                for e in groups:
                    sp.wait_ge(copies[e], nth(CHAIN_ACT, "y", i))
                apart(c, sp)
                sp.dma_start(y_out[:, :, columns(i, P)], y_t[:, :, columns(i, P)]).then_inc(stored, 16)

            rolled(sp, turns, turn)
            following.load_first(sp)
            for i in (TILES - 2, TILES - 1):
                store(i)
            sp.wait_ge(stored, 16 * TILES)

        @block.gpsimd
        def _(pool):
            for g in groups:
                for m in (ak[g], rk[g], ab[g], rb[g], n_p[g], u_b[g]):
                    pool.memset(m[:], 0.0).then_inc(cleared, 1)
            pool.memset(v_two[:], 0.0).then_inc(cleared, 1)
            make_levels(c, pool)
            pool.memset(state[:], 0.0).then_inc(cleared, 1)

        @block.tensor
        def _(pe):
            pe.wait_ge(cleared, 14)

            def scores(q, i):
                rows = [slice(0, 64), slice(64, P)]
                for ct in range(CT):
                    for g in groups:
                        last = pe.matmul(ps[:, n_bank[g], ct * P:(ct + 1) * P], a_r[rows[g], q, ct, 0],
                                         b_in[rows[g], q, ct], start=True, stop=True)
                        if ct == CT - 1:
                            last.then_inc(products[g], 1)
                pe.wait_ge(natural, i * 4 + 4)
                for operand, banks in ((k_in, k_banks), (b_in, b_banks)):
                    if operand is b_in:
                        for g in groups:
                            pe.wait_ge(masks[g], nth(DVE_EVENTS, "n", i))
                    for ct in range(CT):
                        for g in groups:
                            pair = ps[:, banks[g]].rearrange("p b (h m) -> p (b h) m", m=2 * P)
                            last = pe.matmul(pair[:, ct], operand[rows[g], q, ct],
                                             a_r[rows[g], q, ct].rearrange("p a n -> p (a n)"), start=True, stop=True)
                            if ct == CT - 1:
                                last.then_inc(products[g], 1)

            def chunk(i, q, use):
                pe.wait_ge(loaded[q], use * 80 + 80)
                for e in groups:
                    wait(pe, states[e], nth(CHAIN_DVE, "s_new", i - 1))
                    wait(pe, copies[e], nth(CHAIN_ACT, "y", i - 1))
                for b, (n, part) in enumerate((("v", v_in), ("k", k_in), ("b", b_in))):
                    for ct in range(CT):
                        last = pe.transpose(ps[:, (3, 6, 7)[b], ct * P:(ct + 1) * P], part[:, q, ct], c.ident[:])
                    last.then_inc(turned, 1)
                scores(q, i)
                for g in groups:
                    pe.wait_ge(masks[g], nth(DVE_EVENTS, "rk", i))
                for e in groups:
                    out = ps[:, 6 + e]
                    for k in range(2):
                        ct = 2 * e + k
                        pe.matmul(out[:, k * P:(k + 1) * P], a_r[:, q, ct, 0], state[:, ct], start=True, stop=False,
                                  skip_group_check=True)
                        for g in groups:
                            last = pe.matmul(out[:, k * P:(k + 1) * P], ak[g][:, ct], v_two[:, ct, g * P:(g + 1) * P],
                                             start=False, stop=g == 1, skip_group_check=True)
                    last.then_inc(chained[e], 1)
                for n in range(1, LEVELS):
                    for g in groups:
                        if n == 1:
                            pe.wait_ge(masks[1], nth(DVE_EVENTS, "rb", i))
                        inverse_pe(pe, n, products[g], masks[g], i, DVE_EVENTS, level_banks[g], ab[g], t[g])
                    for g in groups:
                        inverse_pe_update(pe, n, products[g], masks[g], i, DVE_EVENTS, level_banks[g], t[g], t_t[g], x[g])
                for g in groups:
                    pe.wait_ge(masks[g], nth(DVE_EVENTS, f"tt{LEVELS - 1}", i))
                for e in groups:
                    pe.wait_ge(copies[e], nth(CHAIN_ACT, "u", i))
                    for k in range(2):
                        for g in groups:
                            last = pe.matmul(ps[:, e, k * P:(k + 1) * P], t_t[g][:, 2 * e + k], u_b[e][:, k, g * P:(g + 1) * P],
                                             start=g == 0, stop=g == 1, skip_group_check=True)
                    last.then_inc(chained[e], 1)
                for e in groups:
                    pe.wait_ge(copies[e], nth(CHAIN_ACT, "sa", i))
                    for k in range(2):
                        ct = 2 * e + k
                        o = ps[:, 2 + e, k * P:(k + 1) * P]
                        pe.matmul(o, nat["b"][:, ct], sa[e][:, k], start=True, stop=False, skip_group_check=True)
                        last = pe.matmul(o, nat["k"][:, ct], nat["v"][:, ct], start=False, stop=True, skip_group_check=True)
                    last.then_inc(chained[e], 1)
                    for k in range(2):
                        ct = 2 * e + k
                        cut = slice(k * P, (k + 1) * P)
                        pe.matmul(ps[:, 4 + e, cut], state[:, ct], a_r[:, q, ct, 1], start=True, stop=False,
                                  skip_group_check=True)
                        for g in groups:
                            rows = slice(64 * g, 64 * g + 64)
                            pe.matmul(ps[rows, 4 + e, cut], sa[e][:, k, rows], rb[g][:, ct], start=False,
                                      stop=False, skip_group_check=True)
                            last = pe.matmul(ps[rows, 4 + e, cut], nat["v"][:, ct, rows], rk[g][:, ct], start=False,
                                             stop=True, skip_group_check=True)
                    last.then_inc(chained[e], 1)

            def turn(j):
                for q in range(2):
                    chunk(j * 2 + q, q, j)

            rolled(pe, turns, turn)

        @block.scalar
        def _(act):
            act.activation(factor[:], c.lend[:], ACT.Exp).then_inc(factored, 1)

            def chunk(i):
                for b, n in enumerate("vkb"):
                    act.wait_ge(turned, i * 3 + (b + 1))
                    act.copy(nat[n][:], heads_of(ps[:, (3, 6, 7)[b]])).then_inc(natural, 1)
                    if n == "v":
                        act.copy(own(v_two[:]), ps[:, 3].rearrange("p (c x y) -> p c x y", x=2, y=64)).then_inc(natural, 1)
                for bank, name, into in ((6, "u", u_b), (0, "sa", sa), (4, "y", None)):
                    for e in groups:
                        act.wait_ge(chained[e], nth(CHAIN_PE, name, i))
                        if name == "y":
                            apart(c, act)
                            dst = y_t[:, 2 * e:2 * e + 2, columns(i, P)]
                        else:
                            dst = into[e][:]
                        src_ = ps[:, bank + e, 0:2 * P]
                        if name == "u":
                            act.copy(own(dst), src_.rearrange("p (k x y) -> p k x y", x=2, y=64)).then_inc(copies[e], 1)
                        else:
                            act.copy(dst, src_.rearrange("p (k n) -> p k n", n=P)).then_inc(copies[e], 1)

            def turn(j):
                for q in range(2):
                    chunk(j * 2 + q)

            rolled(act, turns, turn)

        @block.vector
        def _(dve):
            dve.wait_ge(cleared, 14)
            dve.wait_ge(factored, 1)

            def over(m):
                return m[:].unsqueeze(1).broadcast_to([P, 4, P]).bitcast(mybir.dt.int32)

            def pair(banks):
                return ps[:, banks].rearrange("p b (h a n) -> p (b h) a n", a=2, n=P)

            def chunk(i):
                for e in groups:
                    wait(dve, chained[e], nth(CHAIN_PE, "y", i - 1))
                for g in groups:
                    dve.wait_ge(products[g], nth(PE_EVENTS, "n", i))
                    apart(c, dve)
                    dve.copy_predicated(n_p[g][:], over(c.lower), heads_of(ps[:, n_bank[g]])).then_inc(masks[g], 1)
                for g in groups:
                    dve.wait_ge(products[g], nth(PE_EVENTS, "k", i))
                    apart(c, dve)
                    dve.copy_predicated(ak[g][:], over(c.upper), pair(k_banks[g])[:, :, 0]).then_inc(masks[g], 1)
                    dve.copy_predicated(rk[g][:], over(c.upper_eq), pair(k_banks[g])[:, :, 1]).then_inc(masks[g], 1)
                for g in groups:
                    dve.wait_ge(products[g], nth(PE_EVENTS, "b", i))
                    apart(c, dve)
                    dve.copy_predicated(ab[g][:], over(c.upper), pair(b_banks[g])[:, :, 0]).then_inc(masks[g], 1)
                    dve.copy_predicated(rb[g][:], over(c.upper_eq), pair(b_banks[g])[:, :, 1]).then_inc(masks[g], 1)
                for g in groups:
                    inverse_start_dve(c, dve, masks[g], i, DVE_EVENTS, n_p[g], ab[g], t[g], t_t[g])
                for n in range(1, LEVELS):
                    for g in groups:
                        inverse_mask_dve(c, dve, n, products[g], masks[g], i, PE_EVENTS, level_banks[g], x[g])
                    for g in groups:
                        inverse_add_dve(dve, n, products[g], masks[g], i, PE_EVENTS, level_banks[g], t[g], t_t[g])
                for e in groups:
                    two = slice(2 * e, 2 * e + 2)
                    dve.wait_ge(chained[e], nth(CHAIN_PE, "y", i))
                    dve.tensor_tensor(state[:, two], state[:, two], ps[:, 2 + e, 0:2 * P].rearrange("p (k n) -> p k n", n=P),
                                      ALU.add).then_inc(states[e], 1)
                    dve.wait_ge(states[e], nth(CHAIN_DVE, "s_sum", i))
                    for k in range(2):
                        last = dve.scalar_tensor_tensor(
                            out=state[:, 2 * e + k], in0=state[:, 2 * e + k],
                            scalar=factor[:, 2 * e + k, bass.ds(i, 1)], in1=c.ones_64[:], op0=ALU.mult, op1=ALU.mult)
                    last.then_inc(states[e], 1)

            def turn(j):
                for q in range(2):
                    chunk(j * 2 + q)

            rolled(dve, turns, turn)


def tail(c, off, name, shape, dt=F32):
    return at(c, 2 * BRANCH + off, name, shape, dt)


BRANCH = KT * SEQ * 4


def place(buf, i, h):
    return buf[:, bass.ds(i, 1), h * HALF:(h + 1) * HALF].rearrange("p a n -> p (a n)")


class RwkvOutput:

    def __init__(self, c):
        self.c = c
        free = 4 * CT * SEQ
        self.dev, self.root, self.bonus, self.gate, self.y, self.sq = (
            at(c, free + 2048 * n, f"ro_{name}", [P, HALF]) for n, name in enumerate(("dev", "root", "bonus", "gate", "y", "sq")))
        self.centred, self.squared, self.rooted = c.sem("ro_centred"), c.sem("ro_squared"), c.sem("ro_rooted")
        self.summed, self.made, self.rounded, self.split = (c.sem(f"ro_{n}") for n in ("summed", "made", "rounded", "split"))
        self.loaded = c.sem("ro_loaded")
        self.src = [c.scratch[f"rwkv_{n}"] for n in ("y", "bonus_t", "gate_t")]

    def load(self, sp, i, h):
        wait(sp, self.made, i * 2 + h)
        apart(self.c, sp)
        cut = slice(h * HALF, (h + 1) * HALF)
        for part, dst in zip(self.src, (self.y, self.bonus, self.gate)):
            sp.dma_start(dst[:], part[bass.ds(i, 1), :, cut].rearrange("a p n -> p (a n)")).then_inc(self.loaded, 16)

    def pe_before(self, pe, i, h):
        pe.wait_ge(self.loaded, i * 96 + (48 * h + 48))
        wait(pe, self.centred, i * 2 + h)
        pe.matmul(self.c.ps[:, 4], self.c.ones_64[:], self.y[:], start=True, stop=True).then_inc(self.summed, 1)

    def pe_after(self, pe, i, h):
        pe.wait_ge(self.squared, i * 2 + (h + 1))
        wait(pe, self.rooted, i * 2 + h)
        pe.matmul(self.c.ps[:, 5], self.c.ones_64[:], self.sq[:], start=True, stop=True).then_inc(self.summed, 1)

    def act_before(self, act, i, h):
        act.wait_ge(self.centred, i * 2 + (h + 1))
        wait(act, self.summed, i * 4 + 2 * h)
        act.activation(self.sq[:], self.dev[:], ACT.Square).then_inc(self.squared, 1)

    def act_after(self, act, i, h):
        act.wait_ge(self.summed, i * 4 + (2 * h + 2))
        wait(act, self.made, i * 2 + h)
        act.activation(self.root[:], self.c.ps[:, 5], ACT.Sqrt, bias=self.c.eps[:, 1:2], scale=1.0 / HEAD).then_inc(self.rooted, 1)

    def act_late(self, act, i, h):
        act.wait_ge(self.made, i * 2 + (h + 1))
        apart(self.c, act)
        act.copy(place(self.c.br_hi, i, h), self.dev[:]).then_inc(self.rounded, 1)

    def dve(self, dve, i, h):
        c, v, dev = self.c, self.c.v_steps, self.dev[:]
        dve.wait_ge(self.summed, i * 4 + (2 * h + 1))
        wait(dve, self.split, i * 2 + h)
        dve.scalar_tensor_tensor(out=dev, in0=c.ps[:, 4], scalar=-1.0 / HEAD, in1=self.y[:],
                                 op0=ALU.mult, op1=ALU.add).then_inc(self.centred, 1)
        dve.wait_ge(self.rooted, i * 2 + (h + 1))
        v.mark(dve.reciprocal(self.root[:], self.root[:]))
        v.wait(dve)
        v.mark(dve.tensor_tensor(dev, dev, self.root[:], ALU.mult))
        v.wait(dve)
        v.mark(dve.tensor_scalar(dev, dev, vec(c, "ln_x_w", i), vec(c, "ln_x_b", i), ALU.mult, ALU.add))
        v.wait(dve)
        v.mark(dve.tensor_tensor(dev, dev, self.bonus[:], ALU.add))
        v.wait(dve)
        dve.tensor_tensor(dev, dev, self.gate[:], ALU.mult).then_inc(self.made, 1)
        dve.wait_ge(self.rounded, i * 2 + (h + 1))
        dve.tensor_tensor(place(c.br_lo, i, h), dev, place(c.br_hi, i, h).bitcast(F32), ALU.subtract).then_inc(self.split, 1)


class DeltaOutput:

    def __init__(self, c):
        self.c = c
        self.o, self.z, self.sq = (tail(c, 2048 * n, f"do_{name}", [P, HALF]) for n, name in enumerate(("o", "z", "sq")))
        self.root = self.sq
        self.squared, self.rooted, self.summed = c.sem("do_squared"), c.sem("do_rooted"), c.sem("do_summed")
        self.loaded, self.made, self.rounded, self.split = (c.sem(f"do_{n}") for n in ("loaded", "made", "rounded", "split"))
        self.src = [c.scratch[f"second_{n}"] for n in ("oa", "z")]

    def load(self, sp, i, h):
        wait(sp, self.split, i * 2 + h)
        apart(self.c, sp)
        cut = slice(h * HALF, (h + 1) * HALF)
        for part, dst in zip(self.src, (self.o, self.z)):
            sp.dma_start(dst[:], part[bass.ds(i, 1), :, cut].rearrange("a p n -> p (a n)")).then_inc(self.loaded, 16)

    def pe_before(self, pe, i, h):
        pass

    def pe_after(self, pe, i, h):
        pe.wait_ge(self.squared, i * 2 + (h + 1))
        wait(pe, self.rooted, i * 2 + h)
        pe.matmul(self.c.ps[:, 4], self.c.ones[:], self.sq[:], start=True, stop=True).then_inc(self.summed, 1)

    def act_before(self, act, i, h):
        act.wait_ge(self.loaded, i * 64 + (32 * h + 32))
        wait(act, self.made, i * 2 + h)
        act.activation(self.sq[:], self.o[:], ACT.Square).then_inc(self.squared, 1)

    def act_after(self, act, i, h):
        act.wait_ge(self.summed, i * 2 + (h + 1))
        act.activation(self.root[:], self.c.ps[:, 4], ACT.Sqrt, bias=self.c.eps[:, 0:1], scale=1.0 / P).then_inc(self.rooted, 1)

    def act_late(self, act, i, h):
        act.wait_ge(self.made, i * 2 + (h + 1))
        apart(self.c, act)
        act.copy(place(self.c.br_hi, i, h), self.o[:]).then_inc(self.rounded, 1)

    def dve(self, dve, i, h):
        c, v, o = self.c, self.c.v_steps, self.o[:]
        dve.wait_ge(self.rooted, i * 2 + (h + 1))
        v.mark(dve.reciprocal(self.root[:], self.root[:]))
        v.wait(dve)
        v.mark(dve.scalar_tensor_tensor(out=o, in0=o, scalar=vec(c, "dn_out_gain_2"), in1=self.root[:],
                                        op0=ALU.mult, op1=ALU.mult))
        v.wait(dve)
        dve.tensor_tensor(o, o, self.z[:], ALU.mult).then_inc(self.made, 1)
        dve.wait_ge(self.rounded, i * 2 + (h + 1))
        dve.tensor_tensor(place(c.br_lo, i, h), o, place(c.br_hi, i, h).bitcast(F32), ALU.subtract).then_inc(self.split, 1)


class ShortConv:

    def __init__(self, c, side, following):
        self.c, self.side, self.following = c, side, following
        tile = tile_of(c.dram["w_in"][0], RWKV_COLS)
        self.weights = Weights(c, [lambda i, o=o: tile(i, 1, o * CT) for o in (1, 2, 0)], CT)
        self.u, self.y = tail(c, 0, "conv_u", [P, HALF + 2]), tail(c, 2080, "conv_y", [P, HALF])
        self.copied, self.product, self.ended, self.made, self.rounded, self.split = (
            c.sem(f"conv_{n}") for n in ("copied", "product", "ended", "made", "rounded", "split"))

    def load(self, sp):
        self.weights.load_all(sp)
        sp.wait_ge(self.c.w_split, self.weights.t0 + self.weights.total)
        self.following.load_first(sp)

    def pe(self, pe):
        c, w = self.c, self.weights

        def turn(i):
            for n in range(3):
                w.ready(pe, i, n)
                wait(pe, (self.copied, self.product, self.made)[n], i * 2)
                w.multiply(pe, n, [c.ps[:, 2 * n], c.ps[:, 2 * n + 1]], c.h_hi, c.h_lo).then_inc(c.tile_done, 1)

        rolled(pe, CT, turn)

    def act(self, act):
        c = self.c
        act.wait_ge(self.side.split, 2 * CT)

        def turn(i):
            for h in range(2):
                self.weights.done(act, i, 0)
                wait(act, self.ended, i * 2 + h)
                act.copy(self.u[:, 2:HALF + 2], c.ps[:, h]).then_inc(self.copied, 1)
                act.wait_ge(self.made, i * 2 + (h + 1))
                apart(c, act)
                act.copy(place(c.br_hi, i + CT, h), self.y[:]).then_inc(self.rounded, 1)

        rolled(act, CT, turn)

    def dve(self, dve):
        c, v, u, y = self.c, self.c.v_steps, self.u, self.y

        def turn(i):
            v.mark(dve.memset(u[:, 0:2], 0.0))
            for h in range(2):
                self.weights.done(dve, i, 1)
                dve.wait_ge(self.copied, i * 2 + (h + 1))
                v.wait(dve)
                dve.tensor_tensor(u[:, 2:HALF + 2], u[:, 2:HALF + 2], c.ps[:, 2 + h], ALU.mult).then_inc(self.product, 1)
                dve.wait_ge(self.product, i * 2 + (h + 1))
                wait(dve, self.split, i * 2 + h)
                v.mark(dve.tensor_scalar(y[:], u[:, 2:HALF + 2], vec(c, "conv_w", i + 2 * CT), None, ALU.mult))
                for tap in (1, 0):
                    v.wait(dve)
                    v.mark(dve.scalar_tensor_tensor(out=y[:], in0=u[:, tap:HALF + tap], scalar=vec(c, "conv_w", i + tap * CT),
                                                    in1=y[:], op0=ALU.mult, op1=ALU.add))
                v.wait(dve)
                v.mark(dve.tensor_copy(u[:, 0:2], u[:, HALF:HALF + 2]))
                v.wait(dve)
                dve.sem_inc(self.ended, 1)
                self.weights.done(dve, i, 2)
                dve.tensor_tensor(y[:], y[:], c.ps[:, 4 + h], ALU.mult).then_inc(self.made, 1)
                dve.wait_ge(self.rounded, i * 2 + (h + 1))
                dve.tensor_tensor(place(c.br_lo, i + CT, h), y[:], place(c.br_hi, i + CT, h).bitcast(F32),
                                  ALU.subtract).then_inc(self.split, 1)

        rolled(dve, CT, turn, v)


def gates(c, name, w_in, first_column, bias):
    nc = c.nc
    tile = tile_of(w_in, first_column)
    per = 4
    weights = Weights(c, [lambda i, k=k, g=g: tile(i, 2, k + g * KT) for k in range(2) for g in range(2)], KT // 2)
    out = scratch(c, f"{name}_gates", [2, KT, P, SEQ])

    def build(side, sig, after=None, following=None):
        weights.begin()
        if after:
            after.weights.begin()
        gated = c.sem(f"{name}_gated")
        stored = [c.sem(f"{name}_stored{n}") for n in range(len(sig))]
        share = per // len(sig)
        with nc.Block() as block:

            @block.sync
            def _(sp):
                def store(i, u):
                    sp.wait_ge(gated, i * per + (u + 1))
                    apart(c, sp)
                    sp.dma_start(out[u % 2, bass.ds(i * 2 + u // 2, 1)].rearrange("a p n -> p (a n)"),
                                 sig[u % len(sig)]).then_inc(stored[u % len(sig)], 16)

                def turn(i, last=False):
                    for u in range(per):
                        if not (last and u >= 2):
                            sp.wait_ge(c.w_split, weights.t0 + i * per + (u + 1))
                            apart(c, sp)
                            weights.fetch(sp, (u + 2) % per, i + (u + 2) // per)
                        if u:
                            store(i, u - 1)
                        elif not first(i):
                            store(i - 1, per - 1)
                        if u == 1:
                            side.load(sp, i, 1)
                        if u == 3 and not last:
                            side.load(sp, i + 1, 0)

                side.load(sp, 0, 0)
                rolled(sp, weights.turns - 1, turn)
                turn(weights.turns - 1, last=True)
                store(weights.turns - 1, per - 1)
                if after:
                    after.load(sp)
                else:
                    following.load_first(sp)
                for n in range(len(sig)):
                    sp.wait_ge(stored[n], 16 * weights.turns * share)

            @block.gpsimd
            def _(pool):
                weights.split(pool)
                if after:
                    after.weights.split(pool)

            @block.tensor
            def _(pe):
                def turn(i):
                    for u in range(per):
                        if u % 2 == 0:
                            side.pe_before(pe, i, u // 2)
                        weights.ready(pe, i, u)
                        wait(pe, gated, i * per + (u - 1))
                        b = 2 * (u % 2)
                        weights.multiply(pe, u, [c.ps[:, b], c.ps[:, b + 1]], c.h_hi, c.h_lo).then_inc(c.tile_done, 1)
                        if u % 2 == 0:
                            side.pe_after(pe, i, u // 2)

                rolled(pe, weights.turns, turn)
                if after:
                    pe.wait_ge(gated, weights.total)
                    after.pe(pe)

            @block.scalar
            def _(act):
                def turn(i):
                    for u in range(per):
                        h = u // 2
                        if u % 2 == 0:
                            side.act_before(act, i, h)
                        else:
                            side.act_late(act, i, h)
                        weights.done(act, i, u)
                        wait(act, stored[u % len(sig)], i * (16 * share) + 16 * (u // len(sig)))
                        apart(c, act)
                        act.activation(sig[u % len(sig)], c.ps[:, 2 * (u % 2):2 * (u % 2) + 2].rearrange("p b n -> p (b n)"),
                                       ACT.Sigmoid, bias=vec(c, bias, i * 2 + (u // 2 + (u % 2) * KT))).then_inc(gated, 1)
                        if u % 2 == 0:
                            side.act_after(act, i, h)

                rolled(act, weights.turns, turn)
                if after:
                    after.act(act)

            @block.vector
            def _(dve):
                def turn(i):
                    for h in range(2):
                        side.dve(dve, i, h)

                rolled(dve, weights.turns, turn, c.v_steps)
                if after:
                    after.dve(dve)

    return weights, build


def merge(c, name, w_a, w_b):
    nc = c.nc
    top, low = w_a.rearrange("(k p) n -> p k n", p=P), w_b.rearrange("(k p) n -> p k n", p=P)
    weights = Weights(c, [lambda i, u=u: tuple(w[:, :, bass.ds(i * (2 * P) + u * P, P)] for w in (top, low)) for u in range(2)],
                      KT // 2)
    gate_b = tail(c, 0, f"{name}_gate_b", [P, 2, HALF])
    gate_a = c.w_raw[:, 2].rearrange("p (h k) n -> p h (k n)", h=2)
    src = c.scratch[f"{name}_gates"]

    def build(following):
        weights.begin()
        loaded, scaled, made = ([c.sem(f"{name}_{n}{h}") for h in range(2)] for n in ("loaded", "scaled", "made"))
        rounded, split = ([c.sem(f"{name}_{n}{h}") for h in range(2)] for n in ("rounded", "split"))
        with nc.Block() as block:

            @block.sync
            def _(sp):
                def turn(i, last=False):
                    for u in range(2):
                        for h in range(2):
                            wait(sp, split[h], i * 2 + u)
                            apart(c, sp)
                            for g, dst in enumerate((gate_a, gate_b)):
                                view = src[g, bass.ds(i * 2 + u, 1), :, h * HALF:(h + 1) * HALF]
                                sp.dma_start(dst[:, h], view.rearrange("a p n -> p (a n)")).then_inc(loaded[h], 16)
                        if not last:
                            sp.wait_ge(c.w_split, weights.t0 + i * 2 + (u + 1))
                            apart(c, sp)
                            weights.fetch(sp, u, i + 1)

                rolled(sp, weights.turns - 1, turn)
                turn(weights.turns - 1, last=True)
                sp.wait_ge(c.w_split, weights.t0 + weights.total)
                following.load_first(sp)

            @block.gpsimd
            def _(pool):
                weights.split(pool)

            @block.tensor
            def _(pe):
                def turn(i):
                    for u in range(2):
                        weights.ready(pe, i, u)
                        for h in range(2):
                            wait(pe, scaled[h], i * 4 + (2 * u - 2))
                        b = 4 * u
                        weights.multiply(pe, u, [c.ps[:, b], c.ps[:, b + 1]], c.br_hi, c.br_lo, kts=range(KT // 2))
                        weights.multiply(pe, u, [c.ps[:, b + 2], c.ps[:, b + 3]], c.br_hi, c.br_lo,
                                         kts=range(KT // 2, KT)).then_inc(c.tile_done, 1)

                rolled(pe, weights.turns, turn)

            @block.scalar
            def _(act):
                def turn(i):
                    for u in range(2):
                        for h in range(2):
                            act.wait_ge(made[h], i * 2 + (u + 1))
                            apart(c, act)
                            act.copy(place(c.h_hi, i * 2 + u, h), gate_a[:, h]).then_inc(rounded[h], 1)

                rolled(act, weights.turns, turn)

            @block.vector
            def _(dve):
                def turn(i):
                    for u in range(2):
                        weights.done(dve, i, u)
                        for h in range(2):
                            dve.wait_ge(loaded[h], i * 64 + (32 * u + 32))
                            for g, buf in enumerate((gate_a, gate_b)):
                                dve.tensor_tensor(buf[:, h], buf[:, h], c.ps[:, 4 * u + 2 * g + h], ALU.mult).then_inc(scaled[h], 1)
                        for h in range(2):
                            dve.wait_ge(scaled[h], i * 4 + (2 * u + 2))
                            dve.tensor_tensor(gate_a[:, h], gate_a[:, h], gate_b[:, h], ALU.add).then_inc(made[h], 1)
                        for h in range(2):
                            dve.wait_ge(rounded[h], i * 2 + (u + 1))
                            hi = place(c.h_hi, i * 2 + u, h)
                            dve.tensor_tensor(place(c.h_lo, i * 2 + u, h), gate_a[:, h], hi.bitcast(F32),
                                              ALU.subtract).then_inc(split[h], 1)

                rolled(dve, weights.turns, turn)

    return weights, build


def residual_weights(c, w):
    tile = tile_of(w)
    return Weights(c, [lambda i, u=u: tile(i, 2, u) for u in range(2)], KT // 2)


N_XHEADS = 4
XD = D // N_XHEADS


def memory_keys(c):
    nc, d = c.nc, c.dram
    tile = tile_of(d["w_kv"][0])
    keys = Weights(c, [lambda i, u=u: tile(i, 2, u) for u in range(2)], KT // 2)
    values = Weights(c, [lambda i, u=u: tile(i, 2, KT + u) for u in range(2)], KT // 2)
    mem_hi = at(c, 0, "mem_hi", [P, KT, N_MEM], F32R)
    mem_lo = at(c, 8192, "mem_lo", [P, KT, N_MEM], F32R)
    k_all = at(c, 24576, "k_all", [P, KT, N_MEM])
    v_all = at(c, 32768, "v_all", [P, 2, D])
    scratch(c, "mem_k", [KT, P, N_MEM])
    scratch(c, "mem_v", [2, P, D])
    copied, stored = [c.sem("mem_copied0"), c.sem("mem_copied1")], c.sem("mem_stored")
    memory_norm(c, mem_hi, mem_lo, keys)
    sq = at(c, 40960, "mix_sq", [P, SEQ])

    def build(following, norm):
        for w in (keys, values):
            w.begin()
        with nc.Block() as block:

            @block.sync
            def _(sp):
                keys.load_rest(sp)
                values.load_all(sp)
                sp.wait_ge(c.w_split, c.tiles)
                following.load_first(sp)
                for s in range(2):
                    sp.wait_ge(copied[s], KT)
                sp.dma_start(c.scratch["mem_k"].rearrange("k p n -> p k n"), k_all[:]).then_inc(stored, 16)
                sp.dma_start(c.scratch["mem_v"].rearrange("m p n -> p m n"), v_all[:]).then_inc(stored, 16)
                sp.wait_ge(stored, 32)

            @block.scalar
            def _(act):
                keys.round_on(act)
                values.round_on(act)

            @block.gpsimd
            def _(pool):
                g = c.g_steps
                for k in range(KT):
                    dst = sq[:] if k else norm.acc[:]
                    g.mark(pool.tensor_tensor(dst, c.x[:, k], c.x[:, k], ALU.mult))
                    g.wait(pool)
                    if k:
                        g.mark(pool.tensor_tensor(norm.acc[:], norm.acc[:], dst, ALU.add))
                        g.wait(pool)

            @block.tensor
            def _(pe):
                def key_turn(i):
                    for u in range(2):
                        keys.ready(pe, i, u)
                        wait(pe, copied[u], i)
                        keys.multiply(pe, u, [c.ps[:, u, 0:N_MEM]], mem_hi, mem_lo, width=N_MEM).then_inc(c.tile_done, 1)

                def value_turn(i):
                    for u in range(2):
                        values.ready(pe, i, u)
                        wait(pe, copied[u], i + KT // 2)
                    for m in range(2):
                        rows = slice(m * P, (m + 1) * P)
                        for k in range(KT):
                            for a, w in ((mem_hi, c.w_hi), (mem_lo, c.w_hi), (mem_hi, c.w_lo)):
                                last = pe.matmul(c.ps[:, 2 + m, 0:2 * P].rearrange("p (u n) -> p u n", n=P), a[:, k, rows], w[:, 0:2, k],
                                                 start=(k == 0 and w is c.w_hi and a is mem_hi),
                                                 stop=(k == KT - 1 and w is c.w_lo))
                    last.then_inc(c.tile_done, 2)

                rolled(pe, KT // 2, key_turn)
                rolled(pe, KT // 2, value_turn)

            @block.vector
            def _(dve):
                def copy_key(i, u):
                    keys.done(dve, i, u)
                    apart(c, dve)
                    dve.tensor_copy(k_all[:, bass.ds(i * 2 + u, 1), :].rearrange("p a n -> p (a n)"),
                                    c.ps[:, u, 0:N_MEM]).then_inc(copied[u], 1)

                def copy_value(i, u):
                    values.done(dve, i, u)
                    apart(c, dve)
                    dve.tensor_copy(v_all[:, :, bass.ds(i * (2 * P) + u * P, P)],
                                    c.ps[:, 2:4, u * P:(u + 1) * P]).then_inc(copied[u], 1)

                def behind(copy):
                    return lambda i, u: None if first(i) else copy(i - 1, u)

                keys.subtract(dve, behind(copy_key))
                for u in range(2):
                    copy_key(KT // 2 - 1, u)
                values.subtract(dve, behind(copy_value))
                for u in range(2):
                    copy_value(KT // 2 - 1, u)

    return build


def queries(c):
    nc = c.nc
    weights = residual_weights(c, c.dram["w_q"][0])
    out = scratch(c, "queries", [KT, P, SEQ])
    q_b = at(c, 0, "q_tile", [P, 2, SEQ])
    copied = [c.sem("q_copied0"), c.sem("q_copied1")]
    stored = [c.sem("q_stored0"), c.sem("q_stored1")]

    def build(norm):
        weights.begin()
        with nc.Block() as block:

            @block.sync
            def _(sp):
                def store(i):
                    for u in range(2):
                        sp.wait_ge(copied[u], i + 1)
                        apart(c, sp)
                        sp.dma_start(out[bass.ds(i * 2 + u, 1)].rearrange("a p n -> p (a n)"), q_b[:, u]).then_inc(stored[u], 16)

                def turn(i):
                    for u in range(2):
                        sp.wait_ge(c.w_split, weights.t0 + i * 2 + (u + 1))
                        apart(c, sp)
                        weights.fetch(sp, u, i + 1)
                    store(i)

                rolled(sp, KT // 2 - 1, turn)
                store(KT // 2 - 1)
                for u in range(2):
                    sp.wait_ge(stored[u], 16 * KT // 2)

            @block.gpsimd
            def _(pool):
                weights.split(pool)

            @block.tensor
            def _(pe):
                norm.pe_sums(pe)

                def turn(i):
                    if first(i):
                        norm.first_tiles(pe, weights)
                        return
                    for u in range(2):
                        weights.ready(pe, i, u)
                        wait(pe, copied[u], i)
                        weights.multiply(pe, u, [c.ps[:, 2 * u], c.ps[:, 2 * u + 1]], c.h_hi, c.h_lo).then_inc(c.tile_done, 1)

                rolled(pe, KT // 2, turn)

            @block.scalar
            def _(act):
                norm.act(act)

                def turn(i):
                    for u in range(2):
                        weights.done(act, i, u)
                        wait(act, stored[u], i * 16)
                        act.activation(q_b[:, u], c.ps[:, 2 * u:2 * u + 2].rearrange("p b n -> p (b n)"), ACT.Copy,
                                       scale=XD ** -0.5).then_inc(copied[u], 1)

                rolled(act, KT // 2, turn)

            @block.vector
            def _(dve):
                norm.dve(dve)

    return weights, build


def attention(c, following):
    nc = c.nc
    q_in = at(c, 0, "xa_q", [P, 2, 2, SEQ])
    k_in = at(c, 16384, "xa_k", [P, 2, 2, N_MEM])
    v_in = at(c, 20480, "xa_v", [P, 2, 2, XD])
    prob = at(c, 24576, "xa_prob", [P, 4, N_MEM])
    p_t = at(c, 28672, "xa_prob_t", [P, 2, 2, HALF])
    top, neg, total = (at(c, 36864 + 32 * n, f"xa_{name}", [P, 4]) for n, name in enumerate(("top", "neg", "total")))
    loaded = [c.sem("xa_loaded0"), c.sem("xa_loaded1")]
    scored, turned, summed = c.sem("xa_scored"), c.sem("xa_turned"), c.sem("xa_summed")
    exps, copied, rounded = c.sem("xa_exps"), c.sem("xa_copied"), c.sem("xa_rounded")
    tops, normed, split = c.sem("xa_tops"), c.sem("xa_normed"), c.sem("xa_split")
    ps = c.ps
    q_src, k_src, v_src = c.scratch["queries"], c.scratch["mem_k"], c.scratch["mem_v"]
    n_steps = N_XHEADS * TILES
    quads = n_steps // 4

    with nc.Block() as block:

        @block.sync
        def _(sp):
            following.load_first(sp)
            for hd in range(N_XHEADS):
                s = hd % 2
                wait(sp, summed, 2 * (hd - 1))
                sp.dma_start(q_in[:, s], q_src[2 * hd:2 * hd + 2].rearrange("k p n -> p k n")).then_inc(loaded[s], 16)
                sp.dma_start(k_in[:, s], k_src[2 * hd:2 * hd + 2].rearrange("k p n -> p k n")).then_inc(loaded[s], 16)
                sp.dma_start(v_in[:, s], v_src[:, :, hd * XD:(hd + 1) * XD].rearrange("m p n -> p m n")).then_inc(loaded[s], 16)

        @block.tensor
        def _(pe):
            def score(n):
                hd, t = divmod(n, TILES)
                pe.wait_ge(loaded[hd % 2], (hd // 2 + 1) * 48)
                wait(pe, exps, n - 3)
                for k in range(2):
                    last = pe.matmul(ps[:, n % 4, 0:N_MEM], q_in[:, hd % 2, k, t * P:(t + 1) * P], k_in[:, hd % 2, k],
                                     start=k == 0, stop=k == 1)
                last.then_inc(scored, 1)

            def sum_values(g):
                hd = g // 2
                pe.wait_ge(copied, 4 * g + 4)
                wait(pe, split, 2 * g)
                for e in range(2):
                    for m in range(2):
                        last = pe.matmul(ps[:, 6 + e], v_in[:, hd % 2, m, e * P:(e + 1) * P], p_t[:, g % 2, m],
                                         start=m == 0, stop=m == 1)
                last.then_inc(summed, 1)

            for n in range(3):
                score(n)
            for n in range(n_steps):
                if n + 3 < n_steps:
                    score(n + 3)
                pe.wait_ge(normed, n + 1)
                wait(pe, copied, n - 1)
                for m in range(2):
                    last = pe.transpose(ps[:, 4 + n % 2, m * P:(m + 1) * P], prob[:, n % 4, m * P:(m + 1) * P], c.ident[:])
                last.then_inc(turned, 1)
                if n % 4 == 1 and n > 4:
                    sum_values(n // 4 - 1)
            sum_values(quads - 1)

        @block.scalar
        def _(act):
            def exp(n):
                act.wait_ge(tops, 2 * n + 2)
                wait(act, turned, n - 3)
                one = slice(n % 4, n % 4 + 1)
                act.activation(prob[:, n % 4], ps[:, n % 4, 0:N_MEM], ACT.Exp, bias=neg[:, one],
                               accum_out=total[:, one]).then_inc(exps, 1)

            def round_sums(g):
                hd, h = divmod(g, 2)
                act.wait_ge(summed, g + 1)
                for e in range(2):
                    act.copy(c.h_hi[:, 2 * hd + e, h * HALF:(h + 1) * HALF], ps[:, 6 + e]).then_inc(rounded, 1)

            exp(0)
            for n in range(n_steps):
                if n + 1 < n_steps:
                    exp(n + 1)
                act.wait_ge(turned, n + 1)
                wait(act, summed, n // 4 - 1)
                act.copy(p_t[:, n // 4 % 2, :, (n % 4) * P:(n % 4 + 1) * P],
                         ps[:, 4 + n % 2, 0:2 * P].rearrange("p (m n) -> p m n", n=P)).then_inc(copied, 1)
                if n % 4 == 2 and n > 4:
                    round_sums(n // 4 - 1)
            round_sums(quads - 1)

        @block.vector
        def _(dve):
            v = c.v_steps

            def peak(n):
                one = slice(n % 4, n % 4 + 1)
                dve.wait_ge(scored, n + 1)
                dve.tensor_reduce(top[:, one], ps[:, n % 4, 0:N_MEM], AX_X, ALU.max).then_inc(tops, 1)
                dve.wait_ge(tops, 2 * n + 1)
                wait(dve, exps, n - 3)
                dve.tensor_scalar(neg[:, one], top[:, one], -1.0, None, ALU.mult).then_inc(tops, 1)

            def take_rest(g):
                hd, h = divmod(g, 2)
                for e in range(2):
                    cut = slice(h * HALF, (h + 1) * HALF)
                    dve.wait_ge(rounded, 2 * g + e + 1)
                    dve.tensor_tensor(c.h_lo[:, 2 * hd + e, cut], ps[:, 6 + e], c.h_hi[:, 2 * hd + e, cut].bitcast(F32),
                                      ALU.subtract).then_inc(split, 1)

            peak(0)
            peak(1)
            for n in range(n_steps):
                if n + 2 < n_steps:
                    peak(n + 2)
                one = slice(n % 4, n % 4 + 1)
                dve.wait_ge(exps, n + 1)
                v.mark(dve.reciprocal(total[:, one], total[:, one]))
                v.wait(dve)
                dve.tensor_scalar(prob[:, n % 4], prob[:, n % 4], total[:, one], None, ALU.mult).then_inc(normed, 1)
                if n % 4 == 3 and n > 4:
                    take_rest(n // 4 - 1)
            take_rest(quads - 1)


DN_HEADS = 4
SB_HEAD = 64
BETA_COLUMN = 4 * D_RWKV
SB_COLUMN = BETA_COLUMN + 2 * DN_HEADS
GATE_COLUMN_2 = SB_COLUMN + 4 * D_RWKV


def second_projections(c):
    nc, d = c.nc, c.dram
    w = d["w_in_2"][0]
    kinds = ["q", "z", "k", "v", "sq", "sv", "sk", "zb"]
    at_column = dict(q=0, k=D_RWKV, v=2 * D_RWKV, z=3 * D_RWKV, sq=SB_COLUMN, sk=SB_COLUMN + D_RWKV,
                     sv=SB_COLUMN + 2 * D_RWKV, zb=SB_COLUMN + 3 * D_RWKV)
    conv_row = dict(q=0, k=CT, v=2 * CT)
    out = {n: scratch(c, f"second_{n}", [CT, P, SEQ]) for n in kinds}
    rows_out = {n: scratch(c, f"second_{n}", [2 * DN_HEADS, SEQ]) for n in ("beta", "decay")}
    weights = Weights(c, [tile_of(w, at_column[n]) for n in kinds], CT)
    raw = at(c, 0, "p2_raw", [P, 2, SEQ + 8])
    y = at(c, 8256, "p2_y", [P, 4, SEQ])
    sig = at(c, 24640, "p2_sig", [P, SEQ])
    sq = at(c, 28736, "p2_sq", [P, SEQ])
    root = at(c, 32832, "p2_root", [P, SEQ])
    n_rows = 2 * DN_HEADS
    beta, pre, soft, cum, keep = (at(c, 36928 + 4096 * n, f"p2_{name}", [n_rows, SEQ])
                                  for n, name in enumerate(("beta", "pre", "soft", "cum", "keep")))
    few = at(c, 57408, "p2_few", [P, KT, n_rows])
    few_hi = at(c, 57664, "p2_few_hi", [P, KT, n_rows], F32R)
    few_lo = at(c, 57920, "p2_few_lo", [P, KT, n_rows], F32R)
    params = at(c, 58176, "p2_params", [n_rows, 4])
    cols = at(c, 58208, "p2_cols", [P, TILES, 2, n_rows])
    ACT_EVENTS = ["q_copy", "z_copy", "q_root", "z_sig", "k_copy", "v_copy", "k_root", "sq_copy", "sv_copy", "sq_root",
                  "sk_copy", "zb_copy", "sk_root", "zb_sig"]
    few_loaded, prepared, few_split = c.sem("p2_few_loaded"), c.sem("p2_prepared"), c.sem("p2_few_split")
    rows_made, turned, cols_made = c.sem("p2_rows"), c.sem("p2_turned"), c.sem("p2_cols_made")
    few_done = c.sem("p2_few_done")
    copied, sigmoid, squared, summed, rooted = (c.sem(f"p2_{n}") for n in ("copied", "sigmoid", "squared", "summed", "rooted"))
    tapped, gated, normed, plain = (c.sem(f"p2_{n}") for n in ("tapped", "gated", "normed", "plain"))
    stored = [c.sem(f"p2_stored{s}") for s in range(4)]
    rows_stored = c.sem("p2_rows_stored")
    CONV, NORM, SILU = ["q", "k", "v"], ["q", "k", "sq", "sk"], ["q", "z", "k", "v", "zb"]
    gain = dict(sq="sb_q_gain_2", sk="sb_k_gain_2")

    def finished(eng, n, i):
        if n in NORM:
            eng.wait_ge(normed, nth(NORM, n, i))
        elif n in SILU:
            eng.wait_ge(gated, nth(SILU, n, i))
        else:
            eng.wait_ge(plain, i + 1)

    def build(norm):
        weights.begin()
        with nc.Block() as block:

            @block.sync
            def _(sp):
                sp.dma_start(few[:], w.rearrange("(k p) n -> p k n", p=P)[:, :, BETA_COLUMN:SB_COLUMN]).then_inc(few_loaded, 16)
                sp.wait_ge(prepared, 1)
                for k, name in enumerate(("dt_bias_2", "a_log_2")):
                    sp.dma_start(params[DN_HEADS:n_rows, k:k + 1], d[name].rearrange("a n -> n a")).then_inc(few_loaded, 16)

                def store(u, i):
                    finished(sp, kinds[u], i)
                    apart(c, sp)
                    sp.dma_start(out[kinds[u]][bass.ds(i, 1)].rearrange("a p n -> p (a n)"), y[:, u % 4]).then_inc(stored[u % 4], 16)

                def fetch(u, i):
                    v = u + 2
                    sp.wait_ge(c.w_split, weights.t0 + i * len(kinds) + (u + 1))
                    apart(c, sp)
                    weights.fetch(sp, v % len(kinds), i + v // len(kinds))

                def turn(i):
                    for u in range(len(kinds)):
                        fetch(u, i)
                        if u >= 2:
                            store(u - 2, i)
                    for u in (6, 7):
                        store(u, i)

                rolled(sp, CT - 1, turn)
                for u in range(len(kinds)):
                    if u < 6:
                        fetch(u, CT - 1)
                    if u >= 2:
                        store(u - 2, CT - 1)
                for u in (6, 7):
                    store(u, CT - 1)
                sp.wait_ge(rows_made, 9)
                for n, src in (("beta", beta), ("decay", cum)):
                    sp.dma_start(rows_out[n], src[:]).then_inc(rows_stored, 16)
                for s in range(4):
                    sp.wait_ge(stored[s], 16 * 2 * CT)
                sp.wait_ge(rows_stored, 32)

            @block.gpsimd
            def _(pool):
                pool.memset(params[:], 0.0).then_inc(prepared, 1)
                pool.memset(keep[:], 1.0).then_inc(prepared, 1)
                pool.wait_ge(prepared, 2)
                pool.memset(keep[:].rearrange("p (t n) -> p t n", n=P)[:, :, 0:1], 0.0).then_inc(prepared, 1)
                pool.memset(raw[:, :, 0:8], 0.0).then_inc(prepared, 1)
                weights.split(pool)

            @block.tensor
            def _(pe):
                norm.pe_sums(pe)

                def few_rows():
                    pe.wait_ge(few_split, 2)
                    for k in range(KT):
                        for wt, a in ((few_hi, c.h_hi), (few_hi, c.h_lo), (few_lo, c.h_hi)):
                            for h in range(2):
                                last = pe.matmul(c.ps[0:n_rows, 6 + h], wt[:, k], a[:, k, h * HALF:(h + 1) * HALF],
                                                 start=(k == 0 and wt is few_hi and a is c.h_hi),
                                                 stop=(k == KT - 1 and wt is few_lo))
                    last.then_inc(few_done, 1)

                def sums(n, i):
                    ones = c.ones if n in CONV else c.ones_64
                    pe.wait_ge(squared, nth(NORM, n, i))
                    wait(pe, rooted, nth(NORM, n, i) - 1)
                    for h in range(2):
                        last = pe.matmul(c.ps[:, 4 + h], ones[:], sq[:, h * HALF:(h + 1) * HALF], start=True, stop=True)
                    last.then_inc(summed, 1)

                def turn(i):
                    for u, n in enumerate(kinds):
                        s = u % 2
                        if first(i) and u == 0:
                            norm.first_tiles(pe, weights)
                        elif not first(i) or u > 1:
                            weights.ready(pe, i, u)
                            wait(pe, copied, i * len(kinds) + (u - 1))
                            weights.multiply(pe, u, [c.ps[:, 2 * s], c.ps[:, 2 * s + 1]], c.h_hi, c.h_lo).then_inc(c.tile_done, 1)
                        if first(i) and u == 2:
                            few_rows()
                        if u and kinds[u - 1] in NORM:
                            sums(kinds[u - 1], i)

                rolled(pe, CT, turn)
                pe.wait_ge(rows_made, 9)
                for t in range(TILES):
                    for b, src in enumerate((beta, cum)):
                        last = pe.transpose(c.ps[:, 6, (2 * t + b) * n_rows:(2 * t + b + 1) * n_rows],
                                            src[:, t * P:(t + 1) * P], c.ident[0:n_rows, 0:n_rows])
                last.then_inc(turned, 1)

            @block.scalar
            def _(act):
                act.wait_ge(few_loaded, 48)
                act.copy(few_hi[:], few[:]).then_inc(few_split, 1)
                act.activation(params[:, 2:3], params[:, 1:2], ACT.Exp).then_inc(rows_made, 1)

                def rows_act():
                    act.wait_ge(few_done, 1)
                    act.activation(beta[:], c.ps[0:n_rows, 6:8].rearrange("p b n -> p (b n)"), ACT.Sigmoid).then_inc(rows_made, 1)
                    act.wait_ge(rows_made, 3)
                    act.activation(soft[:], pre[:], ACT.Abs).then_inc(rows_made, 1)
                    act.wait_ge(rows_made, 4)
                    act.activation(soft[:], soft[:], ACT.Exp, scale=-1.0).then_inc(rows_made, 1)
                    act.wait_ge(rows_made, 5)
                    act.activation(soft[:], soft[:], ACT.Ln, bias=c.eps[0:n_rows, 2:3]).then_inc(rows_made, 1)

                norm.act(act)
                act.wait_ge(prepared, 4)

                def turn(i):
                    for u, n in enumerate(kinds):
                        ps = c.ps[:, 2 * (u % 2):2 * (u % 2) + 2].rearrange("p b n -> p (b n)")
                        weights.done(act, i, u)
                        if n == "sv":
                            wait(act, stored[u % 4], i * 32 + (u // 4) * 16)
                            act.copy(y[:, u % 4], ps).then_inc(plain, 1)
                            act.wait_ge(plain, i + 1)
                            act.sem_inc(copied, 1)
                        else:
                            if u >= 2:
                                finished(act, kinds[u - 2], i)
                            elif not first(i):
                                finished(act, kinds[u + 6], i - 1)
                            act.copy(raw[:, u % 2, 8:SEQ + 8], ps).then_inc(copied, 1)
                        if u and kinds[u - 1] in NORM:
                            m = kinds[u - 1]
                            act.wait_ge(summed, nth(NORM, m, i))
                            wait(act, normed, nth(NORM, m, i) - 1)
                            act.activation(root[:], c.ps[:, 4:6].rearrange("p b n -> p (b n)"), ACT.Sqrt,
                                           bias=c.eps[:, 4:5] if m == "sq" else c.eps[:, 0:1],
                                           scale=1.0 / SB_HEAD if m == "sk" else 1.0).then_inc(rooted, 1)
                        if n in SILU:
                            wait(act, gated, nth(SILU, n, i) - 1)
                            if n in CONV:
                                act.wait_ge(tapped, nth(CONV, n, i))
                                act.activation(sig[:], y[:, u % 4], ACT.Sigmoid).then_inc(sigmoid, 1)
                            else:
                                act.wait_ge(copied, i * len(kinds) + (u + 1))
                                act.activation(sig[:], raw[:, u % 2, 8:SEQ + 8], ACT.Sigmoid).then_inc(sigmoid, 1)
                        if n in NORM:
                            wait(act, summed, nth(NORM, n, i) - 1)
                            if n in CONV:
                                act.wait_ge(gated, nth(SILU, n, i))
                                src = y[:, u % 4]
                            else:
                                act.wait_ge(copied, i * len(kinds) + (u + 1))
                                src = raw[:, u % 2, 8:SEQ + 8]
                            act.activation(sq[:], src, ACT.Square).then_inc(squared, 1)
                        if first(i) and u == 3:
                            rows_act()

                rolled(act, CT, turn)
                act.wait_ge(turned, 1)
                act.copy(cols[:].rearrange("p t b n -> p (t b n)"), c.ps[:, 6, 0:TILES * 2 * n_rows]).then_inc(cols_made, 1)
                act.wait_ge(cols_made, 1)
                act.activation(c.beta_decay[:], cols[:, :, 1, DN_HEADS:n_rows], ACT.Exp).then_inc(cols_made, 1)

            @block.vector
            def _(dve):
                v = c.v_steps
                dve.wait_ge(few_split, 1)
                dve.tensor_tensor(few_lo[:], few[:], few_hi[:].bitcast(F32), ALU.subtract).then_inc(few_split, 1)

                def rows_dve():
                    dve.wait_ge(few_done, 1)
                    dve.wait_ge(rows_made, 2)
                    dve.tensor_scalar(pre[:], c.ps[0:n_rows, 6:8].rearrange("p b n -> p (b n)"), params[:, 0:1], None,
                                      ALU.add).then_inc(rows_made, 1)
                    dve.wait_ge(rows_made, 6)
                    dve.scalar_tensor_tensor(out=pre[:], in0=pre[:], scalar=0.0, in1=soft[:], op0=ALU.max,
                                             op1=ALU.add).then_inc(rows_made, 1)
                    dve.wait_ge(rows_made, 7)
                    dve.tensor_scalar(pre[:], pre[:], params[:, 2:3], -1.0, ALU.mult, ALU.mult).then_inc(rows_made, 1)
                    dve.wait_ge(rows_made, 8)
                    dve.wait_ge(prepared, 3)
                    dve.tensor_tensor_scan(cum[:], keep[:], pre[:], 0.0, ALU.mult, ALU.add).then_inc(rows_made, 1)

                norm.dve(dve)

                def turn(i):
                    for u, n in enumerate(kinds):
                        dst = y[:, u % 4]
                        if n != "sv":
                            wait(dve, stored[u % 4], i * 32 + (u // 4) * 16)
                        if n in CONV:
                            dve.wait_ge(copied, i * len(kinds) + (u + 1))
                            for tap in (3, 2, 1, 0):
                                scale = vec(c, "conv_w_2", i + (tap * 3 * CT + conv_row[n]))
                                src = raw[:, u % 2, 5 + tap:5 + tap + SEQ]
                                if tap == 3:
                                    ins = dve.tensor_scalar(dst, src, scale, None, ALU.mult)
                                else:
                                    v.wait(dve)
                                    ins = dve.scalar_tensor_tensor(out=dst, in0=src, scalar=scale, in1=dst,
                                                                   op0=ALU.mult, op1=ALU.add)
                                v.mark(ins)
                            v.wait(dve)
                            dve.sem_inc(tapped, 1)
                        if u and kinds[u - 1] in NORM:
                            m, p = kinds[u - 1], u - 1
                            dve.wait_ge(rooted, nth(NORM, m, i))
                            v.mark(dve.reciprocal(root[:], root[:]))
                            v.wait(dve)
                            o = y[:, p % 4]
                            if m in CONV:
                                dve.scalar_tensor_tensor(out=o, in0=o, scalar=P ** -0.5 if m == "q" else 1.0, in1=root[:],
                                                         op0=ALU.mult, op1=ALU.mult).then_inc(normed, 1)
                            else:
                                dve.scalar_tensor_tensor(out=o, in0=raw[:, p % 2, 8:SEQ + 8], scalar=vec(c, gain[m]),
                                                         in1=root[:], op0=ALU.mult, op1=ALU.mult).then_inc(normed, 1)
                        if n in SILU:
                            dve.wait_ge(sigmoid, nth(SILU, n, i))
                            src = dst if n in CONV else raw[:, u % 2, 8:SEQ + 8]
                            dve.tensor_tensor(dst, src, sig[:], ALU.mult).then_inc(gated, 1)
                        if first(i) and u == 3:
                            rows_dve()

                rolled(dve, CT, turn, v)
                dve.wait_ge(cols_made, 2)
                v.mark(dve.tensor_copy(c.beta_col[:], cols[:, :, 0, 0:DN_HEADS]))
                v.mark(dve.tensor_copy(c.decay_col[:], cols[:, :, 1, DN_HEADS:n_rows]))
                v.mark(dve.scalar_tensor_tensor(out=c.beta_decay[:], in0=c.beta_decay[:], scalar=-1.0,
                                                in1=cols[:, :, 0, 0:DN_HEADS], op0=ALU.mult, op1=ALU.mult))
                v.wait(dve)

    return weights, build


def delta_rule(c, following):
    nc = c.nc
    base, w_off = 0, 0
    wide = [P, DN_HEADS, P]

    def buf(name):
        nonlocal base
        b = at(c, base, f"dn_{name}", wide)
        base += 4 * DN_HEADS * P
        return b

    def buf_w(name, shape):
        nonlocal w_off
        b = nc.alloc_sbuf_tensor_at(f"dn_{name}", shape, F32, offset=c.w_base + w_off)
        n = 4
        for m in shape[1:]:
            n *= m
        w_off += n
        return b

    groups = range(2)
    q_in, k_in, v_in, g_in, b_in = ([buf(f"{n}_in{g}") for g in groups] for n in ("q", "k", "v", "decay", "beta"))
    low, up, q_dec, a_t, q_k = ([buf(f"{n}{g}") for g in groups] for n in ("low", "up", "q_dec", "a_t", "q_k"))
    t, t_t, x = ([buf(f"{n}{g}") for g in groups] for n in ("t", "tt", "x"))
    v_beta, k_dec = ([buf(f"{n}{g}") for g in groups] for n in ("v_beta", "k_dec"))
    rest, v_new, o_b = ([buf_w(f"{n}{g}", wide) for g in groups] for n in ("rest", "v_new", "o"))
    state = buf_w("state", wide)
    c.level = buf_w("level", [P, LEVELS, P])
    ends = [buf_w(f"ends{g}", [P, 2, DN_HEADS]) for g in groups]
    assert w_off <= 24576 and c.aux_base + 32 + base <= 229376

    PE_EVENTS = ["kk", "qk", "k_nat", "v_nat"] + LEVEL_PE + ["ks", "v_new", "o", "s"]
    DVE_EVENTS = ["low_in", "up_in", "ends_in", "low_beta", "n", "qm", "qk", "up_beta", "up_mask", "n_t", "q_dec", "v_beta", "k_dec",
                  "t_block", "t0", "tt_block", "tt0"] + LEVEL_DVE + ["rest", "s_new"]
    ACT_EVENTS = ["low", "up", "grown", "end", "to_end", "v_new", "o"]
    loaded, stored = ([c.sem(f"dn_{n}{g}") for g in groups] for n in ("loaded", "stored"))
    products, masks, acts = ([c.sem(f"dn_{n}{g}") for g in groups] for n in ("products", "masks", "acts"))
    cleared = c.sem("dn_cleared")
    src = {n: c.scratch[f"second_{n}"].rearrange("h p n -> p h n") for n in "qkv"}
    row_src = {n: c.scratch[f"second_{n}"] for n in ("decay", "beta")}
    out = scratch(c, "second_oa", [CT, P, SEQ])
    ps = c.ps
    level_banks = [(ps[:, g], ps[:, 2 + g], ps[:, 4 + g]) for g in groups]
    turns = TILES // 2

    def over(m):
        return m.unsqueeze(1).broadcast_to(wide)

    with nc.Block() as block:

        @block.sync
        def _(sp):
            def load(j, g):
                cut = columns(j * 2 + g, P)
                for n, dst in (("q", q_in), ("k", k_in), ("v", v_in)):
                    sp.dma_start(dst[g][:], src[n][:, :, cut]).then_inc(loaded[g], 16)
                for n, dst, r in (("decay", g_in, DN_HEADS), ("beta", b_in, 0)):
                    rows = row_src[n][r:r + DN_HEADS, cut]
                    sp.dma_start(dst[g][:], rows.unsqueeze(0).broadcast_to(wide)).then_inc(loaded[g], 16)

            def store(j, g):
                sp.wait_ge(acts[g], nth(ACT_EVENTS, "o", j))
                apart(c, sp)
                sp.dma_start(out.rearrange("h p n -> p h n")[:, :, columns(j * 2 + g, P)], o_b[g][:]).then_inc(stored[g], 16)

            def turn(j):
                for g in groups:
                    sp.wait_ge(products[g], nth(PE_EVENTS, "ks", j))
                    apart(c, sp)
                    load(j + 1, g)
                    store(j, g)

            for g in groups:
                load(0, g)
            rolled(sp, turns - 1, turn)
            following.load_first(sp)
            for g in groups:
                store(turns - 1, g)
            for g in groups:
                sp.wait_ge(stored[g], 16 * turns)

        @block.gpsimd
        def _(pool):
            make_levels(c, pool)
            pool.memset(state[:], 0.0).then_inc(cleared, 1)

        @block.tensor
        def _(pe):
            def four(out, lhs, rhs, start=True, stop=True):
                for h in range(DN_HEADS):
                    last = pe.matmul(out[:, h * P:(h + 1) * P], lhs[:, h], rhs[:, h], start=start and h == 0, stop=stop,
                                     skip_group_check=True)
                return last

            def turn(j):
                for g in groups:
                    pe.wait_ge(loaded[g], j * 80 + 80)
                    wait(pe, masks[g], nth(DVE_EVENTS, "s_new", j - 1))
                    wait(pe, acts[g], nth(ACT_EVENTS, "o", j - 1))
                    four(ps[:, 6 + g], k_in[g], k_in[g]).then_inc(products[g], 1)
                    four(ps[:, 4 + g], k_in[g], q_in[g]).then_inc(products[g], 1)
                    for bank, part in ((g, k_in), (2 + g, v_in)):
                        for h in range(DN_HEADS):
                            last = pe.transpose(ps[:, bank, h * P:(h + 1) * P], part[g][:, h], c.ident[:])
                        last.then_inc(products[g], 1)
                for n in range(1, LEVELS):
                    for g in groups:
                        inverse_pe(pe, n, products[g], masks[g], j, DVE_EVENTS, level_banks[g], a_t[g], t[g])
                    for g in groups:
                        inverse_pe_update(pe, n, products[g], masks[g], j, DVE_EVENTS, level_banks[g], t[g], t_t[g], x[g])
                for g in groups:
                    if g == 0:
                        pe.wait_ge(cleared, 1)
                        wait(pe, masks[1], nth(DVE_EVENTS, "s_new", j - 1))
                    else:
                        pe.wait_ge(masks[0], nth(DVE_EVENTS, "s_new", j))
                    four(ps[:, 6 + g], k_in[g], state).then_inc(products[g], 1)
                    pe.wait_ge(masks[g], nth(DVE_EVENTS, "rest", j))
                    four(ps[:, g], t_t[g], rest[g]).then_inc(products[g], 1)
                    four(ps[:, 2 + g], state, q_dec[g], stop=False)
                    pe.wait_ge(acts[g], nth(ACT_EVENTS, "v_new", j))
                    four(ps[:, 2 + g], v_new[g], q_k[g], start=False).then_inc(products[g], 1)
                    four(ps[:, 4 + g], k_dec[g], v_new[g]).then_inc(products[g], 1)

            rolled(pe, turns, turn)

        @block.scalar
        def _(act):
            def turn(j):
                for g in groups:
                    act.wait_ge(masks[g], nth(DVE_EVENTS, "low_in", j))
                    act.activation(low[g][:], low[g][:], ACT.Exp, scale=-1.0).then_inc(acts[g], 1)
                    act.wait_ge(masks[g], nth(DVE_EVENTS, "up_in", j))
                    act.activation(up[g][:], up[g][:], ACT.Exp).then_inc(acts[g], 1)
                    wait(act, products[g], nth(PE_EVENTS, "o", j - 1))
                    act.activation(q_dec[g][:], g_in[g][:], ACT.Exp).then_inc(acts[g], 1)
                    act.wait_ge(masks[g], nth(DVE_EVENTS, "ends_in", j))
                    act.activation(ends[g][:, 1], g_in[g][:, :, P - 1], ACT.Exp).then_inc(acts[g], 1)
                    act.activation(ends[g][:, 0], ends[g][:, 0], ACT.Exp).then_inc(acts[g], 1)
                for g in groups:
                    act.wait_ge(products[g], nth(PE_EVENTS, "v_new", j))
                    act.copy(v_new[g][:], heads_of(ps[:, g])).then_inc(acts[g], 1)
                    act.wait_ge(products[g], nth(PE_EVENTS, "o", j))
                    wait(act, stored[g], j * 16)
                    act.copy(o_b[g][:], heads_of(ps[:, 2 + g])).then_inc(acts[g], 1)

            rolled(act, turns, turn)

        @block.vector
        def _(dve):
            dve.wait_ge(cleared, 1)

            def turn(j):
                def col(buf, g, h):
                    return buf[:, bass.ds(j * 2 + g, 1), h:h + 1].rearrange("p a b -> p (a b)")

                def after(g, name):
                    dve.wait_ge(masks[g], nth(DVE_EVENTS, name, j))

                for g in groups:
                    dve.wait_ge(loaded[g], j * 80 + 80)
                    wait(dve, products[g], nth(PE_EVENTS, "s", j - 1))
                    wait(dve, masks[g], nth(DVE_EVENTS, "s_new", j - 1))
                    for buf, op, in ((low, ALU.max), (up, ALU.min)):
                        for h in range(DN_HEADS):
                            last = dve.tensor_scalar(buf[g][:, h], g_in[g][:, h], col(c.decay_col, g, h), 0.0, ALU.subtract, op)
                        last.then_inc(masks[g], 1)
                    dve.tensor_tensor(ends[g][:, 0], g_in[g][:, :, P - 1],
                                      c.decay_col[:, bass.ds(j * 2 + g, 1), :].rearrange("p a n -> p (a n)"),
                                      ALU.subtract).then_inc(masks[g], 1)
                for g in groups:
                    dve.wait_ge(acts[g], nth(ACT_EVENTS, "low", j))
                    for h in range(DN_HEADS):
                        last = dve.scalar_tensor_tensor(out=low[g][:, h], in0=low[g][:, h], scalar=col(c.beta_col, g, h),
                                                        in1=c.lower[:], op0=ALU.mult, op1=ALU.mult)
                    last.then_inc(masks[g], 1)
                    after(g, "low_beta")
                    dve.wait_ge(products[g], nth(PE_EVENTS, "kk", j))
                    dve.scalar_tensor_tensor(out=low[g][:], in0=heads_of(ps[:, 6 + g]), scalar=-1.0, in1=low[g][:],
                                             op0=ALU.mult, op1=ALU.mult).then_inc(masks[g], 1)
                    dve.wait_ge(acts[g], nth(ACT_EVENTS, "up", j))
                    dve.tensor_tensor(q_k[g][:], up[g][:], over(c.upper_eq[:]), ALU.mult).then_inc(masks[g], 1)
                    after(g, "qm")
                    dve.wait_ge(products[g], nth(PE_EVENTS, "qk", j))
                    dve.tensor_tensor(q_k[g][:], heads_of(ps[:, 4 + g]), q_k[g][:], ALU.mult).then_inc(masks[g], 1)
                    dve.scalar_tensor_tensor(out=a_t[g][:], in0=up[g][:], scalar=-1.0, in1=b_in[g][:],
                                             op0=ALU.mult, op1=ALU.mult).then_inc(masks[g], 1)
                    after(g, "up_beta")
                    dve.tensor_tensor(a_t[g][:], a_t[g][:], over(c.upper[:]), ALU.mult).then_inc(masks[g], 1)
                    after(g, "up_mask")
                    dve.tensor_tensor(a_t[g][:], heads_of(ps[:, 6 + g]), a_t[g][:], ALU.mult).then_inc(masks[g], 1)
                    dve.wait_ge(acts[g], nth(ACT_EVENTS, "grown", j))
                    dve.tensor_tensor(q_dec[g][:], q_in[g][:], q_dec[g][:], ALU.mult).then_inc(masks[g], 1)
                    dve.wait_ge(products[g], nth(PE_EVENTS, "v_nat", j))
                    beta = c.beta_col[:, bass.ds(j * 2 + g, 1), :].rearrange("p a n -> p (a n)")
                    dve.tensor_tensor(v_beta[g][:], heads_of(ps[:, 2 + g]), beta.unsqueeze(2).broadcast_to(wide),
                                      ALU.mult).then_inc(masks[g], 1)
                    dve.wait_ge(acts[g], nth(ACT_EVENTS, "to_end", j))
                    dve.tensor_tensor(k_dec[g][:], heads_of(ps[:, g]), ends[g][:, 0].unsqueeze(2).broadcast_to(wide),
                                      ALU.mult).then_inc(masks[g], 1)
                for g in groups:
                    inverse_start_dve(c, dve, masks[g], j, DVE_EVENTS, low[g], a_t[g], t[g], t_t[g])
                for n in range(1, LEVELS):
                    for g in groups:
                        inverse_mask_dve(c, dve, n, products[g], masks[g], j, PE_EVENTS, level_banks[g], x[g])
                    for g in groups:
                        inverse_add_dve(dve, n, products[g], masks[g], j, PE_EVENTS, level_banks[g], t[g], t_t[g])
                for g in groups:
                    dve.wait_ge(products[g], nth(PE_EVENTS, "ks", j))
                    for h in range(DN_HEADS):
                        last = dve.scalar_tensor_tensor(out=rest[g][:, h], in0=ps[:, 6 + g, h * P:(h + 1) * P],
                                                        scalar=col(c.beta_decay, g, h), in1=v_beta[g][:, h],
                                                        op0=ALU.mult, op1=ALU.add)
                    last.then_inc(masks[g], 1)
                    dve.wait_ge(products[g], nth(PE_EVENTS, "s", j))
                    for h in range(DN_HEADS):
                        last = dve.scalar_tensor_tensor(out=state[:, h], in0=state[:, h], scalar=ends[g][:, 1, h:h + 1],
                                                        in1=ps[:, 4 + g, h * P:(h + 1) * P], op0=ALU.mult, op1=ALU.add)
                    last.then_inc(masks[g], 1)

            rolled(dve, turns, turn)


def stick_breaking(c):
    nc = c.nc
    offset = 0

    def buf(name, shape):
        nonlocal offset
        b = at_h(c, offset, f"sb_{name}", shape)
        n = 4
        for m in shape[1:]:
            n *= m
        offset += n
        return b

    heads = range(2)
    keep, weight, weight_t = (buf(n, [P, 2, 2, HALF]) for n in ("keep", "weight", "weight_t"))
    left = buf("left", [P, 2, 2, HALF + 8])
    v_nat = buf("v_nat", [P, 2, SEQ])
    z_in, o_b = buf("z_in", [P, 2, HALF]), buf("o", [P, 2, HALF])
    forbid = buf("forbid", [P, P])
    assert offset <= 65536
    q_in, k_in, v_in = (nc.alloc_sbuf_tensor_at(f"sb_{n}_in", [P, 2, SEQ], F32, offset=c.w_base + 8192 * k)
                        for k, n in enumerate("qkv"))
    steps = [(ct, qb, kh, min(HALF, (qb + 1) * P - kh * HALF), kh == qb // 4)
             for ct in range(CT) for qb in range(TILES) for kh in range(qb // 4, -1, -1)]
    n_steps = len(steps)
    per = n_steps // CT
    halves = [(st[0], st[1] // 4) for st in steps]
    begins = [n for n in range(n_steps) if n == 0 or halves[n] != halves[n - 1]]
    ends = [n - 1 for n in begins[1:]] + [n_steps - 1]
    early = (8, 10)
    loaded = [c.sem("sb_loaded0"), c.sem("sb_loaded1")]
    made, scored, kept, weighted = (c.sem(f"sb_{n}") for n in ("made", "scored", "kept", "weighted"))
    turned, copied, summed = (c.sem(f"sb_{n}") for n in ("turned", "copied", "summed"))
    values_turned, natural = c.sem("sb_values_turned"), c.sem("sb_natural")
    gates_in, taken, rounded, split = ([c.sem(f"sb_{n}{h}") for h in range(2)] for n in ("gates_in", "taken", "rounded", "split"))
    src = [c.scratch[f"second_{n}"] for n in ("sq", "sk", "sv")]
    z_src = c.scratch["second_zb"]
    ps = c.ps

    with nc.Block() as block:

        @block.sync
        def _(sp):
            def load(ct):
                for part, dst in zip(src, (q_in, k_in, v_in)):
                    sp.dma_start(dst[:, ct % 2], part[ct]).then_inc(loaded[ct % 2], 16)

            def load_gates(ct):
                for h in range(2):
                    wait(sp, taken[h], ct)
                    sp.dma_start(z_in[:, h], z_src[ct, :, h * HALF:(h + 1) * HALF]).then_inc(gates_in[h], 16)

            load(0)
            load(1)
            load_gates(0)
            for ct in range(1, CT):
                load_gates(ct)
                if ct + 1 < CT:
                    load(ct + 1)

        @block.gpsimd
        def _(pool):
            pool.memset(forbid[:], -1e30).then_inc(made, 1)
            pool.wait_ge(made, 1)
            pool.affine_select(out=forbid[:], in_=forbid[:], compare_op=ALU.is_ge, fill=0.0, base=0, pattern=[[1, P]],
                               channel_multiplier=-1).then_inc(made, 1)

        @block.tensor
        def _(pe):
            pe.wait_ge(made, 2)

            def turn_values(ct, h):
                pe.wait_ge(loaded[ct % 2], (ct // 2 + 1) * 48)
                wait(pe, natural, ct * 2 + h)
                wait(pe, taken[0], ct)
                for t in range(4):
                    last = pe.transpose(ps[:, 6, t * P:(t + 1) * P], v_in[:, ct % 2, (4 * h + t) * P:(4 * h + t + 1) * P],
                                        c.ident[:])
                last.then_inc(values_turned, 1)

            def score(n):
                ct, qb, kh, width, diagonal = steps[n]
                pe.wait_ge(loaded[ct % 2], (ct // 2 + 1) * 48)
                wait(pe, kept, 2 * (n - 1))
                for hd in heads:
                    rows = slice(SB_HEAD * hd, SB_HEAD * (hd + 1))
                    last = pe.matmul(ps[:, 2 * (n % 2) + hd, 0:width], q_in[rows, ct % 2, qb * P:(qb + 1) * P],
                                     k_in[rows, ct % 2, kh * HALF:kh * HALF + width], start=True, stop=not diagonal,
                                     skip_group_check=True)
                for hd in heads if diagonal else ():
                    last = pe.matmul(ps[:, 2 * (n % 2) + hd, width - P:width], c.ident[:], forbid[:], start=False, stop=True,
                                     skip_group_check=True)
                last.then_inc(scored, 1)

            def turn_weights(n):
                ct, qb, kh, width, diagonal = steps[n]
                pe.wait_ge(weighted, n + 1)
                wait(pe, copied, n)
                for hd in heads:
                    for t in range(width // P):
                        cut = slice(t * P, (t + 1) * P)
                        last = pe.transpose(ps[:, 4 + hd, cut], weight[:, n % 2, hd, cut], c.ident[:])
                last.then_inc(turned, 1)

            def sum_values(n):
                ct, qb, kh, width, diagonal = steps[n]
                pe.wait_ge(copied, n + 1)
                h = qb // 4
                if n in begins:
                    wait(pe, taken[h], ct)
                    pe.wait_ge(natural, ct * 2 + 2)
                queries_at = slice((qb % 4) * P, (qb % 4 + 1) * P)
                for t in range(width // P):
                    for hd in heads:
                        rows = slice(SB_HEAD * hd, SB_HEAD * (hd + 1))
                        at_key = kh * HALF + t * P
                        last = pe.matmul(ps[rows, 6 + h, queries_at], v_nat[:, ct % 2, at_key:at_key + P][:, rows],
                                         weight_t[:, n % 2, hd, t * P:(t + 1) * P], start=n in begins and t == 0,
                                         stop=n in ends and t == 3, skip_group_check=True)
                last.then_inc(summed, 1)

            for h in range(2):
                turn_values(0, h)
            score(0)
            for n in range(n_steps):
                if n + 1 < n_steps:
                    score(n + 1)
                if n:
                    sum_values(n - 1)
                turn_weights(n)
                ct, at_step = divmod(n, per)
                if at_step in early and ct + 1 < CT:
                    turn_values(ct + 1, early.index(at_step))
            sum_values(n_steps - 1)

        @block.scalar
        def _(act):
            def copy_values(ct, h):
                act.wait_ge(values_turned, ct * 2 + (h + 1))
                act.copy(v_nat[:, ct % 2, h * HALF:(h + 1) * HALF], ps[:, 6]).then_inc(natural, 1)

            def sigmoids(n):
                ct, qb, kh, width, diagonal = steps[n]
                act.wait_ge(scored, n + 1)
                wait(act, turned, n - 1)
                z = ps[:, 2 * (n % 2):2 * (n % 2) + 2, 0:width]
                act.activation(keep[:, n % 2, :, 0:width], z, ACT.Sigmoid, scale=-1.0).then_inc(kept, 1)
                act.activation(weight[:, n % 2, :, 0:width], z, ACT.Sigmoid).then_inc(kept, 1)

            def round_sums(ct, h):
                act.wait_ge(taken[h], ct + 1)
                act.copy(c.br_hi[:, ct + CT, h * HALF:(h + 1) * HALF], o_b[:, h]).then_inc(rounded[h], 1)

            for h in range(2):
                copy_values(0, h)
            sigmoids(0)
            for n, (ct, qb, kh, width, diagonal) in enumerate(steps):
                if n + 1 < n_steps:
                    sigmoids(n + 1)
                act.wait_ge(turned, n + 1)
                wait(act, summed, n - 1)
                act.copy(weight_t[:, n % 2, :, 0:width], ps[:, 4:6, 0:width]).then_inc(copied, 1)
                if n - 3 in ends:
                    round_sums(*halves[n - 3])
                if n % per in early and ct + 1 < CT:
                    copy_values(ct + 1, early.index(n % per))
            round_sums(CT - 1, 1)

        @block.vector
        def _(dve):
            v = c.v_steps

            def take(ct, h):
                dve.wait_ge(summed, ends[2 * ct + h] + 1)
                dve.wait_ge(gates_in[h], ct * 16 + 16)
                wait(dve, split[h], ct)
                dve.tensor_tensor(o_b[:, h], z_in[:, h], ps[:, 6 + h], ALU.mult).then_inc(taken[h], 1)

            def take_rest(ct, h):
                cut = slice(h * HALF, (h + 1) * HALF)
                dve.wait_ge(rounded[h], ct + 1)
                dve.tensor_tensor(c.br_lo[:, ct + CT, cut], o_b[:, h], c.br_hi[:, ct + CT, cut].bitcast(F32),
                                  ALU.subtract).then_inc(split[h], 1)

            for n, (ct, qb, kh, width, diagonal) in enumerate(steps):
                l = left[:, n % 2]
                if diagonal:
                    v.mark(dve.memset(l[:, :, width:width + 1], 1.0))
                else:
                    v.mark(dve.tensor_copy(l[:, :, width:width + 1], left[:, (n - 1) % 2, :, 0:1]))
                v.wait(dve)
                dve.wait_ge(kept, 2 * n + 1)
                for hd in heads:
                    v.mark(dve.tensor_tensor_scan(l[:, hd, 0:width][:, ::-1], keep[:, n % 2, hd, 0:width][:, ::-1],
                                                  c.ones[:, 0:1].broadcast_to([P, width]), l[:, hd, width:width + 1],
                                                  ALU.mult, ALU.mult))
                v.wait(dve)
                dve.wait_ge(kept, 2 * n + 2)
                dve.tensor_tensor(weight[:, n % 2, :, 0:width], weight[:, n % 2, :, 0:width], l[:, :, 1:width + 1],
                                  ALU.mult).then_inc(weighted, 1)
                dve.wait_ge(weighted, n + 1)
                if n - 2 in ends:
                    take(*halves[n - 2])
                if n - 5 in ends:
                    take_rest(*halves[n - 5])
            take(CT - 1, 1)
            take_rest(CT - 1, 1)


def renew(c):
    c.nc.clear_and_free_semaphores(c.stage_sems)
    c.stage_sems = []
    with c.nc.Block() as block:

        @block.gpsimd
        def _(pool):
            pass


def final_norm(c, norm, following):
    sq = at(c, 0, "final_sq", [P, 4, HALF])
    squared, summed = c.sem("final_squared"), c.sem("final_summed")
    with c.nc.Block() as block:

        @block.sync
        def _(sp):
            following.load_first(sp)

        @block.tensor
        def _(pe):
            norm.pe_sums(pe)
            norm.wait(pe, "rooted", 2)
            for n in range(2 * KT):
                h, k = divmod(n, KT)
                pe.wait_ge(squared, n + 1)
                pe.matmul(c.ps[:, 4 + h], c.ones[:], sq[:, n % 4], start=k == 0, stop=k == KT - 1).then_inc(summed, 1)

        @block.scalar
        def _(act):
            norm.act_roots(act)
            for n in range(2 * KT):
                h, k = divmod(n, KT)
                norm.wait(act, "scaled", n + 1)
                wait(act, summed, n - 3)
                act.activation(sq[:, n % 4], c.x[:, k, h * HALF:(h + 1) * HALF], ACT.Square).then_inc(squared, 1)

        @block.vector
        def _(dve):
            v = c.v_steps
            for h in range(2):
                norm.wait(dve, "rooted", h + 1)
                v.mark(dve.reciprocal(norm.root[:, h], norm.root[:, h]))
                v.wait(dve)
                for k in range(KT):
                    x = c.x[:, k, h * HALF:(h + 1) * HALF]
                    norm.mark(dve.scalar_tensor_tensor(out=x, in0=x, scalar=vec(c, norm.gain, k), in1=norm.root[:, h],
                                                       op0=ALU.mult, op1=ALU.mult), "scaled")


def second_block(c, out, final):
    d = c.dram
    norm = Norm(c, "norm_gain_2", "norm_gain_2", events=("rooted", "scaled", "rounded", "split"))
    first_weights, project = second_projections(c)
    final_norm(c, final, first_weights)
    project(norm)
    gate_weights, gate = gates(c, "mix_2", d["w_in_2"][0], GATE_COLUMN_2, "b_gate_2")
    delta_rule(c, gate_weights)
    c.br_hi = at(c, 0, "branch_2_hi", [P, KT, SEQ], F32R)
    c.br_lo = at(c, BRANCH, "branch_2_lo", [P, KT, SEQ], F32R)
    merge_weights, merge_2 = merge(c, "mix_2", d["w_up_a_2"][0], d["w_up_b_2"][0])
    gate(DeltaOutput(c), [c.w_raw[:, 2].rearrange("p k n -> p (k n)")], following=merge_weights)
    stick_breaking(c)
    out_weights = residual_weights(c, d["w_out_2"][0])
    merge_2(out_weights)
    add_product(c, "out_2", out_weights, None)
    finish(c, out)


def first_block(c):
    d = c.dram
    memory = memory_keys(c)
    norm = Norm(c, "norm_mix", "norm_mix", events=("summed", "rooted", "scaled", "rounded", "split"))
    lora_weights, lora = rwkv_lora_inputs(c)
    memory(lora_weights, norm)
    feature_weights, features = rwkv_features(c)
    lora(feature_weights, norm)
    features(lambda sp: None)
    gate_weights, gate = gates(c, "mix", d["w_in"][0], RWKV_COLS + 3 * D_RWKV, "b_gate")
    rwkv_scan(c, gate_weights)
    c.br_hi = at(c, 0, "branch_hi", [P, KT, SEQ], F32R)
    c.br_lo = at(c, BRANCH, "branch_lo", [P, KT, SEQ], F32R)
    side = RwkvOutput(c)
    merge_weights, merge_1 = merge(c, "mix", d["w_proj_a"][0], d["w_proj_b"][0])
    sig = [at(c, BRANCH + 4 * (CT + n) * SEQ, f"mix_sig{n}", [P, SEQ])[:] for n in range(2)]
    gate(side, sig, after=ShortConv(c, side, merge_weights))
    out_weights = residual_weights(c, d["w_out_mix"][0])
    merge_1(out_weights)
    norm = Norm(c, "norm_xattn", "norm_xattn")
    query_weights, query = queries(c)
    add_product(c, "out_mix", out_weights, query_weights, norm)
    query(norm)
    xo_weights = residual_weights(c, d["w_xo"][0])
    attention(c, xo_weights)
    up_weights, hidden = mlp(c)
    norm = Norm(c, "norm_mlp", "norm_mlp")
    add_product(c, "xo", xo_weights, up_weights, norm)
    final = Norm(c, "norm_final", "norm_final", events=("squared", "added", "summed", "rooted", "scaled"),
                 acc=tail(c, 0, "final_acc", [P, SEQ]))
    hidden(norm, final)
    return final


def build(nc, dram, out):
    with ExitStack() as ctx:
        c = open_core(nc, ctx, dram)
        setup(c)
        final = first_block(c)
        renew(c)
        second_block(c, out, final)


def kernel(**inputs):
    from concourse import bacc
    from concourse.bass_utils import run_bass_kernel_spmd
    import numpy as np

    arrays = {f"in_{name}_dram": np.ascontiguousarray(inputs[name]) for name in _INS}
    nc = bacc.Bacc("TRN2", target_bir_lowering=False, num_devices=1)
    dram = {name: nc.dram_tensor(f"in_{name}_dram", list(arrays[f"in_{name}_dram"].shape), F32, kind="ExternalInput").ap()
            for name in _INS}
    out = nc.dram_tensor("out_0_dram", [1, SEQ, D], F32, kind="ExternalOutput").ap()
    build(nc, dram, out)
    nc.finalize()
    results = run_bass_kernel_spmd(nc, [arrays], core_ids=[0])
    return results.results[0]["out_0_dram"]
```

```python
from contextlib import ExitStack

import concourse.bass as bass
from concourse import mybir

F32 = mybir.dt.float32
F32R = mybir.dt.float32r
ALU = mybir.AluOpType
ACT = mybir.ActivationFunctionType
AX_X = mybir.AxisListType.X

P = 128
SEQ = 1024
HALF = 512
D = 1024
KT = D // P
N_MEM = 256
EPS = 1e-6
LN_X_EPS = 64e-5

_INS = [
    "x", "mem", "norm_mix", "w_in", "b_gate", "mu_shift", "w0", "w_lora_w", "a0", "w_lora_a", "w_lora_g",
    "k_k", "k_a", "r_k", "ln_x_w", "ln_x_b", "conv_w", "w_proj_a", "w_proj_b", "w_out_mix", "norm_xattn",
    "norm_mem", "w_q", "w_kv", "w_xo", "norm_mlp", "w_up", "w_down", "norm_final", "norm_gain_2", "w_in_2",
    "b_gate_2", "conv_w_2", "a_log_2", "dt_bias_2", "dn_out_gain_2", "sb_q_gain_2", "sb_k_gain_2",
    "w_up_a_2", "w_up_b_2", "w_out_2",
]

VECTORS = [
    ("norm_mix", 8), ("b_gate", 16), ("mu_shift", 15), ("w0", 4), ("a0", 4), ("k_k", 4), ("k_a", 4),
    ("r_k", 4), ("ln_x_w", 4), ("ln_x_b", 4), ("conv_w", 12), ("norm_xattn", 8), ("norm_mem", 8),
    ("norm_mlp", 8), ("norm_final", 8), ("norm_gain_2", 8),
    ("b_gate_2", 16), ("conv_w_2", 48), ("dn_out_gain_2", 1), ("sb_q_gain_2", 1), ("sb_k_gain_2", 1),
]


def wait(eng, sem, value):
    if not (isinstance(value, int) and value <= 0):
        eng.wait_ge(sem, value)


def apart(c, eng):
    eng.sem_inc(c.passed, 1)


class Steps:

    def __init__(self, sem):
        self.sem, self.total, self.shift = sem, 0, 0

    def mark(self, ins):
        ins.then_inc(self.sem, 1)
        self.total += 1
        return self.total + self.shift

    def wait(self, eng, value=None):
        wait(eng, self.sem, self.total + self.shift if value is None else value)


def rolled(eng, n, body, *steps):
    starts = [s.total for s in steps]
    body(0)
    if n > 1:
        per = [s.total - a for s, a in zip(steps, starts)]
        with eng.Fori(1, n) as i:
            for s, a, p in zip(steps, starts, per):
                s.total, s.shift = a, i * p
            body(i)
        assert [s.total - a for s, a in zip(steps, starts)] == per, "turns count alike"
        for s, a, p in zip(steps, starts, per):
            s.total, s.shift = a + n * p, 0


def first(i):
    return isinstance(i, int) and i == 0


def columns(i, width):
    return bass.ds(i * width, width)


class Weights:

    def __init__(self, core, sources, turns, shift=0):
        self.core, self.sources, self.turns, self.shift = core, sources, turns, shift
        self.per = len(sources)
        self.begun, self.ahead = False, 0
        self.slots = 3 if self.per % 3 == 0 else 2
        self.total = self.per * turns
        self.parts = [2 if isinstance(s(0), tuple) else 1 for s in sources]
        assert self.per % self.slots == 0

    def begin(self):
        if self.begun:
            return
        self.begun = True
        self.t0 = self.core.tiles
        self.l0 = list(self.core.loads)
        self.core.tiles += self.total
        for s in range(self.slots):
            self.core.loads[s] += self.total // self.slots * self.parts[s]

    def slot(self, u):
        return (u + self.shift) % self.slots

    def fetch(self, sp, u, i):
        c, s, src = self.core, self.slot(u), self.sources[u](i)
        if self.parts[u] == 2:
            for half, part in enumerate(src):
                sp.dma_start(c.w_raw[:, s, half * KT // 2:(half + 1) * KT // 2], part).then_inc(c.w_loaded[s], 16)
        else:
            sp.dma_start(c.w_raw[:, s], src).then_inc(c.w_loaded[s], 16)

    def load_first(self, sp):
        for u in range(self.slots):
            self.fetch(sp, u, 0)

    def load_all(self, sp):
        for u in range(self.slots):
            sp.wait_ge(self.core.w_split, self.t0 + (u - self.slots + 1))
            self.fetch(sp, u, 0)
        self.load_rest(sp)

    def load_rest(self, sp):
        c, n = self.core, self.slots

        def turn(i):
            for u in range(self.per):
                if first(i) and u < n:
                    continue
                sp.wait_ge(c.w_split, self.t0 + i * self.per + (u - n + 1))
                apart(c, sp)
                self.fetch(sp, u, i)

        rolled(sp, self.turns, turn)

    def split_tile(self, pool, i, u):
        c, n, s = self.core, self.slots, self.slot(u)
        each = 16 * self.parts[u]
        pool.wait_ge(c.w_loaded[s], 16 * self.l0[s] + i * (each * (self.per // n)) + each * (u // n + 1))
        wait(pool, c.tile_done, self.t0 + i * self.per + (u - n + 1))
        pool.tensor_tensor(c.w_hi[:, s], c.w_raw[:, s], c.ones[:].unsqueeze(1).broadcast_to([P, KT, P]),
                           ALU.mult).then_inc(c.w_rounded, 1)
        pool.wait_ge(c.w_rounded, self.t0 + i * self.per + (u + 1))
        pool.tensor_tensor(c.w_lo[:, s], c.w_raw[:, s], c.w_hi[:, s].bitcast(F32), ALU.subtract).then_inc(c.w_split, 1)

    def split_first(self, pool):
        self.begin()
        self.ahead = self.slots
        for u in range(self.ahead):
            self.split_tile(pool, 0, u)

    def share_first(self):
        self.ahead = 1

    def round_first(self, act):
        c, s = self.core, self.slot(0)
        act.wait_ge(c.w_loaded[s], 16 * self.l0[s] + 16 * self.parts[0])
        wait(act, c.tile_done, self.t0 + (1 - self.slots))
        act.copy(c.w_hi[:, s], c.w_raw[:, s]).then_inc(c.w_rounded, 1)

    def subtract_first(self, dve):
        c, s = self.core, self.slot(0)
        dve.wait_ge(c.w_rounded, self.t0 + 1)
        dve.tensor_tensor(c.w_lo[:, s], c.w_raw[:, s], c.w_hi[:, s].bitcast(F32), ALU.subtract).then_inc(c.w_split, 1)

    def split(self, pool, beside=None):
        def turn(i):
            for u in range(self.per):
                if not (first(i) and u < self.ahead):
                    if first(i) and u == self.ahead:
                        wait(pool, self.core.w_split, self.t0 + u if u else 0)
                    self.split_tile(pool, i, u)
                if beside:
                    beside(i, u)

        rolled(pool, self.turns, turn)

    def round_on(self, act):
        c, n = self.core, self.slots

        def turn(i):
            for u in range(self.per):
                s = self.slot(u)
                act.wait_ge(c.w_loaded[s], 16 * self.l0[s] + i * (16 * (self.per // n)) + 16 * (u // n + 1))
                wait(act, c.tile_done, self.t0 + i * self.per + (u - n + 1))
                act.copy(c.w_hi[:, s], c.w_raw[:, s]).then_inc(c.w_rounded, 1)

        rolled(act, self.turns, turn)

    def subtract(self, eng, beside=None):
        c = self.core

        def turn(i):
            for u in range(self.per):
                s = self.slot(u)
                eng.wait_ge(c.w_rounded, self.t0 + i * self.per + (u + 1))
                eng.tensor_tensor(c.w_lo[:, s], c.w_raw[:, s], c.w_hi[:, s].bitcast(F32),
                                   ALU.subtract).then_inc(c.w_split, 1)
                if beside:
                    beside(i, u)

        rolled(eng, self.turns, turn)

    def ready(self, pe, i, u):
        pe.wait_ge(self.core.w_split, self.t0 + i * self.per + (u + 1))

    def done(self, eng, i, u):
        eng.wait_ge(self.core.tile_done, self.t0 + i * self.per + (u + 1))

    def multiply(self, pe, u, out, hi, lo, kts=range(KT), offset=0, width=HALF, before=None, half=0):
        c, s = self.core, self.slot(u)
        kts = list(kts)
        for k in kts:
            if before:
                before(k)
            for w, a in ((c.w_hi, hi), (c.w_hi, lo), (c.w_lo, hi)):
                for h, o in enumerate(out):
                    last = pe.matmul(o, w[:, s, k], a[:, k - offset, (half + h) * width:(half + h + 1) * width],
                                     start=(k == kts[0] and w is c.w_hi and a is hi),
                                     stop=(k == kts[-1] and w is c.w_lo))
        return last


NORM_EVENTS = dict(squared=KT, added=KT, summed=2, rooted=2, scaled=2 * KT, rounded=2 * KT, split=2 * KT)
NORM_AT = 59392


class Norm:

    def __init__(self, c, name, gain, events=tuple(NORM_EVENTS), acc=None):
        self.c, self.gain = c, gain
        self.root = at(c, NORM_AT, f"{name}_root", [P, 2, HALF])
        self.whole = at(c, NORM_AT + 4096, f"{name}_whole", [P, 2, HALF])
        self.acc = acc if acc is not None else at(c, NORM_AT + 8192, f"{name}_acc", [P, SEQ])
        self.events = events
        self.before = dict(c.norm_totals)
        for n in events:
            c.norm_totals[n] += NORM_EVENTS[n]

    def wait(self, eng, name, n):
        wait(eng, self.c.norm_sems[name], self.before[name] + n)

    def mark(self, ins, name):
        ins.then_inc(self.c.norm_sems[name], 1)

    def square(self, act, dst, src, n):
        self.mark(act.activation(dst, src, ACT.Square), "squared")

    def add_squares(self, pool, sq, n):
        self.wait(pool, "squared", n + 1)
        self.wait(pool, "added", n)
        self.mark(pool.tensor_tensor(self.acc[:], self.acc[:], sq, ALU.add), "added")

    def pe_sums(self, pe):
        for h in range(2) if "summed" in self.events else ():
            self.mark(pe.matmul(self.c.ps[:, 4 + h], self.c.ones[:], self.acc[:, h * HALF:(h + 1) * HALF], start=True, stop=True),
                      "summed")

    def act_roots(self, act):
        for h in range(2):
            if "summed" in self.events:
                self.wait(act, "summed", h + 1)
            self.mark(act.activation(self.root[:, h], self.c.ps[:, 4 + h], ACT.Sqrt, bias=self.c.eps[:, 0:1], scale=1.0 / D),
                      "rooted")

    def act(self, act):
        self.act_roots(act)
        for n in range(2 * KT):
            self.wait(act, "scaled", n + 1)
            h, k = divmod(n, KT)
            self.mark(act.copy(self.c.h_hi[:, k, h * HALF:(h + 1) * HALF], self.whole[:, n % 2]), "rounded")

    def dve(self, dve):
        c, v = self.c, self.c.v_steps

        def take(n):
            h, k = divmod(n, KT)
            cut = slice(h * HALF, (h + 1) * HALF)
            self.wait(dve, "rounded", n + 1)
            self.mark(dve.tensor_tensor(c.h_lo[:, k, cut], self.whole[:, n % 2], c.h_hi[:, k, cut].bitcast(F32), ALU.subtract),
                      "split")

        for n in range(2 * KT):
            h, k = divmod(n, KT)
            if k == 0:
                if n:
                    take(n - 1)
                self.wait(dve, "rooted", h + 1)
                v.mark(dve.reciprocal(self.root[:, h], self.root[:, h]))
                v.wait(dve)
            if n >= 2:
                self.wait(dve, "split", n - 1)
            self.mark(dve.scalar_tensor_tensor(out=self.whole[:, n % 2], in0=c.x[:, k, h * HALF:(h + 1) * HALF],
                                               scalar=vec(c, self.gain, k), in1=self.root[:, h], op0=ALU.mult, op1=ALU.mult),
                      "scaled")
            if k:
                take(n - 1)
        take(2 * KT - 1)

    def first_tiles(self, pe, weights):
        c = self.c
        for h in range(2):
            for u in range(2):
                if h == 0:
                    weights.ready(pe, 0, u)
                last = weights.multiply(pe, u, [c.ps[:, 2 * u + h]], c.h_hi, c.h_lo, half=h,
                                        before=(lambda k: self.wait(pe, "split", h * KT + k + 1)) if u == 0 else None)
                if h:
                    last.then_inc(c.tile_done, 1)


class Core:
    pass


def open_core(nc, ctx, dram):
    c = Core()
    c.nc, c.ctx, c.dram = nc, ctx, dram

    def sb(name, shape, dt=F32):
        return ctx.enter_context(nc.sbuf_tensor(name, shape, dt))

    c.sb = sb
    c.stage_sems = []

    def sem(name):
        c.stage_sems.append(ctx.enter_context(nc.semaphore(name)))
        return c.stage_sems[-1]

    c.sem = sem
    c.x = sb("x_t", [P, KT, SEQ])
    c.h_base = (nc.sbuf_base + 31) // 32 * 32
    c.h_hi = sb("h_hi", [P, KT, SEQ], F32R)
    c.h_lo = sb("h_lo", [P, KT, SEQ], F32R)
    c.w_raw = sb("w_raw", [P, 3, KT, P])
    c.w_base = (nc.sbuf_base + 31) // 32 * 32
    c.w_hi = sb("w_hi", [P, 3, KT, P], F32R)
    c.w_lo = sb("w_lo", [P, 3, KT, P], F32R)
    c.vec = sb("vec", [P, 2 * P])
    c.ident = sb("ident", [P, P])
    c.ones = sb("ones", [P, P])
    c.ones_64 = sb("ones_64", [P, P])
    c.upper = sb("upper", [P, P])
    c.upper_eq = sb("upper_eq", [P, P])
    c.lower = sb("lower", [P, P])
    c.level_t = sb("level_t", [P, P])
    c.eps = sb("eps", [P, 5])
    c.lmid = sb("lmid", [P, CT, TILES + 1])
    c.lend = sb("lend", [P, CT, TILES])
    c.beta_col, c.decay_col, c.beta_decay = (sb(n, [P, TILES, DN_HEADS]) for n in ("beta_col", "decay_col", "beta_decay"))
    c.aux_base = nc.sbuf_base
    c.ps = ctx.enter_context(nc.psum_tensor("ps", [P, 8, HALF], F32))
    c.w_loaded = [c.sem(f"w_loaded{s}") for s in range(3)]
    c.w_rounded, c.w_split, c.tile_done = c.sem("w_rounded"), c.sem("w_split"), c.sem("tile_done")
    c.tiles, c.loads = 0, [0, 0, 0]
    c.a_steps, c.v_steps = Steps(c.sem("act_steps")), Steps(c.sem("dve_steps"))
    c.g_steps, c.t_steps = Steps(c.sem("pool_steps")), Steps(c.sem("pe_steps"))
    c.norm_sems = {n: c.sem(f"norm_{n}") for n in NORM_EVENTS}
    c.norm_totals = dict.fromkeys(NORM_EVENTS, 0)
    c.begun, c.passed = c.sem("ident_ready"), c.sem("waits_passed")
    c.scratch = {}
    c.col, row = {}, 0
    for name, rows in VECTORS:
        c.col[name] = row
        row += rows
    assert row <= 2 * P
    c.stage_sems = []
    return c


def at(c, off, name, shape, dt=F32):
    return c.nc.alloc_sbuf_tensor_at(name, shape, dt, offset=(c.aux_base + 31) // 32 * 32 + off)


def at_h(c, off, name, shape, dt=F32):
    return c.nc.alloc_sbuf_tensor_at(name, shape, dt, offset=c.h_base + off)


def nth(events, name, i=0):
    return i * len(events) + (events.index(name) + 1)


def scratch(c, name, shape):
    c.scratch[name] = c.nc.dram_tensor(name, shape, F32, kind="Internal").ap()
    return c.scratch[name]


def vec(c, name, i=0):
    k = c.col[name]
    return c.vec[:, k + i:k + i + 1] if isinstance(i, int) else c.vec[:, bass.ds(i + k, 1)]


def setup(c):
    nc, d = c.nc, c.dram
    rows = at(c, 0, "vec_rows", [P, 2, P])
    tiles = [d["x"][0, t * P:(t + 1) * P, :] for t in range(TILES)] + [d["mem"][0, t * P:(t + 1) * P, :] for t in range(2)]
    xin = at(c, 24576, "x_in", [P, len(tiles), D])
    c.mem_t = at(c, 16384, "mem_t", [P, KT, N_MEM])
    cleared, rows_in = c.sem("rows_cleared"), c.sem("rows_loaded")
    x_in = [c.sem(f"x_loaded{t}") for t in range(len(tiles))]
    ident_ready, turned, copied = c.begun, c.sem("tile_turned"), c.sem("tile_copied")
    n_rows = [0]
    with nc.Block() as block:

        @block.sync
        def _(sp):
            for t, src in enumerate(tiles):
                sp.dma_start(xin[:, t], src).then_inc(x_in[t], 16)
            sp.wait_ge(cleared, 1)
            for name, n in VECTORS:
                r = c.col[name]
                flat = d[name]
                if name == "mu_shift":
                    mu = flat.rearrange("a n -> (a n)")
                    parts = [(r, mu[0:14 * P].rearrange("(n p) -> n p", p=P)),
                             (r + 14, mu[14 * P:1824].rearrange("(n p) -> n p", n=1))]
                elif name.startswith("sb_"):
                    parts = [(r, flat), (r, flat)]
                elif len(flat.shape) == 1:
                    parts = [(r, flat.rearrange("(n p) -> n p", p=P))]
                elif len(flat.shape) == 2:
                    parts = [(r, flat.rearrange("a (n p) -> (a n) p", p=P))]
                elif name == "r_k":
                    parts = [(r, flat.rearrange("a (n b) p -> (a n) (b p)", b=2))]
                elif len(flat.shape) == 3:
                    parts = [(r, flat.rearrange("a t (n p) -> (a t n) p", p=P))]
                else:
                    parts = [(r, flat.rearrange("a t b (n p) -> (a t b n) p", p=P))]
                for k, (at_row, src) in enumerate(parts):
                    done = 0
                    while done < src.shape[0]:
                        s, q = divmod(at_row + done, P)
                        m = min(src.shape[0] - done, P - q)
                        w = src.shape[1]
                        first = k * 64 if name.startswith("sb_") else 0
                        sp.dma_start(rows[q:q + m, s, first:first + w], src[done:done + m, :]).then_inc(rows_in, 16)
                        n_rows[0] += 1
                        done += m

        @block.gpsimd
        def _(pool):
            g = c.g_steps

            def fill(buf, value):
                return g.mark(pool.memset(buf, value))

            def keep(buf, pattern, base, mult, op=ALU.is_ge, fill=0.0):
                g.mark(pool.affine_select(out=buf, in_=buf, compare_op=op, fill=fill, base=base,
                                          pattern=pattern, channel_multiplier=mult))
                g.wait(pool)

            pool.memset(rows[:], 0.0).then_inc(cleared, 1)
            for buf, value in ((c.ident, 0.0), (c.ones, 1.0), (c.ones_64, 1.0), (c.upper, 1.0),
                               (c.upper_eq, 1.0), (c.lower, 1.0), (c.level_t, 0.0)):
                fill(buf[:], value)
            for k, value in enumerate((EPS, LN_X_EPS, 1.0, 0.0, EPS * SB_HEAD)):
                fill(c.eps[:, k:k + 1], value)
            g.wait(pool)
            pool.affine_select(out=c.ident[:], in_=c.ident[:], compare_op=ALU.not_equal, fill=1.0, base=0,
                               pattern=[[-1, P]], channel_multiplier=1).then_inc(ident_ready, 1)
            keep(c.ones_64[:, 0:64], [[0, 64]], 63, -1)
            keep(c.ones_64[:, 64:128], [[0, 64]], -64, 1)
            keep(c.upper[:], [[1, P]], -1, -1)
            keep(c.upper_eq[:], [[1, P]], 0, -1)
            keep(c.lower[:], [[-1, P]], -1, 1)
            odd = c.level_t[:].rearrange("p (b w) -> p b w", w=2)[:, :, 1:2]
            keep(odd, [[-2, P // 2]], 0, 1, op=ALU.not_equal, fill=1.0)

        @block.tensor
        def _(pe):
            pe.wait_ge(ident_ready, 1)
            for t in range(len(tiles)):
                pe.wait_ge(x_in[t], 16)
                wait(pe, copied, t - 1)
                for k in range(KT):
                    last = pe.transpose(c.ps[:, 2 * (t % 2) + k // 4, (k % 4) * P:(k % 4 + 1) * P],
                                        xin[:, t, k * P:(k + 1) * P], c.ident[:])
                last.then_inc(turned, 1)
            pe.wait_ge(rows_in, 16 * n_rows[0])
            for s in range(2):
                last = pe.transpose(c.ps[:, 4, s * P:(s + 1) * P], rows[:, s, :], c.ident[:])
            last.then_inc(turned, 1)

        @block.scalar
        def _(act):
            for t in range(SEQ // P + 2):
                act.wait_ge(turned, t + 1)
                dst = c.x[:, :, t * P:(t + 1) * P] if t < 8 else c.mem_t[:, :, (t - 8) * P:(t - 7) * P]
                act.copy(dst, c.ps[:, 2 * (t % 2):2 * (t % 2) + 2, :]
                         .rearrange("p b (k n) -> p (b k) n", n=P)).then_inc(copied, 1)
            act.wait_ge(turned, SEQ // P + 3)
            act.copy(c.vec[:], c.ps[:, 4, 0:2 * P]).then_inc(copied, 1)


def memory_norm(c, hi, lo, following):
    gain, src, width = "norm_mem", c.mem_t, N_MEM
    sq = at(c, 40960, "mem_sq", [P, KT, width])
    root = at(c, 49152, "mem_root", [P, width])
    whole = at(c, 50176, "mem_whole", [P, KT, width])
    squared, summed, rooted, scaled, rounded, split = (
        c.sem(f"mem_{n}") for n in ("squared", "summed", "rooted", "scaled", "rounded", "split"))
    with c.nc.Block() as block:

        @block.sync
        def _(sp):
            following.load_first(sp)

        @block.tensor
        def _(pe):
            for k in range(KT):
                pe.wait_ge(squared, k + 1)
                pe.matmul(c.ps[:, 0, 0:width], c.ones[:], sq[:, k], start=k == 0, stop=k == KT - 1).then_inc(summed, 1)

        @block.scalar
        def _(act):
            for k in range(KT):
                act.activation(sq[:, k], src[:, k], ACT.Square).then_inc(squared, 1)
            act.wait_ge(summed, KT)
            act.activation(root[:], c.ps[:, 0, 0:width], ACT.Sqrt, bias=c.eps[:, 0:1], scale=1.0 / D).then_inc(rooted, 1)
            for k in range(KT):
                act.wait_ge(scaled, k + 1)
                act.copy(hi[:, k], whole[:, k]).then_inc(rounded, 1)

        @block.vector
        def _(dve):
            v = c.v_steps
            dve.wait_ge(rooted, 1)
            v.mark(dve.reciprocal(root[:], root[:]))
            v.wait(dve)
            for k in range(KT):
                dve.scalar_tensor_tensor(out=whole[:, k], in0=src[:, k], scalar=vec(c, gain, k), in1=root[:],
                                         op0=ALU.mult, op1=ALU.mult).then_inc(scaled, 1)
            for k in range(KT):
                dve.wait_ge(rounded, k + 1)
                dve.tensor_tensor(lo[:, k], whole[:, k], hi[:, k].bitcast(F32), ALU.subtract).then_inc(split, 1)


def add_product(c, name, weights, following, norm=None):
    nc = c.nc
    weights.begin()
    free = [c.sem(f"{name}_free{q}") for q in range(2)]
    cleared = c.sem(f"{name}_cleared")
    sq = at(c, 0, f"{name}_sq", [P, 2, SEQ])

    def row(k):
        return c.x[:, bass.ds(k, 1), :].rearrange("p a n -> p (a n)")

    with nc.Block() as block:

        @block.sync
        def _(sp):
            weights.load_rest(sp)
            if following:
                sp.wait_ge(c.w_split, weights.t0 + weights.total)
                following.load_first(sp)

        @block.gpsimd
        def _(pool):
            if not norm:
                weights.split(pool)
                return
            pool.memset(norm.acc[:], 0.0).then_inc(cleared, 1)
            pool.wait_ge(cleared, 1)

            def beside(i, u):
                if not first(i):
                    norm.add_squares(pool, sq[:, u], i * 2 + (u - 2))

            weights.split(pool, beside)
            for k in (KT - 2, KT - 1):
                norm.add_squares(pool, sq[:, k % 2], k)

        @block.tensor
        def _(pe):
            def turn(i):
                for u in range(2):
                    weights.ready(pe, i, u)
                    wait(pe, free[u], i)
                    weights.multiply(pe, u, [c.ps[:, 2 * u], c.ps[:, 2 * u + 1]], c.h_hi, c.h_lo).then_inc(c.tile_done, 1)

            rolled(pe, weights.turns, turn)

        @block.scalar
        def _(act):
            def turn(i):
                for u in range(2):
                    act.wait_ge(free[u], i + 1)
                    if not first(i):
                        norm.wait(act, "added", i * 2 + (u - 1))
                    apart(c, act)
                    norm.square(act, sq[:, u], row(i * 2 + u), i * 2 + u)

            if norm:
                rolled(act, weights.turns, turn)

        @block.vector
        def _(dve):
            def turn(i):
                for u in range(2):
                    weights.done(dve, i, u)
                    dve.tensor_tensor(row(i * 2 + u), row(i * 2 + u), c.ps[:, 2 * u:2 * u + 2, :].rearrange("p b n -> p (b n)"),
                                      ALU.add).then_inc(free[u], 1)

            rolled(dve, weights.turns, turn)


def tile_of(src, first=0):
    view = src.rearrange("(k p) n -> p k n", p=P)
    return lambda i, step=1, off=0: view[:, :, bass.ds(i * (step * P) + (first + off * P), P)]


def finish(c, out):
    nc = c.nc
    tok = at(c, 0, "out_tok", [P, 2, D])
    turned, copied = c.sem("out_turned"), c.sem("out_copied")
    stored = [c.sem("out_stored0"), c.sem("out_stored1")]
    with nc.Block() as block:

        @block.tensor
        def _(pe):
            for t in range(SEQ // P):
                wait(pe, copied, t - 1)
                for k in range(KT):
                    last = pe.transpose(c.ps[:, 2 * (t % 2) + k // 4, (k % 4) * P:(k % 4 + 1) * P],
                                        c.x[:, k, t * P:(t + 1) * P], c.ident[:])
                last.then_inc(turned, 1)

        @block.scalar
        def _(act):
            for t in range(SEQ // P):
                act.wait_ge(turned, t + 1)
                wait(act, stored[t % 2], 16 * (t // 2))
                act.copy(tok[:, t % 2], c.ps[:, 2 * (t % 2):2 * (t % 2) + 2, :].rearrange("p b n -> p (b n)")).then_inc(copied, 1)

        @block.sync
        def _(sp):
            for t in range(SEQ // P):
                sp.wait_ge(copied, t + 1)
                sp.dma_start(out[0, t * P:(t + 1) * P, :], tok[:, t % 2]).then_inc(stored[t % 2], 16)
            for s in range(2):
                sp.wait_ge(stored[s], 16 * (SEQ // P // 2))


def mlp(c):
    nc, d = c.nc, c.dram
    groups, pairs = 4, KT // 2
    up, down = tile_of(d["w_up"][0]), d["w_down"][0]
    hid_hi = at(c, 0, "hid_hi", [P, KT, SEQ], F32R)
    hid_lo = at(c, 32768, "hid_lo", [P, KT, SEQ], F32R)
    relu = c.w_raw[:, 2].rearrange("p (h k) n -> p h (k n)", h=2)
    rectified, squared, rounded = c.sem("hid_rectified"), c.sem("hid_squared"), c.sem("hid_rounded")
    ready, cleared = c.sem("hid_ready"), c.sem("final_cleared")
    sq = c.w_raw[:, 2].rearrange("p k n -> p (k n)")
    down_free = [c.sem("down_free0"), c.sem("down_free1")]
    streams = []
    for g in range(groups):
        rows = tile_of(down[g * D:(g + 1) * D, :])
        streams.append((Weights(c, [lambda i, g=g, u=u: up(i, 2, g * KT + u) for u in range(2)], pairs),
                        Weights(c, [lambda i, rows=rows, u=u: rows(i, 2, u) for u in range(2)], pairs)))

    def build(norm, after):
        for pair in streams:
            for w in pair:
                w.begin()
        every = [w for pair in streams for w in pair]
        with nc.Block() as block:

            @block.sync
            def _(sp):
                every[0].load_rest(sp)
                for w in every[1:]:
                    w.load_all(sp)

            @block.gpsimd
            def _(pool):
                for w in every[:-1]:
                    w.split(pool)
                pool.memset(after.acc[:], 0.0).then_inc(cleared, 1)
                pool.wait_ge(cleared, 1)

                def beside(i, u):
                    if not first(i):
                        after.add_squares(pool, sq, i * 2 + (u - 2))

                every[-1].split(pool, beside)
                for k in (KT - 2, KT - 1):
                    after.add_squares(pool, sq, k)

            @block.tensor
            def _(pe):
                norm.pe_sums(pe)
                for g, (w_up, w_down) in enumerate(streams):
                    def up_turn(i):
                        if g == 0 and first(i):
                            norm.first_tiles(pe, w_up)
                            return
                        for u in range(2):
                            w_up.ready(pe, i, u)
                            wait(pe, rectified, (g * pairs + i) * 4 + (2 * u - 2))
                            w_up.multiply(pe, u, [c.ps[:, 2 * u], c.ps[:, 2 * u + 1]], c.h_hi,
                                          c.h_lo).then_inc(c.tile_done, 1)

                    def down_turn(i):
                        for u in range(2):
                            w_down.ready(pe, i, u)
                            wait(pe, down_free[u], g * pairs + i)
                            waits = first(i) and u == 0
                            w_down.multiply(pe, u, [c.ps[:, 4 + 2 * u], c.ps[:, 5 + 2 * u]], hid_hi, hid_lo,
                                            before=(lambda k: pe.wait_ge(ready, g * 16 + 2 * k + 2)) if waits
                                            else None).then_inc(c.tile_done, 1)

                    rolled(pe, pairs, up_turn)
                    rolled(pe, pairs, down_turn)

            @block.scalar
            def _(act):
                norm.act(act)
                for g, (w_up, w_down) in enumerate(streams):
                    def turn(i):
                        for u in range(2):
                            w_up.done(act, i, u)
                            k = bass.ds(i * 2 + u, 1)
                            n = (g * pairs + i) * 4 + 2 * u
                            for h in range(2):
                                wait(act, ready, n + (h - 1))
                                act.activation(relu[:, h], c.ps[:, 2 * u + h], ACT.Relu).then_inc(rectified, 1)
                            for h in range(2):
                                act.wait_ge(squared, n + (h + 1))
                                act.copy(hid_hi[:, k, h * HALF:(h + 1) * HALF].rearrange("p a n -> p (a n)"),
                                         relu[:, h]).then_inc(rounded, 1)

                    rolled(act, pairs, turn)

                def squares(i):
                    for u in range(2):
                        act.wait_ge(down_free[u], (groups - 1) * pairs + i + 1)
                        if u or not first(i):
                            after.wait(act, "added", i * 2 + u)
                        apart(c, act)
                        after.square(act, sq, c.x[:, bass.ds(i * 2 + u, 1), :].rearrange("p a n -> p (a n)"), i * 2 + u)

                act.wait_ge(ready, groups * pairs * 4)
                rolled(act, pairs, squares)

            @block.vector
            def _(dve):
                norm.dve(dve)
                for g, (w_up, w_down) in enumerate(streams):
                    def up_turn(i):
                        for u in range(2):
                            k = bass.ds(i * 2 + u, 1)
                            n = (g * pairs + i) * 4 + 2 * u
                            for h in range(2):
                                dve.wait_ge(rectified, n + (h + 1))
                                dve.tensor_tensor(relu[:, h], relu[:, h], relu[:, h], ALU.mult).then_inc(squared, 1)
                            for h in range(2):
                                dve.wait_ge(rounded, n + (h + 1))
                                cut = slice(h * HALF, (h + 1) * HALF)
                                dve.tensor_tensor(hid_lo[:, k, cut].rearrange("p a n -> p (a n)"), relu[:, h],
                                                  hid_hi[:, k, cut].rearrange("p a n -> p (a n)").bitcast(F32),
                                                  ALU.subtract).then_inc(ready, 1)

                    def down_turn(i):
                        for u in range(2):
                            w_down.done(dve, i, u)
                            if g:
                                dve.wait_ge(down_free[u], (g - 1) * pairs + i + 1)
                            rows = c.x[:, bass.ds(i * 2 + u, 1), :].rearrange("p a n -> p (a n)")
                            dve.tensor_tensor(rows, rows, c.ps[:, 4 + 2 * u:6 + 2 * u, :].rearrange("p b n -> p (b n)"),
                                              ALU.add).then_inc(down_free[u], 1)

                    rolled(dve, pairs, up_turn)
                    rolled(dve, pairs, down_turn)

    return streams[0][0], build


N_HEADS = 8
HEAD = 64
D_RWKV = N_HEADS * HEAD
CT = D_RWKV // P
RWKV_COLS = 3 * D_RWKV + 288
TILES = SEQ // P
DECAY = -0.6065306597126334
STORED = ["a_t", "r_t", "k_t", "b_t", "v_t", "bonus_t", "gate_t"]


def rwkv_lora_inputs(c):
    nc, d = c.nc, c.dram
    tile = tile_of(d["w_in"][0])
    c.lora_in = at(c, 0, "lora_in", [P, SEQ])
    c.gate_in = at(c, 4096, "gate_in", [P, SEQ])
    c.gate_in2 = at(c, 8192, "gate_in2", [P, SEQ])
    c.gate_w2 = c.gate_in2[32:64, 0:D_RWKV]
    c.lora_w = at(c, 12288, "lora_w", [P, D_RWKV])
    c.gate_w = at(c, 14336, "gate_w", [P, D_RWKV])
    plain = at(c, 20480, "lora_plain", [P, 3, SEQ + 1])
    mixed = at(c, 20480 + 12320, "lora_mixed", [P, 3, SEQ])
    weights = Weights(c, [lambda i, u=u: tile(i, 3, 12 + u) for u in range(3)], 1)
    cleared, copied, moved = c.sem("lora_cleared"), c.sem("lora_copied"), c.sem("lora_mixed_done")
    c.lora_loaded = c.sem("lora_loaded")
    mu = c.col["mu_shift"] + 12

    def build(following, norm):
        weights.begin()
        with nc.Block() as block:

            @block.sync
            def _(sp):
                weights.load_rest(sp)
                sp.dma_start(c.lora_w[0:64, :], d["w_lora_w"][0]).then_inc(c.lora_loaded, 16)
                sp.dma_start(c.lora_w[64:128, :], d["w_lora_a"][0]).then_inc(c.lora_loaded, 16)
                sp.dma_start(c.gate_w[:], d["w_lora_g"][0, 0:P, :]).then_inc(c.lora_loaded, 16)
                sp.dma_start(c.gate_w2, d["w_lora_g"][0, P:160, :]).then_inc(c.lora_loaded, 16)
                sp.wait_ge(c.w_split, weights.t0 + weights.total)
                following.load_first(sp)
                sp.wait_ge(c.values_stored, 16)

            @block.gpsimd
            def _(pool):
                pool.memset(plain[:, :, 0:1], 0.0).then_inc(cleared, 1)
                weights.split(pool)
                following.split_first(pool)

            @block.tensor
            def _(pe):
                norm.pe_sums(pe)
                norm.first_tiles(pe, weights)
                weights.ready(pe, 0, 2)
                weights.multiply(pe, 2, [c.ps[:, 4], c.ps[:, 5]], c.h_hi, c.h_lo).then_inc(c.tile_done, 1)

            @block.scalar
            def _(act):
                norm.act(act)
                for u in range(3):
                    weights.done(act, 0, u)
                    act.copy(plain[:, u, 1:SEQ + 1], c.ps[:, 2 * u:2 * u + 2].rearrange("p b n -> p (b n)")).then_inc(copied, 1)
                act.wait_ge(moved, 1)
                act.activation(c.lora_in[0:64, :], mixed[0:64, 0, :], ACT.Tanh)
                act.copy(c.lora_in[64:128, :], mixed[64:128, 0, :])
                act.wait_ge(moved, 2)
                act.activation(c.gate_in[:], mixed[:, 1, :], ACT.Sigmoid)
                act.wait_ge(moved, 3)
                act.activation(c.gate_in2[0:32, :], mixed[0:32, 2, :], ACT.Sigmoid)

            @block.vector
            def _(dve):
                v = c.v_steps
                norm.dve(dve)
                dve.wait_ge(cleared, 1)
                for u in range(3):
                    dve.wait_ge(copied, u + 1)
                    v.mark(dve.tensor_tensor(mixed[:, u], plain[:, u, 0:SEQ], plain[:, u, 1:SEQ + 1], ALU.subtract))
                    v.wait(dve)
                    dve.scalar_tensor_tensor(out=mixed[:, u], in0=mixed[:, u], scalar=c.vec[:, mu + u:mu + u + 1],
                                             in1=plain[:, u, 1:SEQ + 1], op0=ALU.mult, op1=ALU.add).then_inc(moved, 1)

    return weights, build


def rwkv_features(c):
    nc, d = c.nc, c.dram
    tile = tile_of(d["w_in"][0])
    out = [scratch(c, f"rwkv_{name}", [CT, P, SEQ]) for name in STORED]
    order = [4, 0, 8]
    weights = Weights(c, [lambda i, o=o: tile(i, 1, o) for o in order], CT)
    mid = SEQ // TILES // 2 - 1
    base = 16384

    def buf(name, width=HALF):
        nonlocal base
        b = at(c, base, f"rw_{name}", [P, width])
        base += 4 * ((width + 7) // 8 * 8)
        return b

    plain = [[buf(f"plain_{n}{h}", HALF + 1) for h in range(2)] for n in "krv"]
    log_w, a_gate, gate = buf("log_w", SEQ), buf("a_gate", SEQ), buf("gate", SEQ)
    k, r, v_b, kk, kf, b_b, bonus, root, rk, l_b, l_prev, e_neg = (
        buf(n) for n in ("k", "r", "v", "kk", "kf", "b", "bonus", "root", "rk", "l", "l_prev", "e_neg"))
    lora_s = buf("lora_s", 3 * P)
    assert base <= 229368 - c.aux_base, base
    copied, mixed, cleared = c.sem("rw_copied"), c.sem("rw_mixed"), c.sem("rw_cleared")
    aux, taken = [[c.sem(f"rw_{n}{h}") for h in range(2)] for n in ("aux", "taken")]
    staged, squared, keyed = c.sem("rw_staged"), c.sem("rw_squared"), c.sem("rw_keyed")
    decayed, negated, exps = c.sem("rw_decayed"), c.sem("rw_negated"), c.sem("rw_exps")
    made, stored, half_done = c.sem("rw_made"), c.sem("rw_stored"), c.sem("rw_half_done")

    def build(following):
        weights.begin()
        with nc.Block() as block:

            @block.sync
            def _(sp):
                def store(i, h):
                    sp.wait_ge(taken[h], i * 5 + 3)
                    apart(c, sp)
                    sp.wait_ge(made, i * 2 + (h + 1))
                    apart(c, sp)
                    cut = slice(h * HALF, (h + 1) * HALF)
                    for dst, src in zip(out, (kk[:], r[:], kf[:], b_b[:], v_b[:], bonus[:], gate[:, cut])):
                        view = dst[bass.ds(i, 1), :, cut].rearrange("a p n -> p (a n)")
                        sp.dma_start(view, src).then_inc(stored, 16)

                def turn(i):
                    for u in range(3):
                        sp.wait_ge(c.w_split, weights.t0 + i * 3 + (u + 1))
                        apart(c, sp)
                        sp.dma_start(c.w_raw[:, u], weights.sources[u](i + 1)).then_inc(c.w_loaded[u], 16)
                    for h in range(2):
                        store(i, h)

                rolled(sp, CT - 1, turn)
                for h in range(2):
                    store(CT - 1, h)
                following(sp)
                sp.wait_ge(stored, 16 * 7 * 2 * CT)

            @block.gpsimd
            def _(pool):
                pool.memset(c.lmid[:], 0.0).then_inc(cleared, 1)
                for n in range(3):
                    pool.memset(plain[n][0][:, 0:1], 0.0).then_inc(cleared, 1)
                weights.split(pool)

            @block.tensor
            def _(pe):
                def lora(i, n, h):
                    wait(pe, taken[h], i * 5 + n)
                    cut = slice(h * HALF, (h + 1) * HALF)
                    o = c.ps[:, 6 + h]
                    if n == 0:
                        last = pe.matmul(o, lora_s[0:64, 0:P], c.lora_in[0:64, cut], start=True, stop=True)
                    elif n == 1:
                        last = pe.matmul(o, lora_s[64:128, 0:P], c.lora_in[64:128, cut], start=True, stop=True)
                    else:
                        pe.matmul(o, lora_s[:, P:2 * P], c.gate_in[:, cut], start=True, stop=False)
                        last = pe.matmul(o, lora_s[0:32, 2 * P:3 * P], c.gate_in2[0:32, cut], start=False, stop=True)
                    last.then_inc(aux[h], 1)

                def sums_of(i, h):
                    wait(pe, taken[h], i * 5 + 3)
                    pe.wait_ge(squared, i * 2 + (h + 1))
                    pe.matmul(c.ps[:, 6 + h], c.ones_64[:], root[:], start=True, stop=True).then_inc(aux[h], 1)
                    wait(pe, taken[h], i * 5 + 4)
                    pe.wait_ge(keyed, i * 2 + (h + 1))
                    pe.matmul(c.ps[:, 6 + h], c.ones_64[:], rk[:], start=True, stop=True).then_inc(aux[h], 1)

                def turn(i):
                    for u in range(3):
                        weights.ready(pe, i, u)
                        wait(pe, copied, i * 6 + (2 * u - 4))
                        if u == 2:
                            weights.multiply(pe, u, [c.ps[:, 4]], c.h_hi, c.h_lo).then_inc(half_done, 1)
                            weights.multiply(pe, u, [c.ps[:, 5]], c.h_hi, c.h_lo, half=1).then_inc(c.tile_done, 1)
                        else:
                            weights.multiply(pe, u, [c.ps[:, 2 * u], c.ps[:, 2 * u + 1]], c.h_hi, c.h_lo).then_inc(c.tile_done, 1)
                        if u == 1:
                            if not first(i):
                                sums_of(i - 1, 1)
                            pe.wait_ge(staged, i + 1)
                            for n in range(3):
                                for h in range(2):
                                    lora(i, n, h)
                    sums_of(i, 0)

                rolled(pe, CT, turn)
                sums_of(CT - 1, 1)

            @block.scalar
            def _(act):
                act.wait_ge(c.lora_loaded, 64)
                act.wait_ge(cleared, 4)
                a = c.a_steps

                def copies(i, n):
                    for h in range(2):
                        if n == 2 and h == 0:
                            act.wait_ge(half_done, i + 1)
                        else:
                            weights.done(act, i, n)
                        wait(act, mixed, (i - 1) * 6 + (3 * h + n + 1) if not first(i) else 0)
                        flat = c.ps[:, 2 * n:2 * n + 2].rearrange("p b m -> p (b m)")
                        if h == 0:
                            act.copy(plain[n][0][:, 1:HALF + 1], flat[:, 0:HALF]).then_inc(copied, 1)
                        else:
                            act.copy(plain[n][1][:], flat[:, HALF - 1:SEQ]).then_inc(copied, 1)

                def half(i, h):
                    act.wait_ge(mixed, i * 6 + (3 * h + 1))
                    if h == 0:
                        wait(act, made, i * 2)
                    else:
                        act.wait_ge(made, i * 2 + 1)
                    act.activation(root[:], kk[:], ACT.Square).then_inc(squared, 1)
                    act.wait_ge(aux[h], i * 5 + 4)
                    act.activation(root[:], c.ps[:, 6 + h], ACT.Sqrt, bias=c.eps[:, 3:4]).then_inc(taken[h], 1)
                    act.wait_ge(decayed, i * 2 + (h + 1))
                    act.activation(l_prev[:], l_prev[:], ACT.Exp)
                    act.activation(e_neg[:], l_b[:], ACT.Exp, scale=-1.0).then_inc(negated, 1)
                    act.wait_ge(negated, i * 2 + (h + 1))
                    act.activation(l_b[:], l_b[:], ACT.Exp).then_inc(exps, 1)

                def turn(i):
                    wait(act, aux[1], i * 5 - 2)
                    apart(c, act)
                    at_i = columns(i, P)
                    a.mark(act.copy(lora_s[:, 0:P], c.lora_w[:, at_i]))
                    a.mark(act.copy(lora_s[:, P:2 * P], c.gate_w[:, at_i]))
                    a.mark(act.copy(lora_s[0:32, 2 * P:3 * P], c.gate_in2[32:64, at_i]))
                    a.wait(act)
                    act.sem_inc(staged, 1)
                    for n in range(2):
                        copies(i, n)
                    if not first(i):
                        half(i - 1, 1)
                    for n, (dst, bias) in enumerate(((log_w, vec(c, "w0", i)), (a_gate, vec(c, "a0", i)))):
                        for h in range(2):
                            act.wait_ge(aux[h], i * 5 + (n + 1))
                            wait(act, made, (i - 1) * 2 + (h + 1) if not first(i) else 0)
                            apart(c, act)
                            act.activation(dst[:, h * HALF:(h + 1) * HALF], c.ps[:, 6 + h], ACT.Sigmoid,
                                           bias=bias).then_inc(taken[h], 1)
                    for h in range(2):
                        act.wait_ge(aux[h], i * 5 + 3)
                        wait(act, stored, i * (16 * 14) + (h - 1) * 16 * 7 if not first(i) else 0)
                        act.copy(gate[:, h * HALF:(h + 1) * HALF], c.ps[:, 6 + h]).then_inc(taken[h], 1)
                    copies(i, 2)
                    half(i, 0)

                rolled(act, CT, turn, a)
                half(CT - 1, 1)

            @block.vector
            def _(dve):
                v = c.v_steps
                mu = c.col["mu_shift"]
                dve.wait_ge(cleared, 4)

                def mix(i, n, h, dst):
                    p = plain[n][h]
                    dve.wait_ge(copied, i * 6 + (2 * n + h + 1))
                    v.mark(dve.tensor_tensor(dst[:], p[:, 0:HALF], p[:, 1:HALF + 1], ALU.subtract))
                    v.wait(dve)
                    col = i + (mu + order[n])
                    scale = c.vec[:, col:col + 1] if isinstance(i, int) else c.vec[:, bass.ds(col, 1)]
                    v.mark(dve.scalar_tensor_tensor(out=dst[:], in0=dst[:], scalar=scale, in1=p[:, 1:HALF + 1],
                                                    op0=ALU.mult, op1=ALU.add))
                    v.wait(dve)

                def half(i, h):
                    cut = slice(h * HALF, (h + 1) * HALF)
                    dve.wait_ge(taken[h], i * 5 + 2)
                    v.mark(dve.tensor_scalar(log_w[:, cut], log_w[:, cut], DECAY, None, ALU.mult))
                    v.wait(dve)
                    for q in range(HALF // P):
                        chunk = slice(q * P, (q + 1) * P)
                        v.mark(dve.tensor_tensor_scan(l_b[:, chunk], c.ones[:], log_w[:, cut][:, chunk], 0.0,
                                                      ALU.mult, ALU.add))
                    v.wait(dve)
                    chunks = l_b[:].rearrange("p (t n) -> p t n", n=P)
                    t0 = h * (TILES // 2)
                    mids = c.lmid[:, bass.ds(i, 1), t0:t0 + 4].rearrange("p a t -> p (a t)")
                    v.mark(dve.tensor_copy(mids, chunks[:, :, mid]))
                    v.wait(dve)
                    v.mark(dve.tensor_tensor(chunks, chunks, mids.unsqueeze(2).broadcast_to([P, 4, P]), ALU.subtract))
                    v.wait(dve)
                    v.mark(dve.tensor_copy(c.lend[:, bass.ds(i, 1), t0:t0 + 4].rearrange("p a t -> p (a t)"),
                                           chunks[:, :, P - 1]))
                    v.mark(dve.tensor_tensor(l_prev[:], l_b[:], log_w[:, cut], ALU.subtract))
                    v.wait(dve)
                    dve.sem_inc(decayed, 1)
                    mix(i, 0, h, k)
                    if h == 0:
                        wait(dve, stored, i * (16 * 14))
                    else:
                        dve.wait_ge(stored, i * (16 * 14) + 16 * 7)
                    dve.tensor_scalar(kk[:], k[:], vec(c, "k_k", i), None, ALU.mult).then_inc(mixed, 1)
                    v.mark(dve.tensor_scalar(kf[:], a_gate[:, cut], -1.0, vec(c, "k_a", i), ALU.add, ALU.mult))
                    v.wait(dve)
                    v.mark(dve.scalar_tensor_tensor(out=kf[:], in0=kf[:], scalar=1.0, in1=k[:], op0=ALU.add, op1=ALU.mult))
                    mix(i, 1, h, r)
                    dve.sem_inc(mixed, 1)
                    v.mark(dve.scalar_tensor_tensor(out=rk[:], in0=r[:], scalar=vec(c, "r_k", i), in1=kf[:],
                                                    op0=ALU.mult, op1=ALU.mult))
                    v.wait(dve)
                    dve.sem_inc(keyed, 1)
                    mix(i, 2, h, v_b)
                    dve.sem_inc(mixed, 1)
                    dve.wait_ge(taken[h], i * 5 + 4)
                    v.mark(dve.tensor_scalar(root[:], root[:], 1e-12, None, ALU.max))
                    v.wait(dve)
                    v.mark(dve.reciprocal(root[:], root[:]))
                    v.wait(dve)
                    v.mark(dve.tensor_tensor(kk[:], kk[:], root[:], ALU.mult))
                    v.wait(dve)
                    v.mark(dve.tensor_tensor(b_b[:], kk[:], a_gate[:, cut], ALU.mult))
                    dve.wait_ge(aux[h], i * 5 + 5)
                    v.mark(dve.tensor_tensor(bonus[:], c.ps[:, 6 + h], v_b[:], ALU.mult))
                    v.wait(dve)
                    dve.sem_inc(taken[h], 1)
                    dve.wait_ge(exps, i * 2 + (h + 1))
                    v.mark(dve.tensor_tensor(r[:], r[:], l_b[:], ALU.mult))
                    v.mark(dve.scalar_tensor_tensor(out=kk[:], in0=kk[:], scalar=-1.0, in1=l_prev[:], op0=ALU.mult, op1=ALU.mult))
                    v.mark(dve.tensor_tensor(kf[:], kf[:], e_neg[:], ALU.mult))
                    v.mark(dve.tensor_tensor(b_b[:], b_b[:], e_neg[:], ALU.mult))
                    v.wait(dve)
                    dve.sem_inc(made, 1)

                def turn(i):
                    for h in range(2):
                        half(i, h)

                rolled(dve, CT, turn, v)
                v.mark(dve.tensor_tensor(c.lend[:], c.lend[:], c.lmid[:, :, 1:TILES + 1], ALU.add))

    return weights, build


def make_levels(c, pool, levels):
    g = c.g_steps
    if 0 in levels:
        g.mark(pool.memset(c.level[:], 0.0))
    for n in levels:
        s = 1 << n
        blocks = P // (2 * s)
        quarter = c.level[:, n, :].rearrange("p (b w) -> p b w", w=2 * s)[:, :, 0:s]
        g.wait(pool)
        g.mark(pool.memset(quarter, 1.0))
        for pattern, base, sign in (([[-2 * s, blocks], [0, s]], -s, 1), ([[2 * s, blocks], [0, s]], 2 * s - 1, -1)):
            g.wait(pool)
            g.mark(pool.affine_select(out=quarter, in_=quarter, compare_op=ALU.is_ge, fill=0.0, base=base,
                                      pattern=pattern, channel_multiplier=sign))
    g.wait(pool)


LEVELS = 7
LEVEL_PE = [f"{what}{n}" for n in range(1, LEVELS) for what in ("x", "t")]
LEVEL_DVE = [f"{what}{n}" for n in range(1, LEVELS) for what in (("xm", "t", "tt") if n < LEVELS - 1 else ("xm", "tt"))]


def side_of(buf, n, which):
    return buf.rearrange("p (b two s) -> p b two s", two=2, s=1 << n)[:, :, which]


def inverse_pe(pe, n, products, masks, i, dve_events, banks, n_t, t, start="tt0"):
    pe.wait_ge(masks, nth(dve_events, start if n == 1 else f"tt{n - 1}", i))
    for h in range(4):
        cut = slice(h * P, (h + 1) * P)
        last = pe.matmul(banks[0][:, cut], n_t[:, h], t[:, h], start=True, stop=True)
    last.then_inc(products, 1)


def inverse_pe_update(pe, n, products, masks, i, dve_events, banks, t_t, x):
    pe.wait_ge(masks, nth(dve_events, f"xm{n}", i))
    for h in range(4):
        cut = slice(h * P, (h + 1) * P)
        if n < LEVELS - 1:
            pe.matmul(banks[1][:, cut], t_t[:, h], x[:, h], start=True, stop=True)
        last = pe.matmul(banks[2][:, cut], x[:, h], t_t[:, h], start=True, stop=True)
    last.then_inc(products, 1)


def heads_of(bank):
    return bank.rearrange("p (h n) -> p h n", n=P)


def inverse_mask_dve(c, dve, n, products, masks, i, pe_events, banks, x):
    dve.wait_ge(products, nth(pe_events, f"x{n}", i))
    dve.tensor_tensor(x[:], heads_of(banks[0]), c.level[:, n].unsqueeze(1).broadcast_to([P, 4, P]),
                      ALU.mult).then_inc(masks, 1)


def inverse_add_dve(dve, n, products, masks, i, pe_events, banks, t, t_t):
    dve.wait_ge(products, nth(pe_events, f"t{n}", i))
    for bank, buf, which in ((banks[1], t, 0), (banks[2], t_t, 1)):
        if which or n < LEVELS - 1:
            dst = side_of(buf[:].rearrange("p h n -> p (h n)"), n, which)
            dve.tensor_tensor(dst, dst, side_of(bank, n, which), ALU.add).then_inc(masks, 1)


def rwkv_scan(c, following):
    nc = c.nc
    base = 0

    def buf(name, shape):
        nonlocal base
        b = at(c, base, f"scan_{name}", shape)
        n = 4
        for m in shape[1:]:
            n *= m
        base += n
        return b

    a_r, k_in, b_in, v_in = (buf("a_r", [P, 2, CT, 2, P]), buf("k", [P, 2, CT, P]), buf("b", [P, 2, CT, P]),
                             buf("v", [P, 2, CT, P]))
    nat = {n: buf(f"{n}_nat", [P, CT, P]) for n in "vkb"}
    groups = range(2)
    ak, rk, ab, rb = ([buf(f"{n}{g}", [P, 4, P]) for g in groups] for n in ("ak", "rk", "ab", "rb"))
    t, t_t, x = ([buf(f"{n}{g}", [P, 4, P]) for g in groups] for n in ("t", "tt", "x"))
    u_b = [buf(f"u{g}", [P, 2, 2 * P]) for g in groups]
    sa = [buf(f"sa{g}", [P, 2, P]) for g in groups]
    state = buf("state", [P, CT, P])
    factor = c.lend
    assert c.aux_base + base <= 229376
    y_t = c.nc.alloc_sbuf_tensor_at("y_t", [P, CT, SEQ], F32, offset=c.w_base)
    c.level = c.nc.alloc_sbuf_tensor_at("scan_level", [P, LEVELS, P], F32, offset=c.w_base + 16384)
    v_two = c.nc.alloc_sbuf_tensor_at("scan_v_two", [P, CT, 2 * P], F32, offset=c.w_base + 16384 + 3584)

    def own(two):
        return two.rearrange("p c (x y) -> p c x y", y=64)[:, :, 0:4:3]

    PE_EVENTS = ["n", "b", "k"] + LEVEL_PE
    DVE_EVENTS = ["t0", "n_t", "rb", "tt0", "ak", "rk"] + LEVEL_DVE
    CHAIN_PE, CHAIN_DVE, CHAIN_ACT = ["u", "sa", "s", "y"], ["s_sum", "s_new"], ["u", "sa", "y"]
    UNIT_EVENTS = ["t", "tt"]
    loaded = [c.sem("scan_loaded0"), c.sem("scan_loaded1")]
    turned, natural, cleared, levels_made = (c.sem(f"scan_{n}") for n in ("turned", "natural", "cleared", "levels_made"))
    products, masks, units = ([c.sem(f"scan_{n}{g}") for g in groups] for n in ("products", "masks", "units"))
    chained, copies, states = ([c.sem(f"scan_{n}{e}") for e in groups] for n in ("chained", "copies", "states"))
    factored, stored = c.sem("scan_factored"), c.sem("scan_stored")
    y_out = scratch(c, "rwkv_y", [CT, P, SEQ]).rearrange("a p n -> p a n")
    ps = c.ps
    src = [c.scratch[f"rwkv_{n}"].rearrange("a p n -> p a n") for n in STORED[:5]]
    level_banks = [(ps[:, 2 * g], ps[:, 2 * g + 1], ps[:, 4 + g]) for g in groups]
    n_bank = [4, 5]
    b_banks = [slice(0, 2), slice(2, 4)]
    k_banks = [slice(4, 6), slice(6, 8)]
    turns = TILES // 2

    with nc.Block() as block:

        @block.sync
        def _(sp):
            def turn(j):
                for q in range(2):
                    i = j * 2 + q
                    if not first(j):
                        for e in groups:
                            sp.wait_ge(chained[e], nth(CHAIN_PE, "y", i - 2))
                        apart(c, sp)
                        store(i - 2)
                    cut = columns(i, P)
                    for part, dst in zip(src, (a_r[:, q, :, 0], a_r[:, q, :, 1], k_in[:, q], b_in[:, q], v_in[:, q])):
                        sp.dma_start(dst, part[:, :, cut]).then_inc(loaded[q], 16)

            def store(i):
                for e in groups:
                    sp.wait_ge(copies[e], nth(CHAIN_ACT, "y", i))
                apart(c, sp)
                sp.dma_start(y_out[:, :, columns(i, P)], y_t[:, :, columns(i, P)]).then_inc(stored, 16)

            rolled(sp, turns, turn)
            following.load_first(sp)
            for i in (TILES - 2, TILES - 1):
                store(i)
            sp.wait_ge(stored, 16 * TILES)

        @block.gpsimd
        def _(pool):
            def unit(buf, g):
                pool.tensor_tensor(buf[g][:], c.ident[:].unsqueeze(1).broadcast_to([P, 4, P]),
                                   c.ones[:].unsqueeze(1).broadcast_to([P, 4, P]), ALU.mult).then_inc(units[g], 1)

            def renew_units(i):
                for g in groups:
                    pool.wait_ge(products[g], nth(PE_EVENTS, f"x{LEVELS - 1}", i))
                    unit(t, g)
                for e in groups:
                    pool.wait_ge(chained[e], nth(CHAIN_PE, "sa", i))
                for g in groups:
                    unit(t_t, g)

            make_levels(c, pool, range(1))
            for g in groups:
                unit(t, g)
            for g in groups:
                unit(t_t, g)
            make_levels(c, pool, range(1, LEVELS))
            pool.sem_inc(levels_made, 1)
            rolled(pool, TILES - 1, renew_units)

        @block.tensor
        def _(pe):

            def scores(q, i):
                rows = [slice(0, 64), slice(64, P)]
                for ct in range(CT):
                    for g in groups:
                        last = pe.matmul(ps[:, n_bank[g], ct * P:(ct + 1) * P], a_r[rows[g], q, ct, 0],
                                         b_in[rows[g], q, ct], start=True, stop=True)
                        if ct == CT - 1:
                            last.then_inc(products[g], 1)
                pe.wait_ge(natural, i * 4 + 4)
                for operand, banks in ((b_in, b_banks), (k_in, k_banks)):
                    if operand is k_in:
                        for g in groups:
                            pe.wait_ge(masks[g], nth(DVE_EVENTS, "t0", i))
                    for ct in range(CT):
                        for g in groups:
                            pair = ps[:, banks[g]].rearrange("p b (h m) -> p (b h) m", m=2 * P)
                            last = pe.matmul(pair[:, ct], operand[rows[g], q, ct],
                                             a_r[rows[g], q, ct].rearrange("p a n -> p (a n)"), start=True, stop=True)
                            if ct == CT - 1:
                                last.then_inc(products[g], 1)

            def from_state(q):
                for e in groups:
                    out = ps[:, 6 + e]
                    for k in range(2):
                        ct = 2 * e + k
                        pe.matmul(out[:, k * P:(k + 1) * P], a_r[:, q, ct, 0], state[:, ct], start=True, stop=False,
                                  skip_group_check=True)
                        for g in groups:
                            last = pe.matmul(out[:, k * P:(k + 1) * P], ak[g][:, ct], v_two[:, ct, g * P:(g + 1) * P],
                                             start=False, stop=g == 1, skip_group_check=True)
                    last.then_inc(chained[e], 1)

            def chunk(i, q, use):
                pe.wait_ge(loaded[q], use * 80 + 80)
                for n, part, bank in (("k", k_in, 6), ("b", b_in, 7), ("v", v_in, 3)):
                    if n == "v":
                        for e in groups:
                            wait(pe, states[e], nth(CHAIN_DVE, "s_sum", i - 1))
                    for ct in range(CT):
                        last = pe.transpose(ps[:, bank, ct * P:(ct + 1) * P], part[:, q, ct], c.ident[:])
                    last.then_inc(turned, 1)
                for e in groups:
                    wait(pe, copies[e], nth(CHAIN_ACT, "y", i - 1))
                scores(q, i)
                if first(i):
                    pe.wait_ge(cleared, 12)
                for n in range(1, LEVELS):
                    for g in groups:
                        inverse_pe(pe, n, products[g], masks[g], i, DVE_EVENTS, level_banks[g], ab[g], t[g])
                    for g in groups:
                        if n == 1:
                            pe.wait_ge(masks[0], nth(DVE_EVENTS, "rk", i))
                        inverse_pe_update(pe, n, products[g], masks[g], i, DVE_EVENTS, level_banks[g], t_t[g], x[g])
                    if n == 1:
                        pe.wait_ge(masks[1], nth(DVE_EVENTS, "rk", i))
                        for e in groups:
                            wait(pe, states[e], nth(CHAIN_DVE, "s_new", i - 1))
                        from_state(q)
                for g in groups:
                    pe.wait_ge(masks[g], nth(DVE_EVENTS, f"tt{LEVELS - 1}", i))
                for e in groups:
                    pe.wait_ge(copies[e], nth(CHAIN_ACT, "u", i))
                    for k in range(2):
                        for g in groups:
                            last = pe.matmul(ps[:, e, k * P:(k + 1) * P], t_t[g][:, 2 * e + k], u_b[e][:, k, g * P:(g + 1) * P],
                                             start=g == 0, stop=g == 1, skip_group_check=True)
                    last.then_inc(chained[e], 1)
                for e in groups:
                    pe.wait_ge(copies[e], nth(CHAIN_ACT, "sa", i))
                    for k in range(2):
                        ct = 2 * e + k
                        o = ps[:, 2 + e, k * P:(k + 1) * P]
                        pe.matmul(o, nat["b"][:, ct], sa[e][:, k], start=True, stop=False, skip_group_check=True)
                        last = pe.matmul(o, nat["k"][:, ct], nat["v"][:, ct], start=False, stop=True, skip_group_check=True)
                    last.then_inc(chained[e], 1)
                    for k in range(2):
                        ct = 2 * e + k
                        cut = slice(k * P, (k + 1) * P)
                        pe.matmul(ps[:, 4 + e, cut], state[:, ct], a_r[:, q, ct, 1], start=True, stop=False,
                                  skip_group_check=True)
                        for g in groups:
                            rows = slice(64 * g, 64 * g + 64)
                            pe.matmul(ps[rows, 4 + e, cut], sa[e][:, k, rows], rb[g][:, ct], start=False,
                                      stop=False, skip_group_check=True)
                            last = pe.matmul(ps[rows, 4 + e, cut], nat["v"][:, ct, rows], rk[g][:, ct], start=False,
                                             stop=True, skip_group_check=True)
                    last.then_inc(chained[e], 1)

            def turn(j):
                for q in range(2):
                    chunk(j * 2 + q, q, j)

            rolled(pe, turns, turn)

        @block.scalar
        def _(act):
            act.activation(factor[:], c.lend[:], ACT.Exp).then_inc(factored, 1)
            act.wait_ge(cleared, 3)

            def chunk(i):
                for b, n in enumerate("kbv"):
                    act.wait_ge(turned, i * 3 + (b + 1))
                    act.copy(nat[n][:], heads_of(ps[:, (6, 7, 3)[b]])).then_inc(natural, 1)
                    if n == "v":
                        act.copy(own(v_two[:]), ps[:, 3].rearrange("p (c x y) -> p c x y", x=2, y=64)).then_inc(natural, 1)
                for bank, name, into in ((6, "u", u_b), (0, "sa", sa), (4, "y", None)):
                    for e in groups:
                        act.wait_ge(chained[e], nth(CHAIN_PE, name, i))
                        if name == "y":
                            apart(c, act)
                            dst = y_t[:, 2 * e:2 * e + 2, columns(i, P)]
                        else:
                            dst = into[e][:]
                        src_ = ps[:, bank + e, 0:2 * P]
                        if name == "u":
                            act.copy(own(dst), src_.rearrange("p (k x y) -> p k x y", x=2, y=64)).then_inc(copies[e], 1)
                        else:
                            act.copy(dst, src_.rearrange("p (k n) -> p k n", n=P)).then_inc(copies[e], 1)

            def turn(j):
                for q in range(2):
                    chunk(j * 2 + q)

            rolled(act, turns, turn)

        @block.vector
        def _(dve):
            for m in (v_two, *u_b, *ab, *rb, *ak, *rk, state):
                dve.memset(m[:], 0.0).then_inc(cleared, 1)
            dve.wait_ge(cleared, 12)
            dve.wait_ge(factored, 1)

            def over(m):
                return m.unsqueeze(1).broadcast_to([P, 4, P]).bitcast(mybir.dt.int32)

            def pair(banks):
                return ps[:, banks].rearrange("p b (h a n) -> p (b h) a n", a=2, n=P)

            def chunk(i):
                def keep(dst, mask, src, g):
                    apart(c, dve)
                    dve.copy_predicated(dst[g][:], over(mask), src).then_inc(masks[g], 1)

                for e in groups:
                    wait(dve, chained[e], nth(CHAIN_PE, "y", i - 1))
                for g in groups:
                    dve.wait_ge(units[g], nth(UNIT_EVENTS, "t", i))
                    dve.wait_ge(products[g], nth(PE_EVENTS, "n", i))
                    keep(t, c.level[:, 0], heads_of(ps[:, n_bank[g]]), g)
                for g in groups:
                    dve.wait_ge(products[g], nth(PE_EVENTS, "b", i))
                    keep(ab, c.upper[:], pair(b_banks[g])[:, :, 0], g)
                    keep(rb, c.upper_eq[:], pair(b_banks[g])[:, :, 1], g)
                    dve.wait_ge(units[g], nth(UNIT_EVENTS, "tt", i))
                    keep(t_t, c.level_t[:], pair(b_banks[g])[:, :, 0], g)
                if first(i):
                    dve.wait_ge(levels_made, 1)
                for n in range(1, LEVELS):
                    for g in groups:
                        if n == 1:
                            dve.wait_ge(products[g], nth(PE_EVENTS, "k", i))
                            keep(ak, c.upper[:], pair(k_banks[g])[:, :, 0], g)
                            keep(rk, c.upper_eq[:], pair(k_banks[g])[:, :, 1], g)
                        inverse_mask_dve(c, dve, n, products[g], masks[g], i, PE_EVENTS, level_banks[g], x[g])
                    for g in groups:
                        inverse_add_dve(dve, n, products[g], masks[g], i, PE_EVENTS, level_banks[g], t[g], t_t[g])
                for e in groups:
                    two = slice(2 * e, 2 * e + 2)
                    dve.wait_ge(chained[e], nth(CHAIN_PE, "y", i))
                    dve.tensor_tensor(state[:, two], state[:, two], ps[:, 2 + e, 0:2 * P].rearrange("p (k n) -> p k n", n=P),
                                      ALU.add).then_inc(states[e], 1)
                    dve.wait_ge(states[e], nth(CHAIN_DVE, "s_sum", i))
                    for k in range(2):
                        last = dve.scalar_tensor_tensor(
                            out=state[:, 2 * e + k], in0=state[:, 2 * e + k],
                            scalar=factor[:, 2 * e + k, bass.ds(i, 1)], in1=c.ones_64[:], op0=ALU.mult, op1=ALU.mult)
                    last.then_inc(states[e], 1)

            def turn(j):
                for q in range(2):
                    chunk(j * 2 + q)

            rolled(dve, turns, turn)


def tail(c, off, name, shape, dt=F32):
    return at(c, 2 * BRANCH + off, name, shape, dt)


BRANCH = KT * SEQ * 4


def place(buf, i, h):
    return buf[:, bass.ds(i, 1), h * HALF:(h + 1) * HALF].rearrange("p a n -> p (a n)")


class RwkvOutput:

    def __init__(self, c):
        self.c = c
        free = 4 * CT * SEQ
        self.dev, self.root, self.bonus, self.gate, self.y, self.sq = (
            at(c, free + 2048 * n, f"ro_{name}", [P, HALF]) for n, name in enumerate(("dev", "root", "bonus", "gate", "y", "sq")))
        self.centred, self.squared, self.rooted = c.sem("ro_centred"), c.sem("ro_squared"), c.sem("ro_rooted")
        self.summed, self.made, self.rounded, self.split = (c.sem(f"ro_{n}") for n in ("summed", "made", "rounded", "split"))
        self.loaded, self.loaded_late = c.sem("ro_loaded"), c.sem("ro_loaded_late")
        self.src = [c.scratch[f"rwkv_{n}"] for n in ("y", "bonus_t", "gate_t")]

    def load(self, sp, i, h):
        wait(sp, self.centred, i * 2 + h)
        apart(self.c, sp)
        cut = slice(h * HALF, (h + 1) * HALF)
        sp.dma_start(self.y[:], self.src[0][bass.ds(i, 1), :, cut].rearrange("a p n -> p (a n)")).then_inc(self.loaded, 16)

    def load_late(self, sp, i, h):
        wait(sp, self.made, i * 2 + h)
        apart(self.c, sp)
        cut = slice(h * HALF, (h + 1) * HALF)
        for part, dst in zip(self.src[1:], (self.bonus, self.gate)):
            sp.dma_start(dst[:], part[bass.ds(i, 1), :, cut].rearrange("a p n -> p (a n)")).then_inc(self.loaded_late, 16)

    def pe_before(self, pe, i, h):
        pe.wait_ge(self.loaded, i * 32 + (16 * h + 16))
        wait(pe, self.centred, i * 2 + h)
        pe.matmul(self.c.ps[:, 4], self.c.ones_64[:], self.y[:], start=True, stop=True).then_inc(self.summed, 1)

    def pe_after(self, pe, i, h):
        pe.wait_ge(self.squared, i * 2 + (h + 1))
        wait(pe, self.rooted, i * 2 + h)
        pe.matmul(self.c.ps[:, 5], self.c.ones_64[:], self.sq[:], start=True, stop=True).then_inc(self.summed, 1)

    def act_before(self, act, i, h):
        act.wait_ge(self.centred, i * 2 + (h + 1))
        wait(act, self.summed, i * 4 + 2 * h)
        act.activation(self.sq[:], self.dev[:], ACT.Square).then_inc(self.squared, 1)

    def act_after(self, act, i, h):
        act.wait_ge(self.summed, i * 4 + (2 * h + 2))
        wait(act, self.made, i * 2 + h)
        act.activation(self.root[:], self.c.ps[:, 5], ACT.Sqrt, bias=self.c.eps[:, 1:2], scale=1.0 / HEAD).then_inc(self.rooted, 1)

    def act_late(self, act, i, h):
        act.wait_ge(self.made, i * 2 + (h + 1))
        apart(self.c, act)
        act.copy(place(self.c.br_hi, i, h), self.dev[:]).then_inc(self.rounded, 1)

    def dve(self, dve, i, h):
        c, v, dev = self.c, self.c.v_steps, self.dev[:]
        dve.wait_ge(self.summed, i * 4 + (2 * h + 1))
        wait(dve, self.split, i * 2 + h)
        dve.scalar_tensor_tensor(out=dev, in0=c.ps[:, 4], scalar=-1.0 / HEAD, in1=self.y[:],
                                 op0=ALU.mult, op1=ALU.add).then_inc(self.centred, 1)
        dve.wait_ge(self.rooted, i * 2 + (h + 1))
        v.mark(dve.reciprocal(self.root[:], self.root[:]))
        v.wait(dve)
        v.mark(dve.tensor_tensor(dev, dev, self.root[:], ALU.mult))
        v.wait(dve)
        v.mark(dve.tensor_scalar(dev, dev, vec(c, "ln_x_w", i), vec(c, "ln_x_b", i), ALU.mult, ALU.add))
        v.wait(dve)
        dve.wait_ge(self.loaded_late, i * 64 + (32 * h + 32))
        apart(c, dve)
        v.mark(dve.tensor_tensor(dev, dev, self.bonus[:], ALU.add))
        v.wait(dve)
        dve.tensor_tensor(dev, dev, self.gate[:], ALU.mult).then_inc(self.made, 1)
        dve.wait_ge(self.rounded, i * 2 + (h + 1))
        dve.tensor_tensor(place(c.br_lo, i, h), dev, place(c.br_hi, i, h).bitcast(F32), ALU.subtract).then_inc(self.split, 1)


class DeltaOutput:

    def __init__(self, c):
        self.c = c
        self.o, self.z, self.sq = (tail(c, 2048 * n, f"do_{name}", [P, HALF]) for n, name in enumerate(("o", "z", "sq")))
        self.root = self.sq
        self.squared, self.rooted, self.summed = c.sem("do_squared"), c.sem("do_rooted"), c.sem("do_summed")
        self.loaded, self.made, self.rounded, self.split = (c.sem(f"do_{n}") for n in ("loaded", "made", "rounded", "split"))
        self.src = [c.scratch[f"second_{n}"] for n in ("oa", "z")]

    def load(self, sp, i, h):
        wait(sp, self.split, i * 2 + h)
        apart(self.c, sp)
        cut = slice(h * HALF, (h + 1) * HALF)
        for part, dst in zip(self.src, (self.o, self.z)):
            sp.dma_start(dst[:], part[bass.ds(i, 1), :, cut].rearrange("a p n -> p (a n)")).then_inc(self.loaded, 16)

    def load_late(self, sp, i, h):
        pass

    def pe_before(self, pe, i, h):
        pass

    def pe_after(self, pe, i, h):
        pe.wait_ge(self.squared, i * 2 + (h + 1))
        wait(pe, self.rooted, i * 2 + h)
        pe.matmul(self.c.ps[:, 4], self.c.ones[:], self.sq[:], start=True, stop=True).then_inc(self.summed, 1)

    def act_before(self, act, i, h):
        act.wait_ge(self.loaded, i * 64 + (32 * h + 32))
        wait(act, self.made, i * 2 + h)
        act.activation(self.sq[:], self.o[:], ACT.Square).then_inc(self.squared, 1)

    def act_after(self, act, i, h):
        act.wait_ge(self.summed, i * 2 + (h + 1))
        act.activation(self.root[:], self.c.ps[:, 4], ACT.Sqrt, bias=self.c.eps[:, 0:1], scale=1.0 / P).then_inc(self.rooted, 1)

    def act_late(self, act, i, h):
        act.wait_ge(self.made, i * 2 + (h + 1))
        apart(self.c, act)
        act.copy(place(self.c.br_hi, i, h), self.o[:]).then_inc(self.rounded, 1)

    def dve(self, dve, i, h):
        c, v, o = self.c, self.c.v_steps, self.o[:]
        dve.wait_ge(self.rooted, i * 2 + (h + 1))
        v.mark(dve.reciprocal(self.root[:], self.root[:]))
        v.wait(dve)
        v.mark(dve.scalar_tensor_tensor(out=o, in0=o, scalar=vec(c, "dn_out_gain_2"), in1=self.root[:],
                                        op0=ALU.mult, op1=ALU.mult))
        v.wait(dve)
        dve.tensor_tensor(o, o, self.z[:], ALU.mult).then_inc(self.made, 1)
        dve.wait_ge(self.rounded, i * 2 + (h + 1))
        dve.tensor_tensor(place(c.br_lo, i, h), o, place(c.br_hi, i, h).bitcast(F32), ALU.subtract).then_inc(self.split, 1)


class ShortConv:

    def __init__(self, c, side, following):
        self.c, self.side, self.following = c, side, following
        tile = tile_of(c.dram["w_in"][0], RWKV_COLS)
        self.weights = Weights(c, [lambda i, o=o: tile(i, 1, o * CT) for o in (1, 2, 0)], CT, shift=2)
        self.u = [tail(c, 2080 * h, f"conv_u{h}", [P, HALF + 2]) for h in range(2)]
        self.y = [tail(c, 4160, "conv_y0", [P, HALF]),
                  at(c, BRANCH + 4 * ((2 * CT - 1) * SEQ + HALF), "conv_y1", [P, HALF])]
        self.copied, self.product, self.ended, self.made, self.rounded, self.split = (
            c.sem(f"conv_{n}") for n in ("copied", "product", "ended", "made", "rounded", "split"))

    def load(self, sp):
        self.weights.load_rest(sp)
        sp.wait_ge(self.c.w_split, self.weights.t0 + self.weights.total)
        self.following.load_first(sp)

    def pe(self, pe, gated, gates_before):
        c, w = self.c, self.weights

        def turn(i):
            for n in range(3):
                w.ready(pe, i, n)
                if first(i) and n == 1:
                    pe.wait_ge(gated, gates_before)
                if first(i) and n == 2:
                    pe.wait_ge(self.side.rooted, 2 * CT)
                wait(pe, (self.copied, self.product, self.made)[n], i * 2)
                w.multiply(pe, n, [c.ps[:, 2 * n], c.ps[:, 2 * n + 1]], c.h_hi, c.h_lo).then_inc(c.tile_done, 1)

        rolled(pe, CT, turn)

    def act(self, act):
        c = self.c
        act.wait_ge(self.side.split, 2 * CT)

        def turn(i):
            self.weights.done(act, i, 0)
            for h in range(2):
                wait(act, self.ended, (i - 1) * 2 + (h + 1) if not first(i) else 0)
                act.copy(self.u[h][:, 2:HALF + 2], c.ps[:, h]).then_inc(self.copied, 1)
            for h in range(2):
                act.wait_ge(self.made, i * 2 + (h + 1))
                apart(c, act)
                act.copy(place(c.br_hi, i + CT, h), self.y[h][:]).then_inc(self.rounded, 1)

        rolled(act, CT, turn)

    def dve(self, dve):
        c, v = self.c, self.c.v_steps

        def turn(i):
            v.mark(dve.memset(self.u[0][:, 0:2], 0.0))
            self.weights.done(dve, i, 1)
            for h in range(2):
                u, y = self.u[h], self.y[h]
                dve.wait_ge(self.copied, i * 2 + (h + 1))
                v.wait(dve)
                dve.tensor_tensor(u[:, 2:HALF + 2], u[:, 2:HALF + 2], c.ps[:, 2 + h], ALU.mult).then_inc(self.product, 1)
                dve.wait_ge(self.product, i * 2 + (h + 1))
                wait(dve, self.split, (i - 1) * 2 + (h + 1) if not first(i) else 0)
                v.mark(dve.tensor_scalar(y[:], u[:, 2:HALF + 2], vec(c, "conv_w", i + 2 * CT), None, ALU.mult))
                for tap in (1, 0):
                    v.wait(dve)
                    v.mark(dve.scalar_tensor_tensor(out=y[:], in0=u[:, tap:HALF + tap], scalar=vec(c, "conv_w", i + tap * CT),
                                                    in1=y[:], op0=ALU.mult, op1=ALU.add))
                if h == 0:
                    v.mark(dve.tensor_copy(self.u[1][:, 0:2], u[:, HALF:HALF + 2]))
                v.wait(dve)
                dve.sem_inc(self.ended, 1)
            self.weights.done(dve, i, 2)
            for h in range(2):
                dve.tensor_tensor(self.y[h][:], self.y[h][:], c.ps[:, 4 + h], ALU.mult).then_inc(self.made, 1)
            for h in range(2):
                dve.wait_ge(self.rounded, i * 2 + (h + 1))
                dve.tensor_tensor(place(c.br_lo, i + CT, h), self.y[h][:], place(c.br_hi, i + CT, h).bitcast(F32),
                                  ALU.subtract).then_inc(self.split, 1)

        rolled(dve, CT, turn, v)


def gates(c, name, w_in, first_column, bias):
    nc = c.nc
    tile = tile_of(w_in, first_column)
    per = 4
    weights = Weights(c, [lambda i, k=k, g=g: tile(i, 2, k + g * KT) for k in range(2) for g in range(2)], KT // 2)
    out = scratch(c, f"{name}_gates", [2, KT, P, SEQ])

    def build(side, sig, after=None):
        weights.begin()
        weights.share_first()
        if after:
            after.weights.begin()
        gated = c.sem(f"{name}_gated")
        stored = [c.sem(f"{name}_stored{n}") for n in range(len(sig))]
        share = per // len(sig)
        with nc.Block() as block:

            @block.sync
            def _(sp):
                def store(i, u):
                    sp.wait_ge(gated, i * per + (u + 1))
                    apart(c, sp)
                    sp.dma_start(out[u % 2, bass.ds(i * 2 + u // 2, 1)].rearrange("a p n -> p (a n)"),
                                 sig[u % len(sig)]).then_inc(stored[u % len(sig)], 16)

                def turn(i, last=False):
                    for u in range(per):
                        if not (last and u >= 2):
                            sp.wait_ge(c.w_split, weights.t0 + i * per + (u + 1))
                            apart(c, sp)
                            weights.fetch(sp, (u + 2) % per, i + (u + 2) // per)
                        if u:
                            store(i, u - 1)
                        elif not first(i):
                            store(i - 1, per - 1)
                        if last and after and u:
                            if u > 1:
                                sp.wait_ge(c.w_split, weights.t0 + i * per + (u + 1))
                                apart(c, sp)
                            after.weights.fetch(sp, u - 1, 0)
                        if u % 2 == 0 and (u or not first(i)):
                            side.load_late(sp, i, u // 2)
                        if u == 1:
                            side.load(sp, i, 1)
                        if u == 3 and not last:
                            side.load(sp, i + 1, 0)

                side.load(sp, 0, 0)
                side.load_late(sp, 0, 0)
                rolled(sp, weights.turns - 1, turn)
                turn(weights.turns - 1, last=True)
                store(weights.turns - 1, per - 1)
                if after:
                    after.load(sp)
                    for n in range(len(sig)):
                        sp.wait_ge(stored[n], 16 * weights.turns * share)
                else:
                    c.gates_stored = [(sem, 16 * weights.turns * share) for sem in stored]

            @block.gpsimd
            def _(pool):
                weights.split(pool)
                if after:
                    after.weights.split(pool)
                    after.following.split_first(pool)

            @block.tensor
            def _(pe):
                def turn(i):
                    for u in range(per):
                        if u % 2 == 0:
                            side.pe_before(pe, i, u // 2)
                        weights.ready(pe, i, u)
                        wait(pe, gated, i * per + (u - 1))
                        b = 2 * (u % 2)
                        weights.multiply(pe, u, [c.ps[:, b], c.ps[:, b + 1]], c.h_hi, c.h_lo).then_inc(c.tile_done, 1)
                        if u % 2 == 0:
                            side.pe_after(pe, i, u // 2)

                rolled(pe, weights.turns, turn)
                if after:
                    pe.wait_ge(gated, weights.total - 1)
                    after.pe(pe, gated, weights.total)

            @block.scalar
            def _(act):
                def turn(i):
                    for u in range(per):
                        h = u // 2
                        if u % 2 == 0:
                            side.act_before(act, i, h)
                        else:
                            side.act_late(act, i, h)
                        weights.done(act, i, u)
                        wait(act, stored[u % len(sig)], i * (16 * share) + 16 * (u // len(sig)))
                        apart(c, act)
                        act.activation(sig[u % len(sig)], c.ps[:, 2 * (u % 2):2 * (u % 2) + 2].rearrange("p b n -> p (b n)"),
                                       ACT.Sigmoid, bias=vec(c, bias, i * 2 + (u // 2 + (u % 2) * KT))).then_inc(gated, 1)
                        if u % 2 == 0:
                            side.act_after(act, i, h)

                weights.round_first(act)
                rolled(act, weights.turns, turn)
                if after:
                    after.act(act)

            @block.vector
            def _(dve):
                def turn(i):
                    for h in range(2):
                        side.dve(dve, i, h)

                weights.subtract_first(dve)
                rolled(dve, weights.turns, turn, c.v_steps)
                if after:
                    after.dve(dve)

    return weights, build


def merge(c, name, w_a, w_b):
    nc = c.nc
    top, low = w_a.rearrange("(k p) n -> p k n", p=P), w_b.rearrange("(k p) n -> p k n", p=P)
    weights = Weights(c, [lambda i, u=u: tuple(w[:, :, bass.ds(i * (2 * P) + u * P, P)] for w in (top, low)) for u in range(2)],
                      KT // 2)
    gate_b = tail(c, 0, f"{name}_gate_b", [P, 2, HALF])
    gate_a = c.w_raw[:, 2].rearrange("p (h k) n -> p h (k n)", h=2)
    src = c.scratch[f"{name}_gates"]

    def build(following):
        weights.begin()
        shared = not weights.ahead
        if shared:
            weights.share_first()
        loaded, scaled, made = ([c.sem(f"{name}_{n}{h}") for h in range(2)] for n in ("loaded", "scaled", "made"))
        rounded, split = ([c.sem(f"{name}_{n}{h}") for h in range(2)] for n in ("rounded", "split"))
        with nc.Block() as block:

            @block.sync
            def _(sp):
                def turn(i, last=False):
                    for u in range(2):
                        for h in range(2):
                            wait(sp, split[h], i * 2 + u)
                            apart(c, sp)
                            for g, dst in enumerate((gate_a, gate_b)):
                                view = src[g, bass.ds(i * 2 + u, 1), :, h * HALF:(h + 1) * HALF]
                                sp.dma_start(dst[:, h], view.rearrange("a p n -> p (a n)")).then_inc(loaded[h], 16)
                        if not last:
                            sp.wait_ge(c.w_split, weights.t0 + i * 2 + (u + 1))
                            apart(c, sp)
                            weights.fetch(sp, u, i + 1)

                rolled(sp, weights.turns - 1, turn)
                turn(weights.turns - 1, last=True)
                sp.wait_ge(c.w_split, weights.t0 + weights.total)
                following.load_first(sp)

            @block.gpsimd
            def _(pool):
                weights.split(pool)
                following.split_first(pool)

            @block.tensor
            def _(pe):
                def turn(i):
                    for u in range(2):
                        weights.ready(pe, i, u)
                        for h in range(2):
                            wait(pe, scaled[h], i * 4 + (2 * u - 2))
                        b = 4 * u
                        weights.multiply(pe, u, [c.ps[:, b], c.ps[:, b + 1]], c.br_hi, c.br_lo, kts=range(KT // 2))
                        weights.multiply(pe, u, [c.ps[:, b + 2], c.ps[:, b + 3]], c.br_hi, c.br_lo,
                                         kts=range(KT // 2, KT)).then_inc(c.tile_done, 1)

                rolled(pe, weights.turns, turn)

            @block.scalar
            def _(act):
                def turn(i):
                    for u in range(2):
                        for h in range(2):
                            act.wait_ge(made[h], i * 2 + (u + 1))
                            apart(c, act)
                            act.copy(place(c.h_hi, i * 2 + u, h), gate_a[:, h]).then_inc(rounded[h], 1)

                if shared:
                    weights.round_first(act)
                rolled(act, weights.turns, turn)

            @block.vector
            def _(dve):
                def turn(i):
                    for u in range(2):
                        weights.done(dve, i, u)
                        for h in range(2):
                            dve.wait_ge(loaded[h], i * 64 + (32 * u + 32))
                            for g, buf in enumerate((gate_a, gate_b)):
                                dve.tensor_tensor(buf[:, h], buf[:, h], c.ps[:, 4 * u + 2 * g + h], ALU.mult).then_inc(scaled[h], 1)
                        for h in range(2):
                            dve.wait_ge(scaled[h], i * 4 + (2 * u + 2))
                            dve.tensor_tensor(gate_a[:, h], gate_a[:, h], gate_b[:, h], ALU.add).then_inc(made[h], 1)
                        for h in range(2):
                            dve.wait_ge(rounded[h], i * 2 + (u + 1))
                            hi = place(c.h_hi, i * 2 + u, h)
                            dve.tensor_tensor(place(c.h_lo, i * 2 + u, h), gate_a[:, h], hi.bitcast(F32),
                                              ALU.subtract).then_inc(split[h], 1)

                if shared:
                    weights.subtract_first(dve)
                rolled(dve, weights.turns, turn)

    return weights, build


def residual_weights(c, w):
    tile = tile_of(w)
    return Weights(c, [lambda i, u=u: tile(i, 2, u) for u in range(2)], KT // 2)


N_XHEADS = 4
XD = D // N_XHEADS


def memory_keys(c):
    nc, d = c.nc, c.dram
    tile = tile_of(d["w_kv"][0])
    weights = Weights(c, [lambda i, u=u: tile(i, 2, u) for u in range(2)], KT)
    mem_hi = at(c, 0, "mem_hi", [P, KT, N_MEM], F32R)
    mem_lo = at(c, 8192, "mem_lo", [P, KT, N_MEM], F32R)
    both = at(c, 24576, "keys_values", [P, 2 * KT, N_MEM])
    v_all = at(c, 50176, "v_all", [P, 2, D])
    scratch(c, "mem_k", [KT, P, N_MEM])
    scratch(c, "mem_v", [2, P, D])
    copied, stored = [c.sem("mem_copied0"), c.sem("mem_copied1")], c.sem("mem_stored")
    c.values_stored, turned, taken = c.sem("mem_values_stored"), c.sem("mem_turned"), c.sem("mem_taken")
    memory_norm(c, mem_hi, mem_lo, weights)
    sq = at(c, 40960, "mix_sq", [P, SEQ])

    def build(following, norm):
        weights.begin()
        with nc.Block() as block:

            @block.sync
            def _(sp):
                weights.load_rest(sp)
                for s in range(2):
                    sp.wait_ge(copied[s], KT // 2)
                sp.dma_start(c.scratch["mem_k"].rearrange("k p n -> p k n"), both[:, 0:KT]).then_inc(stored, 16)
                sp.wait_ge(c.w_split, c.tiles)
                following.load_first(sp)
                sp.wait_ge(taken, KT)
                sp.dma_start(c.scratch["mem_v"].rearrange("m p n -> p m n"), v_all[:]).then_inc(c.values_stored, 16)
                sp.wait_ge(stored, 16)

            @block.scalar
            def _(act):
                weights.round_on(act)

            @block.gpsimd
            def _(pool):
                g = c.g_steps
                for k in range(KT):
                    dst = sq[:] if k else norm.acc[:]
                    g.mark(pool.tensor_tensor(dst, c.x[:, k], c.x[:, k], ALU.mult))
                    g.wait(pool)
                    if k:
                        g.mark(pool.tensor_tensor(norm.acc[:], norm.acc[:], dst, ALU.add))
                        g.wait(pool)

            @block.tensor
            def _(pe):
                def turn(i):
                    for u in range(2):
                        weights.ready(pe, i, u)
                        wait(pe, copied[u], i)
                        weights.multiply(pe, u, [c.ps[:, u, 0:N_MEM]], mem_hi, mem_lo, width=N_MEM).then_inc(c.tile_done, 1)

                rolled(pe, KT, turn)
                for n in range(KT):
                    pe.wait_ge(copied[n % 2], (KT + n) // 2 + 1)
                    wait(pe, taken, n - 3)
                    for m in range(2):
                        last = pe.transpose(c.ps[:, 2 + n % 4, m * P:(m + 1) * P], both[:, KT + n, m * P:(m + 1) * P], c.ident[:])
                    last.then_inc(turned, 1)

            @block.vector
            def _(dve):
                def copy_tile(i, u):
                    weights.done(dve, i, u)
                    apart(c, dve)
                    dve.tensor_copy(both[:, bass.ds(i * 2 + u, 1), :].rearrange("p a n -> p (a n)"),
                                    c.ps[:, u, 0:N_MEM]).then_inc(copied[u], 1)

                weights.subtract(dve, lambda i, u: None if first(i) else copy_tile(i - 1, u))
                for u in range(2):
                    copy_tile(KT - 1, u)
                for n in range(KT):
                    dve.wait_ge(turned, n + 1)
                    dve.tensor_copy(v_all[:, :, n * P:(n + 1) * P],
                                    c.ps[:, 2 + n % 4, 0:2 * P].rearrange("p (m n) -> p m n", n=P)).then_inc(taken, 1)

    return build


def load_head(c, sp, hd):
    s = hd % 2
    sp.dma_start(c.xa_k[:, s], c.scratch["mem_k"][2 * hd:2 * hd + 2].rearrange("k p n -> p k n")).then_inc(c.xa_loaded[s], 16)
    sp.dma_start(c.xa_v[:, s], c.scratch["mem_v"][:, :, hd * XD:(hd + 1) * XD].rearrange("m p n -> p m n")).then_inc(
        c.xa_loaded[s], 16)


def queries(c):
    nc = c.nc
    weights = residual_weights(c, c.dram["w_q"][0])
    c.q = at(c, 0, "queries", [P, KT, SEQ])
    c.xa_k, c.xa_v = at(c, 32768, "xa_k", [P, 2, 2, N_MEM]), at(c, 36864, "xa_v", [P, 2, 2, XD])
    c.xa_loaded = [c.sem("xa_loaded0"), c.sem("xa_loaded1")]
    copied = [c.sem("q_copied0"), c.sem("q_copied1")]

    def build(norm):
        weights.begin()
        with nc.Block() as block:

            @block.sync
            def _(sp):
                weights.load_rest(sp)
                for hd in range(2):
                    load_head(c, sp, hd)

            @block.gpsimd
            def _(pool):
                weights.split(pool)

            @block.tensor
            def _(pe):
                norm.pe_sums(pe)

                def turn(i):
                    if first(i):
                        norm.first_tiles(pe, weights)
                        return
                    for u in range(2):
                        weights.ready(pe, i, u)
                        wait(pe, copied[u], i)
                        weights.multiply(pe, u, [c.ps[:, 2 * u], c.ps[:, 2 * u + 1]], c.h_hi, c.h_lo).then_inc(c.tile_done, 1)

                rolled(pe, KT // 2, turn)

            @block.scalar
            def _(act):
                norm.act(act)

                def turn(i):
                    for u in range(2):
                        weights.done(act, i, u)
                        apart(c, act)
                        act.activation(c.q[:, bass.ds(i * 2 + u, 1)].rearrange("p a n -> p (a n)"),
                                       c.ps[:, 2 * u:2 * u + 2].rearrange("p b n -> p (b n)"), ACT.Copy,
                                       scale=XD ** -0.5).then_inc(copied[u], 1)

                rolled(act, KT // 2, turn)

            @block.vector
            def _(dve):
                norm.dve(dve)

    return weights, build


def attention(c, following):
    nc = c.nc
    k_in, v_in, loaded = c.xa_k, c.xa_v, c.xa_loaded
    prob = at(c, 40960, "xa_prob", [P, 4, N_MEM])
    p_t = at(c, 45056, "xa_prob_t", [P, 2, 2, HALF])
    top, neg, total = (at(c, 53248 + 32 * n, f"xa_{name}", [P, 4]) for n, name in enumerate(("top", "neg", "total")))
    scored, turned, summed = c.sem("xa_scored"), c.sem("xa_turned"), c.sem("xa_summed")
    exps, copied, rounded = c.sem("xa_exps"), c.sem("xa_copied"), c.sem("xa_rounded")
    tops, normed, split = c.sem("xa_tops"), c.sem("xa_normed"), c.sem("xa_split")
    ps = c.ps
    n_steps = N_XHEADS * TILES
    quads = n_steps // 4

    with nc.Block() as block:

        @block.sync
        def _(sp):
            following.load_first(sp)
            for hd in range(2, N_XHEADS):
                sp.wait_ge(summed, 2 * (hd - 1))
                load_head(c, sp, hd)

        @block.gpsimd
        def _(pool):
            following.split_first(pool)

        @block.tensor
        def _(pe):
            def score(n):
                hd, t = divmod(n, TILES)
                pe.wait_ge(loaded[hd % 2], (hd // 2 + 1) * 32)
                wait(pe, exps, n - 3)
                for k in range(2):
                    last = pe.matmul(ps[:, n % 4, 0:N_MEM], c.q[:, 2 * hd + k, t * P:(t + 1) * P], k_in[:, hd % 2, k],
                                     start=k == 0, stop=k == 1)
                last.then_inc(scored, 1)

            def sum_values(g):
                hd = g // 2
                pe.wait_ge(copied, 4 * g + 4)
                wait(pe, split, 2 * g)
                for e in range(2):
                    for m in range(2):
                        last = pe.matmul(ps[:, 6 + e], v_in[:, hd % 2, m, e * P:(e + 1) * P], p_t[:, g % 2, m],
                                         start=m == 0, stop=m == 1)
                last.then_inc(summed, 1)

            for n in range(3):
                score(n)
            for n in range(n_steps):
                if n + 3 < n_steps:
                    score(n + 3)
                pe.wait_ge(normed, n + 1)
                wait(pe, copied, n - 1)
                for m in range(2):
                    last = pe.transpose(ps[:, 4 + n % 2, m * P:(m + 1) * P], prob[:, n % 4, m * P:(m + 1) * P], c.ident[:])
                last.then_inc(turned, 1)
                if n % 4 == 1 and n > 4:
                    sum_values(n // 4 - 1)
            sum_values(quads - 1)

        @block.scalar
        def _(act):
            def exp(n):
                act.wait_ge(tops, 2 * n + 2)
                wait(act, turned, n - 3)
                one = slice(n % 4, n % 4 + 1)
                act.activation(prob[:, n % 4], ps[:, n % 4, 0:N_MEM], ACT.Exp, bias=neg[:, one],
                               accum_out=total[:, one]).then_inc(exps, 1)

            def round_sums(g):
                hd, h = divmod(g, 2)
                act.wait_ge(summed, g + 1)
                for e in range(2):
                    act.copy(c.h_hi[:, 2 * hd + e, h * HALF:(h + 1) * HALF], ps[:, 6 + e]).then_inc(rounded, 1)

            exp(0)
            for n in range(n_steps):
                if n + 1 < n_steps:
                    exp(n + 1)
                act.wait_ge(turned, n + 1)
                wait(act, summed, n // 4 - 1)
                act.copy(p_t[:, n // 4 % 2, :, (n % 4) * P:(n % 4 + 1) * P],
                         ps[:, 4 + n % 2, 0:2 * P].rearrange("p (m n) -> p m n", n=P)).then_inc(copied, 1)
                if n % 4 == 2 and n > 4:
                    round_sums(n // 4 - 1)
            round_sums(quads - 1)

        @block.vector
        def _(dve):
            v = c.v_steps

            def peak(n):
                one = slice(n % 4, n % 4 + 1)
                dve.wait_ge(scored, n + 1)
                dve.tensor_reduce(top[:, one], ps[:, n % 4, 0:N_MEM], AX_X, ALU.max).then_inc(tops, 1)
                dve.wait_ge(tops, 2 * n + 1)
                wait(dve, exps, n - 3)
                dve.tensor_scalar(neg[:, one], top[:, one], -1.0, None, ALU.mult).then_inc(tops, 1)

            def take_rest(g):
                hd, h = divmod(g, 2)
                for e in range(2):
                    cut = slice(h * HALF, (h + 1) * HALF)
                    dve.wait_ge(rounded, 2 * g + e + 1)
                    dve.tensor_tensor(c.h_lo[:, 2 * hd + e, cut], ps[:, 6 + e], c.h_hi[:, 2 * hd + e, cut].bitcast(F32),
                                      ALU.subtract).then_inc(split, 1)

            peak(0)
            peak(1)
            for n in range(n_steps):
                if n + 2 < n_steps:
                    peak(n + 2)
                one = slice(n % 4, n % 4 + 1)
                dve.wait_ge(exps, n + 1)
                v.mark(dve.reciprocal(total[:, one], total[:, one]))
                v.wait(dve)
                dve.tensor_scalar(prob[:, n % 4], prob[:, n % 4], total[:, one], None, ALU.mult).then_inc(normed, 1)
                if n % 4 == 3 and n > 4:
                    take_rest(n // 4 - 1)
            take_rest(quads - 1)


DN_HEADS = 4
SB_HEAD = 64
BETA_COLUMN = 4 * D_RWKV
SB_COLUMN = BETA_COLUMN + 2 * DN_HEADS
GATE_COLUMN_2 = SB_COLUMN + 4 * D_RWKV


def second_projections(c):
    nc, d = c.nc, c.dram
    w = d["w_in_2"][0]
    kinds = ["q", "z", "k", "v", "sq", "sv", "sk", "zb"]
    at_column = dict(q=0, k=D_RWKV, v=2 * D_RWKV, z=3 * D_RWKV, sq=SB_COLUMN, sk=SB_COLUMN + D_RWKV,
                     sv=SB_COLUMN + 2 * D_RWKV, zb=SB_COLUMN + 3 * D_RWKV)
    conv_row = dict(q=0, k=CT, v=2 * CT)
    out = {n: scratch(c, f"second_{n}", [CT, P, SEQ]) for n in kinds}
    rows_out = {n: scratch(c, f"second_{n}", [2 * DN_HEADS, SEQ]) for n in ("beta", "decay")}
    weights = Weights(c, [tile_of(w, at_column[n]) for n in kinds], CT)
    raw = at(c, 0, "p2_raw", [P, 2, SEQ + 8])
    y = at(c, 8256, "p2_y", [P, 4, SEQ])
    sig = at(c, 24640, "p2_sig", [P, SEQ])
    sq = at(c, 28736, "p2_sq", [P, SEQ])
    root = at(c, 32832, "p2_root", [P, SEQ])
    n_rows = 2 * DN_HEADS
    beta, pre, soft, cum, keep = (at(c, 36928 + 4096 * n, f"p2_{name}", [n_rows, SEQ])
                                  for n, name in enumerate(("beta", "pre", "soft", "cum", "keep")))
    few = at(c, 57408, "p2_few", [P, KT, n_rows])
    few_hi = at(c, 57664, "p2_few_hi", [P, KT, n_rows], F32R)
    few_lo = at(c, 57920, "p2_few_lo", [P, KT, n_rows], F32R)
    params = at(c, 58176, "p2_params", [n_rows, 4])
    cols = at(c, 58208, "p2_cols", [P, TILES, 2, n_rows])
    few_loaded, prepared, few_split = c.sem("p2_few_loaded"), c.sem("p2_prepared"), c.sem("p2_few_split")
    rows_made, turned, cols_made = c.sem("p2_rows"), c.sem("p2_turned"), c.sem("p2_cols_made")
    few_done = c.sem("p2_few_done")
    copied, sigmoid, squared, summed, rooted = (c.sem(f"p2_{n}") for n in ("copied", "sigmoid", "squared", "summed", "rooted"))
    tapped, gated, normed, plain = (c.sem(f"p2_{n}") for n in ("tapped", "gated", "normed", "plain"))
    stored = [c.sem(f"p2_stored{s}") for s in range(4)]
    rows_stored = c.sem("p2_rows_stored")
    CONV, NORM, SILU = ["q", "k", "v"], ["q", "k", "sq", "sk"], ["q", "z", "k", "v", "zb"]
    gain = dict(sq="sb_q_gain_2", sk="sb_k_gain_2")
    EARLY = ["sq", "sk"]

    def finished(eng, n, i):
        if n in NORM:
            eng.wait_ge(normed, nth(NORM, n, i))
        elif n in SILU:
            eng.wait_ge(gated, nth(SILU, n, i))
        else:
            eng.wait_ge(plain, i + 1)

    def build(norm):
        weights.begin()
        with nc.Block() as block:

            @block.sync
            def _(sp):
                sp.dma_start(few[:], w.rearrange("(k p) n -> p k n", p=P)[:, :, BETA_COLUMN:SB_COLUMN]).then_inc(few_loaded, 16)
                sp.wait_ge(prepared, 1)
                for k, name in enumerate(("dt_bias_2", "a_log_2")):
                    sp.dma_start(params[DN_HEADS:n_rows, k:k + 1], d[name].rearrange("a n -> n a")).then_inc(few_loaded, 16)

                def store(u, i):
                    finished(sp, kinds[u], i)
                    apart(c, sp)
                    sp.dma_start(out[kinds[u]][bass.ds(i, 1)].rearrange("a p n -> p (a n)"), y[:, u % 4]).then_inc(stored[u % 4], 16)

                def fetch(u, i):
                    v = u + 2
                    sp.wait_ge(c.w_split, weights.t0 + i * len(kinds) + (u + 1))
                    apart(c, sp)
                    weights.fetch(sp, v % len(kinds), i + v // len(kinds))

                def turn(i):
                    for u in range(len(kinds)):
                        fetch(u, i)
                        if u >= 2:
                            store(u - 2, i)
                    for u in (6, 7):
                        store(u, i)

                rolled(sp, CT - 1, turn)
                for u in range(len(kinds)):
                    if u < 6:
                        fetch(u, CT - 1)
                    if u >= 2:
                        store(u - 2, CT - 1)
                for u in (6, 7):
                    store(u, CT - 1)
                sp.wait_ge(rows_made, 9)
                for n, src in (("beta", beta), ("decay", cum)):
                    sp.dma_start(rows_out[n], src[:]).then_inc(rows_stored, 16)
                for s in range(4):
                    sp.wait_ge(stored[s], 16 * 2 * CT)
                sp.wait_ge(rows_stored, 32)

            @block.gpsimd
            def _(pool):
                pool.memset(params[:], 0.0).then_inc(prepared, 1)
                pool.memset(keep[:], 1.0).then_inc(prepared, 1)
                pool.wait_ge(prepared, 2)
                pool.memset(keep[:].rearrange("p (t n) -> p t n", n=P)[:, :, 0:1], 0.0).then_inc(prepared, 1)
                pool.memset(raw[:, :, 0:8], 0.0).then_inc(prepared, 1)
                weights.split(pool)

            @block.tensor
            def _(pe):
                norm.pe_sums(pe)

                def few_rows():
                    pe.wait_ge(few_split, 2)
                    for k in range(KT):
                        for wt, a in ((few_hi, c.h_hi), (few_hi, c.h_lo), (few_lo, c.h_hi)):
                            for h in range(2):
                                last = pe.matmul(c.ps[0:n_rows, 6 + h], wt[:, k], a[:, k, h * HALF:(h + 1) * HALF],
                                                 start=(k == 0 and wt is few_hi and a is c.h_hi),
                                                 stop=(k == KT - 1 and wt is few_lo))
                    last.then_inc(few_done, 1)

                def sums(n, i):
                    ones = c.ones if n in CONV else c.ones_64
                    pe.wait_ge(squared, nth(NORM, n, i))
                    wait(pe, rooted, nth(NORM, n, i) - 1)
                    for h in range(2):
                        last = pe.matmul(c.ps[:, 4 + h], ones[:], sq[:, h * HALF:(h + 1) * HALF], start=True, stop=True)
                    last.then_inc(summed, 1)

                def turn(i):
                    for u, n in enumerate(kinds):
                        s = u % 2
                        if first(i) and u == 0:
                            norm.first_tiles(pe, weights)
                        elif not first(i) or u > 1:
                            weights.ready(pe, i, u)
                            wait(pe, copied, i * len(kinds) + (u - 1))
                            amid = u and kinds[u - 1] in EARLY
                            weights.multiply(pe, u, [c.ps[:, 2 * s], c.ps[:, 2 * s + 1]], c.h_hi, c.h_lo,
                                             before=(lambda k, m=kinds[u - 1]: sums(m, i) if k == KT // 2 else None) if amid
                                             else None).then_inc(c.tile_done, 1)
                        if first(i) and u == 2:
                            few_rows()
                        if u and kinds[u - 1] in NORM and kinds[u - 1] not in EARLY:
                            sums(kinds[u - 1], i)

                rolled(pe, CT, turn)
                pe.wait_ge(rows_made, 9)
                for t in range(TILES):
                    for b, src in enumerate((beta, cum)):
                        last = pe.transpose(c.ps[:, 6, (2 * t + b) * n_rows:(2 * t + b + 1) * n_rows],
                                            src[:, t * P:(t + 1) * P], c.ident[0:n_rows, 0:n_rows])
                last.then_inc(turned, 1)

            @block.scalar
            def _(act):
                act.wait_ge(few_loaded, 48)
                act.copy(few_hi[:], few[:]).then_inc(few_split, 1)
                act.activation(params[:, 2:3], params[:, 1:2], ACT.Exp).then_inc(rows_made, 1)

                def rows_act():
                    act.wait_ge(few_done, 1)
                    act.activation(beta[:], c.ps[0:n_rows, 6:8].rearrange("p b n -> p (b n)"), ACT.Sigmoid).then_inc(rows_made, 1)
                    act.wait_ge(rows_made, 3)
                    act.activation(soft[:], pre[:], ACT.Abs).then_inc(rows_made, 1)
                    act.wait_ge(rows_made, 4)
                    act.activation(soft[:], soft[:], ACT.Exp, scale=-1.0).then_inc(rows_made, 1)
                    act.wait_ge(rows_made, 5)
                    act.activation(soft[:], soft[:], ACT.Ln, bias=c.eps[0:n_rows, 2:3]).then_inc(rows_made, 1)

                norm.act(act)
                act.wait_ge(prepared, 4)

                def root_of(m, i):
                    act.wait_ge(summed, nth(NORM, m, i))
                    wait(act, normed, nth(NORM, m, i) - 1)
                    act.activation(root[:], c.ps[:, 4:6].rearrange("p b n -> p (b n)"), ACT.Sqrt,
                                   bias=c.eps[:, 4:5] if m == "sq" else c.eps[:, 0:1],
                                   scale=1.0 / SB_HEAD if m == "sk" else 1.0).then_inc(rooted, 1)

                def turn(i):
                    for u, n in enumerate(kinds):
                        ps = c.ps[:, 2 * (u % 2):2 * (u % 2) + 2].rearrange("p b n -> p (b n)")
                        if u and kinds[u - 1] in EARLY:
                            root_of(kinds[u - 1], i)
                        weights.done(act, i, u)
                        if n == "sv":
                            wait(act, stored[u % 4], i * 32 + (u // 4) * 16)
                            act.copy(y[:, u % 4], ps).then_inc(plain, 1)
                            act.wait_ge(plain, i + 1)
                            act.sem_inc(copied, 1)
                        else:
                            if u >= 2:
                                finished(act, kinds[u - 2], i)
                            elif not first(i):
                                finished(act, kinds[u + 6], i - 1)
                            act.copy(raw[:, u % 2, 8:SEQ + 8], ps).then_inc(copied, 1)
                        if u and kinds[u - 1] in NORM and kinds[u - 1] not in EARLY:
                            root_of(kinds[u - 1], i)
                        if n in SILU:
                            wait(act, gated, nth(SILU, n, i) - 1)
                            if n in CONV:
                                act.wait_ge(tapped, nth(CONV, n, i))
                                act.activation(sig[:], y[:, u % 4], ACT.Sigmoid).then_inc(sigmoid, 1)
                            else:
                                act.wait_ge(copied, i * len(kinds) + (u + 1))
                                act.activation(sig[:], raw[:, u % 2, 8:SEQ + 8], ACT.Sigmoid).then_inc(sigmoid, 1)
                        if n in NORM:
                            wait(act, summed, nth(NORM, n, i) - 1)
                            if n in CONV:
                                act.wait_ge(gated, nth(SILU, n, i))
                                src = y[:, u % 4]
                            else:
                                act.wait_ge(copied, i * len(kinds) + (u + 1))
                                src = raw[:, u % 2, 8:SEQ + 8]
                            act.activation(sq[:], src, ACT.Square).then_inc(squared, 1)
                        if first(i) and u == 3:
                            rows_act()

                rolled(act, CT, turn)
                act.wait_ge(turned, 1)
                act.copy(cols[:].rearrange("p t b n -> p (t b n)"), c.ps[:, 6, 0:TILES * 2 * n_rows]).then_inc(cols_made, 1)
                act.wait_ge(cols_made, 1)
                act.activation(c.beta_decay[:], cols[:, :, 1, DN_HEADS:n_rows], ACT.Exp).then_inc(cols_made, 1)

            @block.vector
            def _(dve):
                v = c.v_steps
                dve.wait_ge(few_split, 1)
                dve.tensor_tensor(few_lo[:], few[:], few_hi[:].bitcast(F32), ALU.subtract).then_inc(few_split, 1)

                def rows_dve():
                    dve.wait_ge(few_done, 1)
                    dve.wait_ge(rows_made, 2)
                    dve.tensor_scalar(pre[:], c.ps[0:n_rows, 6:8].rearrange("p b n -> p (b n)"), params[:, 0:1], None,
                                      ALU.add).then_inc(rows_made, 1)
                    dve.wait_ge(rows_made, 6)
                    dve.scalar_tensor_tensor(out=pre[:], in0=pre[:], scalar=0.0, in1=soft[:], op0=ALU.max,
                                             op1=ALU.add).then_inc(rows_made, 1)
                    dve.wait_ge(rows_made, 7)
                    dve.tensor_scalar(pre[:], pre[:], params[:, 2:3], -1.0, ALU.mult, ALU.mult).then_inc(rows_made, 1)
                    dve.wait_ge(rows_made, 8)
                    dve.wait_ge(prepared, 3)
                    dve.tensor_tensor_scan(cum[:], keep[:], pre[:], 0.0, ALU.mult, ALU.add).then_inc(rows_made, 1)

                norm.dve(dve)

                def turn(i):
                    for u, n in enumerate(kinds):
                        dst = y[:, u % 4]
                        if n != "sv":
                            wait(dve, stored[u % 4], i * 32 + (u // 4) * 16)
                        if n in CONV:
                            dve.wait_ge(copied, i * len(kinds) + (u + 1))
                            for tap in (3, 2, 1, 0):
                                scale = vec(c, "conv_w_2", i + (tap * 3 * CT + conv_row[n]))
                                src = raw[:, u % 2, 5 + tap:5 + tap + SEQ]
                                if tap == 3:
                                    ins = dve.tensor_scalar(dst, src, scale, None, ALU.mult)
                                else:
                                    v.wait(dve)
                                    ins = dve.scalar_tensor_tensor(out=dst, in0=src, scalar=scale, in1=dst,
                                                                   op0=ALU.mult, op1=ALU.add)
                                v.mark(ins)
                            v.wait(dve)
                            dve.sem_inc(tapped, 1)
                        if u and kinds[u - 1] in NORM:
                            m, p = kinds[u - 1], u - 1
                            dve.wait_ge(rooted, nth(NORM, m, i))
                            v.mark(dve.reciprocal(root[:], root[:]))
                            v.wait(dve)
                            o = y[:, p % 4]
                            if m in CONV:
                                dve.scalar_tensor_tensor(out=o, in0=o, scalar=P ** -0.5 if m == "q" else 1.0, in1=root[:],
                                                         op0=ALU.mult, op1=ALU.mult).then_inc(normed, 1)
                            else:
                                dve.scalar_tensor_tensor(out=o, in0=raw[:, p % 2, 8:SEQ + 8], scalar=vec(c, gain[m]),
                                                         in1=root[:], op0=ALU.mult, op1=ALU.mult).then_inc(normed, 1)
                        if n in SILU:
                            dve.wait_ge(sigmoid, nth(SILU, n, i))
                            src = dst if n in CONV else raw[:, u % 2, 8:SEQ + 8]
                            dve.tensor_tensor(dst, src, sig[:], ALU.mult).then_inc(gated, 1)
                        if first(i) and u == 3:
                            rows_dve()

                rolled(dve, CT, turn, v)
                dve.wait_ge(cols_made, 2)
                v.mark(dve.tensor_copy(c.beta_col[:], cols[:, :, 0, 0:DN_HEADS]))
                v.mark(dve.tensor_copy(c.decay_col[:], cols[:, :, 1, DN_HEADS:n_rows]))
                v.mark(dve.scalar_tensor_tensor(out=c.beta_decay[:], in0=c.beta_decay[:], scalar=-1.0,
                                                in1=cols[:, :, 0, 0:DN_HEADS], op0=ALU.mult, op1=ALU.mult))
                v.wait(dve)

    return weights, build


OUT_OF_SIGHT = -1e4


def delta_rule(c, following):
    nc = c.nc
    base, w_off = 0, 0
    wide = [P, DN_HEADS, P]

    def buf(name):
        nonlocal base
        b = at(c, base, f"dn_{name}", wide)
        base += 4 * DN_HEADS * P
        return b

    def buf_w(name, shape):
        nonlocal w_off
        b = nc.alloc_sbuf_tensor_at(f"dn_{name}", shape, F32, offset=c.w_base + w_off)
        n = 4
        for m in shape[1:]:
            n *= m
        w_off += n
        return b

    groups = range(2)
    q_in, k_in, v_in, g_in, b_in = ([buf(f"{n}_in{g}") for g in groups] for n in ("q", "k", "v", "decay", "beta"))
    low, up, up_beta, grown, q_dec, a_t, q_k = ([buf(f"{n}{g}") for g in groups] for n in
                                                ("low", "up", "up_beta", "grown", "q_dec", "a_t", "q_k"))
    t, t_t, x = ([buf(f"{n}{g}") for g in groups] for n in ("t", "tt", "x"))
    v_beta, k_dec = ([buf(f"{n}{g}") for g in groups] for n in ("v_beta", "k_dec"))
    rest, v_new, o_b = ([buf_w(f"{n}{g}", wide) for g in groups] for n in ("rest", "v_new", "o"))
    state = buf_w("state", wide)
    c.level = buf_w("level", [P, LEVELS, P])
    ends = buf_w("ends", [P, TILES, DN_HEADS])
    assert w_off <= 24576 and c.aux_base + 32 + base <= 229376, (w_off, c.aux_base + 32 + base)

    PE_EVENTS = ["kk", "qk", "v_nat", "x1", "k_nat"] + LEVEL_PE[1:] + ["ks", "v_new", "o", "s"]
    DVE_EVENTS = ["n_t", "t_block", "t0", "tt_block", "tt0", "qk", "v_beta"] + LEVEL_DVE[:3] + ["k_dec"] + LEVEL_DVE[3:] + \
        ["rest", "s_new"]
    ACT_EVENTS = ["v_new", "o"]
    DECAY_EVENTS = ["low", "up", "grown", "end"]
    FACTOR_EVENTS = ["low_diff", "low_kept", "up_diff", "up_kept", "low_level", "low", "up_beta"]
    loaded, decays_in, stored = ([c.sem(f"dn_{n}{g}") for g in groups] for n in ("loaded", "decays_in", "stored"))
    products, masks, acts = ([c.sem(f"dn_{n}{g}") for g in groups] for n in ("products", "masks", "acts"))
    decays, factors, q_grown = ([c.sem(f"dn_{n}{g}") for g in groups] for n in ("decays", "factors", "q_grown"))
    cleared = c.sem("dn_cleared")
    src = {n: c.scratch[f"second_{n}"].rearrange("h p n -> p h n") for n in "qkv"}
    row_src = {n: c.scratch[f"second_{n}"] for n in ("decay", "beta")}
    out = scratch(c, "second_oa", [CT, P, SEQ])
    ps = c.ps
    level_banks = [(ps[:, g], ps[:, 2 + g], ps[:, 4 + g]) for g in groups]
    turns = TILES // 2

    def over(m):
        return m.unsqueeze(1).broadcast_to(wide)

    def col(buf, j, g, h):
        return buf[:, bass.ds(j * 2 + g, 1), h:h + 1].rearrange("p a b -> p (a b)")

    def cols(buf, j, g):
        return buf[:, bass.ds(j * 2 + g, 1), :].rearrange("p a n -> p (a n)")

    with nc.Block() as block:

        @block.sync
        def _(sp):
            def load_decays(j, g):
                cut = columns(j * 2 + g, P)
                for n, dst, r in (("decay", g_in, DN_HEADS), ("beta", b_in, 0)):
                    rows = row_src[n][r:r + DN_HEADS, cut]
                    sp.dma_start(dst[g][:], rows.unsqueeze(0).broadcast_to(wide)).then_inc(decays_in[g], 16)

            def load(j, g):
                cut = columns(j * 2 + g, P)
                for n, dst in (("k", k_in), ("q", q_in), ("v", v_in)):
                    sp.dma_start(dst[g][:], src[n][:, :, cut]).then_inc(loaded[g], 16)

            def store(j, g):
                sp.wait_ge(acts[g], nth(ACT_EVENTS, "o", j))
                apart(c, sp)
                sp.dma_start(out.rearrange("h p n -> p h n")[:, :, columns(j * 2 + g, P)], o_b[g][:]).then_inc(stored[g], 16)

            def turn(j):
                for g in groups:
                    sp.wait_ge(decays[g], nth(DECAY_EVENTS, "end", j))
                    sp.wait_ge(factors[g], nth(FACTOR_EVENTS, "up_beta", j))
                    apart(c, sp)
                    load_decays(j + 1, g)
                for g in groups:
                    sp.wait_ge(q_grown[g], j + 1)
                    sp.wait_ge(products[g], nth(PE_EVENTS, "ks", j))
                    apart(c, sp)
                    load(j + 1, g)
                    store(j, g)

            for g in groups:
                load_decays(0, g)
            for g in groups:
                load(0, g)
            rolled(sp, turns - 1, turn)
            following.load_first(sp)
            for g in groups:
                store(turns - 1, g)
            for g in groups:
                sp.wait_ge(stored[g], 16 * turns)

        @block.gpsimd
        def _(pool):
            def after(name, j, g):
                pool.wait_ge(factors[g], nth(FACTOR_EVENTS, name, j))

            def make_differences(j, g):
                def keep(buf, pattern, base, mult):
                    apart(c, pool)
                    pool.affine_select(out=buf, in_=buf, compare_op=ALU.is_ge, fill=OUT_OF_SIGHT, base=base, pattern=pattern,
                                       channel_multiplier=mult).then_inc(factors[g], 1)

                own = cols(c.decay_col, j, g).unsqueeze(2).broadcast_to(wide)
                pool.wait_ge(decays_in[g], j * 32 + 32)
                wait(pool, masks[g], nth(DVE_EVENTS, "t_block", j - 1))
                apart(c, pool)
                pool.tensor_tensor(low[g][:], own, g_in[g][:], ALU.subtract).then_inc(factors[g], 1)
                after("low_diff", j, g)
                keep(low[g][:], [[0, DN_HEADS], [-1, P]], -1, 1)
                wait(pool, masks[g], nth(DVE_EVENTS, "k_dec", j - 1))
                apart(c, pool)
                pool.tensor_tensor(up[g][:], g_in[g][:], own, ALU.subtract).then_inc(factors[g], 1)
                after("up_diff", j, g)
                keep(up[g][:], [[0, DN_HEADS], [1, P]], 0, -1)

            def make_factors(j, g):
                pool.wait_ge(decays[g], nth(DECAY_EVENTS, "low", j))
                pool.tensor_tensor(low[g][:], low[g][:], over(c.level[:, 0]), ALU.mult).then_inc(factors[g], 1)
                after("low_level", j, g)
                apart(c, pool)
                pool.tensor_tensor(low[g][:], low[g][:], cols(c.beta_col, j, g).unsqueeze(2).broadcast_to(wide),
                                   ALU.mult).then_inc(factors[g], 1)
                pool.wait_ge(decays_in[g], j * 32 + 32)
                wait(pool, masks[g], nth(DVE_EVENTS, "n_t", j - 1))
                pool.wait_ge(decays[g], nth(DECAY_EVENTS, "up", j))
                pool.tensor_tensor(up_beta[g][:], up[g][:], b_in[g][:], ALU.mult).then_inc(factors[g], 1)

            def grow_q(j, g):
                pool.wait_ge(loaded[g], j * 48 + 48)
                pool.wait_ge(decays[g], nth(DECAY_EVENTS, "grown", j))
                wait(pool, products[g], nth(PE_EVENTS, "o", j - 1))
                pool.tensor_tensor(q_dec[g][:], q_in[g][:], grown[g][:], ALU.mult).then_inc(q_grown[g], 1)

            def turn(j):
                for g in groups:
                    grow_q(j, g)
                for g in groups:
                    make_differences(j + 1, g)
                for g in groups:
                    make_factors(j + 1, g)

            make_levels(c, pool, range(1))
            for g in groups:
                make_differences(0, g)
            for g in groups:
                make_factors(0, g)
            make_levels(c, pool, range(1, LEVELS))
            pool.memset(state[:], 0.0).then_inc(cleared, 1)
            rolled(pool, turns - 1, turn)
            for g in groups:
                grow_q(turns - 1, g)

        @block.tensor
        def _(pe):
            def four(out, lhs, rhs, start=True, stop=True):
                for h in range(DN_HEADS):
                    last = pe.matmul(out[:, h * P:(h + 1) * P], lhs[:, h], rhs[:, h], start=start and h == 0, stop=stop,
                                     skip_group_check=True)
                return last

            def turned(out, part):
                for h in range(DN_HEADS):
                    last = pe.transpose(out[:, h * P:(h + 1) * P], part[:, h], c.ident[:])
                return last

            def turn(j):
                for g in groups:
                    pe.wait_ge(loaded[g], j * 48 + 48)
                    wait(pe, masks[g], nth(DVE_EVENTS, "s_new", j - 1))
                    wait(pe, acts[g], nth(ACT_EVENTS, "o", j - 1))
                    four(ps[:, 6 + g], k_in[g], k_in[g]).then_inc(products[g], 1)
                    four(ps[:, 4 + g], k_in[g], q_in[g]).then_inc(products[g], 1)
                    turned(ps[:, 2 + g], v_in[g]).then_inc(products[g], 1)
                for n in range(1, LEVELS):
                    for g in groups:
                        inverse_pe(pe, n, products[g], masks[g], j, DVE_EVENTS, level_banks[g], a_t[g], t[g], start="t0")
                    if n == 1:
                        for g in groups:
                            pe.wait_ge(masks[g], nth(DVE_EVENTS, "t_block", j))
                            turned(ps[:, 6 + g], k_in[g]).then_inc(products[g], 1)
                    for g in groups:
                        inverse_pe_update(pe, n, products[g], masks[g], j, DVE_EVENTS, level_banks[g], t_t[g], x[g])
                for g in groups:
                    if g == 0:
                        pe.wait_ge(cleared, 1)
                        wait(pe, masks[1], nth(DVE_EVENTS, "s_new", j - 1))
                    else:
                        pe.wait_ge(masks[0], nth(DVE_EVENTS, "s_new", j))
                    four(ps[:, 6 + g], k_in[g], state).then_inc(products[g], 1)
                    pe.wait_ge(q_grown[g], j + 1)
                    four(ps[:, 2 + g], state, q_dec[g], stop=False)
                    pe.wait_ge(masks[g], nth(DVE_EVENTS, "rest", j))
                    four(ps[:, g], t_t[g], rest[g]).then_inc(products[g], 1)
                    pe.wait_ge(acts[g], nth(ACT_EVENTS, "v_new", j))
                    four(ps[:, 4 + g], k_dec[g], v_new[g])
                    four(ps[:, 2 + g], v_new[g], q_k[g], start=False).then_inc(products[g], 2)

            rolled(pe, turns, turn)

        @block.scalar
        def _(act):
            def make_decays(j, g):
                act.wait_ge(factors[g], nth(FACTOR_EVENTS, "low_kept", j))
                act.activation(low[g][:], low[g][:], ACT.Exp).then_inc(decays[g], 1)
                act.wait_ge(factors[g], nth(FACTOR_EVENTS, "up_kept", j))
                act.activation(up[g][:], up[g][:], ACT.Exp).then_inc(decays[g], 1)
                wait(act, q_grown[g], j)
                act.activation(grown[g][:], g_in[g][:], ACT.Exp).then_inc(decays[g], 1)
                act.activation(cols(ends, j, g), g_in[g][:, :, P - 1], ACT.Exp).then_inc(decays[g], 1)

            def take_out(j):
                for g in groups:
                    act.wait_ge(products[g], nth(PE_EVENTS, "v_new", j))
                    act.copy(v_new[g][:], heads_of(ps[:, g])).then_inc(acts[g], 1)
                    act.wait_ge(products[g], nth(PE_EVENTS, "o", j))
                    wait(act, stored[g], j * 16)
                    act.copy(o_b[g][:], heads_of(ps[:, 2 + g])).then_inc(acts[g], 1)

            def turn(j):
                for g in groups:
                    make_decays(j + 1, g)
                take_out(j)

            for g in groups:
                make_decays(0, g)
            rolled(act, turns - 1, turn)
            take_out(turns - 1)

        @block.vector
        def _(dve):
            def turn(j):
                def after(g, name):
                    dve.wait_ge(masks[g], nth(DVE_EVENTS, name, j))

                def scores(g):
                    dve.wait_ge(decays[g], nth(DECAY_EVENTS, "up", j))
                    dve.wait_ge(products[g], nth(PE_EVENTS, "qk", j))
                    dve.tensor_tensor(q_k[g][:], heads_of(ps[:, 4 + g]), up[g][:], ALU.mult).then_inc(masks[g], 1)
                    dve.wait_ge(products[g], nth(PE_EVENTS, "v_nat", j))
                    dve.tensor_tensor(v_beta[g][:], heads_of(ps[:, 2 + g]), cols(c.beta_col, j, g).unsqueeze(2).broadcast_to(wide),
                                      ALU.mult).then_inc(masks[g], 1)

                for g in groups:
                    wait(dve, products[g], nth(PE_EVENTS, "s", j - 1))
                    wait(dve, masks[g], nth(DVE_EVENTS, "s_new", j - 1))
                    dve.wait_ge(factors[g], nth(FACTOR_EVENTS, "up_beta", j))
                    dve.wait_ge(products[g], nth(PE_EVENTS, "kk", j))
                    for into, factor in ((a_t, up_beta), (t, low)):
                        dve.scalar_tensor_tensor(out=into[g][:], in0=heads_of(ps[:, 6 + g]), scalar=-1.0, in1=factor[g][:],
                                                 op0=ALU.mult, op1=ALU.mult).then_inc(masks[g], 1)
                    after(g, "t_block")
                    dve.tensor_tensor(t[g][:], t[g][:], over(c.ident[:]), ALU.add).then_inc(masks[g], 1)
                    dve.tensor_tensor(t_t[g][:], a_t[g][:], over(c.level_t[:]), ALU.mult).then_inc(masks[g], 1)
                    after(g, "tt_block")
                    dve.tensor_tensor(t_t[g][:], t_t[g][:], over(c.ident[:]), ALU.add).then_inc(masks[g], 1)
                if first(j):
                    dve.wait_ge(cleared, 1)
                for n in range(1, LEVELS):
                    for g in groups:
                        if n == 1:
                            scores(g)
                        inverse_mask_dve(c, dve, n, products[g], masks[g], j, PE_EVENTS, level_banks[g], x[g])
                    for g in groups:
                        inverse_add_dve(dve, n, products[g], masks[g], j, PE_EVENTS, level_banks[g], t[g], t_t[g])
                        if n == 1:
                            dve.wait_ge(products[g], nth(PE_EVENTS, "k_nat", j))
                            dve.tensor_tensor(k_dec[g][:], heads_of(ps[:, 6 + g]),
                                              up[g][:, :, P - 1].unsqueeze(2).broadcast_to(wide), ALU.mult).then_inc(masks[g], 1)
                for g in groups:
                    dve.wait_ge(products[g], nth(PE_EVENTS, "ks", j))
                    for h in range(DN_HEADS):
                        last = dve.scalar_tensor_tensor(out=rest[g][:, h], in0=ps[:, 6 + g, h * P:(h + 1) * P],
                                                        scalar=col(c.beta_decay, j, g, h), in1=v_beta[g][:, h],
                                                        op0=ALU.mult, op1=ALU.add)
                    last.then_inc(masks[g], 1)
                    dve.wait_ge(products[g], nth(PE_EVENTS, "s", j))
                    dve.wait_ge(decays[g], nth(DECAY_EVENTS, "end", j))
                    for h in range(DN_HEADS):
                        last = dve.scalar_tensor_tensor(out=state[:, h], in0=state[:, h],
                                                        scalar=ends[:, bass.ds(j * 2 + g, 1), h:h + 1].rearrange("p a b -> p (a b)"),
                                                        in1=ps[:, 4 + g, h * P:(h + 1) * P], op0=ALU.mult, op1=ALU.add)
                    last.then_inc(masks[g], 1)

            rolled(dve, turns, turn)


def stick_breaking(c, following):
    nc = c.nc
    offset = 0

    def buf(name, shape):
        nonlocal offset
        b = at_h(c, offset, f"sb_{name}", shape)
        n = 4
        for m in shape[1:]:
            n *= m
        offset += n
        return b

    heads = range(2)
    keep, weight, weight_t = (buf(n, [P, 2, 2, HALF]) for n in ("keep", "weight", "weight_t"))
    left = buf("left", [P, 2, 2, HALF + 8])
    v_nat = buf("v_nat", [P, 2, SEQ])
    z_in, o_b = buf("z_in", [P, 2, HALF]), buf("o", [P, 2, HALF])
    forbid = buf("forbid", [P, P])
    assert offset <= 65536
    q_in, k_in, v_in = (nc.alloc_sbuf_tensor_at(f"sb_{n}_in", [P, 2, SEQ], F32, offset=c.w_base + 8192 * k)
                        for k, n in enumerate("qkv"))
    steps = [(ct, qb, kh, min(HALF, (qb + 1) * P - kh * HALF), kh == qb // 4)
             for ct in range(CT) for qb in range(TILES) for kh in range(qb // 4, -1, -1)]
    n_steps = len(steps)
    per = n_steps // CT
    halves = [(st[0], st[1] // 4) for st in steps]
    begins = [n for n in range(n_steps) if n == 0 or halves[n] != halves[n - 1]]
    ends = [n - 1 for n in begins[1:]] + [n_steps - 1]
    early = (8, 10)
    loaded = [c.sem("sb_loaded0"), c.sem("sb_loaded1")]
    made, scored, kept, weighted = (c.sem(f"sb_{n}") for n in ("made", "scored", "kept", "weighted"))
    turned, copied, summed = (c.sem(f"sb_{n}") for n in ("turned", "copied", "summed"))
    values_turned, natural = c.sem("sb_values_turned"), c.sem("sb_natural")
    gates_in, taken, rounded, split = ([c.sem(f"sb_{n}{h}") for h in range(2)] for n in ("gates_in", "taken", "rounded", "split"))
    src = [c.scratch[f"second_{n}"] for n in ("sq", "sk", "sv")]
    z_src = c.scratch["second_zb"]
    ps = c.ps

    with nc.Block() as block:

        @block.sync
        def _(sp):
            def load(ct):
                for part, dst in zip(src, (q_in, k_in, v_in)):
                    sp.dma_start(dst[:, ct % 2], part[ct]).then_inc(loaded[ct % 2], 16)

            def load_gates(ct):
                for h in range(2):
                    wait(sp, taken[h], ct)
                    sp.dma_start(z_in[:, h], z_src[ct, :, h * HALF:(h + 1) * HALF]).then_inc(gates_in[h], 16)

            load(0)
            load_gates(0)
            load(1)
            following.load_first(sp)
            for sem, count in c.gates_stored:
                sp.wait_ge(sem, count)
            for ct in range(1, CT):
                load_gates(ct)
                if ct + 1 < CT:
                    load(ct + 1)

        @block.gpsimd
        def _(pool):
            pool.memset(forbid[:], -1e30).then_inc(made, 1)
            pool.wait_ge(made, 1)
            pool.affine_select(out=forbid[:], in_=forbid[:], compare_op=ALU.is_ge, fill=0.0, base=0, pattern=[[1, P]],
                               channel_multiplier=-1).then_inc(made, 1)

        @block.tensor
        def _(pe):
            pe.wait_ge(made, 2)

            def turn_values(ct, h):
                pe.wait_ge(loaded[ct % 2], (ct // 2 + 1) * 48)
                wait(pe, natural, ct * 2 + h)
                wait(pe, taken[0], ct)
                for t in range(4):
                    last = pe.transpose(ps[:, 6, t * P:(t + 1) * P], v_in[:, ct % 2, (4 * h + t) * P:(4 * h + t + 1) * P],
                                        c.ident[:])
                last.then_inc(values_turned, 1)

            def score(n):
                ct, qb, kh, width, diagonal = steps[n]
                pe.wait_ge(loaded[ct % 2], (ct // 2 + 1) * 48)
                wait(pe, kept, 2 * (n - 1))
                for hd in heads:
                    rows = slice(SB_HEAD * hd, SB_HEAD * (hd + 1))
                    last = pe.matmul(ps[:, 2 * (n % 2) + hd, 0:width], q_in[rows, ct % 2, qb * P:(qb + 1) * P],
                                     k_in[rows, ct % 2, kh * HALF:kh * HALF + width], start=True, stop=not diagonal,
                                     skip_group_check=True)
                for hd in heads if diagonal else ():
                    last = pe.matmul(ps[:, 2 * (n % 2) + hd, width - P:width], c.ident[:], forbid[:], start=False, stop=True,
                                     skip_group_check=True)
                last.then_inc(scored, 1)

            def turn_weights(n):
                ct, qb, kh, width, diagonal = steps[n]
                pe.wait_ge(weighted, n + 1)
                wait(pe, copied, n)
                for hd in heads:
                    for t in range(width // P):
                        cut = slice(t * P, (t + 1) * P)
                        last = pe.transpose(ps[:, 4 + hd, cut], weight[:, n % 2, hd, cut], c.ident[:])
                last.then_inc(turned, 1)

            def sum_values(n):
                ct, qb, kh, width, diagonal = steps[n]
                pe.wait_ge(copied, n + 1)
                h = qb // 4
                if n in begins:
                    wait(pe, taken[h], ct)
                    pe.wait_ge(natural, ct * 2 + 2)
                queries_at = slice((qb % 4) * P, (qb % 4 + 1) * P)
                for t in range(width // P):
                    for hd in heads:
                        rows = slice(SB_HEAD * hd, SB_HEAD * (hd + 1))
                        at_key = kh * HALF + t * P
                        last = pe.matmul(ps[rows, 6 + h, queries_at], v_nat[:, ct % 2, at_key:at_key + P][:, rows],
                                         weight_t[:, n % 2, hd, t * P:(t + 1) * P], start=n in begins and t == 0,
                                         stop=n in ends and t == 3, skip_group_check=True)
                last.then_inc(summed, 1)

            for h in range(2):
                turn_values(0, h)
            score(0)
            for n in range(n_steps):
                if n + 1 < n_steps:
                    score(n + 1)
                if n:
                    sum_values(n - 1)
                turn_weights(n)
                ct, at_step = divmod(n, per)
                if at_step in early and ct + 1 < CT:
                    turn_values(ct + 1, early.index(at_step))
            sum_values(n_steps - 1)

        @block.scalar
        def _(act):
            def copy_values(ct, h):
                act.wait_ge(values_turned, ct * 2 + (h + 1))
                act.copy(v_nat[:, ct % 2, h * HALF:(h + 1) * HALF], ps[:, 6]).then_inc(natural, 1)

            def sigmoids(n):
                ct, qb, kh, width, diagonal = steps[n]
                act.wait_ge(scored, n + 1)
                wait(act, turned, n - 1)
                z = ps[:, 2 * (n % 2):2 * (n % 2) + 2, 0:width]
                act.activation(keep[:, n % 2, :, 0:width], z, ACT.Sigmoid, scale=-1.0).then_inc(kept, 1)
                act.activation(weight[:, n % 2, :, 0:width], z, ACT.Sigmoid).then_inc(kept, 1)

            def round_sums(ct, h):
                act.wait_ge(taken[h], ct + 1)
                act.copy(c.br_hi[:, ct + CT, h * HALF:(h + 1) * HALF], o_b[:, h]).then_inc(rounded[h], 1)

            for h in range(2):
                copy_values(0, h)
            sigmoids(0)
            for n, (ct, qb, kh, width, diagonal) in enumerate(steps):
                if n + 1 < n_steps:
                    sigmoids(n + 1)
                act.wait_ge(turned, n + 1)
                wait(act, summed, n - 1)
                act.copy(weight_t[:, n % 2, :, 0:width], ps[:, 4:6, 0:width]).then_inc(copied, 1)
                if n - 3 in ends:
                    round_sums(*halves[n - 3])
                if n % per in early and ct + 1 < CT:
                    copy_values(ct + 1, early.index(n % per))
            round_sums(CT - 1, 1)

        @block.vector
        def _(dve):
            v = c.v_steps

            def take(ct, h):
                dve.wait_ge(summed, ends[2 * ct + h] + 1)
                dve.wait_ge(gates_in[h], ct * 16 + 16)
                wait(dve, split[h], ct)
                dve.tensor_tensor(o_b[:, h], z_in[:, h], ps[:, 6 + h], ALU.mult).then_inc(taken[h], 1)

            def take_rest(ct, h):
                cut = slice(h * HALF, (h + 1) * HALF)
                dve.wait_ge(rounded[h], ct + 1)
                dve.tensor_tensor(c.br_lo[:, ct + CT, cut], o_b[:, h], c.br_hi[:, ct + CT, cut].bitcast(F32),
                                  ALU.subtract).then_inc(split[h], 1)

            for n, (ct, qb, kh, width, diagonal) in enumerate(steps):
                l = left[:, n % 2]
                if diagonal:
                    v.mark(dve.memset(l[:, :, width:width + 1], 1.0))
                else:
                    v.mark(dve.tensor_copy(l[:, :, width:width + 1], left[:, (n - 1) % 2, :, 0:1]))
                v.wait(dve)
                dve.wait_ge(kept, 2 * n + 1)
                for hd in heads:
                    v.mark(dve.tensor_tensor_scan(l[:, hd, 0:width][:, ::-1], keep[:, n % 2, hd, 0:width][:, ::-1],
                                                  c.ones[:, 0:1].broadcast_to([P, width]), l[:, hd, width:width + 1],
                                                  ALU.mult, ALU.mult))
                v.wait(dve)
                dve.wait_ge(kept, 2 * n + 2)
                dve.tensor_tensor(weight[:, n % 2, :, 0:width], weight[:, n % 2, :, 0:width], l[:, :, 1:width + 1],
                                  ALU.mult).then_inc(weighted, 1)
                dve.wait_ge(weighted, n + 1)
                if n - 2 in ends:
                    take(*halves[n - 2])
                if n - 5 in ends:
                    take_rest(*halves[n - 5])
            take(CT - 1, 1)
            take_rest(CT - 1, 1)


def renew(c):
    c.nc.clear_and_free_semaphores(c.stage_sems)
    c.stage_sems = []
    with c.nc.Block() as block:

        @block.gpsimd
        def _(pool):
            pass


def final_norm(c, norm, following):
    sq = at(c, 0, "final_sq", [P, 4, HALF])
    squared, summed = c.sem("final_squared"), c.sem("final_summed")
    with c.nc.Block() as block:

        @block.sync
        def _(sp):
            following.load_first(sp)

        @block.tensor
        def _(pe):
            norm.pe_sums(pe)
            norm.wait(pe, "rooted", 2)
            for n in range(2 * KT):
                h, k = divmod(n, KT)
                pe.wait_ge(squared, n + 1)
                pe.matmul(c.ps[:, 4 + h], c.ones[:], sq[:, n % 4], start=k == 0, stop=k == KT - 1).then_inc(summed, 1)

        @block.scalar
        def _(act):
            norm.act_roots(act)
            for n in range(2 * KT):
                h, k = divmod(n, KT)
                norm.wait(act, "scaled", n + 1)
                wait(act, summed, n - 3)
                act.activation(sq[:, n % 4], c.x[:, k, h * HALF:(h + 1) * HALF], ACT.Square).then_inc(squared, 1)

        @block.vector
        def _(dve):
            v = c.v_steps
            for h in range(2):
                norm.wait(dve, "rooted", h + 1)
                v.mark(dve.reciprocal(norm.root[:, h], norm.root[:, h]))
                v.wait(dve)
                for k in range(KT):
                    x = c.x[:, k, h * HALF:(h + 1) * HALF]
                    norm.mark(dve.scalar_tensor_tensor(out=x, in0=x, scalar=vec(c, norm.gain, k), in1=norm.root[:, h],
                                                       op0=ALU.mult, op1=ALU.mult), "scaled")


def second_block(c, out, final):
    d = c.dram
    norm = Norm(c, "norm_gain_2", "norm_gain_2", events=("rooted", "scaled", "rounded", "split"))
    first_weights, project = second_projections(c)
    final_norm(c, final, first_weights)
    project(norm)
    gate_weights, gate = gates(c, "mix_2", d["w_in_2"][0], GATE_COLUMN_2, "b_gate_2")
    delta_rule(c, gate_weights)
    c.br_hi = at(c, 0, "branch_2_hi", [P, KT, SEQ], F32R)
    c.br_lo = at(c, BRANCH, "branch_2_lo", [P, KT, SEQ], F32R)
    merge_weights, merge_2 = merge(c, "mix_2", d["w_up_a_2"][0], d["w_up_b_2"][0])
    gate(DeltaOutput(c), [c.w_raw[:, 2].rearrange("p k n -> p (k n)")])
    stick_breaking(c, merge_weights)
    out_weights = residual_weights(c, d["w_out_2"][0])
    merge_2(out_weights)
    add_product(c, "out_2", out_weights, None)
    finish(c, out)


def first_block(c):
    d = c.dram
    memory = memory_keys(c)
    norm = Norm(c, "norm_mix", "norm_mix", events=("summed", "rooted", "scaled", "rounded", "split"))
    lora_weights, lora = rwkv_lora_inputs(c)
    memory(lora_weights, norm)
    feature_weights, features = rwkv_features(c)
    lora(feature_weights, norm)
    features(lambda sp: None)
    gate_weights, gate = gates(c, "mix", d["w_in"][0], RWKV_COLS + 3 * D_RWKV, "b_gate")
    rwkv_scan(c, gate_weights)
    c.br_hi = at(c, 0, "branch_hi", [P, KT, SEQ], F32R)
    c.br_lo = at(c, BRANCH, "branch_lo", [P, KT, SEQ], F32R)
    side = RwkvOutput(c)
    merge_weights, merge_1 = merge(c, "mix", d["w_proj_a"][0], d["w_proj_b"][0])
    sig = [at(c, BRANCH + 4 * (CT + n) * SEQ, f"mix_sig{n}", [P, SEQ])[:] for n in range(2)]
    gate(side, sig, after=ShortConv(c, side, merge_weights))
    out_weights = residual_weights(c, d["w_out_mix"][0])
    merge_1(out_weights)
    norm = Norm(c, "norm_xattn", "norm_xattn")
    query_weights, query = queries(c)
    add_product(c, "out_mix", out_weights, query_weights, norm)
    query(norm)
    xo_weights = residual_weights(c, d["w_xo"][0])
    attention(c, xo_weights)
    up_weights, hidden = mlp(c)
    norm = Norm(c, "norm_mlp", "norm_mlp")
    add_product(c, "xo", xo_weights, up_weights, norm)
    final = Norm(c, "norm_final", "norm_final", events=("squared", "added", "summed", "rooted", "scaled"),
                 acc=tail(c, 0, "final_acc", [P, SEQ]))
    hidden(norm, final)
    return final


def build(nc, dram, out):
    with ExitStack() as ctx:
        c = open_core(nc, ctx, dram)
        setup(c)
        final = first_block(c)
        renew(c)
        second_block(c, out, final)


def kernel(**inputs):
    from concourse import bacc
    from concourse.bass_utils import run_bass_kernel_spmd
    import numpy as np

    arrays = {f"in_{name}_dram": np.ascontiguousarray(inputs[name]) for name in _INS}
    nc = bacc.Bacc("TRN2", target_bir_lowering=False, num_devices=1)
    dram = {name: nc.dram_tensor(f"in_{name}_dram", list(arrays[f"in_{name}_dram"].shape), F32, kind="ExternalInput").ap()
            for name in _INS}
    out = nc.dram_tensor("out_0_dram", [1, SEQ, D], F32, kind="ExternalOutput").ap()
    build(nc, dram, out)
    nc.finalize()
    results = run_bass_kernel_spmd(nc, [arrays], core_ids=[0])
    return results.results[0]["out_0_dram"]
```
